# Optimizing a Trainium2 kernel written in Bass

```python
import math
import jax, jax.numpy as jnp
from jax import lax
import numpy as np

D_MODEL = 1024
BATCH = 1
SEQ = 1024
DEPTH = 1
DEC_BATCH = 8
DEC_SEQ = 4
PAST_LEN = 2048
PAGE_SIZE = 128

A_HEADS = 8
A_HD = 64
A_W = A_HEADS * A_HD
A_LORA_W = 64
A_LORA_A = 64
A_LORA_G = 128
LNX_EPS = 64e-5
L2_EPS = 1e-24
B_GROUPS = 4
B_GW = 128
B_W = B_GROUPS * B_GW
POOL_WINDOWS = (2, 4, 8, 16)
POOL_BUF = 15
C_HEADS = 8
C_HD = 64
C_W = C_HEADS * C_HD
C_KV = 2
C_HPG = C_HEADS // C_KV
C_KVW = C_KV * C_HD
CMP_BLOCK = 64
N_SEL = 16
WINDOW = 512
Q_BLOCK = 128
FORCE_SCORE = 1e4
NEG = -1e30
N_BUCKETS = 32
MAX_DIST = 128
N_MEM = 256
M_HEADS = 4
M_HD = 128
M_W = M_HEADS * M_HD
D_FF = 4 * D_MODEL
RMS_EPS = 1e-6

OFF_R = 0
OFF_WL = OFF_R + A_W
OFF_K = OFF_WL + A_LORA_W
OFF_V = OFF_K + A_W
OFF_AL = OFF_V + A_W
OFF_GL = OFF_AL + A_LORA_A
A_COLS = OFF_GL + A_LORA_G
OFF_POOL = A_COLS
OFF_Q = OFF_POOL + B_W
OFF_KV = OFF_Q + C_W
OFF_CG = OFF_KV + 6 * C_KVW
OFF_MG = OFF_CG + 3 * C_HEADS
N_IN = OFF_MG + 3 * D_MODEL

kernel_name = 'hybrid_rwkv7_pool_nsa_decoder_step'

def rms_norm(x, g):
    xf = x.astype(jnp.float32)
    y = xf * lax.rsqrt(jnp.mean(xf * xf, axis=-1, keepdims=True) + RMS_EPS)
    return (y * g.astype(jnp.float32)).astype(x.dtype)

def rel_bucket(dist):
    n = jnp.maximum(dist, 0)
    exact = N_BUCKETS // 2
    ratio = jnp.log(jnp.maximum(n, 1).astype(jnp.float32) / exact) / math.log(MAX_DIST / exact)
    large = jnp.minimum(exact + (ratio * (N_BUCKETS - exact)).astype(jnp.int32), N_BUCKETS - 1)
    return jnp.where(n < exact, n, large)

def masked_softmax(logits, mask):
    p = jax.nn.softmax(jnp.where(mask, logits.astype(jnp.float32), NEG), axis=-1)
    return p * mask

def rwkv_mix(u, u_last, s0, mu, w0, w2, a0, a2, g2, k_k, k_a, r_k, lnx_g, lnx_b):
    bn, t = u.shape[:2]
    u_prev = jnp.concatenate([u_last[:, None, :].astype(u.dtype), u[:, :-1]], axis=1)
    xs = u + (u_prev - u) * mu
    r = xs[..., OFF_R:OFF_R + A_W]
    wl = xs[..., OFF_WL:OFF_WL + A_LORA_W]
    k = xs[..., OFF_K:OFF_K + A_W]
    v = xs[..., OFF_V:OFF_V + A_W]
    al = xs[..., OFF_AL:OFF_AL + A_LORA_A]
    gl = xs[..., OFF_GL:OFF_GL + A_LORA_G]
    w = -jax.nn.softplus(-(w0 + jnp.tanh(wl) @ w2)) - 0.5
    a = jax.nn.sigmoid(a0 + al @ a2)
    g = jax.nn.sigmoid(gl) @ g2
    heads = lambda z: z.astype(jnp.float32).reshape(bn, t, A_HEADS, A_HD)
    kk = heads(k * k_k)
    kk = kk * lax.rsqrt(jnp.maximum(jnp.sum(kk * kk, -1, keepdims=True), L2_EPS))
    k = k * (1.0 + (a - 1.0) * k_a)
    rh, kh, vh, ah = heads(r), heads(k), heads(v), heads(a)
    decay = jnp.exp(-jnp.exp(heads(w)))

    def step(S, inp):
        r_t, d_t, k_t, v_t, kk_t, a_t = inp
        sa = jnp.einsum('bhij,bhj->bhi', S, -kk_t)
        S = (S * d_t[:, :, None, :] + sa[..., None] * (kk_t * a_t)[:, :, None, :]
             + v_t[..., None] * k_t[:, :, None, :])
        return S, jnp.einsum('bhij,bhj->bhi', S, r_t)

    seq = tuple(jnp.swapaxes(z, 0, 1) for z in (rh, decay, kh, vh, kk, ah))
    s_new, ys = lax.scan(step, s0.astype(jnp.float32), seq)
    y = jnp.swapaxes(ys, 0, 1)
    mean = jnp.mean(y, -1, keepdims=True)
    var = jnp.mean(jnp.square(y - mean), -1, keepdims=True)
    y = ((y - mean) * lax.rsqrt(var + LNX_EPS)).reshape(bn, t, A_W) * lnx_g + lnx_b
    bonus = (jnp.sum(rh * kh * r_k, -1, keepdims=True) * vh).reshape(bn, t, A_W)
    return ((y + bonus) * g).astype(u.dtype), s_new, u[:, -1]

def pool_mix(u, u_buf, pos0, pm, pscale):
    bn, t = u.shape[:2]
    ext = jnp.concatenate([u_buf.astype(u.dtype), u], axis=1).astype(jnp.float32)
    c0 = jnp.concatenate([jnp.zeros((bn, 1, B_W), jnp.float32), jnp.cumsum(ext, axis=1)], axis=1)
    pos = pos0 + jnp.arange(t)
    cur = ext[:, POOL_BUF:]
    outs = []
    for gi, win in enumerate(POOL_WINDOWS):
        sl = slice(gi * B_GW, (gi + 1) * B_GW)
        s = c0[:, POOL_BUF + 1:, sl] - c0[:, POOL_BUF + 1 - win:POOL_BUF + 1 - win + t, sl]
        cnt = jnp.minimum(win, pos + 1).astype(jnp.float32)
        outs.append(s / cnt[None, :, None] - cur[..., sl])
    d = jnp.stack(outs, axis=2)
    z = jnp.einsum('btgc,gcd->btgd', d, pm).reshape(bn, t, B_W) * pscale
    return z.astype(u.dtype), ext[:, -POOL_BUF:].astype(u.dtype)

def nsa_inputs(proj, q_g, k_g):
    bn, t = proj.shape[:2]
    q = rms_norm(proj[..., OFF_Q:OFF_Q + C_W].reshape(bn, t, C_HEADS, C_HD), q_g)
    kv = proj[..., OFF_KV:OFF_KV + 6 * C_KVW].reshape(bn, t, 6, C_KV, C_HD)
    k_cmp, v_cmp = kv[:, :, 0], kv[:, :, 1]
    k_slc, v_slc = rms_norm(kv[:, :, 2], k_g[1]), kv[:, :, 3]
    k_win, v_win = rms_norm(kv[:, :, 4], k_g[2]), kv[:, :, 5]
    gates = proj[..., OFF_CG:OFF_CG + 3 * C_HEADS]
    return q, gates, (k_cmp, v_cmp, k_slc, v_slc, k_win, v_win)

def compress_kv(k_raw, v, kg):
    bn, tk = k_raw.shape[:2]
    nb = -(-tk // CMP_BLOCK)
    pad = nb * CMP_BLOCK - tk

    def blk_mean(z):
        z = jnp.pad(z.astype(jnp.float32), ((0, 0), (0, pad), (0, 0), (0, 0)))
        return z.reshape(bn, nb, CMP_BLOCK, C_KV, C_HD).mean(axis=2)

    return rms_norm(blk_mean(k_raw), kg), blk_mean(v)

def to_blocks(z):
    bn, tk = z.shape[:2]
    nb = -(-tk // CMP_BLOCK)
    z = jnp.pad(z, ((0, 0), (0, nb * CMP_BLOCK - tk), (0, 0), (0, 0)))
    return z.reshape(bn, nb, CMP_BLOCK, C_KV, C_HD).transpose(0, 3, 1, 2, 4)

def nsa_query_block(q, qpos, gates, kc, vc, ksb, vsb, kw, vw, kwpos, rel_bias):
    bn, tq = q.shape[:2]
    nb = kc.shape[1]
    scale = C_HD ** -0.5
    qg = q.reshape(bn, tq, C_KV, C_HPG, C_HD)
    rb = rel_bias.reshape(N_BUCKETS, C_KV, C_HPG)
    endpos = jnp.arange(nb) * CMP_BLOCK + (CMP_BLOCK - 1)
    dist_c = qpos[:, None] - endpos[None, :]
    bias_c = rb[rel_bucket(dist_c)].transpose(2, 3, 0, 1)
    lc = jnp.einsum('btgnd,bjgd->bgntj', qg, kc).astype(jnp.float32) * scale + bias_c
    pc = masked_softmax(lc, dist_c >= 0)
    o_cmp = jnp.einsum('bgntj,bjgd->btgnd', pc, vc)
    blk = jnp.arange(nb)
    cur = (qpos // CMP_BLOCK)[:, None]
    forced = (blk == 0) | (blk == cur) | (blk == cur - 1)
    score = jnp.where(blk > cur, NEG, jnp.where(forced, FORCE_SCORE, pc.sum(axis=2)))
    ksel = min(N_SEL, nb)
    top_val, top_idx = lax.top_k(score, ksel)
    bi = jnp.arange(bn)[:, None, None, None]
    gi = jnp.arange(C_KV)[None, :, None, None]
    n_sel_keys = ksel * CMP_BLOCK
    ks = ksb[bi, gi, top_idx].reshape(bn, C_KV, tq, n_sel_keys, C_HD)
    vs = vsb[bi, gi, top_idx].reshape(bn, C_KV, tq, n_sel_keys, C_HD)
    kpos5 = top_idx[..., None] * CMP_BLOCK + jnp.arange(CMP_BLOCK)
    valid = ((top_val > 0.5 * NEG)[..., None] & (kpos5 <= qpos[None, None, :, None, None]))
    valid = valid.reshape(bn, C_KV, tq, n_sel_keys)
    dist_s = qpos[None, None, :, None] - kpos5.reshape(bn, C_KV, tq, n_sel_keys)
    bias_s = rb[rel_bucket(dist_s), gi].transpose(0, 1, 4, 2, 3)
    ls = jnp.einsum('btgnd,bgtsd->bgnts', qg, ks).astype(jnp.float32) * scale + bias_s
    ps = masked_softmax(ls, valid[:, :, None])
    o_slc = jnp.einsum('bgnts,bgtsd->btgnd', ps, vs)
    dist_w = qpos[:, None] - kwpos[None, :]
    mask_w = (dist_w >= 0) & (dist_w < WINDOW) & (kwpos >= 0)[None, :]
    bias_w = rb[rel_bucket(dist_w)].transpose(2, 3, 0, 1)
    lw = jnp.einsum('btgnd,bsgd->bgnts', qg, kw).astype(jnp.float32) * scale + bias_w
    pw = masked_softmax(lw, mask_w)
    o_win = jnp.einsum('bgnts,bsgd->btgnd', pw, vw)
    gt = jax.nn.sigmoid(gates.astype(jnp.float32)).reshape(bn, tq, 3, C_KV, C_HPG)[..., None]
    o = gt[:, :, 0] * o_cmp + gt[:, :, 1] * o_slc + gt[:, :, 2] * o_win
    return o.reshape(bn, tq, C_W).astype(q.dtype)

def nsa_prompt(q, gates, k_cmp, v_cmp, k_slc, v_slc, k_win, v_win, kg_cmp, rel_bias):
    bn, t = q.shape[:2]
    kc, vc = compress_kv(k_cmp, v_cmp, kg_cmp)
    ksb, vsb = to_blocks(k_slc), to_blocks(v_slc)
    zpad = jnp.zeros((bn, WINDOW, C_KV, C_HD), k_win.dtype)
    kwp = jnp.concatenate([zpad, k_win], axis=1)
    vwp = jnp.concatenate([zpad.astype(v_win.dtype), v_win], axis=1)

    def body(i):
        s = i * Q_BLOCK
        sl = lambda z, n: lax.dynamic_slice_in_dim(z, s, n, axis=1)
        qpos = s + jnp.arange(Q_BLOCK)
        kwpos = s - WINDOW + jnp.arange(WINDOW + Q_BLOCK)
        return nsa_query_block(sl(q, Q_BLOCK), qpos, sl(gates, Q_BLOCK), kc, vc, ksb, vsb,
                               sl(kwp, WINDOW + Q_BLOCK), sl(vwp, WINDOW + Q_BLOCK), kwpos, rel_bias)

    out = lax.map(body, jnp.arange(t // Q_BLOCK, dtype=jnp.int32))
    return jnp.swapaxes(out, 0, 1).reshape(bn, t, C_W)

def nsa_sample(q, gates, k_cmp, v_cmp, k_slc, v_slc, k_win, v_win, pool_ck, pool_cv, pool_sk, pool_sv,
               win_k, win_v, page_table, kg_cmp, rel_bias):
    bn, tq = q.shape[:2]
    past = page_table.shape[1] * PAGE_SIZE

    def logical(pool, new):
        rows = pool[page_table].reshape((bn, past) + pool.shape[2:])
        return jnp.concatenate([rows.astype(new.dtype), new], axis=1)

    kc, vc = compress_kv(logical(pool_ck, k_cmp), logical(pool_cv, v_cmp), kg_cmp)
    ksb, vsb = to_blocks(logical(pool_sk, k_slc)), to_blocks(logical(pool_sv, v_slc))
    kw = jnp.concatenate([win_k.astype(k_win.dtype), k_win], axis=1)
    vw = jnp.concatenate([win_v.astype(v_win.dtype), v_win], axis=1)
    wbuf = win_k.shape[1]
    kwpos = past - wbuf + jnp.arange(wbuf + tq)
    qpos = past + jnp.arange(tq)
    out = nsa_query_block(q, qpos, gates, kc, vc, ksb, vsb, kw, vw, kwpos, rel_bias)
    return out, kw[:, -wbuf:], vw[:, -wbuf:]

def merge_branches(x, proj, o_a, o_b, o_c, wa, wb, wc, wo):
    bn, t = x.shape[:2]
    gate = jax.nn.sigmoid(proj[..., OFF_MG:OFF_MG + 3 * D_MODEL].reshape(bn, t, 3, D_MODEL))
    h = gate[:, :, 0] * (o_a @ wa) + gate[:, :, 1] * (o_b @ wb) + gate[:, :, 2] * (o_c @ wc)
    return x + h @ wo

def mem_kv(mem, g_mem, w_k, w_v, k_g):
    bn, m = mem.shape[:2]
    mn = rms_norm(mem, g_mem)
    k = rms_norm((mn @ w_k).reshape(bn, m, M_HEADS, M_HD), k_g)
    v = (mn @ w_v).reshape(bn, m, M_HEADS, M_HD)
    return k, v

def mem_ffn(x, mk, mv, g_x, w_q, q_g, w_o, g_f, w1, w2):
    bn, t = x.shape[:2]
    q = rms_norm((rms_norm(x, g_x) @ w_q).reshape(bn, t, M_HEADS, M_HD), q_g)
    logits = jnp.einsum('bthd,bmhd->bhtm', q, mk).astype(jnp.float32) * (M_HD ** -0.5)
    p = jax.nn.softmax(logits, axis=-1)
    o = jnp.einsum('bhtm,bmhd->bthd', p, mv).reshape(bn, t, M_W).astype(x.dtype)
    x = x + o @ w_o
    h = jnp.square(jax.nn.relu(rms_norm(x, g_f) @ w1))
    return x + h @ w2

def setup_inputs(seed: int = 0) -> dict:
    key = jax.random.key(seed)
    ks = iter(jax.random.split(key, 64))
    nrm = lambda shape, s: jax.random.normal(next(ks), shape, jnp.float32) * s
    uni = lambda shape, lo, hi: jax.random.uniform(next(ks), shape, jnp.float32, lo, hi)
    gain = lambda shape: 1.0 + nrm(shape, 0.05)
    n_pages = PAST_LEN // PAGE_SIZE
    n_phys = (DEC_BATCH * n_pages * 5) // 4
    wbuf = min(WINDOW, PAST_LEN)
    perm = jax.random.permutation(next(ks), n_phys)
    page_table = perm[:DEC_BATCH * n_pages].reshape(DEC_BATCH, n_pages).astype(jnp.int32)
    pool_shape = (DEPTH, n_phys, PAGE_SIZE, C_KV, C_HD)
    return {
        'x_prompt': nrm((BATCH, SEQ, D_MODEL), 1.0),
        'x_sample': nrm((DEC_BATCH, DEC_SEQ, D_MODEL), 1.0),
        'state_rwkv': nrm((DEPTH, DEC_BATCH, A_HEADS, A_HD, A_HD), 0.3),
        'state_shift': nrm((DEPTH, DEC_BATCH, A_COLS), 1.0),
        'state_pool': nrm((DEPTH, DEC_BATCH, POOL_BUF, B_W), 1.0),
        'cache_cmp_k': nrm(pool_shape, 1.0),
        'cache_cmp_v': nrm(pool_shape, 1.0),
        'cache_slc_k': nrm(pool_shape, 1.0),
        'cache_slc_v': nrm(pool_shape, 1.0),
        'cache_win_k': nrm((DEPTH, DEC_BATCH, wbuf, C_KV, C_HD), 1.0),
        'cache_win_v': nrm((DEPTH, DEC_BATCH, wbuf, C_KV, C_HD), 1.0),
        'cache_mem_k': nrm((DEPTH, DEC_BATCH, N_MEM, M_HEADS, M_HD), 1.0),
        'cache_mem_v': nrm((DEPTH, DEC_BATCH, N_MEM, M_HEADS, M_HD), 1.0),
        'page_table': page_table,
        'mem_prompt': nrm((BATCH, N_MEM, D_MODEL), 1.0),
        'rel_bias': nrm((N_BUCKETS, C_HEADS), 0.5),
        'norm_mix_g': gain((DEPTH, D_MODEL)),
        'w_in': nrm((DEPTH, D_MODEL, N_IN), D_MODEL ** -0.5),
        'shift_mu': uni((DEPTH, A_COLS), 0.0, 1.0),
        'rwkv_w0': uni((DEPTH, A_W), -3.0, 0.0),
        'rwkv_w2': nrm((DEPTH, A_LORA_W, A_W), 0.1),
        'rwkv_a0': nrm((DEPTH, A_W), 0.5),
        'rwkv_a2': nrm((DEPTH, A_LORA_A, A_W), 0.1),
        'rwkv_g2': nrm((DEPTH, A_LORA_G, A_W), A_LORA_G ** -0.5),
        'rwkv_kk': 0.85 + nrm((DEPTH, A_W), 0.05),
        'rwkv_ka': 1.0 + nrm((DEPTH, A_W), 0.1),
        'rwkv_rk': nrm((DEPTH, A_HEADS, A_HD), 0.1),
        'rwkv_lnx_g': gain((DEPTH, A_W)),
        'rwkv_lnx_b': nrm((DEPTH, A_W), 0.01),
        'pool_w': nrm((DEPTH, B_GROUPS, B_GW, B_GW), B_GW ** -0.5),
        'pool_scale': 1.0 + nrm((DEPTH, B_W), 0.1),
        'nsa_q_g': gain((DEPTH, C_HD)),
        'nsa_k_g': gain((DEPTH, 3, C_HD)),
        'w_br_a': nrm((DEPTH, A_W, D_MODEL), A_W ** -0.5),
        'w_br_b': nrm((DEPTH, B_W, D_MODEL), B_W ** -0.5),
        'w_br_c': nrm((DEPTH, C_W, D_MODEL), C_W ** -0.5),
        'w_out': nrm((DEPTH, D_MODEL, D_MODEL), D_MODEL ** -0.5),
        'norm_memx_g': gain((DEPTH, D_MODEL)),
        'norm_mem_g': gain((DEPTH, D_MODEL)),
        'w_mq': nrm((DEPTH, D_MODEL, M_W), D_MODEL ** -0.5),
        'w_mk': nrm((DEPTH, D_MODEL, M_W), D_MODEL ** -0.5),
        'w_mv': nrm((DEPTH, D_MODEL, M_W), D_MODEL ** -0.5),
        'mem_q_g': gain((DEPTH, M_HD)),
        'mem_k_g': gain((DEPTH, M_HD)),
        'w_mo': nrm((DEPTH, M_W, D_MODEL), M_W ** -0.5),
        'norm_ffn_g': gain((DEPTH, D_MODEL)),
        'w_ff1': nrm((DEPTH, D_MODEL, D_FF), D_MODEL ** -0.5),
        'w_ff2': nrm((DEPTH, D_FF, D_MODEL), D_FF ** -0.5),
    }

def reference(x_prompt, x_sample, state_rwkv, state_shift, state_pool,
              cache_cmp_k, cache_cmp_v, cache_slc_k, cache_slc_v,
              cache_win_k, cache_win_v, cache_mem_k, cache_mem_v, page_table,
              mem_prompt, rel_bias, norm_mix_g, w_in, shift_mu,
              rwkv_w0, rwkv_w2, rwkv_a0, rwkv_a2, rwkv_g2, rwkv_kk, rwkv_ka,
              rwkv_rk, rwkv_lnx_g, rwkv_lnx_b, pool_w, pool_scale,
              nsa_q_g, nsa_k_g, w_br_a, w_br_b, w_br_c, w_out,
              norm_memx_g, norm_mem_g, w_mq, w_mk, w_mv, mem_q_g, mem_k_g, w_mo,
              norm_ffn_g, w_ff1, w_ff2):
    bp, t = x_prompt.shape[:2]
    past = page_table.shape[1] * PAGE_SIZE
    wbuf_p = min(WINDOW, t)
    xp, xsm = x_prompt, x_sample
    p_rwkv, p_shift, p_pool, p_ck, p_cv, p_sk, p_sv, p_wk, p_wv, p_mk, p_mv = ([] for _ in range(11))
    s_rwkv, s_shift, s_pool, s_ck, s_cv, s_sk, s_sv, s_wk, s_wv = ([] for _ in range(9))
    for l in range(DEPTH):
        rw = (shift_mu[l], rwkv_w0[l], rwkv_w2[l], rwkv_a0[l], rwkv_a2[l], rwkv_g2[l],
              rwkv_kk[l], rwkv_ka[l], rwkv_rk[l], rwkv_lnx_g[l], rwkv_lnx_b[l])
        proj = rms_norm(xp, norm_mix_g[l]) @ w_in[l]
        o_a, s_a, last_a = rwkv_mix(proj[..., :A_COLS], jnp.zeros((bp, A_COLS), proj.dtype),
                                    jnp.zeros((bp, A_HEADS, A_HD, A_HD), jnp.float32), *rw)
        o_b, buf_b = pool_mix(proj[..., OFF_POOL:OFF_POOL + B_W], jnp.zeros((bp, POOL_BUF, B_W), proj.dtype),
                              0, pool_w[l], pool_scale[l])
        q, gates, (kc_, vc_, ks_, vs_, kw_, vw_) = nsa_inputs(proj, nsa_q_g[l], nsa_k_g[l])
        o_c = nsa_prompt(q, gates, kc_, vc_, ks_, vs_, kw_, vw_, nsa_k_g[l][0], rel_bias)
        xp = merge_branches(xp, proj, o_a, o_b, o_c, w_br_a[l], w_br_b[l], w_br_c[l], w_out[l])
        mk, mv = mem_kv(mem_prompt, norm_mem_g[l], w_mk[l], w_mv[l], mem_k_g[l])
        xp = mem_ffn(xp, mk, mv, norm_memx_g[l], w_mq[l], mem_q_g[l], w_mo[l],
                     norm_ffn_g[l], w_ff1[l], w_ff2[l])
        p_rwkv.append(s_a); p_shift.append(last_a); p_pool.append(buf_b)
        p_ck.append(kc_); p_cv.append(vc_); p_sk.append(ks_); p_sv.append(vs_)
        p_wk.append(kw_[:, -wbuf_p:]); p_wv.append(vw_[:, -wbuf_p:]); p_mk.append(mk); p_mv.append(mv)
        proj = rms_norm(xsm, norm_mix_g[l]) @ w_in[l]
        o_a, s_a, last_a = rwkv_mix(proj[..., :A_COLS], state_shift[l], state_rwkv[l], *rw)
        o_b, buf_b = pool_mix(proj[..., OFF_POOL:OFF_POOL + B_W], state_pool[l], past,
                              pool_w[l], pool_scale[l])
        q, gates, (kc_, vc_, ks_, vs_, kw_, vw_) = nsa_inputs(proj, nsa_q_g[l], nsa_k_g[l])
        o_c, wk_new, wv_new = nsa_sample(q, gates, kc_, vc_, ks_, vs_, kw_, vw_,
                                         cache_cmp_k[l], cache_cmp_v[l], cache_slc_k[l], cache_slc_v[l],
                                         cache_win_k[l], cache_win_v[l], page_table, nsa_k_g[l][0], rel_bias)
        xsm = merge_branches(xsm, proj, o_a, o_b, o_c, w_br_a[l], w_br_b[l], w_br_c[l], w_out[l])
        xsm = mem_ffn(xsm, cache_mem_k[l], cache_mem_v[l], norm_memx_g[l], w_mq[l], mem_q_g[l], w_mo[l],
                      norm_ffn_g[l], w_ff1[l], w_ff2[l])
        s_rwkv.append(s_a); s_shift.append(last_a); s_pool.append(buf_b)
        s_ck.append(kc_); s_cv.append(vc_); s_sk.append(ks_); s_sv.append(vs_)
        s_wk.append(wk_new); s_wv.append(wv_new)
    return (xp, xsm,
            jnp.stack(p_rwkv), jnp.stack(p_shift), jnp.stack(p_pool),
            jnp.stack(p_ck), jnp.stack(p_cv), jnp.stack(p_sk), jnp.stack(p_sv),
            jnp.stack(p_wk), jnp.stack(p_wv), jnp.stack(p_mk), jnp.stack(p_mv),
            jnp.stack(s_rwkv), jnp.stack(s_shift), jnp.stack(s_pool),
            jnp.stack(s_ck), jnp.stack(s_cv), jnp.stack(s_sk), jnp.stack(s_sv),
            jnp.stack(s_wk), jnp.stack(s_wv))


_drawn_inputs = setup_inputs


def setup_inputs(seed=0):
    import zlib

    import numpy as np

    out = dict(_drawn_inputs(seed))
    spreads = {}
    factors = {'cache_cmp_k': 4.658,
     'cache_cmp_v': 5.915,
     'cache_slc_k': 4.598,
     'cache_slc_v': 3.782,
     'rel_bias': 3.049,
     'rwkv_kk': 8.512,
     'rwkv_lnx_g': 4.32,
     'rwkv_lnx_b': 21.724,
     'nsa_q_g': 8.0,
     'norm_memx_g': 8.0,
     'mem_q_g': 8.0}
    for name, (base, spread) in spreads.items():
        noise = np.random.default_rng([zlib.crc32(name.encode()), seed]).standard_normal(out[name].shape)
        drawn = base * np.exp(spread * noise) if base else spread * noise
        out[name] = __import__('jax').numpy.asarray(drawn.astype(out[name].dtype))
    for name, factor in factors.items():
        out[name] = (out[name] * factor).astype(out[name].dtype)
    return out
```

```python
from contextlib import ExitStack

import numpy as np

import concourse.bass as bass
from concourse import mybir


class Shared:
    pass


F32 = mybir.dt.float32
I32 = mybir.dt.int32
ALU = mybir.AluOpType
ACT = mybir.ActivationFunctionType
AX = mybir.AxisListType

P = 128
D = 1024
KD = D // P
TP = 1024
DB, DT = 8, 4
TS = DB * DT
T = TP + TS
NC3 = 3
NW = T // NC3
TAIL = 15 + TS
T0 = T - TAIL
NTI = TP // P
A_COLS = 1792
OFF_POOL = A_COLS
OFF_Q = OFF_POOL + 512
OFF_KV = OFF_Q + 512
OFF_CG = OFF_KV + 768
OFF_MG = OFF_CG + 24
KVG = 768 + 24
PAST = 2048
PAGE = 128
NPG = PAST // PAGE
NEG = -1e30
RMS_EPS = 1e-6
LNX_EPS = 64e-5
DECAY = float(np.exp(-0.5))
REV = 2111
BVL = REV + 1025

BLOCKS = ([[(128 * c, 128)] for c in range(4)] + [[(576 + 128 * c, 128)] for c in range(4)]
          + [[(1088 + 128 * c, 128)] for c in range(4)] + [[(512, 64), (1600, 64)], [(1664, 128)]]
          + [[(OFF_POOL + 128 * c, 128)] for c in range(4)] + [[(OFF_Q + 128 * c, 128)] for c in range(4)])
B_R, B_K, B_V, B_WA, B_G, B_POOL, B_Q = 0, 4, 8, 12, 13, 14, 18
NSHIFT = 14

PARAMS = [("norm_mix_g", 8), ("shift_mu", NSHIFT), ("rwkv_w0", 4), ("rwkv_a0", 4), ("rwkv_kk", 4), ("rwkv_ka", 4),
          ("rwkv_rk", 4), ("rwkv_lnx_g", 4), ("rwkv_lnx_b", 4), ("pool_scale", 4), ("norm_memx_g", 8),
          ("norm_mem_g", 8), ("norm_ffn_g", 8), ("mem_q_g", 1), ("nsa_q_g", 1), ("kg_cmp", 1)]
PCOL = {}
_at = 0
for _n, _c in PARAMS:
    PCOL[_n] = _at
    _at += _c
NPAR = _at


def shape_constants():
    cols, sheets = {}, []

    def put(name, a):
        b = np.zeros((P, a.shape[1]), np.float32)
        b[:a.shape[0]] = a
        cols[name] = (sum(s.shape[1] for s in sheets), a.shape[1])
        sheets.append(b)

    r = np.arange(P)
    put("ident", np.eye(P))
    put("flip", np.eye(P)[::-1])
    put("headsum", (r[:, None] // 64 == r[None, :] // 64).astype(np.float32))
    put("ones", np.ones((P, P)))

    def chunk_masks(tag, n, levels, size):
        i, t = np.arange(n)[:, None], np.arange(n)[None, :]
        same = i // size == t // size
        put("strict" + tag, (same & (i < t)) * 1.0)
        put("incl" + tag, (same & (i <= t)) * 1.0)
        for l in range(levels):
            s = 1 << l
            m = (i // (2 * s) == t // (2 * s)) & (t // s % 2 == 1) & (i // s % 2 == 0)
            put(f"lvl{l}" + tag, m * 1.0)
        put("low0" + tag, ((t // 2 == i // 2) & (i % 2 == 1) & (t % 2 == 0)) * 1.0)
    chunk_masks("P", 128, 7, 128)
    chunk_masks("S", TS, 2, DT)
    i = np.arange(TS)
    put("batch", (i[:, None] // DT == np.arange(DB)[None, :]) * 1.0)
    put("batchcol", np.repeat(np.kron(np.eye(DB), np.ones((1, DT))).reshape(1, -1), P, 0))
    put("edge", np.where(r[:, None] < r[None, :], 0.0, NEG))
    put("poolcnt", np.concatenate([np.repeat((1.0 / np.minimum(w, np.arange(16) + 1))[None], P, 0)
                                   for w in (2, 4, 8, 16)], 1))
    m = np.zeros((P, 64))
    m[:64, 30] = 1 / 64
    m[64:, 31] = 1 / 64
    put("blk", m)
    t = r % 4
    put("edgeS", np.where(np.arange(4)[None, :] <= t[:, None], NEG, 0.0))
    put("grp", (r[:, None] % 32 // 16 == np.arange(2)[None, :]) * 1.0)
    put("mhead", (r[:, None] % 32 // 4 == np.arange(4)[None, :]) * 1.0)
    put("heads4", ((r[:, None] // 16 == r[None, :] // 16) & (t[:, None] == t[None, :])) * 1.0)
    m = np.arange(-14, 16)
    put("cmask", (r[:, None] - 64 * m[None, :] - 63 >= 0) * 1.0)
    keep = np.ones((1, T))
    keep[0, 0:TP:P] = 0
    keep[0, TP:T:DT] = 0
    dist = REV - np.arange(BVL)
    n = np.maximum(dist, 0)
    ratio = np.log(np.maximum(n, 1) / 16) / np.log(8)
    bucket = np.where(n < 16, n, np.minimum(16 + (ratio * 16).astype(np.int64), 31))
    onehot = (bucket[None, :] == np.arange(32)[:, None]) & (dist >= 0)[None]
    onehot = np.concatenate([onehot, (dist < 0)[None]], 0)
    return cols, np.concatenate(sheets, 1).astype(np.float32), keep.astype(np.float32), onehot.astype(np.float32)


CCOL, SHEET, KEEP, ONEHOT = shape_constants()


def stage_load(nc, K):
    ctx = ExitStack()
    with ctx:
        xin = ctx.enter_context(nc.sbuf_tensor("xin", [P, NTI + 1, D], F32))
        prow = ctx.enter_context(nc.sbuf_tensor("prow", [NPAR, P], F32))
        srow = ctx.enter_context(nc.sbuf_tensor("srow", [DB, A_COLS], F32))
        block = ctx.enter_context(nc.Block())
        s_const, s_prow, s_x = K.sem("const_in"), K.sem("param_rows_in"), K.sems("x_in", NTI + 1)
        s_par, s_parc = K.sem("params_turned"), K.sem("params_copied")
        s_xt, s_xa, s_xv = K.sem("x_turned"), K.sem("x_copied_act"), K.sem("x_copied_dve")
        s_sh = K.sem("shift_turned")

        @block.sync
        def _(e):
            e.dma_start(K.cst[:, :], K.d["sheet"]).then_inc(s_const, 16)
            e.dma_start(K.keep[:, :], K.d["keep"].partition_broadcast(P)).then_inc(s_const, 16)
            e.dma_start(srow[:, :], K.d["state_shift"][0]).then_inc(s_const, 16)
            for i in range(NTI):
                e.dma_start(xin[:, i, :], K.d["x_prompt"][0, P * i:P * i + P, :]).then_inc(s_x[i], 16)
            e.dma_start(xin[0:TS, NTI, :], K.d["x_sample"].rearrange("b t d -> (b t) d")).then_inc(s_x[NTI], 16)

        @block.scalar
        def _(e):
            for name, cnt in PARAMS:
                if name in ("nsa_q_g", "kg_cmp"):
                    src = K.d["nsa_q_g"][0:1, :] if name == "nsa_q_g" else K.d["nsa_k_g"][0, 0:1, :]
                    for z in range(2):
                        e.dma_start(prow[PCOL[name]:PCOL[name] + 1, 64 * z:64 * z + 64], src).then_inc(s_prow, 16)
                    continue
                if name == "shift_mu":
                    for b in range(NSHIFT):
                        at = 0
                        for c0, w in BLOCKS[b]:
                            e.dma_start(prow[PCOL[name] + b:PCOL[name] + b + 1, at:at + w],
                                        K.d["shift_mu"][0:1, c0:c0 + w]).then_inc(s_prow, 16)
                            at += w
                    continue
                src = K.d[name]
                if name == "rwkv_rk":
                    src = src.rearrange("a (c h) d -> (a c) (h d)", c=cnt)
                else:
                    src = src.rearrange("a (c p) -> (a c) p", p=P)
                e.dma_start(prow[PCOL[name]:PCOL[name] + cnt, :], src).then_inc(s_prow, 16)
            for i in range(NTI + 1):
                n = P if i < NTI else TS
                e.wait_ge(s_xt, i + 1)
                e.activation(K.xT[:, 0:4, P * i:P * i + n],
                             K.ps[:, 2 * (i % 2), :].rearrange("p (k n) -> p k n", k=4)[:, :, 0:n],
                             ACT.Copy).then_inc(s_xa, 1)

        @block.tensor
        def _(e):
            e.wait_ge(s_const, 48)
            ident = K.c("ident")
            e.wait_ge(s_prow, 16 * K.n_prow)
            e.transpose(K.ps[:, 4, 0:NPAR], prow[:, :], ident[0:NPAR, 0:NPAR]).then_inc(s_par, 1)
            for b in range(NSHIFT):
                at = 0
                for c0, w in BLOCKS[b]:
                    if at == 0:
                        mm = e.transpose(K.ps[0:w, 5, 8 * b:8 * b + 8], srow[:, c0:c0 + w], ident[0:DB, 0:DB])
                    else:
                        mm = e.transpose(K.ps[0:w, 6, 0:8], srow[:, c0:c0 + w], ident[0:DB, 0:DB])
                    at += w
            mm.then_inc(s_sh, 1)
            for i in range(NTI + 1):
                n = P if i < NTI else TS
                e.wait_ge(s_x[i], 16)
                if i >= 2:
                    e.wait_ge(s_xa, i - 1)
                    e.wait_ge(s_xv, i - 1)
                for k in range(KD):
                    mm = e.transpose(K.ps[:, 2 * (i % 2) + k // 4, P * (k % 4):P * (k % 4) + n],
                                     xin[0:n, i, P * k:P * k + P], ident[0:n, 0:n])
                mm.then_inc(s_xt, 1)

        @block.vector
        def _(e):
            e.wait_ge(s_par, 1)
            e.tensor_copy(K.par[:, 0:NPAR], K.ps[:, 4, 0:NPAR])
            e.wait_ge(s_sh, 1)
            e.tensor_copy(K.shT[:, 0:B_WA, :], K.ps[:, 5, 0:8 * B_WA].rearrange("p (b n) -> p b n", n=8))
            e.tensor_copy(K.shT[:, B_G, :], K.ps[:, 5, 8 * B_G:8 * B_G + 8])
            e.tensor_copy(K.shT[0:64, B_WA, :], K.ps[0:64, 5, 8 * B_WA:8 * B_WA + 8])
            e.tensor_copy(K.shT[64:128, B_WA, :], K.ps[0:64, 6, 0:8])
            for i in range(NTI + 1):
                n = P if i < NTI else TS
                e.wait_ge(s_xt, i + 1)
                e.tensor_copy(K.xT[:, 4:8, P * i:P * i + n],
                              K.ps[:, 2 * (i % 2) + 1, :].rearrange("p (k n) -> p k n", k=4)[:, :, 0:n]).then_inc(s_xv, 1)


def stage_rms(nc, K, name, src, dst, gain, ntok):
    nchunk = -(-ntok // NW)
    w = ntok // nchunk
    ctx = ExitStack()
    with ctx:
        sq = ctx.enter_context(nc.sbuf_tensor(name + "_sq", [P, KD, w], F32))
        rstd = ctx.enter_context(nc.sbuf_tensor(name + "_rstd", [P, 2, w], F32))
        block = ctx.enter_context(nc.Block())
        s_sq, s_sum = K.sem(name + "_squared"), K.sem(name + "_summed")
        s_var, s_root = K.sem(name + "_mean"), K.sem(name + "_root")

        @block.scalar
        def _(e):
            for c in range(nchunk):
                if c >= 1:
                    e.wait_ge(s_sum, c)
                e.activation(sq[:, :, :], src[:, :, w * c:w * c + w], ACT.Square).then_inc(s_sq, 1)
                e.wait_ge(s_var, c + 1)
                e.activation(rstd[:, c % 2, :], rstd[:, c % 2, :], ACT.Sqrt).then_inc(s_root, 1)

        @block.tensor
        def _(e):
            for c in range(nchunk):
                e.wait_ge(s_sq, c + 1)
                if c >= 2:
                    e.wait_ge(s_var, c - 1)
                for k in range(KD):
                    mm = e.matmul(K.ps[:, c % 2, 0:w], K.c("ones"), sq[:, k, :], start=k == 0, stop=k == KD - 1)
                mm.then_inc(s_sum, 1)

        @block.vector
        def _(e):
            for c in range(nchunk):
                e.wait_ge(s_sum, c + 1)
                e.tensor_scalar(rstd[:, c % 2, :], K.ps[:, c % 2, 0:w], 1.0 / D, RMS_EPS,
                                ALU.mult, ALU.add).then_inc(s_var, 1)
                e.wait_ge(s_root, c + 1)
                e.reciprocal(rstd[:, c % 2, :], rstd[:, c % 2, :])
                e.drain()
                for k in range(KD):
                    e.scalar_tensor_tensor(dst[:, k, w * c:w * c + w], src[:, k, w * c:w * c + w],
                                           K.p(gain, k), rstd[:, c % 2, :], ALU.mult, ALU.mult)
                e.drain()


def project(e, K, ring, s_in, s_mm, s_free, nblk, kb, rhs, use_slot, bank=0):
    for m in range(nblk):
        slot, turn, off, last = use_slot(m)
        e.wait_ge(s_in[slot], 16 * turn)
        if m >= 2:
            for s, per in s_free:
                e.wait_ge(s, per * (m - 1))
        for c in range(NC3):
            for k in range(kb):
                mm = e.matmul(K.ps[:, 3 * (m % 2) + c, 0:NW], ring[:, slot, k, off:off + P],
                              rhs[:, k, NW * c:NW * c + NW], start=k == 0, stop=k == kb - 1)
        mm.then_inc(s_mm, 1)


def stage_proj_a(nc, K, xs, first, count):
    NS = 4
    ctx = ExitStack()
    tag = f"pj{first}"
    with ctx:
        ring = ctx.enter_context(nc.sbuf_tensor(tag + "_w", [P, NS, KD, P], F32))
        u = ctx.enter_context(nc.sbuf_tensor(tag + "_u", [P, 2, 1 + TP + DB * (DT + 1)], F32))
        dlt = ctx.enter_context(nc.sbuf_tensor(tag + "_d", [P, T], F32))
        block = ctx.enter_context(nc.Block())
        s_in = K.sems(tag + "_weights_in", NS)
        s_mm, s_raw, s_used = K.sem(tag + "_product"), K.sem(tag + "_raw_copied"), K.sem(tag + "_raw_used")
        shifted = first == 0

        @block.sync
        def _(e):
            for m in range(count):
                if m >= NS:
                    e.wait_ge(s_mm, m - NS + 1)
                at = 0
                pieces = BLOCKS[first + m]
                for c0, w in pieces:
                    e.dma_start(ring[:, m % NS, :, at:at + w],
                                K.d["w_in"][0, :, c0:c0 + w].rearrange("(k p) n -> p k n", p=P)).then_inc(s_in[m % NS], 16)
                    at += w

        @block.tensor
        def _(e):
            turns = {}
            for m in range(count):
                n = turns.get(m % NS, 0) + len(BLOCKS[first + m])
                turns[m % NS] = n
                K.turn[m] = n
            project(e, K, ring, s_in, s_mm, [(s_raw, 1)], count, KD, K.xn, lambda m: (m % NS, K.turn[m], 0, True))

        @block.scalar
        def _(e):
            for m in range(count):
                e.wait_ge(s_mm, m + 1)
                bank = K.ps[:, 3 * (m % 2):3 * (m % 2) + 3, :]
                if shifted:
                    if m >= 2:
                        e.wait_ge(s_used, m - 1)
                    for c in range(2):
                        e.activation(u[:, m % 2, 1 + NW * c:1 + NW * c + NW], bank[:, c, 0:NW], ACT.Copy)
                    e.activation(u[:, m % 2, 1 + 2 * NW:1 + TP], bank[:, 2, 0:TP - 2 * NW], ACT.Copy)
                    us = u[:, m % 2, 1 + TP:].rearrange("p (b t) -> p b t", t=DT + 1)
                    e.activation(us[:, :, 1:], bank[:, 2, TP - 2 * NW:NW].rearrange("p (b t) -> p b t", t=DT), ACT.Copy)
                else:
                    e.activation(xs[:, m, :].rearrange("p (c n) -> p c n", c=NC3), bank[:, :, 0:NW], ACT.Copy)
                if first + m < B_Q:
                    e.activation(K.utail[:, first + m, :], bank[:, 2, NW - TAIL:NW], ACT.Copy).then_inc(s_raw, 1)
                else:
                    e.drain().then_inc(s_raw, 1)

        if shifted:
            @block.vector
            def _(e):
                e.memset(u[:, 0, 0:1], 0.0)
                e.memset(u[:, 1, 0:1], 0.0)
                for m in range(count):
                    us = u[:, m % 2, 1 + TP:].rearrange("p (b t) -> p b t", t=DT + 1)
                    e.tensor_copy(us[:, :, 0:1], K.shT[:, m, :].unsqueeze(2))
                    e.wait_ge(s_raw, m + 1)
                    e.drain()
                    up = u[:, m % 2, 0:1 + TP]
                    e.tensor_tensor(dlt[:, 0:TP], up[:, 0:TP], up[:, 1:1 + TP], ALU.subtract)
                    e.tensor_tensor(dlt[:, TP:T].rearrange("p (b t) -> p b t", t=DT), us[:, :, 0:DT], us[:, :, 1:DT + 1],
                                    ALU.subtract)
                    e.drain()
                    e.scalar_tensor_tensor(xs[:, m, 0:TP], dlt[:, 0:TP], K.p("shift_mu", m), up[:, 1:1 + TP],
                                           ALU.mult, ALU.add)
                    e.scalar_tensor_tensor(xs[:, m, TP:T].rearrange("p (b t) -> p b t", t=DT),
                                           dlt[:, TP:T].rearrange("p (b t) -> p b t", t=DT), K.p("shift_mu", m),
                                           us[:, :, 1:DT + 1], ALU.mult, ALU.add).then_inc(s_used, 1)
                    e.drain()


def stage_rwkv_prep(nc, K, xs, ld):
    KK, A, L = K.oA, K.oB, K.oC
    ctx = ExitStack()
    with ctx:
        w2 = ctx.enter_context(nc.sbuf_tensor("rw_w2a2", [P, 512], F32))
        sq = ctx.enter_context(nc.sbuf_tensor("rw_sq", [P, T], F32))
        inv = ctx.enter_context(nc.sbuf_tensor("rw_inv", [P, T], F32))
        block = ctx.enter_context(nc.Block())
        s_w, s_th = K.sem("rw_lora_in"), K.sem("rw_tanh")
        s_z, s_sig = K.sem("rw_lora_product"), K.sem("rw_sigmoid")
        s_kk, s_sq, s_ss = K.sem("rw_kk_scaled"), K.sem("rw_kk_squared"), K.sem("rw_kk_summed")
        s_mx, s_rt = K.sem("rw_sum_guarded"), K.sem("rw_root")

        @block.sync
        def _(e):
            e.dma_start(w2[0:64, :], K.d["rwkv_w2"][0]).then_inc(s_w, 16)
            e.dma_start(w2[64:128, :], K.d["rwkv_a2"][0]).then_inc(s_w, 16)

        @block.scalar
        def _(e):
            e.activation(xs[0:64, B_WA, :], xs[0:64, B_WA, :], ACT.Tanh).then_inc(s_th, 1)
            for m in range(8):
                e.wait_ge(s_z, m + 1)
                dst = (ld if m < 4 else A)[:, m % 4, :].rearrange("p (c n) -> p c n", c=NC3)
                e.activation(dst, K.ps[:, 3 * (m % 2):3 * (m % 2) + 3, 0:NW], ACT.Sigmoid,
                             bias=K.p("rwkv_w0" if m < 4 else "rwkv_a0", m % 4)).then_inc(s_sig, 1)
            for c in range(4):
                e.wait_ge(s_kk, c + 1)
                if c >= 1:
                    e.wait_ge(s_ss, c)
                e.activation(sq[:, :], KK[:, c, :], ACT.Square).then_inc(s_sq, 1)
                e.wait_ge(s_mx, c + 1)
                e.activation(inv[:, :], inv[:, :], ACT.Sqrt).then_inc(s_rt, 1)

        @block.tensor
        def _(e):
            e.wait_ge(s_w, 32)
            e.wait_ge(s_th, 1)
            for m in range(8):
                o = 0 if m < 4 else 64
                if m >= 2:
                    e.wait_ge(s_sig, m - 1)
                for c in range(NC3):
                    mm = e.matmul(K.ps[:, 3 * (m % 2) + c, 0:NW], w2[o:o + 64, 128 * (m % 4):128 * (m % 4) + 128],
                                  xs[o:o + 64, B_WA, NW * c:NW * c + NW], start=True, stop=True)
                mm.then_inc(s_z, 1)
            e.wait_ge(s_sig, 8)
            for c in range(4):
                e.wait_ge(s_sq, c + 1)
                if c >= 1:
                    e.wait_ge(s_mx, c)
                for n in range(NC3):
                    mm = e.matmul(K.ps[:, n, 0:NW], K.c("headsum"), sq[:, NW * n:NW * n + NW], start=True, stop=True)
                mm.then_inc(s_ss, 1)

        @block.vector
        def _(e):
            for c in range(4):
                e.tensor_scalar(KK[:, c, :], xs[:, B_K + c, :], K.p("rwkv_kk", c), None, ALU.mult).then_inc(s_kk, 1)
            e.tensor_scalar(K.par[:, NPAR:NPAR + 4], K.par[:, PCOL["rwkv_ka"]:PCOL["rwkv_ka"] + 4], -1.0, 1.0,
                            ALU.mult, ALU.add)
            for c in range(4):
                e.wait_ge(s_sig, c + 1)
                e.tensor_scalar(ld[:, c, :], ld[:, c, :], -DECAY, None, ALU.mult)
                e.drain()
                e.tensor_tensor_scan(L[:, c, :], K.keep[:, :], ld[:, c, :], 0.0, ALU.mult, ALU.add)
            for c in range(4):
                e.wait_ge(s_ss, c + 1)
                e.tensor_scalar(inv[:, :].rearrange("p (c n) -> p c n", c=NC3), K.ps[:, 0:3, 0:NW], 1e-24, None,
                                ALU.max).then_inc(s_mx, 1)
                e.wait_ge(s_rt, c + 1)
                e.reciprocal(inv[:, :], inv[:, :])
                e.drain()
                e.tensor_tensor(KK[:, c, :], KK[:, c, :], inv[:, :], ALU.mult)
                e.drain()
                e.tensor_scalar(inv[:, :], A[:, c, :], K.p("rwkv_ka", c), K.par[:, NPAR + c:NPAR + c + 1],
                                ALU.mult, ALU.add)
                e.drain()
                e.tensor_tensor(xs[:, B_K + c, :], xs[:, B_K + c, :], inv[:, :], ALU.mult)
                e.tensor_tensor(A[:, c, :], A[:, c, :], KK[:, c, :], ALU.mult)
                e.drain()


def stage_rwkv_scan(nc, K, xs, ld, tag, n, levels, nchunk, tbase, S0, mid):
    KK, B, L = K.oA, K.oB, K.oC
    sample = tag == "S"
    ctx = ExitStack()
    with ctx:
        sb = lambda nm, sh: ctx.enter_context(nc.sbuf_tensor("sc" + tag + nm, sh, F32))
        D1, D2 = sb("D1", [P, 4, n]), sb("D2", [P, 4, n])
        EN = sb("EN", [P, 4, n])
        KtR = sb("KtR", [P, 4, 2, n])
        Bt, Kc, Vc = sb("Bt", [P, 4, n]), sb("Kc", [P, 4, n]), sb("Vc", [P, 4, n])
        fac = sb("fac", [P, 4])
        BtT, KcT, VT = sb("BtT", [n, 512]), sb("KcT", [n, 512]), sb("VT", [n, 512])
        MT, RBT, NT, RKT = (sb(x, [n, 8, n]) for x in ("MT", "RBT", "NT", "RKT"))
        X, XT, T1 = (sb(x, [n, 8, n]) for x in ("X", "XT", "T1"))
        Mn = [sb(f"Mn{z}", [n, 8, n]) for z in range(2 if sample else 1)]
        RH, SA = sb("RH", [n, 512]), sb("SA", [n, 512])
        if sample:
            KtB = sb("KtB", [P, 4, DB, TS])
            RB4 = sb("RB4", [P, 4, DB, TS])
            SAB = sb("SAB", [n, 2, DB, 64])
        block = ctx.enter_context(nc.Block())
        sem = lambda nm: K.sem(f"sc{tag}_{nm}")
        s_d, s_e = sem("exponents"), sem("decays")
        s_prep, s_vc = sem("operands"), sem("values_copied")
        s_tr, s_trc = sem("turned"), sem("turned_copied")
        s_ab, s_msk = sem("scores"), sem("scores_masked")
        s_mn, s_t1, s_t1c, s_z, s_x = sem("level_masked"), sem("level_half"), sem("level_half_copied"), sem("level_step"), sem("inverse_updated")
        s_rh, s_rhc, s_sa, s_sac = sem("rhs"), sem("rhs_copied"), sem("corrections"), sem("corrections_copied")
        s_y, s_yc, s_st, s_stu = sem("outputs"), sem("outputs_copied"), sem("state_sum"), sem("state_updated")
        NLV = levels - 1
        ps = K.ps
        bank = lambda h: 2 * (h % 2) + h // 4
        pos = lambda h: (h // 2) % 2

        def tok(i):
            return bass.ds(tbase + n * i, n) if not isinstance(i, int) else slice(tbase + n * i, tbase + n * i + n)

        def col(i, at):
            return bass.ds(tbase + n * i + at, 1) if not isinstance(i, int) else slice(tbase + n * i + at, tbase + n * i + at + 1)

        msk = lambda nm: K.c(nm + tag)[0:n, 0:n].unsqueeze(1)

        def mid_of(i):
            return L[:, :, col(i, mid)].to_broadcast([P, 4, n])

        @block.vector
        def _(e):
            for i in range(nchunk):
                if i >= 1:
                    e.wait_ge(s_e, 2 * i)
                if sample:
                    e.tensor_copy(D1[:, :, :], L[:, :, tok(i)])
                else:
                    e.tensor_tensor(D1[:, :, :], L[:, :, tok(i)], mid_of(i), ALU.subtract)
                e.drain()
                e.tensor_tensor(D2[:, :, :], D1[:, :, :], ld[:, :, tok(i)], ALU.subtract).then_inc(s_d, 1)
                e.wait_ge(s_e, 2 * i + 1)
                if i >= 1:
                    e.wait_ge(s_y, i)
                e.tensor_tensor(KtR[:, :, 0, :], KK[:, :, tok(i)], D2[:, :, :], ALU.mult)
                e.tensor_tensor(KtR[:, :, 1, :], xs[:, B_R:B_R + 4, tok(i)], D1[:, :, :], ALU.mult)
                e.tensor_tensor(Bt[:, :, :], B[:, :, tok(i)], EN[:, :, :], ALU.mult)
                e.tensor_tensor(Kc[:, :, :], xs[:, B_K:B_K + 4, tok(i)], EN[:, :, :], ALU.mult)
                if not sample:
                    e.tensor_tensor(fac[:, :].unsqueeze(2), L[:, :, col(i, n - 1)], L[:, :, col(i, mid)], ALU.subtract)
                    if i < nchunk - 1:
                        e.drain()
                        e.tensor_tensor(fac[:, :].unsqueeze(2), fac[:, :].unsqueeze(2), L[:, :, col(i + 1, mid)], ALU.add)
                e.drain().then_inc(s_prep, 1)
                if sample:
                    bc = K.c("batchcol").rearrange("p (b t) -> p b t", b=DB)
                    for q in range(4):
                        for dst, z in ((KtB, 0), (RB4, 1)):
                            e.tensor_tensor(dst[:, q, :, :], KtR[:, q, z, :].unsqueeze(1).to_broadcast([P, DB, TS]), bc, ALU.mult)
                    e.drain().then_inc(s_prep, 1)
                for h in range(8):
                    e.wait_ge(s_ab, 24 * i + 8)
                    v = ps[0:n, bank(h), :].rearrange("p (z n) -> p z n", z=2)[:, pos(h), 0:2 * n]
                    e.scalar_tensor_tensor(MT[:, h, :], v[:, 0:n], 3e38, K.c("strict" + tag)[0:n, 0:n], ALU.min, ALU.mult)
                    e.scalar_tensor_tensor(RBT[:, h, :], v[:, n:2 * n], 3e38, K.c("incl" + tag)[0:n, 0:n], ALU.min, ALU.mult).then_inc(s_msk, 1)
                for h in range(8):
                    e.wait_ge(s_ab, 24 * i + 16)
                    v = ps[0:n, 4 + bank(h), :].rearrange("p (z n) -> p z n", z=2)[:, pos(h), 0:2 * n]
                    e.scalar_tensor_tensor(NT[:, h, :], v[:, 0:n], 3e38, K.c("strict" + tag)[0:n, 0:n], ALU.min, ALU.mult)
                    e.scalar_tensor_tensor(RKT[:, h, :], v[:, n:2 * n], 3e38, K.c("incl" + tag)[0:n, 0:n], ALU.min, ALU.mult).then_inc(s_msk, 1)
                e.wait_ge(s_ab, 24 * i + 24)
                for z in range(2):
                    v = ps[0:n, z, 0:4 * n].rearrange("p (h n) -> p h n", h=4)
                    e.scalar_tensor_tensor(X[:, z::2, :], v, 3e38, msk("low0").to_broadcast([n, 4, n]), ALU.min, ALU.mult)
                e.tensor_tensor(XT[:, :, :], MT[:, :, :], msk("lvl0").to_broadcast([n, 8, n]), ALU.mult)
                e.drain()
                idn = K.c("ident")[0:n, 0:n].unsqueeze(1).to_broadcast([n, 8, n])
                e.tensor_tensor(X[:, :, :], idn, X[:, :, :], ALU.subtract)
                e.tensor_tensor(XT[:, :, :], idn, XT[:, :, :], ALU.subtract)
                e.drain().then_inc(s_x, 2)
                for l in range(NLV):
                    for z in range(2):
                        e.wait_ge(s_z, 2 * (NLV * i + l) + z + 1)
                        zz = ps[0:n, 2 + z, 0:4 * n].rearrange("p (h n) -> p h n", h=4)
                        e.tensor_tensor(X[:, 4 * z:4 * z + 4, :], X[:, 4 * z:4 * z + 4, :], zz, ALU.subtract)
                        zt = ps[0:n, 4 + z, 0:4 * n].rearrange("p (h n) -> p h n", h=4)
                        e.tensor_tensor(XT[:, 4 * z:4 * z + 4, :], XT[:, 4 * z:4 * z + 4, :], zt, ALU.subtract)
                        e.drain().then_inc(s_x, 1)
                e.wait_ge(s_sa, i + 1)
                e.tensor_copy(SA[:, :].rearrange("p (h z d) -> p h z d", z=2, d=64),
                              ps[0:n, 0:2, 0:256].rearrange("p z (h d) -> p h z d", d=64)).then_inc(s_sac, 1)
                if sample:
                    e.drain()
                    bm = K.c("batch")[0:n, :].unsqueeze(2).to_broadcast([n, DB, 64])
                    for h in range(8):
                        e.wait_ge(s_st, h) if h else None
                        e.tensor_tensor(SAB[:, 0, :, :], SA[:, 64 * h:64 * h + 64].unsqueeze(1).to_broadcast([n, DB, 64]), bm, ALU.mult)
                        e.tensor_tensor(SAB[:, 1, :, :], VT[:, 64 * h:64 * h + 64].unsqueeze(1).to_broadcast([n, DB, 64]), bm, ALU.mult)
                        e.drain().then_inc(s_sac, 1)
                        e.wait_ge(s_st, h + 1)
                        pp = 64 * (h % 2)
                        st = S0[pp:pp + 64, h // 2, :, :]
                        e.tensor_tensor(st, st, ps[pp:pp + 64, 4 + h % 2, :].rearrange("p (b d) -> p b d", b=DB), ALU.add)
                        e.drain()
                        e.tensor_tensor(st, st, D1[pp:pp + 64, h // 2, DT - 1::DT].unsqueeze(2).to_broadcast([64, DB, 64]), ALU.mult)
                        e.drain()
                else:
                    e.wait_ge(s_st, i + 1)
                    e.tensor_tensor(S0[:, :, :], S0[:, :, :], ps[:, 4, 0:256].rearrange("p (c d) -> p c d", c=4), ALU.add)
                    e.wait_ge(s_e, 2 * i + 2)
                    e.drain()
                    e.tensor_tensor(S0[:, :, :], S0[:, :, :], fac[:, :].unsqueeze(2).to_broadcast([P, 4, 64]), ALU.mult)
                    e.drain().then_inc(s_stu, 1)

        @block.scalar
        def _(e):
            for i in range(nchunk):
                e.wait_ge(s_d, i + 1)
                if i >= 1:
                    e.wait_ge(s_prep, i)
                e.activation(EN[:, :, :], D1[:, :, :], ACT.Exp, scale=-1.0)
                e.drain()
                e.activation(D1[:, :, :], D1[:, :, :], ACT.Exp)
                e.activation(D2[:, :, :], D2[:, :, :], ACT.Exp)
                e.drain().then_inc(s_e, 1)
                if sample:
                    e.wait_ge(s_prep, 1)
                else:
                    e.wait_ge(s_prep, i + 1)
                    e.activation(fac[:, :], fac[:, :], ACT.Exp).then_inc(s_e, 1)
                for z, dst in enumerate((BtT, KcT, VT)):
                    e.wait_ge(s_tr, 3 * i + z + 1)
                    e.activation(dst[:, :], ps[0:n, z, :], ACT.Copy).then_inc(s_trc, 1)
                for l in range(2 * NLV):
                    z = l % 2
                    e.wait_ge(s_t1, 2 * NLV * i + l + 1)
                    e.activation(T1[:, 4 * z:4 * z + 4, :], ps[0:n, z, 0:4 * n].rearrange("p (h n) -> p h n", h=4),
                                 ACT.Copy).then_inc(s_t1c, 1)
                e.wait_ge(s_rh, i + 1)
                e.activation(RH[:, :].rearrange("p (h z d) -> p h z d", z=2, d=64),
                             ps[0:n, 6:8, 0:256].rearrange("p z (h d) -> p h z d", d=64), ACT.Copy, scale=-1.0).then_inc(s_rhc, 1)
                e.wait_ge(s_y, i + 1)
                for z in range(2):
                    e.activation(KK[64 * z:64 * z + 64, :, tok(i)],
                                 ps[64 * z:64 * z + 64, 2 + z, 0:4 * n].rearrange("p (c n) -> p c n", c=4), ACT.Copy)
                e.drain().then_inc(s_yc, 1)

        @block.gpsimd
        def _(e):
            for i in range(nchunk):
                if i >= 1:
                    e.wait_ge(s_y, i)
                e.tensor_copy(Vc[:, :, :], xs[:, B_V:B_V + 4, tok(i)]).then_inc(s_vc, 1)
                e.wait_ge(s_msk, 16 * i + 8)
                for l in range(NLV):
                    if not sample:
                        if NLV * i + l >= 1:
                            e.wait_ge(s_t1, 2 * (NLV * i + l))
                    e.tensor_tensor(Mn[l % len(Mn)][:, :, :], MT[:, :, :], msk(f"lvl{l + 1}").to_broadcast([n, 8, n]),
                                    ALU.mult).then_inc(s_mn, 1)

        @block.tensor
        def _(e):
            ident = K.c("ident")
            for i in range(nchunk):
                e.wait_ge(s_prep, (2 if sample else 1) * (i + 1))
                e.wait_ge(s_vc, i + 1)
                if i >= 1:
                    e.wait_ge(s_stu, i)
                    e.wait_ge(s_yc, i)
                for z, src in enumerate((Bt, Kc, Vc)):
                    for c in range(4):
                        mm = e.transpose(ps[0:n, z, P * c:P * c + P], src[:, c, :], ident)
                    mm.then_inc(s_tr, 1)
                e.wait_ge(s_trc, 3 * i + 3)
                for src, b0 in ((Bt, 0), (Kc, 4)):
                    for h in range(8):
                        pp = 64 * (h % 2)
                        e.matmul(ps[0:n, b0 + bank(h), 256 * pos(h):256 * pos(h) + 2 * n], src[pp:pp + 64, h // 2, :],
                                 KtR[pp:pp + 64, h // 2, :, :].rearrange("p z n -> p (z n)"), start=True, stop=True).then_inc(s_ab, 1)
                e.wait_ge(s_msk, 16 * i + 8)
                for h in range(8):
                    pp = 64 * (h % 2)
                    e.matmul(ps[0:n, h % 2, n * (h // 2):n * (h // 2) + n], KtR[pp:pp + 64, h // 2, 0, :],
                             Bt[pp:pp + 64, h // 2, :], start=True, stop=True).then_inc(s_ab, 1)
                e.wait_ge(s_msk, 16 * i + 16)
                for l in range(NLV):
                    e.wait_ge(s_mn, NLV * i + l + 1)
                    for z in range(2):
                        e.wait_ge(s_x, 2 * ((NLV + 1) * i + l) + z + 1)
                        for h in range(4 * z, 4 * z + 4):
                            mm = e.matmul(ps[0:n, z, n * (h % 4):n * (h % 4) + n], Mn[l % len(Mn)][:, h, :], X[:, h, :], start=True, stop=True)
                        mm.then_inc(s_t1, 1)
                    for z in range(2):
                        e.wait_ge(s_t1c, 2 * (NLV * i + l) + z + 1)
                        for h in range(4 * z, 4 * z + 4):
                            e.matmul(ps[0:n, 2 + z, n * (h % 4):n * (h % 4) + n], XT[:, h, :], T1[:, h, :], start=True, stop=True)
                            mm = e.matmul(ps[0:n, 4 + z, n * (h % 4):n * (h % 4) + n], T1[:, h, :], XT[:, h, :], start=True, stop=True)
                        mm.then_inc(s_z, 1)
                e.wait_ge(s_x, 2 * (NLV + 1) * (i + 1))
                for h in range(8):
                    pp, hh = 64 * (h % 2), h // 2
                    o = ps[0:n, 6 + h % 2, 64 * hh:64 * hh + 64]
                    if sample:
                        for b in range(DB):
                            e.matmul(o, KtB[pp:pp + 64, hh, b, :], S0[pp:pp + 64, hh, b, :], start=b == 0, stop=False)
                    else:
                        e.matmul(o, KtR[pp:pp + 64, hh, 0, :], S0[pp:pp + 64, hh, :], start=True, stop=False)
                    mm = e.matmul(o, NT[:, h, :], VT[:, 64 * h:64 * h + 64], start=False, stop=True)
                mm.then_inc(s_rh, 1)
                e.wait_ge(s_rhc, i + 1)
                for h in range(8):
                    mm = e.matmul(ps[0:n, h % 2, 64 * (h // 2):64 * (h // 2) + 64], XT[:, h, :], RH[:, 64 * h:64 * h + 64],
                                  start=True, stop=True)
                mm.then_inc(s_sa, 1)
                e.wait_ge(s_sac, i + 1)
                for h in range(8):
                    pp, hh = 64 * (h % 2), h // 2
                    o = ps[pp:pp + 64, 2 + h % 2, n * hh:n * hh + n]
                    if sample:
                        for b in range(DB):
                            e.matmul(o, S0[pp:pp + 64, hh, b, :], RB4[pp:pp + 64, hh, b, :], start=b == 0, stop=False)
                    else:
                        e.matmul(o, S0[pp:pp + 64, hh, :], KtR[pp:pp + 64, hh, 1, :], start=True, stop=False)
                    e.matmul(o, SA[:, 64 * h:64 * h + 64], RBT[:, h, :], start=False, stop=False)
                    mm = e.matmul(o, VT[:, 64 * h:64 * h + 64], RKT[:, h, :], start=False, stop=True)
                mm.then_inc(s_y, 1)
                if sample:
                    for h in range(8):
                        pp = 64 * (h % 2)
                        e.wait_ge(s_sac, h + 2)
                        o = ps[pp:pp + 64, 4 + h % 2, :]
                        e.matmul(o, BtT[:, 64 * h:64 * h + 64], SAB[:, 0, :, :].rearrange("p b d -> p (b d)"), start=True, stop=False)
                        e.matmul(o, KcT[:, 64 * h:64 * h + 64], SAB[:, 1, :, :].rearrange("p b d -> p (b d)"), start=False, stop=True).then_inc(s_st, 1)
                else:
                    for h in range(8):
                        pp, hh = 64 * (h % 2), h // 2
                        o = ps[pp:pp + 64, 4, 64 * hh:64 * hh + 64]
                        e.matmul(o, BtT[:, 64 * h:64 * h + 64], SA[:, 64 * h:64 * h + 64], start=True, stop=False)
                        mm = e.matmul(o, KcT[:, 64 * h:64 * h + 64], VT[:, 64 * h:64 * h + 64], start=False, stop=True)
                    mm.then_inc(s_st, 1)


def stage_rwkv_states(nc, K, tag, S0, src, outs):
    nb = DB if tag == "S" else 1
    ctx = ExitStack()
    nm = f"st{tag}{'i' if src is not None else 'o'}"
    with ctx:
        rows = ctx.enter_context(nc.sbuf_tensor(nm + "rows", [64, nb, 8, 64], F32))
        low = ctx.enter_context(nc.sbuf_tensor(nm + "low", [64, nb, 8, 64], F32)) if outs is not None else None
        block = ctx.enter_context(nc.Block())
        s_in, s_t, s_c = K.sem(nm + "_in"), K.sem(nm + "_turned"), K.sem(nm + "_copied")
        s_low, s_out = K.sem(nm + "_lowered"), K.out_sem(nm + "_stored")
        st4 = S0 if tag == "S" else S0[:, :, :].unsqueeze(2)
        if src is not None:
            @block.sync
            def _(e):
                e.dma_start(rows[:, :, :, :], src.rearrange("b h i j -> i b h j")).then_inc(s_in, 16)

            @block.tensor
            def _(e):
                e.wait_ge(s_in, 16)
                for b in range(nb):
                    if b >= 2:
                        e.wait_ge(s_c, b - 1)
                    for h in range(8):
                        mm = e.transpose(K.ps[0:64, b % 2, 64 * h:64 * h + 64], rows[:, b, h, :], K.c("ident")[0:64, 0:64])
                    mm.then_inc(s_t, 1)

            @block.vector
            def _(e):
                for b in range(nb):
                    e.wait_ge(s_t, b + 1)
                    for z in range(2):
                        e.tensor_copy(st4[64 * z:64 * z + 64, :, b, :],
                                      K.ps[0:64, b % 2, :].rearrange("p (c z d) -> p c z d", z=2, d=64)[:, :, z, :])
                    e.drain().then_inc(s_c, 1)
        else:
            @block.tensor
            def _(e):
                e.wait_ge(s_low, 1)
                for b in range(nb):
                    if b >= 2:
                        e.wait_ge(s_c, b - 1)
                    for h in range(8):
                        mm = e.transpose(K.ps[0:64, b % 2, 64 * h:64 * h + 64], low[:, b, h, :], K.c("ident")[0:64, 0:64])
                    mm.then_inc(s_t, 1)

            @block.vector
            def _(e):
                for z in range(2):
                    for b in range(nb):
                        e.tensor_copy(low[:, b, z::2, :], st4[64 * z:64 * z + 64, :, b, :])
                e.drain().then_inc(s_low, 1)
                for b in range(nb):
                    e.wait_ge(s_t, b + 1)
                    e.tensor_copy(rows[:, b, :, :], K.ps[0:64, b % 2, :].rearrange("p (h d) -> p h d", h=8)).then_inc(s_c, 1)

            @block.sync
            def _(e):
                e.wait_ge(s_c, nb)
                e.dma_start(outs.rearrange("b h i j -> i b h j"), rows[:, :, :, :]).then_inc(s_out, 16)
                e.wait_ge(s_out, 16)


def stage_rwkv_out(nc, K, xs):
    Y = K.oA
    ctx = ExitStack()
    with ctx:
        g2 = ctx.enter_context(nc.sbuf_tensor("ro_g2", [P, 512], F32))
        sq = ctx.enter_context(nc.sbuf_tensor("ro_sq", [P, 2, T], F32))
        rt = ctx.enter_context(nc.sbuf_tensor("ro_root", [P, T], F32))
        block = ctx.enter_context(nc.Block())
        s_w, s_sg, s_mean, s_cen, s_sq = K.sem("ro_gate_w_in"), K.sem("ro_gate_sig"), K.sem("ro_means"), K.sem("ro_centred"), K.sem("ro_squared")
        s_rk, s_var, s_ve, s_rt, s_bon, s_g, s_fin = (K.sem("ro_" + x) for x in
                                                   ("rk", "variances", "variance_eps", "rooted", "bonus_sum", "gate", "final"))
        c3 = lambda ap: ap.rearrange("p (c n) -> p c n", c=NC3)

        @block.sync
        def _(e):
            e.dma_start(g2[:, :], K.d["rwkv_g2"][0]).then_inc(s_w, 16)

        @block.scalar
        def _(e):
            e.activation(xs[:, B_G, :], xs[:, B_G, :], ACT.Sigmoid).then_inc(s_sg, 1)
            for c in range(4):
                e.wait_ge(s_cen, c + 1)
                e.activation(sq[:, 0, :], Y[:, c, :], ACT.Square).then_inc(s_sq, 1)
                e.wait_ge(s_ve, c + 1)
                e.activation(rt[:, :], rt[:, :], ACT.Sqrt).then_inc(s_rt, 1)

        @block.tensor
        def _(e):
            hs = K.c("headsum")
            e.wait_ge(s_w, 16)
            for c in range(4):
                if c >= 1:
                    e.wait_ge(s_fin, c)
                for n in range(NC3):
                    mm = e.matmul(K.ps[:, n, 0:NW], hs, Y[:, c, NW * n:NW * n + NW], start=True, stop=True)
                mm.then_inc(s_mean, 1)
                e.wait_ge(s_rk, c + 1)
                for n in range(NC3):
                    mm = e.matmul(K.ps[:, 3 + n, 0:NW], hs, sq[:, 1, NW * n:NW * n + NW], start=True, stop=True)
                mm.then_inc(s_bon, 1)
                e.wait_ge(s_sq, c + 1)
                for n in range(NC3):
                    mm = e.matmul(K.ps[:, n, 0:NW], hs, sq[:, 0, NW * n:NW * n + NW], start=True, stop=True)
                mm.then_inc(s_var, 1)
                e.wait_ge(s_sg, 1)
                e.wait_ge(s_ve, c + 1)
                for n in range(NC3):
                    mm = e.matmul(K.ps[:, n, 0:NW], g2[:, P * c:P * c + P], xs[:, B_G, NW * n:NW * n + NW], start=True, stop=True)
                mm.then_inc(s_g, 1)

        @block.vector
        def _(e):
            for c in range(4):
                e.wait_ge(s_mean, c + 1)
                e.scalar_tensor_tensor(c3(Y[:, c, :]), K.ps[:, 0:3, 0:NW], -1.0 / 64, c3(Y[:, c, :]), ALU.mult, ALU.add).then_inc(s_cen, 1)
                e.tensor_tensor(sq[:, 1, :], xs[:, B_R + c, :], xs[:, B_K + c, :], ALU.mult)
                e.drain()
                e.tensor_scalar(sq[:, 1, :], sq[:, 1, :], K.p("rwkv_rk", c), None, ALU.mult).then_inc(s_rk, 1)
                e.wait_ge(s_var, c + 1)
                e.tensor_scalar(c3(rt[:, :]), K.ps[:, 0:3, 0:NW], 1.0 / 64, LNX_EPS, ALU.mult, ALU.add).then_inc(s_ve, 1)
                e.wait_ge(s_bon, c + 1)
                e.tensor_tensor(c3(xs[:, B_V + c, :]), c3(xs[:, B_V + c, :]), K.ps[:, 3:6, 0:NW], ALU.mult)
                e.wait_ge(s_rt, c + 1)
                e.reciprocal(rt[:, :], rt[:, :])
                e.drain()
                e.tensor_tensor(Y[:, c, :], Y[:, c, :], rt[:, :], ALU.mult)
                e.drain()
                e.tensor_scalar(Y[:, c, :], Y[:, c, :], K.p("rwkv_lnx_g", c), K.p("rwkv_lnx_b", c), ALU.mult, ALU.add)
                e.drain()
                e.tensor_tensor(Y[:, c, :], Y[:, c, :], xs[:, B_V + c, :], ALU.add)
                e.drain()
                e.wait_ge(s_g, c + 1)
                e.tensor_tensor(c3(Y[:, c, :]), c3(Y[:, c, :]), K.ps[:, 0:3, 0:NW], ALU.mult)
                e.drain().then_inc(s_fin, 1)


def stage_move(nc, K, name, dst, src):
    with nc.Block() as block:
        s_moved = K.sem(name)

        @block.sync
        def _(e):
            e.dma_start(dst, src).then_inc(s_moved, 16)
            e.wait_ge(s_moved, 16)


def stage_tail_rows(nc, K):
    ctx = ExitStack()
    with ctx:
        rows = ctx.enter_context(nc.sbuf_tensor("tail_rows", [TAIL, B_Q, P], F32))
        block = ctx.enter_context(nc.Block())
        s_t, s_c, s_out = K.sem("tail_turned"), K.sem("tail_copied"), K.out_sem("tail_stored")

        @block.tensor
        def _(e):
            for b in range(B_Q):
                mm = e.transpose(K.ps[0:TAIL, b // 4, P * (b % 4):P * (b % 4) + P], K.utail[:, b, :], K.c("ident"))
            mm.then_inc(s_t, 1)

        @block.vector
        def _(e):
            e.wait_ge(s_t, 1)
            e.tensor_copy(rows[:, :, :].rearrange("p b n -> p (b n)"),
                          K.ps[0:TAIL, 0:5, :].rearrange("p a n -> p (a n)")[:, 0:B_Q * P]).then_inc(s_c, 1)

        @block.sync
        def _(e):
            n = 0
            e.wait_ge(s_c, 1)
            for b in range(NSHIFT):
                at = 0
                for c0, w in BLOCKS[b]:
                    e.dma_start(K.d["p_state_shift"][0, :, c0:c0 + w], rows[14:15, b, at:at + w]).then_inc(s_out, 16)
                    e.dma_start(K.d["s_state_shift"][0, :, c0:c0 + w], rows[15 + DT - 1:TAIL:DT, b, at:at + w]).then_inc(s_out, 16)
                    at += w
                    n += 2
            e.dma_start(K.d["p_state_pool"][0, 0].rearrange("t (b n) -> t b n", n=P), rows[0:15, B_POOL:B_Q, :]).then_inc(s_out, 16)
            e.dma_start(K.d["s_state_pool"][0, :, 0:15 - DT, :], K.d["state_pool"][0, :, DT:15, :]).then_inc(s_out, 16)
            for b in range(DB):
                e.dma_start(K.d["s_state_pool"][0, b, 15 - DT:15, :].rearrange("t (b n) -> t b n", n=P),
                            rows[15 + DT * b:15 + DT * b + DT, B_POOL:B_Q, :]).then_inc(s_out, 16)
            n += 2 + DB
            e.wait_ge(s_out, 16 * n)


def stage_pool(nc, K, up):
    ctx = ExitStack()
    with ctx:
        sb = lambda nm, sh: ctx.enter_context(nc.sbuf_tensor("po_" + nm, sh, F32))
        srow = sb("state", [DB * 15, 512])
        pw = sb("w", [P, 4, P])
        EP, ES = sb("ext", [P, 4, 15 + TP]), sb("exts", [P, 4, DB, 15 + DT])
        TPp, TSs = sb("sums", [P, 2, 15 + TP]), sb("sumss", [P, 2, DB, 15 + DT])
        dd = sb("diff", [P, 4, T])
        block = ctx.enter_context(nc.Block())
        s_in, s_t, s_cp, s_c2 = K.sem("po_in"), K.sem("po_turned"), K.sem("po_extended"), K.sem("po_state_copied")
        s_d, s_z, s_w = K.sem("po_differences"), K.sem("po_mapped"), K.sem("po_scaled")

        @block.sync
        def _(e):
            e.dma_start(srow[:, :], K.d["state_pool"][0].rearrange("b t n -> (b t) n")).then_inc(s_in, 16)
            e.dma_start(pw[:, :, :], K.d["pool_w"][0].rearrange("g c n -> c g n")).then_inc(s_in, 16)

        @block.scalar
        def _(e):
            e.activation(EP[:, :, 15:], up[:, :, 0:TP], ACT.Copy)
            for g in range(4):
                e.activation(ES[:, g, :, 15:], up[:, g, TP:T].rearrange("p (b t) -> p b t", t=DT), ACT.Copy)
            e.drain().then_inc(s_cp, 1)
            for g in range(4):
                e.wait_ge(s_z, g + 1)
                e.activation(K.oB[:, g, :].rearrange("p (c n) -> p c n", c=NC3),
                             K.ps[:, 3 * (g % 2):3 * (g % 2) + 3, 0:NW], ACT.Copy, scale=K.p("pool_scale", g)).then_inc(s_w, 1)

        @block.tensor
        def _(e):
            e.wait_ge(s_in, 32)
            for g in range(4):
                mm = e.transpose(K.ps[:, 7, 120 * g:120 * g + 120], srow[:, P * g:P * g + P], K.c("ident")[0:120, 0:120])
            mm.then_inc(s_t, 1)
            for g in range(4):
                e.wait_ge(s_d, g + 1)
                if g >= 2:
                    e.wait_ge(s_w, g - 1)
                for c in range(NC3):
                    mm = e.matmul(K.ps[:, 3 * (g % 2) + c, 0:NW], pw[:, g, :], dd[:, g, NW * c:NW * c + NW], start=True, stop=True)
                mm.then_inc(s_z, 1)

        @block.vector
        def _(e):
            e.memset(EP[:, :, 0:15], 0.0)
            e.wait_ge(s_t, 1)
            for g in range(4):
                e.tensor_copy(ES[:, g, :, 0:15], K.ps[:, 7, 120 * g:120 * g + 120].rearrange("p (b t) -> p b t", t=15))
            e.wait_ge(s_cp, 1)
            e.drain()
            LP, LS = 15 + TP, 15 + DT
            for g in range(4):
                a, s = EP[:, g, :], ES[:, g, :, :]
                for l in range(g + 1):
                    w, o = 1 << l, (2 << l) - 1
                    e.tensor_tensor(TPp[:, l % 2, o:LP], a[:, o:LP], a[:, o - w:LP - w], ALU.add)
                    e.tensor_tensor(TSs[:, l % 2, :, o:LS], s[:, :, o:LS], s[:, :, o - w:LS - w], ALU.add)
                    e.drain()
                    a, s = TPp[:, l % 2, :], TSs[:, l % 2, :, :]
                inv = 1.0 / (2 << g)
                e.scalar_tensor_tensor(dd[:, g, 16:TP], a[:, 31:LP], inv, EP[:, g, 31:LP], ALU.mult, ALU.subtract)
                e.tensor_tensor(dd[:, g, 0:16], a[:, 15:31], K.c("poolcnt")[:, 16 * g:16 * g + 16], ALU.mult)
                e.scalar_tensor_tensor(dd[:, g, TP:T].rearrange("p (b t) -> p b t", t=DT), s[:, :, 15:], inv,
                                       ES[:, g, :, 15:], ALU.mult, ALU.subtract)
                e.drain()
                e.tensor_tensor(dd[:, g, 0:16], dd[:, g, 0:16], EP[:, g, 15:31], ALU.subtract)
                e.drain().then_inc(s_d, 1)


def stage_head_rms(nc, K, name, q, nblk, mask, width, gain, scale):
    ctx = ExitStack()
    with ctx:
        sq = ctx.enter_context(nc.sbuf_tensor(name + "_sq", [P, 2, T], F32))
        rt = ctx.enter_context(nc.sbuf_tensor(name + "_root", [P, 2, T], F32))
        block = ctx.enter_context(nc.Block())
        s_sq, s_sum, s_me, s_rt = (K.sem(f"{name}_{x}") for x in ("squared", "summed", "mean", "rooted"))

        @block.scalar
        def _(e):
            def squares(c):
                if c >= 2:
                    e.wait_ge(s_sum, c - 1)
                e.activation(sq[:, c % 2, :], q[:, c, :], ACT.Square).then_inc(s_sq, 1)
            squares(0)
            for c in range(nblk):
                if c + 1 < nblk:
                    squares(c + 1)
                e.wait_ge(s_me, c + 1)
                e.activation(rt[:, c % 2, :], rt[:, c % 2, :], ACT.Sqrt).then_inc(s_rt, 1)

        @block.tensor
        def _(e):
            for c in range(nblk):
                e.wait_ge(s_sq, c + 1)
                if c >= 2:
                    e.wait_ge(s_me, c - 1)
                for n in range(NC3):
                    mm = e.matmul(K.ps[:, 3 * (c % 2) + n, 0:NW], K.c(mask), sq[:, c % 2, NW * n:NW * n + NW], start=True, stop=True)
                mm.then_inc(s_sum, 1)

        @block.vector
        def _(e):
            for c in range(nblk):
                e.wait_ge(s_sum, c + 1)
                e.tensor_scalar(rt[:, c % 2, :].rearrange("p (c n) -> p c n", c=NC3), K.ps[:, 3 * (c % 2):3 * (c % 2) + 3, 0:NW],
                                1.0 / width / scale ** 2, RMS_EPS / scale ** 2, ALU.mult, ALU.add).then_inc(s_me, 1)
                e.wait_ge(s_rt, c + 1)
                e.reciprocal(rt[:, c % 2, :], rt[:, c % 2, :])
                e.drain()
                e.scalar_tensor_tensor(q[:, c, :], q[:, c, :], K.p(gain, 0), rt[:, c % 2, :], ALU.mult, ALU.mult)
                e.drain()


def stage_kv(nc, K, kvt):
    ctx = ExitStack()
    with ctx:
        w = ctx.enter_context(nc.sbuf_tensor("kv_w", [P, KD, KVG], F32))
        kg = ctx.enter_context(nc.sbuf_tensor("kv_gain", [P, 2, 64], F32))
        sq = ctx.enter_context(nc.sbuf_tensor("kv_sq", [P, 2, 8, 2, 64], F32))
        ss = ctx.enter_context(nc.sbuf_tensor("kv_ss", [P, 2, 2, 16], F32))
        block = ctx.enter_context(nc.Block())
        s_in, s_g, s_mm, s_cp = K.sem("kv_w_in"), K.sem("kv_gain_in"), K.sem("kv_product"), K.sem("kv_copied")
        s_v, s_r, s_k, s_out = K.sem("kv_mean"), K.sem("kv_rooted"), K.sem("kv_normed"), K.out_sem("kv_stored")
        HW = KVG // 2

        @block.sync
        def _(e):
            for k in range(KD):
                e.dma_start(w[:, k, :], K.d["w_in"][0, P * k:P * k + P, OFF_KV:OFF_KV + KVG]).then_inc(s_in, 16)
            e.dma_start(kg[:, :, :], K.d["nsa_k_g"][0, 1:3, :].partition_broadcast(P)).then_inc(s_g, 16)
            e.wait_ge(s_k, 1)
            pr = lambda name: K.d[name][0, 0].rearrange("(i p) g d -> p i (g d)", p=P)
            n = 0
            for z, nm in enumerate(("cmp_k", "cmp_v", "slc_k", "slc_v", "win_k", "win_v")):
                lo = NTI - 4 if z >= 4 else 0
                e.dma_start(pr("p_" + nm), kvt[:, lo:NTI, P * z:P * z + P]).then_inc(s_out, 16)
                n += 1
                if z < 4:
                    e.dma_start(K.d["s_" + nm][0].rearrange("b t g d -> (b t) (g d)"), kvt[0:TS, NTI, P * z:P * z + P]).then_inc(s_out, 16)
                    n += 1
                else:
                    e.dma_start(K.d["s_" + nm][0, :, 0:512 - DT], K.d["cache_" + nm][0, :, DT:512]).then_inc(s_out, 16)
                    n += 1
                    for b in range(DB):
                        e.dma_start(K.d["s_" + nm][0, b, 512 - DT:512].rearrange("t g d -> t (g d)"),
                                    kvt[DT * b:DT * b + DT, NTI, P * z:P * z + P]).then_inc(s_out, 16)
                        n += 1
            e.wait_ge(s_out, 16 * n)

        @block.tensor
        def _(e):
            e.wait_ge(s_in, 16 * KD)
            for i in range(NTI + 1):
                n = P if i < NTI else TS
                if i >= 3:
                    e.wait_ge(s_cp, i - 2)
                for z in range(2):
                    for k in range(KD):
                        mm = e.matmul(K.ps[0:n, 2 * (i % 3) + z, 0:HW], K.xn[:, k, P * i:P * i + n], w[:, k, HW * z:HW * z + HW],
                                      start=k == 0, stop=k == KD - 1)
                mm.then_inc(s_mm, 1)

        @block.scalar
        def _(e):
            for i in range(NTI + 1):
                n = P if i < NTI else TS
                e.wait_ge(s_mm, i + 1)
                e.activation(kvt[0:n, i, :].rearrange("p (z n) -> p z n", z=2),
                             K.ps[0:n, 2 * (i % 3):2 * (i % 3) + 2, 0:HW], ACT.Copy).then_inc(s_cp, 1)
            for z in range(2):
                e.wait_ge(s_v, z + 1)
                m, cnt = (P, 16) if z == 0 else (TS, 2)
                e.activation(ss[0:m, z, :, 0:cnt], ss[0:m, z, :, 0:cnt], ACT.Sqrt).then_inc(s_r, 1)
            e.activation(kvt[:, 0:NTI, 768:KVG], kvt[:, 0:NTI, 768:KVG], ACT.Sigmoid)
            e.activation(kvt[0:TS, NTI, 768:KVG], kvt[0:TS, NTI, 768:KVG], ACT.Sigmoid)

        @block.vector
        def _(e):
            e.wait_ge(s_cp, NTI + 1)
            e.wait_ge(s_g, 16)
            for z, (m, lo, hi) in enumerate(((P, 0, NTI), (TS, NTI, NTI + 1))):
                nt = hi - lo
                for s in range(2):
                    kk = kvt[0:m, lo:hi, 256 + 256 * s:384 + 256 * s].rearrange("p i (g d) -> p i g d", g=2)
                    e.tensor_tensor(sq[0:m, s, 0:nt, :, :], kk, kk, ALU.mult)
                    e.drain()
                    e.tensor_reduce(ss[0:m, z, s, 0:2 * nt], sq[0:m, s, 0:nt, :, :].rearrange("p i g d -> p (i g) d"), AX.X, ALU.add)
                e.drain()
                e.tensor_scalar(ss[0:m, z, :, 0:2 * nt], ss[0:m, z, :, 0:2 * nt], 1.0 / 64, RMS_EPS, ALU.mult, ALU.add).then_inc(s_v, 1)
                e.wait_ge(s_r, z + 1)
                e.reciprocal(ss[0:m, z, :, 0:2 * nt], ss[0:m, z, :, 0:2 * nt])
                e.drain()
                for s in range(2):
                    kk = kvt[0:m, lo:hi, 256 + 256 * s:384 + 256 * s].rearrange("p i (g d) -> p i g d", g=2)
                    e.tensor_tensor(kk, kk, ss[0:m, z, s, 0:2 * nt].rearrange("p (i g) -> p i g", g=2).unsqueeze(3).to_broadcast([m, nt, 2, 64]), ALU.mult)
                    e.drain()
                    gb = kg[0:m, s, :].unsqueeze(1).to_broadcast([m, 2 * nt, 64])
                    for i in range(lo, hi):
                        k2 = kvt[0:m, i, 256 + 256 * s:384 + 256 * s].rearrange("p (g d) -> p g d", g=2)
                        e.tensor_tensor(k2, k2, kg[0:m, s, :].unsqueeze(1).to_broadcast([m, 2, 64]), ALU.mult)
            e.drain().then_inc(s_k, 1)


def stage_bias(nc, K, near, cb, b31):
    ctx = ExitStack()
    with ctx:
        rb = ctx.enter_context(nc.sbuf_tensor("bi_rel", [33, 8], F32))
        oh = ctx.enter_context(nc.sbuf_tensor("bi_onehot", [33, BVL], F32))
        bv = ctx.enter_context(nc.sbuf_tensor("bi_vector", [8, BVL], F32))
        block = ctx.enter_context(nc.Block())
        s_in, s_ms, s_mm, s_c, s_d, s_t, s_fl = (K.sem("bi_" + x) for x in (
            "in", "neg_set", "spread", "copied", "stored", "tiles_in", "tiles_flipped"))
        W = BVL // 7

        @block.sync
        def _(e):
            e.dma_start(oh[:, :], K.d["onehot"]).then_inc(s_in, 16)
            e.wait_ge(s_ms, 1)
            e.dma_start(rb[0:32, :], K.d["rel_bias"]).then_inc(s_in, 16)
            e.dma_start(b31[:, :], K.d["rel_bias"][31, :].partition_broadcast(P)).then_inc(s_t, 16)
            e.wait_ge(s_c, 1)
            e.dma_start(K.bvec, bv[:, :]).then_inc(s_d, 16)
            e.wait_ge(s_d, 16)
            v = K.bvec.tensor
            for h in range(8):
                e.dma_start(near[:, h, :], bass.AP(tensor=v, offset=h * BVL + REV - 2 * P + 1, ap=[[1, P], [1, 2 * P]])).then_inc(s_t, 16)
                e.dma_start(cb[:, h, :], bass.AP(tensor=v, offset=h * BVL + REV + 63 - 64 * 14 - P + 1, ap=[[1, P], [64, 30]]),
                            allow_slow_non_contiguous=True).then_inc(s_t, 16)

        @block.vector
        def _(e):
            e.memset(rb[:, :], NEG).then_inc(s_ms, 1)
            e.wait_ge(s_mm, 1)
            e.tensor_copy(bv[:, :].rearrange("p (z n) -> p z n", z=7), K.ps[0:8, 0:7, 0:W]).then_inc(s_c, 1)
            e.wait_ge(s_fl, 1)
            e.tensor_copy(near[:, :, :].rearrange("p (a h) n -> p a (h n)", h=2), K.ps[:, 0:4, :])
            e.tensor_copy(cb[:, :, :].rearrange("p h n -> p (h n)"), K.ps[:, 4, 0:240])

        @block.tensor
        def _(e):
            e.wait_ge(s_in, 32)
            for z in range(7):
                mm = e.matmul(K.ps[0:8, z, 0:W], rb[:, :], oh[:, W * z:W * z + W], start=True, stop=True)
            mm.then_inc(s_mm, 1)
            e.wait_ge(s_t, 16 * 17)
            e.wait_ge(s_c, 1)
            for a in range(4):
                e.matmul(K.ps[:, a, :], K.c("flip"), near[:, 2 * a:2 * a + 2, :].rearrange("p h n -> p (h n)"), start=True, stop=True)
            e.matmul(K.ps[:, 4, 0:240], K.c("flip"), cb[:, :, :].rearrange("p h n -> p (h n)"), start=True, stop=True).then_inc(s_fl, 1)


def stage_nsa_keys(nc, K, kvt, kcd, vc, ksd, kwd, ksn, kwn):
    ctx = ExitStack()
    with ctx:
        kc = ctx.enter_context(nc.sbuf_tensor("nk_kc", [P, 16], F32))
        sq = ctx.enter_context(nc.sbuf_tensor("nk_sq", [P, 16], F32))
        rt = ctx.enter_context(nc.sbuf_tensor("nk_rt", [P, 16], F32))
        block = ctx.enter_context(nc.Block())
        s_t, s_c, s_new, s_m, s_sq, s_s, s_v, s_r = (K.sem("nk_" + x) for x in (
            "turned", "copied", "new_turned", "means", "squared", "summed", "mean_sq", "rooted"))
        CUT = ((0, 0), (1, 1))

        @block.tensor
        def _(e):
            blk, ident = K.c("blk"), K.c("ident")
            for i in range(NTI):
                e.matmul(K.ps[:, 4, 2 * i:2 * i + 2], kvt[:, i, 0:P], blk[:, 30:32], start=True, stop=True)
            for i in range(NTI):
                mm = e.matmul(K.ps[0:16, 5, 0:P], blk[:, 30 - 2 * i:46 - 2 * i], kvt[:, i, P:2 * P], start=i == 0, stop=i == NTI - 1)
            mm.then_inc(s_m, 1)
            for z in range(4):
                for i in range(4):
                    mm = e.transpose(K.ps[:, z, P * i:P * i + P], kvt[:, 4 * (z % 2) + i, 256 + 256 * (z // 2):384 + 256 * (z // 2)], ident)
                mm.then_inc(s_t, 1)
            e.transpose(K.ps[:, 6, 0:TS], kvt[0:TS, NTI, 256:384], ident[0:TS, 0:TS])
            e.transpose(K.ps[:, 6, TS:2 * TS], kvt[0:TS, NTI, 512:640], ident[0:TS, 0:TS]).then_inc(s_new, 1)
            e.wait_ge(s_sq, 1)
            e.matmul(K.ps[:, 7, 0:16], K.c("headsum"), sq[:, :], start=True, stop=True).then_inc(s_s, 1)

        @block.scalar
        def _(e):
            e.wait_ge(s_v, 1)
            e.activation(rt[:, :], rt[:, :], ACT.Sqrt).then_inc(s_r, 1)
            for z in range(4):
                e.wait_ge(s_t, z + 1)
                dst = (ksd, kwd)[z // 2]
                cs = slice(512 * (z % 2), 512 * (z % 2) + 512)
                e.activation(dst[0:64, 0, cs], K.ps[0:64, z, :], ACT.Copy)
                e.activation(dst[64:128, 0, cs], K.ps[0:64, z, :], ACT.Copy).then_inc(s_c, 1)

        @block.vector
        def _(e):
            e.wait_ge(s_m, 1)
            e.tensor_copy(kc[:, :], K.ps[:, 4, 0:16])
            e.tensor_copy(vc[:, :], K.ps[0:16, 5, 0:P])
            e.drain()
            e.tensor_tensor(sq[:, :], kc[:, :], kc[:, :], ALU.mult).then_inc(s_sq, 1)
            e.wait_ge(s_s, 1)
            e.tensor_scalar(rt[:, :], K.ps[:, 7, 0:16], 1.0 / 64, RMS_EPS, ALU.mult, ALU.add).then_inc(s_v, 1)
            e.wait_ge(s_r, 1)
            e.reciprocal(rt[:, :], rt[:, :])
            e.drain()
            e.scalar_tensor_tensor(kc[:, :], kc[:, :], K.p("kg_cmp", 0), rt[:, :], ALU.mult, ALU.mult)
            e.drain()
            for g in range(2):
                for half in range(2):
                    e.tensor_copy(kcd[64 * half:64 * half + 64, g, :], kc[64 * g:64 * g + 64, :])
            for z in range(4):
                e.wait_ge(s_t, z + 1)
                e.wait_ge(s_c, z + 1)
                dst = (ksd, kwd)[z // 2]
                cs = slice(512 * (z % 2), 512 * (z % 2) + 512)
                e.tensor_copy(dst[0:64, 1, cs], K.ps[64:128, z, :])
                e.tensor_copy(dst[64:128, 1, cs], K.ps[64:128, z, :])
            e.wait_ge(s_new, 1)
            e.tensor_copy(ksn[:, :], K.ps[:, 6, 0:TS])
            e.tensor_copy(kwn[:, :], K.ps[:, 6, TS:2 * TS])


def stage_nsa_prompt(nc, K, qT, kvt, kcd, vc, ksd, kwd, near, cb, b31):
    units = [(i, h) for i in range(NTI) for h in range(8)]
    NU = len(units)
    SW = TP + 5 * P + 16
    win = lambda i: list(range(max(0, i - 4), i + 1))
    cols = lambda i: (P * (i + 1), P * len(win(i)))

    def blocks(i):
        return [("s", j) for j in range(i + 1)] + [("w", j) for j in win(i)] + [("c", 0)]

    groups = lambda i: [blocks(i)[a:a + 4] for a in range(0, len(blocks(i)), 4)]
    gbase = [0]
    for i, h in units:
        gbase.append(gbase[-1] + len(groups(i)))
    ctx = ExitStack()
    with ctx:
        sb = lambda nm, sh: ctx.enter_context(nc.sbuf_tensor("np_" + nm, sh, F32))
        S = sb("scores", [P, 2, SW])
        nm = sb("negmax", [P, 2, 3])
        sm = sb("sums", [P, 2, 3])
        PT = sb("probsT", [P, 2, 512])
        co = sb("coef", [P, 2, 3])
        O = sb("out", [P, 2, 512])
        block = ctx.enter_context(nc.Block())
        s_s, s_ev, s_mx, s_ex = K.sem("np_scores"), K.sem("np_scores_out"), K.sem("np_max"), K.sem("np_exps")
        s_cm, s_pt, s_pc, s_o, s_oc = K.sem("np_masked"), K.sem("np_turned"), K.sem("np_turned_copied"), K.sem("np_values"), K.sem("np_combined")
        s_ot, s_oe = K.sem("np_out_turned"), K.sem("np_out_copied")

        def col_of(i, kind, j):
            return {"s": P * j, "w": TP + P * (j - win(i)[0]), "c": TP + 5 * P}[kind]

        @block.tensor
        def _(e):
            ident = K.c("ident")

            def scores(u):
                i, h = units[u]
                g, pp, c = h // 4, 64 * (h % 2), h // 2
                q = qT[pp:pp + 64, c, P * i:P * i + P]
                if u >= 1:
                    e.wait_ge(s_ev, u)
                ns, nw = cols(i)
                for a in range(0, ns, 512):
                    e.matmul(K.ps[:, a // 512, 0:min(512, ns - a)], q, ksd[pp:pp + 64, g, a:min(a + 512, ns)], start=True, stop=True)
                lo = P * win(i)[0]
                for a in range(0, nw, 512):
                    e.matmul(K.ps[:, 2 + a // 512, 0:min(512, nw - a)], q, kwd[pp:pp + 64, g, lo + a:lo + min(a + 512, nw)], start=True, stop=True)
                e.matmul(K.ps[:, 3, 256:272], q, kcd[pp:pp + 64, g, :], start=True, stop=True).then_inc(s_s, 1)

            def values(u):
                i, h = units[u]
                g = h // 4
                e.wait_ge(s_ex, u + 1)
                e.wait_ge(s_cm, u + 1)
                if u >= 2:
                    e.wait_ge(s_oc, u - 1)
                gs = groups(i)
                seen = set()

                def turn(n):
                    G = gbase[u] + n
                    if G >= 2:
                        e.wait_ge(s_pc, G - 1)
                    for z, (kind, j) in enumerate(gs[n]):
                        a = col_of(i, kind, j)
                        m = 16 if kind == "c" else P
                        mm = e.transpose(K.ps[0:m, 4 + G % 2, P * z:P * z + P], S[:, u % 2, a:a + m], ident)
                    mm.then_inc(s_pt, 1)

                turn(0)
                for n in range(len(gs)):
                    if n + 1 < len(gs):
                        turn(n + 1)
                    G = gbase[u] + n
                    e.wait_ge(s_pc, G + 1)
                    for z, (kind, j) in enumerate(gs[n]):
                        b = "swc".index(kind)
                        m = 16 if kind == "c" else P
                        v = vc[:, 64 * g:64 * g + 64] if kind == "c" else \
                            kvt[:, j, (384 if kind == "s" else 640) + 64 * g:(384 if kind == "s" else 640) + 64 * g + 64]
                        last = kind == "c" or j == i
                        mm = e.matmul(K.ps[:, 6 + u % 2, 64 * b:64 * b + 64], PT[0:m, G % 2, P * z:P * z + P], v,
                                      start=kind not in seen, stop=last)
                        seen.add(kind)
                mm.then_inc(s_o, 1)

            def turn_out(i):
                e.wait_ge(s_oc, 8 * i + 8)
                e.wait_ge(s_pc, gbase[8 * i + 8])
                if i == NTI - 1:
                    pass
                for c in range(4):
                    mm = e.transpose(K.ps[:, 7, P * c:P * c + P], O[:, i % 2, P * c:P * c + P], ident)
                mm.then_inc(s_ot, 1)
                e.wait_ge(s_oe, i + 1)

            scores(0)
            for u in range(NU):
                if u + 1 < NU:
                    scores(u + 1)
                values(u)
                if units[u][1] == 7:
                    turn_out(units[u][0])

        @block.vector
        def _(e):
            def softmax_in(u):
                i, h = units[u]
                b = u % 2
                e.wait_ge(s_s, u + 1)
                if u >= 2:
                    e.wait_ge(s_o, u - 1)
                ns, nw = cols(i)
                far = ns - 2 * P
                if far > 0:
                    e.tensor_scalar(S[:, b, 0:far], K.ps[:, 0:2, :].rearrange("p a n -> p (a n)")[:, 0:far], b31[:, h:h + 1], None, ALU.add)
                lo = max(far, 0)
                e.tensor_tensor(S[:, b, lo:ns], K.ps[:, 0:2, :].rearrange("p a n -> p (a n)")[:, lo:ns], near[:, h, 2 * P - (ns - lo):], ALU.add)
                pw = K.ps[:, 2:4, :].rearrange("p a n -> p (a n)")
                at = 0
                if i >= 4:
                    e.scalar_tensor_tensor(S[:, b, TP:TP + P], pw[:, 0:P], b31[:, h:h + 1], K.c("edge"), ALU.add, ALU.add)
                    at = P
                if nw - 2 * P > at:
                    e.tensor_scalar(S[:, b, TP + at:TP + nw - 2 * P], pw[:, at:nw - 2 * P], b31[:, h:h + 1], None, ALU.add)
                lo = max(nw - 2 * P, 0)
                e.tensor_tensor(S[:, b, TP + lo:TP + nw], pw[:, lo:nw], near[:, h, 2 * P - (nw - lo):], ALU.add)
                e.tensor_tensor(S[:, b, TP + 5 * P:SW], pw[:, 768:784], cb[:, h, 14 - 2 * i:30 - 2 * i], ALU.add).then_inc(s_ev, 1)
                e.drain()
                e.tensor_reduce(nm[:, b, 0:1], S[:, b, 0:ns], AX.X, ALU.max, negate=True)
                e.tensor_reduce(nm[:, b, 1:2], S[:, b, TP:TP + nw], AX.X, ALU.max, negate=True)
                e.tensor_reduce(nm[:, b, 2:3], S[:, b, TP + 5 * P:SW], AX.X, ALU.max, negate=True)
                e.drain().then_inc(s_mx, 1)

            def combine(u):
                i, h = units[u]
                b = u % 2
                e.wait_ge(s_ex, u + 1)
                e.reciprocal(co[:, b, :], sm[:, b, :])
                e.drain()
                gt = kvt[:, i, 768:KVG].rearrange("p (z h) -> p z h", z=3)
                e.tensor_tensor(co[:, b, 0:2], co[:, b, 0:2], gt[:, 1:3, h], ALU.mult)
                e.tensor_tensor(co[:, b, 2:3], co[:, b, 2:3], gt[:, 0:1, h], ALU.mult)
                e.wait_ge(s_o, u + 1)
                if h == 0 and i >= 2:
                    e.wait_ge(s_ot, i - 1)
                o = O[:, i % 2, 64 * h:64 * h + 64]
                e.drain()
                e.tensor_scalar(o, K.ps[:, 6 + b, 0:64], co[:, b, 0:1], None, ALU.mult)
                e.drain()
                e.scalar_tensor_tensor(o, K.ps[:, 6 + b, 64:128], co[:, b, 1:2], o, ALU.mult, ALU.add)
                e.drain()
                e.scalar_tensor_tensor(o, K.ps[:, 6 + b, 128:192], co[:, b, 2:3], o, ALU.mult, ALU.add).then_inc(s_oc, 1)
                if h == 7:
                    e.wait_ge(s_ot, i + 1)
                    e.tensor_copy(K.oC[:, :, P * i:P * i + P], K.ps[:, 7, :].rearrange("p (c n) -> p c n", c=4)).then_inc(s_oe, 1)

            softmax_in(0)
            for u in range(NU):
                if u + 1 < NU:
                    softmax_in(u + 1)
                combine(u)

        @block.scalar
        def _(e):
            def exps(u):
                i, h = units[u]
                b = u % 2
                ns, nw = cols(i)
                e.wait_ge(s_mx, u + 1)
                if u >= 2:
                    e.wait_ge(s_oc, u - 1)
                for z, (lo, hi) in enumerate(((0, ns), (TP, TP + nw), (TP + 5 * P, SW))):
                    e.activation(S[:, b, lo:hi], S[:, b, lo:hi], ACT.Exp, bias=nm[:, b, z:z + 1], accum_out=sm[:, b, z:z + 1])
                e.drain().then_inc(s_ex, 1)

            exps(0)
            for u in range(NU):
                gs = groups(units[u][0])
                for n in range(len(gs)):
                    G = gbase[u] + n
                    e.wait_ge(s_pt, G + 1)
                    full = [z for z, (kind, _) in enumerate(gs[n]) if kind != "c"]
                    w = P * len(full)
                    if w:
                        mm = e.activation(PT[:, G % 2, 0:w], K.ps[:, 4 + G % 2, 0:w], ACT.Copy)
                    if len(full) < len(gs[n]):
                        mm = e.activation(PT[0:16, G % 2, w:w + P], K.ps[0:16, 4 + G % 2, w:w + P], ACT.Copy)
                    mm.then_inc(s_pc, 1)
                if u + 1 < NU:
                    exps(u + 1)

        @block.gpsimd
        def _(e):
            for u in range(NU):
                i, h = units[u]
                e.wait_ge(s_ex, u + 1)
                e.tensor_tensor(S[:, u % 2, TP + 5 * P:SW], S[:, u % 2, TP + 5 * P:SW], K.c("cmask")[:, 14 - 2 * i:30 - 2 * i],
                                ALU.mult).then_inc(s_cm, 1)


SS, SWN, SCM = PAST + DT, 512 + DT, 32
SROW = SS + SWN + SCM


def stage_sample_rows(nc, K, kvt, qT, Qbd, bias, grow, vnew):
    with nc.Block() as block:
        s_g, s_b, s_z, s_q = K.sem("sr_gates_stored"), K.sem("sr_in"), K.sem("sr_zeroed"), K.sem("sr_queries")

        @block.sync
        def _(e):
            v = K.bvec.tensor
            n = 0
            e.dma_start(K.gscr, kvt[0:TS, NTI, 768:KVG]).then_inc(s_g, 16)
            for q in range(4):
                for t in range(DT):
                    r = slice(32 * q + t, 32 * q + 32, DT)
                    e.dma_start(bias[r, 0:SS], bass.AP(tensor=v, offset=REV - PAST - t, ap=[[BVL, 8], [1, SS]])).then_inc(s_b, 16)
                    e.dma_start(bias[r, SS:SS + SWN], bass.AP(tensor=v, offset=REV - 512 - t, ap=[[BVL, 8], [1, SWN]])).then_inc(s_b, 16)
                    e.dma_start(bias[r, SS + SWN:SROW], bass.AP(tensor=v, offset=REV - PAST + 63 - t, ap=[[BVL, 8], [64, SCM]]),
                                allow_slow_non_contiguous=True).then_inc(s_b, 16)
                    n += 3
            for b in range(DB):
                for z, c0 in enumerate((384, 640)):
                    e.dma_start(vnew[0:DT, b, z, :], kvt[DT * b:DT * b + DT, NTI, c0:c0 + P]).then_inc(s_b, 16)
                    n += 1
            e.wait_ge(s_g, 16)
            for b in range(DB):
                for h in range(8):
                    r0 = 32 * (b % 4) + 4 * h
                    e.dma_start(grow[r0:r0 + 4, b // 4, :], bass.AP(tensor=K.gscr.tensor, offset=24 * DT * b + h, ap=[[24, DT], [8, 3]]),
                                allow_slow_non_contiguous=True).then_inc(s_b, 16)
                    n += 1
            e.wait_ge(s_b, 16 * n)

        @block.vector
        def _(e):
            e.memset(Qbd[:, :, :], 0.0)
            e.drain()
            for h in range(8):
                g, pp = h // 4, 64 * (h % 2)
                e.tensor_copy(Qbd[64 * g:64 * g + 64, :, 4 * h:4 * h + 4],
                              qT[pp:pp + 64, h // 2, TP:T].rearrange("p (b t) -> p b t", t=DT))


def stage_sample_scores(nc, K, Qbd, bias, S, vcb, ksn, kwn):
    ctx = ExitStack()
    with ctx:
        sb = lambda nm, sh: ctx.enter_context(nc.sbuf_tensor("ss_" + nm, sh, F32))
        pt = ctx.enter_context(nc.sbuf_tensor("ss_pages", [1, DB * NPG], I32))
        ck, cv, sk = (sb(x, [P, NPG, P]) for x in ("ck", "cv", "sk"))
        wk = sb("wk", [P, 4, P])
        KT = sb("KT", [P, SS + SWN])
        kc, sq, rt = sb("kc", [P, SCM]), sb("sq", [P, SCM]), sb("rt", [P, SCM])
        block = ctx.enter_context(nc.Block())
        s_pt, s_pg, s_wk = K.sem("ss_table_in"), K.sem("ss_pages_in"), K.sem("ss_window_in")
        s_used, s_t, s_tc = K.sem("ss_pages_used"), K.sem("ss_turned"), K.sem("ss_turned_copied")
        s_m, s_mc, s_sq, s_sm, s_v, s_r, s_kc = (K.sem("ss_" + x) for x in (
            "means", "means_copied", "squared", "summed", "mean_sq", "rooted", "block_keys"))
        s_s, s_ev = K.sem("ss_scores"), K.sem("ss_scores_out")
        NTG = 5

        @block.sync
        def _(e):
            e.dma_start(pt[:, :], K.d["page_table"].rearrange("b n -> (b n)").unsqueeze(0)).then_inc(s_pt, 16)
            e.wait_ge(s_pt, 16)
            for b in range(DB):
                if b >= 1:
                    e.wait_ge(s_used, b)
                e.dma_start(wk[:, :, :], K.d["cache_win_k"][0, b].rearrange("(i p) g d -> p i (g d)", p=P)).then_inc(s_wk, 16)
                for j in range(NPG):
                    page = e.value_load(pt[0:1, NPG * b + j:NPG * b + j + 1], min_val=0, max_val=159)
                    for dst, src in ((ck, K.d["cache_cmp_k"]), (cv, K.d["cache_cmp_v"]), (sk, K.d["cache_slc_k"])):
                        e.dma_start(dst[:, j, :], src[0, bass.ds(page, 1), :, :, :].rearrange("a p g d -> p (a g d)")).then_inc(s_pg, 16)

        @block.tensor
        def _(e):
            ident, blk = K.c("ident"), K.c("blk")
            for b in range(DB):
                q, bb = b // 4, b % 4
                e.wait_ge(s_pg, 48 * NPG * (b + 1))
                e.wait_ge(s_wk, 16 * (b + 1))
                if b >= 1:
                    e.wait_ge(s_mc, b)
                    e.wait_ge(s_v, b)
                for j in range(NPG):
                    e.matmul(K.ps[:, 6, 2 * j:2 * j + 2], ck[:, j, :], blk[:, 30:32], start=True, stop=True)
                for j in range(NPG):
                    mm = e.matmul(K.ps[0:SCM, 7, 0:P], blk[:, 30 - 2 * j:62 - 2 * j], cv[:, j, :], start=j == 0, stop=j == NPG - 1)
                mm.then_inc(s_m, 1)
                for z in range(NTG):
                    G = NTG * b + z
                    if G >= 2:
                        e.wait_ge(s_tc, G - 1)
                    for j in range(4):
                        src = sk[:, 4 * z + j, :] if z < 4 else wk[:, j, :]
                        mm = e.transpose(K.ps[:, G % 2, P * j:P * j + P], src, ident)
                    mm.then_inc(s_t, 1)
                e.wait_ge(s_sq, b + 1)
                e.matmul(K.ps[:, 5, 0:SCM], K.c("headsum"), sq[:, :], start=True, stop=True).then_inc(s_sm, 1)
                e.wait_ge(s_tc, NTG * (b + 1))
                e.wait_ge(s_kc, b + 1)
                pr = slice(32 * bb, 32 * bb + 32)
                new = slice(DT * b, DT * b + DT)
                qb = Qbd[:, b, :]
                for z in range(4):
                    c = 2 + z % 3
                    if z == 0 and b >= 1:
                        e.wait_ge(s_ev, 6 * b)
                    if z == 3:
                        e.wait_ge(s_ev, 6 * b + 1)
                    e.matmul(K.ps[pr, c, :], qb, KT[:, 512 * z:512 * z + 512], start=True, stop=True).then_inc(s_s, 1)
                e.wait_ge(s_ev, 6 * b + 2)
                e.matmul(K.ps[pr, 3, 0:512], qb, KT[:, SS:SS + 512], start=True, stop=True).then_inc(s_s, 1)
                e.wait_ge(s_ev, 6 * b + 3)
                e.matmul(K.ps[pr, 4, 0:DT], qb, ksn[:, new], start=True, stop=True)
                e.matmul(K.ps[pr, 4, 8:8 + DT], qb, kwn[:, new], start=True, stop=True)
                e.matmul(K.ps[pr, 4, 16:16 + SCM], qb, kc[:, :], start=True, stop=True).then_inc(s_s, 1)

        @block.scalar
        def _(e):
            for b in range(DB):
                for z in range(NTG):
                    G = NTG * b + z
                    e.wait_ge(s_t, G + 1)
                    if z == 0 and b >= 1:
                        e.wait_ge(s_s, 6 * b)
                    lo = 512 * z if z < 4 else SS
                    e.activation(KT[:, lo:lo + 512], K.ps[:, G % 2, :], ACT.Copy).then_inc(s_tc, 1)
                e.wait_ge(s_v, b + 1)
                e.activation(rt[:, :], rt[:, :], ACT.Sqrt).then_inc(s_r, 1)
                e.wait_ge(s_m, b + 1)
                e.drain().then_inc(s_used, 1)

        @block.vector
        def _(e):
            for b in range(DB):
                q, bb = b // 4, b % 4
                pr = slice(32 * bb, 32 * bb + 32)
                e.wait_ge(s_m, b + 1)
                if b >= 1:
                    e.wait_ge(s_s, 6 * b)
                e.tensor_copy(kc[:, :], K.ps[:, 6, 0:SCM])
                e.tensor_copy(vcb[:, b, :], K.ps[0:SCM, 7, 0:P]).then_inc(s_mc, 1)
                e.drain()
                e.tensor_tensor(sq[:, :], kc[:, :], kc[:, :], ALU.mult).then_inc(s_sq, 1)
                e.wait_ge(s_sm, b + 1)
                e.tensor_scalar(rt[:, :], K.ps[:, 5, 0:SCM], 1.0 / 64, RMS_EPS, ALU.mult, ALU.add).then_inc(s_v, 1)
                e.wait_ge(s_r, b + 1)
                e.reciprocal(rt[:, :], rt[:, :])
                e.drain()
                e.scalar_tensor_tensor(kc[:, :], kc[:, :], K.p("kg_cmp", 0), rt[:, :], ALU.mult, ALU.mult).then_inc(s_kc, 1)
                for z in range(4):
                    e.wait_ge(s_s, 6 * b + z + 1)
                    lo = 512 * z
                    e.tensor_tensor(S[pr, q, lo:lo + 512], K.ps[pr, 2 + z % 3, :], bias[pr, lo:lo + 512], ALU.add).then_inc(s_ev, 1)
                e.wait_ge(s_s, 6 * b + 5)
                e.tensor_tensor(S[pr, q, SS:SS + 512], K.ps[pr, 3, :], bias[pr, SS:SS + 512], ALU.add).then_inc(s_ev, 1)
                e.wait_ge(s_s, 6 * b + 6)
                e.tensor_tensor(S[pr, q, PAST:SS], K.ps[pr, 4, 0:DT], bias[pr, PAST:SS], ALU.add)
                e.tensor_tensor(S[pr, q, SS + 512:SS + SWN], K.ps[pr, 4, 8:8 + DT], bias[pr, SS + 512:SS + SWN], ALU.add)
                e.tensor_tensor(S[pr, q, SS + SWN:SROW], K.ps[pr, 4, 16:16 + SCM], bias[pr, SS + SWN:SROW], ALU.add).then_inc(s_ev, 1)


def stage_sample_softmax(nc, K, S, coef, grow):
    ctx = ExitStack()
    with ctx:
        sb = lambda nm, sh: ctx.enter_context(nc.sbuf_tensor("sx_" + nm, sh, F32))
        nm, sm, rc = sb("negmax", [P, 2, 3]), sb("sums", [P, 2, 3]), sb("rec", [P, 2, 3])
        pc, sc, s1, s2 = sb("pc", [P, SCM]), sb("score", [P, 33]), sb("left", [P, 33]), sb("left2", [P, 33])
        m1, m2 = sb("top", [P, 8]), sb("top2", [P, 8])
        block = ctx.enter_context(nc.Block())
        s_mx, s_ex, s_pc, s_sc = K.sem("sx_max"), K.sem("sx_exps"), K.sem("sx_block_probs"), K.sem("sx_block_scores")
        RNG = ((0, SS), (SS, SS + SWN), (SS + SWN, SROW))
        OUT = -3e30

        @block.vector
        def _(e):
            for q in range(2):
                e.tensor_tensor(S[:, q, SS:SS + 4], S[:, q, SS:SS + 4], K.c("edgeS"), ALU.add)
                e.drain()
                for z in (2, 1):
                    lo, hi = RNG[z]
                    e.tensor_reduce(nm[:, q, z:z + 1], S[:, q, lo:hi], AX.X, ALU.max, negate=True).then_inc(s_mx, 1)
                e.wait_ge(s_ex, 3 * q + 1)
                e.reciprocal(rc[:, q, 2:3], sm[:, q, 2:3])
                e.drain()
                e.tensor_scalar(pc[:, :], S[:, q, SS + SWN:SROW], rc[:, q, 2:3], None, ALU.mult).then_inc(s_pc, 1)
                e.wait_ge(s_sc, q + 1)
                e.tensor_copy(sc[:, 0:SCM], K.ps[:, q, 0:SCM])
                e.drain()
                e.memset(sc[:, 0:1], 1e4)
                e.memset(sc[:, 31:33], 1e4)
                e.drain()
                e.max(m1[:, :], sc[:, :])
                e.drain()
                e.match_replace(s1[:, :], m1[:, :], sc[:, :], OUT)
                e.drain()
                e.max(m2[:, :], s1[:, :])
                e.drain()
                e.match_replace(s2[:, :], m2[:, :], s1[:, :], OUT)
                e.drain()
                e.tensor_scalar(s1[:, :], s2[:, :], OUT / 2, NEG, ALU.is_gt, ALU.mult)
                e.drain()
                sv = S[:, q, 0:PAST].rearrange("p (j n) -> p j n", n=64)
                e.tensor_tensor(sv, sv, s1[:, 0:32].unsqueeze(2).to_broadcast([P, 32, 64]), ALU.add)
                e.drain()
                e.tensor_reduce(nm[:, q, 0:1], S[:, q, 0:SS], AX.X, ALU.max, negate=True).then_inc(s_mx, 1)
                e.wait_ge(s_ex, 3 * q + 3)
                e.reciprocal(rc[:, q, 0:2], sm[:, q, 0:2])
                e.drain()
                e.tensor_tensor(coef[:, q, 0:2], rc[:, q, 0:2], grow[:, q, 1:3], ALU.mult)
                e.tensor_tensor(coef[:, q, 2:3], rc[:, q, 2:3], grow[:, q, 0:1], ALU.mult)

        @block.scalar
        def _(e):
            for q in range(2):
                for n, z in enumerate((2, 1, 0)):
                    lo, hi = RNG[z]
                    e.wait_ge(s_mx, 3 * q + n + 1)
                    e.activation(S[:, q, lo:hi], S[:, q, lo:hi], ACT.Exp, bias=nm[:, q, z:z + 1], accum_out=sm[:, q, z:z + 1])
                    e.drain().then_inc(s_ex, 1)

        @block.tensor
        def _(e):
            for q in range(2):
                e.wait_ge(s_pc, q + 1)
                e.matmul(K.ps[:, q, 0:SCM], K.c("heads4"), pc[:, :], start=True, stop=True).then_inc(s_sc, 1)


def stage_sample_values(nc, K, S, coef, vcb, vnew):
    ctx = ExitStack()
    NB4 = 20
    with ctx:
        sb = lambda nm, sh: ctx.enter_context(nc.sbuf_tensor("sv_" + nm, sh, F32))
        pt = ctx.enter_context(nc.sbuf_tensor("sv_pages", [1, DB * NPG], I32))
        sv = sb("v", [P, 2, NPG, P])
        wv = sb("wv", [P, 2, 4, P])
        PT = sb("PT", [P, NB4, P])
        PN = sb("PN", [SCM, 3, P])
        o1, o2 = sb("o1", [P, P]), sb("o2", [P, 64])
        block = ctx.enter_context(nc.Block())
        s_pt, s_wv = K.sem("sv_table_in"), K.sem("sv_window_in")
        s_pgs = K.sems("sv_pages_in", 2)
        s_t, s_tc, s_used, s_o, s_oc, s_ot, s_fin = (K.sem("sv_" + x) for x in (
            "turned", "turned_copied", "values_used", "values", "combined", "out_turned", "out_copied"))

        @block.sync
        def _(e):
            e.dma_start(pt[:, :], K.d["page_table"].rearrange("b n -> (b n)").unsqueeze(0)).then_inc(s_pt, 16)
            e.wait_ge(s_pt, 16)
            for b in range(DB):
                if b >= 2:
                    e.wait_ge(s_used, b - 1)
                e.dma_start(wv[:, b % 2, :, :], K.d["cache_win_v"][0, b].rearrange("(i p) g d -> p i (g d)", p=P)).then_inc(s_pgs[b % 2], 16)
                for j in range(NPG):
                    page = e.value_load(pt[0:1, NPG * b + j:NPG * b + j + 1], min_val=0, max_val=159)
                    e.dma_start(sv[:, b % 2, j, :], K.d["cache_slc_v"][0, bass.ds(page, 1), :, :, :].rearrange("a p g d -> p (a g d)")).then_inc(s_pgs[b % 2], 16)

        @block.tensor
        def _(e):
            ident = K.c("ident")
            for q in range(2):
                if q:
                    e.wait_ge(s_used, 4)
                for z in range(6):
                    G = 6 * q + z
                    if G >= 2:
                        e.wait_ge(s_tc, G - 1)
                    if z < 5:
                        for j in range(4):
                            lo = 512 * z + P * j if z < 4 else SS + P * j
                            mm = e.transpose(K.ps[:, G % 2, P * j:P * j + P], S[:, q, lo:lo + P], ident)
                    else:
                        e.transpose(K.ps[0:DT, G % 2, 0:P], S[:, q, PAST:SS], ident)
                        e.transpose(K.ps[0:DT, G % 2, P:2 * P], S[:, q, SS + 512:SS + SWN], ident)
                        mm = e.transpose(K.ps[0:SCM, G % 2, 2 * P:3 * P], S[:, q, SS + SWN:SROW], ident)
                    mm.then_inc(s_t, 1)
                e.wait_ge(s_tc, 6 * q + 6)
                if q:
                    e.wait_ge(s_oc, 1)
                for bb in range(4):
                    b = 4 * q + bb
                    e.wait_ge(s_pgs[b % 2], 16 * (NPG + 1) * (b // 2 + 1))
                    r = slice(32 * bb, 32 * bb + 32)
                    for j in range(NPG):
                        e.matmul(K.ps[r, 2, 0:P], PT[:, j, r], sv[:, b % 2, j, :], start=j == 0, stop=False)
                    e.matmul(K.ps[r, 2, 0:P], PN[0:DT, 0, r], vnew[0:DT, b, 0, :], start=False, stop=True)
                    for j in range(4):
                        e.matmul(K.ps[r, 3, 0:P], PT[:, NPG + j, r], wv[:, b % 2, j, :], start=j == 0, stop=False)
                    e.matmul(K.ps[r, 3, 0:P], PN[0:DT, 1, r], vnew[0:DT, b, 1, :], start=False, stop=True)
                    e.matmul(K.ps[r, 4, 0:P], PN[:, 2, r], vcb[:, b, :], start=True, stop=True).then_inc(s_used, 1)
                e.wait_ge(s_oc, q + 1)
                e.transpose(K.ps[0:64, 5, 0:P], o2[:, :], ident).then_inc(s_ot, 1)

        @block.scalar
        def _(e):
            for q in range(2):
                if q:
                    e.wait_ge(s_used, 4)
                for z in range(6):
                    G = 6 * q + z
                    e.wait_ge(s_t, G + 1)
                    if z < 5:
                        e.activation(PT[:, 4 * z:4 * z + 4, :].rearrange("p j n -> p (j n)"), K.ps[:, G % 2, :], ACT.Copy).then_inc(s_tc, 1)
                    else:
                        for k, n in enumerate((DT, DT, SCM)):
                            mm = e.activation(PN[0:n, k, :], K.ps[0:n, G % 2, P * k:P * k + P], ACT.Copy)
                        mm.then_inc(s_tc, 1)

        @block.vector
        def _(e):
            for q in range(2):
                e.wait_ge(s_used, 4 * q + 4)
                e.tensor_scalar(o1[:, :], K.ps[:, 2, 0:P], coef[:, q, 0:1], None, ALU.mult)
                e.drain()
                e.scalar_tensor_tensor(o1[:, :], K.ps[:, 3, 0:P], coef[:, q, 1:2], o1[:, :], ALU.mult, ALU.add)
                e.drain()
                e.scalar_tensor_tensor(o1[:, :], K.ps[:, 4, 0:P], coef[:, q, 2:3], o1[:, :], ALU.mult, ALU.add)
                e.drain()
                e.tensor_scalar(o2[:, :], o1[:, 0:64], K.c("grp")[:, 0:1], None, ALU.mult)
                e.drain()
                e.scalar_tensor_tensor(o2[:, :], o1[:, 64:P], K.c("grp")[:, 1:2], o2[:, :], ALU.mult, ALU.add).then_inc(s_oc, 1)
                e.wait_ge(s_ot, q + 1)
                t = K.ps[0:64, 5, 0:P].rearrange("p (b h t) -> p b h t", b=4, h=8)
                for h in range(8):
                    e.tensor_copy(K.oC[64 * (h % 2):64 * (h % 2) + 64, h // 2, TP + 16 * q:TP + 16 * q + 16].rearrange("p (b t) -> p b t", t=DT),
                                  t[:, :, h, :])
                e.drain()


def stage_merge(nc, K, h):
    NS = 4
    names = ("w_br_a", "w_br_b", "w_br_c")
    srcs = (K.oA, K.oB, K.oC)
    ctx = ExitStack()
    with ctx:
        ring = ctx.enter_context(nc.sbuf_tensor("me_w", [P, NS, KD + 4, P], F32))
        sg = ctx.enter_context(nc.sbuf_tensor("me_gate", [P, 2, T], F32))
        tmp = ctx.enter_context(nc.sbuf_tensor("me_tmp", [P, T], F32))
        block = ctx.enter_context(nc.Block())
        s_in = K.sems("me_weights_in", NS)
        s_g, s_b, s_sg, s_h = K.sem("me_gate_product"), K.sem("me_branch_product"), K.sem("me_gate_sigmoid"), K.sem("me_weighted")

        @block.sync
        def _(e):
            for u in range(3 * KD):
                m, br = u // 3, u % 3
                if u >= NS:
                    e.wait_ge(s_b, u - NS + 1)
                c0 = OFF_MG + D * br + P * m
                e.dma_start(ring[:, u % NS, 0:KD, :], K.d["w_in"][0, :, c0:c0 + P].rearrange("(k p) n -> p k n", p=P)).then_inc(s_in[u % NS], 16)
                e.dma_start(ring[:, u % NS, KD:KD + 4, :], K.d[names[br]][0, :, P * m:P * m + P].rearrange("(k p) n -> p k n", p=P)).then_inc(s_in[u % NS], 16)

        @block.tensor
        def _(e):
            for u in range(3 * KD):
                br = u % 3
                e.wait_ge(s_in[u % NS], 32 * (u // NS + 1))
                if u >= 1:
                    e.wait_ge(s_sg, u)
                for c in range(NC3):
                    for k in range(KD):
                        mm = e.matmul(K.ps[:, c, 0:NW], ring[:, u % NS, k, :], K.xn[:, k, NW * c:NW * c + NW], start=k == 0, stop=k == KD - 1)
                mm.then_inc(s_g, 1)
                if u >= 1:
                    e.wait_ge(s_h, u)
                for c in range(NC3):
                    for k in range(4):
                        mm = e.matmul(K.ps[:, 3 + c, 0:NW], ring[:, u % NS, KD + k, :], srcs[br][:, k, NW * c:NW * c + NW], start=k == 0, stop=k == 3)
                mm.then_inc(s_b, 1)

        @block.scalar
        def _(e):
            for u in range(3 * KD):
                e.wait_ge(s_g, u + 1)
                if u >= 2:
                    e.wait_ge(s_h, u - 1)
                e.activation(sg[:, u % 2, :].rearrange("p (c n) -> p c n", c=NC3), K.ps[:, 0:3, 0:NW], ACT.Sigmoid).then_inc(s_sg, 1)

        @block.vector
        def _(e):
            c3 = lambda ap: ap.rearrange("p (c n) -> p c n", c=NC3)
            for u in range(3 * KD):
                m, br = u // 3, u % 3
                e.wait_ge(s_sg, u + 1)
                e.wait_ge(s_b, u + 1)
                dst = h[:, m, :] if br == 0 else tmp[:, :]
                e.tensor_tensor(c3(dst), c3(sg[:, u % 2, :]), K.ps[:, 3:6, 0:NW], ALU.mult).then_inc(s_h, 1)
                e.drain()
                if br:
                    e.tensor_tensor(h[:, m, :], h[:, m, :], tmp[:, :], ALU.add)
                    e.drain()


def stage_product(nc, K, tag, w, kb, nblk, rhs, dst, kind):
    NS = 4
    ctx = ExitStack()
    with ctx:
        ring = ctx.enter_context(nc.sbuf_tensor(tag + "_w", [P, NS, kb, P], F32))
        block = ctx.enter_context(nc.Block())
        s_in = K.sems(tag + "_weights_in", NS)
        s_mm, s_out = K.sem(tag + "_product"), K.sem(tag + "_taken")
        c3 = lambda ap: ap.rearrange("p (c n) -> p c n", c=NC3)
        bank = lambda m: K.ps[:, 3 * (m % 2):3 * (m % 2) + 3, 0:NW]

        @block.sync
        def _(e):
            for m in range(nblk):
                if m >= NS:
                    e.wait_ge(s_mm, m - NS + 1)
                e.dma_start(ring[:, m % NS, :, :], w(m).rearrange("(k p) n -> p k n", p=P)).then_inc(s_in[m % NS], 16)

        @block.tensor
        def _(e):
            project(e, K, ring, s_in, s_mm, [(s_out, 1)], nblk, kb, rhs, lambda m: (m % NS, m // NS + 1, 0, True))

        if kind == "copy":
            @block.scalar
            def _(e):
                for m in range(nblk):
                    e.wait_ge(s_mm, m + 1)
                    e.activation(c3(dst[:, m, :]), bank(m), ACT.Copy).then_inc(s_out, 1)

        if kind == "add":
            @block.vector
            def _(e):
                for m in range(nblk):
                    e.wait_ge(s_mm, m + 1)
                    e.tensor_tensor(c3(dst[:, m, :]), c3(dst[:, m, :]), bank(m), ALU.add).then_inc(s_out, 1)

        if kind == "relu2":
            s_rl = K.sem(tag + "_relu")

            @block.scalar
            def _(e):
                for m in range(nblk):
                    e.wait_ge(s_mm, m + 1)
                    e.activation(c3(dst[:, m, :]), bank(m), ACT.Relu).then_inc(s_rl, 1)
                    e.drain().then_inc(s_out, 1)

            @block.vector
            def _(e):
                for m in range(nblk):
                    e.wait_ge(s_rl, m + 1)
                    e.tensor_tensor(dst[:, m, :], dst[:, m, :], dst[:, m, :], ALU.mult)


def stage_mem_load(nc, K, mT):
    ctx = ExitStack()
    with ctx:
        rows = ctx.enter_context(nc.sbuf_tensor("ml_rows", [P, 2, D], F32))
        block = ctx.enter_context(nc.Block())
        s_in, s_t, s_c = K.sem("ml_in"), K.sem("ml_turned"), K.sem("ml_copied")

        @block.sync
        def _(e):
            e.dma_start(rows[:, :, :], K.d["mem_prompt"][0].rearrange("(i p) d -> p i d", p=P)).then_inc(s_in, 16)

        @block.tensor
        def _(e):
            e.wait_ge(s_in, 16)
            for i in range(2):
                for k in range(KD):
                    mm = e.transpose(K.ps[:, 2 * i + k // 4, P * (k % 4):P * (k % 4) + P], rows[:, i, P * k:P * k + P], K.c("ident"))
                mm.then_inc(s_t, 1)

        @block.vector
        def _(e):
            for i in range(2):
                e.wait_ge(s_t, i + 1)
                for z in range(2):
                    e.tensor_copy(mT[:, 4 * z:4 * z + 4, P * i:P * i + P], K.ps[:, 2 * i + z, :].rearrange("p (k n) -> p k n", k=4))


def stage_mem_kv(nc, K, mn, mkT, mv):
    ctx = ExitStack()
    with ctx:
        sb = lambda nm, sh: ctx.enter_context(nc.sbuf_tensor("mk_" + nm, sh, F32))
        w = sb("w", [P, 2, KD, 512])
        mk = sb("k", [P, 2, 512])
        sq, kg, ss = sb("sq", [P, 2, 512]), sb("gain", [P, P]), sb("ss", [P, 8])
        block = ctx.enter_context(nc.Block())
        s_in, s_g, s_mm, s_c, s_v, s_r, s_k, s_t = (K.sem("mk_" + x) for x in (
            "w_in", "gain_in", "product", "copied", "mean", "rooted", "normed", "turned"))
        s_out = K.out_sem("mk_stored")

        @block.sync
        def _(e):
            e.dma_start(w[:, 0, :, :], K.d["w_mk"][0].rearrange("(k p) n -> p k n", p=P)).then_inc(s_in, 16)
            e.dma_start(w[:, 1, :, :], K.d["w_mv"][0].rearrange("(k p) n -> p k n", p=P)).then_inc(s_in, 16)
            e.dma_start(kg[:, :], K.d["mem_k_g"][0, :].partition_broadcast(P)).then_inc(s_g, 16)
            e.wait_ge(s_k, 1)
            e.dma_start(K.d["p_mem_k"][0, 0].rearrange("(i p) h d -> p i (h d)", p=P), mk[:, :, :]).then_inc(s_out, 16)
            e.wait_ge(s_c, 2)
            e.dma_start(K.d["p_mem_v"][0, 0].rearrange("(i p) h d -> p i (h d)", p=P), mv[:, :, :]).then_inc(s_out, 16)
            e.wait_ge(s_out, 32)

        @block.tensor
        def _(e):
            e.wait_ge(s_in, 32)
            for z in range(2):
                for i in range(2):
                    for k in range(KD):
                        mm = e.matmul(K.ps[:, 2 * z + i, :], mn[:, k, P * i:P * i + P], w[:, z, k, :], start=k == 0, stop=k == KD - 1)
                mm.then_inc(s_mm, 1)
            e.wait_ge(s_k, 1)
            for h in range(4):
                for i in range(2):
                    mm = e.transpose(K.ps[:, 4 + h // 2, 256 * (h % 2) + P * i:256 * (h % 2) + P * i + P], mk[:, i, P * h:P * h + P], K.c("ident"))
            mm.then_inc(s_t, 1)

        @block.scalar
        def _(e):
            for z, dst in ((0, mk), (1, mv)):
                e.wait_ge(s_mm, z + 1)
                e.activation(dst[:, :, :], K.ps[:, 2 * z:2 * z + 2, :], ACT.Copy).then_inc(s_c, 1)
            e.wait_ge(s_v, 1)
            e.activation(ss[:, :], ss[:, :], ACT.Sqrt).then_inc(s_r, 1)

        @block.vector
        def _(e):
            k8 = mk[:, :, :].rearrange("p i (h d) -> p (i h) d", d=P)
            e.wait_ge(s_c, 1)
            e.tensor_tensor(sq[:, :, :], mk[:, :, :], mk[:, :, :], ALU.mult)
            e.drain()
            e.tensor_reduce(ss[:, :], sq[:, :, :].rearrange("p i (h d) -> p (i h) d", d=P), AX.X, ALU.add)
            e.drain()
            e.tensor_scalar(ss[:, :], ss[:, :], 1.0 / P, RMS_EPS, ALU.mult, ALU.add).then_inc(s_v, 1)
            e.wait_ge(s_r, 1)
            e.reciprocal(ss[:, :], ss[:, :])
            e.drain()
            e.tensor_tensor(k8, k8, ss[:, :].unsqueeze(2).to_broadcast([P, 8, P]), ALU.mult)
            e.drain()
            e.wait_ge(s_g, 16)
            e.tensor_tensor(k8, k8, kg[:, :].unsqueeze(1).to_broadcast([P, 8, P]), ALU.mult).then_inc(s_k, 1)
            e.wait_ge(s_t, 1)
            e.tensor_copy(mkT[:, :, :].rearrange("p h n -> p (h n)"), K.ps[:, 4:6, :].rearrange("p a n -> p (a n)"))


def stage_mem_prompt(nc, K, q, mkT, mv, o):
    SC = P ** -0.5
    ctx = ExitStack()
    with ctx:
        sb = lambda nm, sh: ctx.enter_context(nc.sbuf_tensor("mp_" + nm, sh, F32))
        Pr = sb("probs", [P, 2, 4, 256])
        nm, sm = sb("negmax", [P, 2, 4]), sb("sums", [P, 2, 4])
        PT = sb("probsT", [P, 8, P])
        block = ctx.enter_context(nc.Block())
        s_s, s_mx, s_ex, s_pr, s_t, s_tc, s_o, s_oc = (K.sem("mp_" + x) for x in (
            "scores", "max", "exps", "probs", "turned", "turned_copied", "values", "values_copied"))

        def sbank(i):
            return K.ps[:, 2 * (i % 2):2 * (i % 2) + 2, :].rearrange("p a (h n) -> p (a h) n", h=2)

        @block.tensor
        def _(e):
            def scores(i):
                if i >= 2:
                    e.wait_ge(s_ex, i - 1)
                for h in range(4):
                    mm = e.matmul(K.ps[:, 2 * (i % 2) + h // 2, 256 * (h % 2):256 * (h % 2) + 256], q[:, h, P * i:P * i + P], mkT[:, h, :],
                                  start=True, stop=True)
                mm.then_inc(s_s, 1)

            scores(0)
            for i in range(NTI):
                if i + 1 < NTI:
                    scores(i + 1)
                e.wait_ge(s_pr, i + 1)
                if i >= 1:
                    e.wait_ge(s_tc, i)
                for h in range(4):
                    for j in range(2):
                        mm = e.transpose(K.ps[:, 4 + h // 2, 256 * (h % 2) + P * j:256 * (h % 2) + P * j + P],
                                         Pr[:, i % 2, h, P * j:P * j + P], K.c("ident"))
                mm.then_inc(s_t, 1)
                e.wait_ge(s_tc, i + 1)
                if i >= 2:
                    e.wait_ge(s_oc, i - 1)
                for h in range(4):
                    for j in range(2):
                        mm = e.matmul(K.ps[:, 6 + i % 2, P * h:P * h + P], mv[:, j, P * h:P * h + P], PT[:, 2 * h + j, :], start=j == 0, stop=j == 1)
                mm.then_inc(s_o, 1)

        @block.vector
        def _(e):
            def maxes(i):
                e.wait_ge(s_s, i + 1)
                if i >= 2:
                    e.wait_ge(s_ex, i - 1)
                e.tensor_reduce(nm[:, i % 2, :], sbank(i), AX.X, ALU.max, negate=True)
                e.drain()
                e.tensor_scalar(nm[:, i % 2, :], nm[:, i % 2, :], SC, None, ALU.mult).then_inc(s_mx, 1)

            maxes(0)
            for i in range(NTI):
                if i + 1 < NTI:
                    maxes(i + 1)
                e.wait_ge(s_ex, i + 1)
                e.reciprocal(sm[:, i % 2, :], sm[:, i % 2, :])
                e.drain()
                e.tensor_tensor(Pr[:, i % 2, :, :], Pr[:, i % 2, :, :], sm[:, i % 2, :].unsqueeze(2).to_broadcast([P, 4, 256]), ALU.mult).then_inc(s_pr, 1)
                e.wait_ge(s_o, i + 1)
                e.tensor_copy(o[:, :, P * i:P * i + P], K.ps[:, 6 + i % 2, :].rearrange("p (h n) -> p h n", h=4)).then_inc(s_oc, 1)

        @block.scalar
        def _(e):
            for i in range(NTI):
                e.wait_ge(s_mx, i + 1)
                if i >= 2:
                    e.wait_ge(s_t, i - 1)
                for h in range(4):
                    e.activation(Pr[:, i % 2, h, :], sbank(i)[:, h, :], ACT.Exp, bias=nm[:, i % 2, h:h + 1], scale=SC, accum_out=sm[:, i % 2, h:h + 1])
                e.drain().then_inc(s_ex, 1)
                e.wait_ge(s_t, i + 1)
                if i >= 1:
                    e.wait_ge(s_o, i)
                e.activation(PT[:, :, :].rearrange("p (a h) n -> p a (h n)", a=2), K.ps[:, 4:6, :], ACT.Copy).then_inc(s_tc, 1)


def stage_mem_sample(nc, K, q, o):
    SC = P ** -0.5
    ctx = ExitStack()
    with ctx:
        sb = lambda nm, sh: ctx.enter_context(nc.sbuf_tensor("ms_" + nm, sh, F32))
        kb, vb = sb("k", [P, 2, 2, 512]), sb("v", [P, DB, 2, 512])
        KT = sb("KT", [P, 2, 1024])
        Q = sb("Q", [P, 4, DB, 32])
        Pr, PT = sb("probs", [P, 256]), sb("probsT", [P, 2, P])
        nm, sm = sb("negmax", [P, 1]), sb("sums", [P, 1])
        o1 = sb("o1", [P, P])
        block = ctx.enter_context(nc.Block())
        s_k, s_v = K.sems("ms_keys_in", 2), K.sem("ms_values_in")
        s_q, s_t, s_tc, s_s, s_mx, s_ex, s_pr, s_pt, s_ptc, s_o, s_oc, s_ot, s_oe = (K.sem("ms_" + x) for x in (
            "queries", "keys_turned", "keys_copied", "scores", "max", "exps", "probs", "probs_turned", "probs_copied",
            "values", "combined", "out_turned", "out_copied"))

        @block.sync
        def _(e):
            for b in range(DB):
                if b >= 2:
                    e.wait_ge(s_t, b - 1)
                e.dma_start(kb[:, b % 2, :, :], K.d["cache_mem_k"][0, b].rearrange("(i p) h d -> p i (h d)", p=P)).then_inc(s_k[b % 2], 16)
                if b == 1:
                    for z in range(DB):
                        e.dma_start(vb[:, z, :, :], K.d["cache_mem_v"][0, z].rearrange("(i p) h d -> p i (h d)", p=P)).then_inc(s_v, 16)

        @block.tensor
        def _(e):
            ident = K.c("ident")
            e.wait_ge(s_q, 1)
            for b in range(DB):
                qd, bb = b // 4, b % 4
                e.wait_ge(s_k[b % 2], 16 * (b // 2 + 1))
                if b >= 1:
                    e.wait_ge(s_tc, b)
                for h in range(4):
                    for j in range(2):
                        mm = e.transpose(K.ps[:, h // 2, 256 * (h % 2) + P * j:256 * (h % 2) + P * j + P], kb[:, b % 2, j, P * h:P * h + P], ident)
                mm.then_inc(s_t, 1)
                e.wait_ge(s_tc, b + 1)
                if b == 4:
                    e.wait_ge(s_ex, 1)
                for h in range(4):
                    mm = e.matmul(K.ps[32 * bb:32 * bb + 32, 2, 0:256], Q[:, h, b, :], KT[:, b % 2, 256 * h:256 * h + 256], start=h == 0, stop=h == 3)
                mm.then_inc(s_s, 1)
                if bb == 3:
                    e.wait_ge(s_pr, qd + 1)
                    for j in range(2):
                        mm = e.transpose(K.ps[:, 3, P * j:P * j + P], Pr[:, P * j:P * j + P], ident)
                    mm.then_inc(s_pt, 1)
                    e.wait_ge(s_ptc, qd + 1)
                    e.wait_ge(s_v, 16 * DB)
                    if qd:
                        e.wait_ge(s_oc, 1)
                    for z in range(4):
                        for j in range(2):
                            mm = e.matmul(K.ps[32 * z:32 * z + 32, 4, :], PT[:, j, 32 * z:32 * z + 32], vb[:, 4 * qd + z, j, :], start=j == 0, stop=j == 1)
                    mm.then_inc(s_o, 1)
                    e.wait_ge(s_oc, qd + 1)
                    e.transpose(K.ps[:, 5, 0:P], o1[:, :], ident).then_inc(s_ot, 1)

        @block.scalar
        def _(e):
            for b in range(DB):
                qd = b // 4
                e.wait_ge(s_t, b + 1)
                if b >= 2:
                    e.wait_ge(s_s, b - 1)
                e.activation(KT[:, b % 2, :].rearrange("p (a n) -> p a n", a=2), K.ps[:, 0:2, :], ACT.Copy).then_inc(s_tc, 1)
                if b % 4 == 3:
                    e.wait_ge(s_mx, qd + 1)
                    e.activation(Pr[:, :], K.ps[:, 2, 0:256], ACT.Exp, bias=nm[:, :], scale=SC, accum_out=sm[:, :])
                    e.drain().then_inc(s_ex, 1)
                    e.wait_ge(s_pt, qd + 1)
                    e.activation(PT[:, :, :].rearrange("p j n -> p (j n)"), K.ps[:, 3, 0:256], ACT.Copy).then_inc(s_ptc, 1)

        @block.vector
        def _(e):
            e.memset(Q[:, :, :, :], 0.0)
            e.drain()
            for h in range(4):
                e.tensor_copy(Q[:, h, :, 4 * h:4 * h + 4], q[:, h, TP:T].rearrange("p (b t) -> p b t", t=DT))
            e.drain().then_inc(s_q, 1)
            for qd in range(2):
                e.wait_ge(s_s, 4 * qd + 4)
                e.tensor_reduce(nm[:, :], K.ps[:, 2, 0:256], AX.X, ALU.max, negate=True)
                e.drain()
                e.tensor_scalar(nm[:, :], nm[:, :], SC, None, ALU.mult).then_inc(s_mx, 1)
                e.wait_ge(s_ex, qd + 1)
                e.reciprocal(sm[:, :], sm[:, :])
                e.drain()
                e.tensor_scalar(Pr[:, :], Pr[:, :], sm[:, 0:1], None, ALU.mult).then_inc(s_pr, 1)
                e.wait_ge(s_o, qd + 1)
                e.tensor_scalar(o1[:, :], K.ps[:, 4, 0:P], K.c("mhead")[:, 0:1], None, ALU.mult)
                for h in range(1, 4):
                    e.drain()
                    mm = e.scalar_tensor_tensor(o1[:, :], K.ps[:, 4, P * h:P * h + P], K.c("mhead")[:, h:h + 1], o1[:, :], ALU.mult, ALU.add)
                mm.then_inc(s_oc, 1)
                e.wait_ge(s_ot, qd + 1)
                t = K.ps[:, 5, 0:P].rearrange("p (b h t) -> p b h t", b=4, h=8)
                for h in range(4):
                    e.tensor_copy(o[:, h, TP + 16 * qd:TP + 16 * qd + 16].rearrange("p (b t) -> p b t", t=DT), t[:, :, h, :])
                e.drain()


def stage_store(nc, K, x):
    ctx = ExitStack()
    with ctx:
        rows = ctx.enter_context(nc.sbuf_tensor("so_rows", [P, 3, D], F32))
        block = ctx.enter_context(nc.Block())
        s_t, s_a, s_v = K.sem("so_turned"), K.sem("so_copied_act"), K.sem("so_copied_dve")
        s_out = [K.out_sem(f"so_stored{z}") for z in range(3)]

        @block.tensor
        def _(e):
            for i in range(NTI + 1):
                n = P if i < NTI else TS
                if i >= 2:
                    e.wait_ge(s_a, i - 1)
                    e.wait_ge(s_v, i - 1)
                for k in range(KD):
                    mm = e.transpose(K.ps[0:n, 2 * (i % 2) + k // 4, P * (k % 4):P * (k % 4) + P], x[:, k, P * i:P * i + n], K.c("ident"))
                mm.then_inc(s_t, 1)

        @block.scalar
        def _(e):
            for i in range(NTI + 1):
                n = P if i < NTI else TS
                e.wait_ge(s_t, i + 1)
                if i >= 3:
                    e.wait_ge(s_out[i % 3], 16 * (i // 3))
                e.activation(rows[0:n, i % 3, 0:512], K.ps[0:n, 2 * (i % 2), :], ACT.Copy).then_inc(s_a, 1)

        @block.vector
        def _(e):
            for i in range(NTI + 1):
                n = P if i < NTI else TS
                e.wait_ge(s_t, i + 1)
                if i >= 3:
                    e.wait_ge(s_out[i % 3], 16 * (i // 3))
                e.tensor_copy(rows[0:n, i % 3, 512:1024], K.ps[0:n, 2 * (i % 2) + 1, :]).then_inc(s_v, 1)

        @block.sync
        def _(e):
            for i in range(NTI + 1):
                e.wait_ge(s_a, i + 1)
                e.wait_ge(s_v, i + 1)
                if i < NTI:
                    e.dma_start(K.d["y_prompt"][0, P * i:P * i + P, :], rows[:, i % 3, :]).then_inc(s_out[i % 3], 16)
                else:
                    e.dma_start(K.d["y_sample"].rearrange("b t d -> (b t) d"), rows[0:TS, i % 3, :]).then_inc(s_out[i % 3], 16)
            for z in range(3):
                e.wait_ge(s_out[z], 48)


def stage_zero(nc, tile):
    with nc.Block() as block:
        @block.vector
        def _(e):
            e.memset(tile[:, :, :], 0.0)


def build(nc, aps):
    with ExitStack() as ctx:
        K = Shared()
        K.d = aps
        K.turn = {}
        K.n_prow = sum(2 if n in ("nsa_q_g", "kg_cmp") else 15 if n == "shift_mu" else 1 for n, _ in PARAMS)
        K.live = []

        def sem(name):
            K.live.append(nc.alloc_semaphore(name))
            return K.live[-1]

        def reuse_semaphores():
            nc.clear_and_free_semaphores(K.live)
            nc.all_engine_barrier()
            K.live = []

        K.sem = sem
        stores = {n: nc.alloc_semaphore(n) for n in ("tail_stored", "kv_stored", "stPo_stored", "stSo_stored", "stSi_stored",
                                                      "mk_stored", "so_stored0", "so_stored1", "so_stored2")}
        K.out_sem = lambda name: stores[name]
        K.sems = lambda name, n: [K.sem(f"{name}{i}") for i in range(n)]
        K.c = lambda name: K.cst[:, CCOL[name][0]:CCOL[name][0] + CCOL[name][1]]
        K.p = lambda name, k: K.par[:, PCOL[name] + k:PCOL[name] + k + 1]
        sb = lambda name, shape: ctx.enter_context(nc.sbuf_tensor(name, shape, F32))
        K.ps = ctx.enter_context(nc.psum_tensor("ps", [P, 8, 512], F32))
        K.cst = sb("cst", [P, SHEET.shape[1]])
        K.par = sb("par", [P, NPAR + 4])
        K.utail = sb("utail", [P, B_Q, TAIL])
        K.shT = sb("shT", [P, NSHIFT, DB])
        K.oA, K.oB, K.oC = (sb(x, [P, 4, T]) for x in ("oA", "oB", "oC"))
        K.x_dram = nc.dram_tensor("x_channel_major", (P, KD * T), F32).ap()
        K.xn_dram = nc.dram_tensor("xn_channel_major", (P, KD * T), F32).ap()
        flat = lambda t: t[:, :, :].rearrange("p k n -> p (k n)")
        with nc.sbuf_tensor("keep", [P, T], F32) as K.keep, nc.sbuf_tensor("xs", [P, NSHIFT, T], F32) as xs:
            with nc.sbuf_tensor("xT", [P, KD, T], F32) as K.xT:
                stage_load(nc, K)
                stage_move(nc, K, "x_spilled", K.x_dram, flat(K.xT))
                K.xn = K.xT
                stage_rms(nc, K, "mix", K.xT, K.xn, "norm_mix_g", T)
                stage_move(nc, K, "xn_spilled", K.xn_dram, flat(K.xn))
                stage_proj_a(nc, K, xs, 0, NSHIFT)
            with nc.sbuf_tensor("ld", [P, 4, T], F32) as ld:
                stage_rwkv_prep(nc, K, xs, ld)
                with nc.sbuf_tensor("stP", [P, 4, 64], F32) as stP:
                    stage_zero(nc, stP)
                    stage_rwkv_scan(nc, K, xs, ld, "P", 128, 7, NTI, 0, stP, 63)
                    stage_rwkv_states(nc, K, "P", stP, None, K.d["p_state_rwkv"][0])
                with nc.sbuf_tensor("stS", [P, 4, DB, 64], F32) as stS:
                    stage_rwkv_states(nc, K, "S", stS, K.d["state_rwkv"][0], None)
                    stage_rwkv_scan(nc, K, xs, ld, "S", TS, 2, 1, TP, stS, None)
                    stage_rwkv_states(nc, K, "S", stS, None, K.d["s_state_rwkv"][0])
            stage_rwkv_out(nc, K, xs)
        reuse_semaphores()
        K.bvec = nc.dram_tensor("bias_vectors", (8, BVL), F32).ap()
        c1 = ExitStack()
        s1 = lambda name, shape: c1.enter_context(nc.sbuf_tensor(name, shape, F32))
        qT, kvt = s1("qT", [P, 4, T]), s1("kvt", [P, NTI + 1, KVG])
        b31, ksn, kwn = s1("b31", [P, 8]), s1("ksn", [P, TS]), s1("kwn", [P, TS])
        with nc.sbuf_tensor("xnB", [P, KD, T], F32) as K.xn:
            stage_move(nc, K, "xn_back", flat(K.xn), K.xn_dram)
            with nc.sbuf_tensor("up", [P, 4, T], F32) as up:
                stage_proj_a(nc, K, up, B_POOL, 4)
                stage_pool(nc, K, up)
            stage_tail_rows(nc, K)
            stage_proj_a(nc, K, qT, B_Q, 4)
            stage_head_rms(nc, K, "nsaq", qT, 4, "headsum", 64, "nsa_q_g", 0.125)
            stage_kv(nc, K, kvt)
        with ExitStack() as c2:
            sc = lambda name, shape: c2.enter_context(nc.sbuf_tensor(name, shape, F32))
            near, cb = sc("near", [P, 8, 2 * P]), sc("cb", [P, 8, 30])
            kcd, vc = sc("kcd", [P, 2, 16]), sc("vc", [16, P])
            ksd, kwd = sc("ksd", [P, 2, TP]), sc("kwd", [P, 2, TP])
            stage_bias(nc, K, near, cb, b31)
            stage_nsa_keys(nc, K, kvt, kcd, vc, ksd, kwd, ksn, kwn)
            stage_nsa_prompt(nc, K, qT, kvt, kcd, vc, ksd, kwd, near, cb, b31)
        reuse_semaphores()
        K.gscr = nc.dram_tensor("gate_rows", (TS, 24), F32).ap()
        with ExitStack() as c2:
            sc = lambda name, shape: c2.enter_context(nc.sbuf_tensor(name, shape, F32))
            Ssc = sc("s_scores", [P, 2, SROW])
            coef, grow = sc("s_coef", [P, 2, 3]), sc("s_gates", [P, 2, 3])
            vnew, vcb = sc("s_vnew", [DT, DB, 2, P]), sc("s_vcb", [SCM, DB, P])
            with nc.sbuf_tensor("s_qbd", [P, DB, 32], F32) as Qbd, nc.sbuf_tensor("s_bias", [P, SROW], F32) as bias:
                stage_sample_rows(nc, K, kvt, qT, Qbd, bias, grow, vnew)
                stage_sample_scores(nc, K, Qbd, bias, Ssc, vcb, ksn, kwn)
            stage_sample_softmax(nc, K, Ssc, coef, grow)
            stage_sample_values(nc, K, Ssc, coef, vcb, vnew)
        c1.close()
        reuse_semaphores()
        block_of = lambda w: lambda m: w[:, P * m:P * m + P]
        x = sb("x", [P, KD, T])
        with nc.sbuf_tensor("h", [P, KD, T], F32) as h:
            K.xn = x
            stage_move(nc, K, "xn_again", flat(x), K.xn_dram)
            stage_merge(nc, K, h)
            stage_move(nc, K, "x_back", flat(x), K.x_dram)
            stage_product(nc, K, "wo", block_of(K.d["w_out"][0]), KD, KD, h, x, "add")
        mkT, mv = sb("mkT", [P, 4, 256]), sb("mv", [P, 2, 512])
        with nc.sbuf_tensor("mT", [P, KD, 256], F32) as mT:
            stage_mem_load(nc, K, mT)
            stage_rms(nc, K, "mem", mT, mT, "norm_mem_g", 256)
            stage_mem_kv(nc, K, mT, mkT, mv)
        with nc.sbuf_tensor("xm", [P, KD, T], F32) as xm:
            stage_rms(nc, K, "memx", x, xm, "norm_memx_g", T)
            stage_product(nc, K, "mq", block_of(K.d["w_mq"][0]), KD, 4, xm, K.oB, "copy")
        stage_head_rms(nc, K, "memq", K.oB, 4, "ones", P, "mem_q_g", 1.0)
        stage_mem_prompt(nc, K, K.oB, mkT, mv, K.oA)
        stage_mem_sample(nc, K, K.oB, K.oA)
        stage_product(nc, K, "mo", block_of(K.d["w_mo"][0]), 4, KD, K.oA, x, "add")
        reuse_semaphores()
        with nc.sbuf_tensor("xf", [P, KD, T], F32) as xf, nc.sbuf_tensor("hid", [P, KD, T], F32) as hid:
            stage_rms(nc, K, "ffn", x, xf, "norm_ffn_g", T)
            for z in range(4):
                stage_product(nc, K, f"f1{z}", block_of(K.d["w_ff1"][0][:, D * z:D * z + D]), KD, KD, xf, hid, "relu2")
                stage_product(nc, K, f"f2{z}", block_of(K.d["w_ff2"][0][D * z:D * z + D, :]), KD, KD, hid, x, "add")
        stage_store(nc, K, x)


_INS = ["x_prompt", "x_sample", "state_rwkv", "state_shift", "state_pool", "cache_cmp_k", "cache_cmp_v", "cache_slc_k",
        "cache_slc_v", "cache_win_k", "cache_win_v", "cache_mem_k", "cache_mem_v", "page_table", "mem_prompt", "rel_bias",
        "norm_mix_g", "w_in", "shift_mu", "rwkv_w0", "rwkv_w2", "rwkv_a0", "rwkv_a2", "rwkv_g2", "rwkv_kk", "rwkv_ka",
        "rwkv_rk", "rwkv_lnx_g", "rwkv_lnx_b", "pool_w", "pool_scale", "nsa_q_g", "nsa_k_g", "w_br_a", "w_br_b", "w_br_c",
        "w_out", "norm_memx_g", "norm_mem_g", "w_mq", "w_mk", "w_mv", "mem_q_g", "mem_k_g", "w_mo", "norm_ffn_g",
        "w_ff1", "w_ff2"]
_OUTS = [("y_prompt", (1, TP, D)), ("y_sample", (DB, DT, D)),
         ("p_state_rwkv", (1, 1, 8, 64, 64)), ("p_state_shift", (1, 1, A_COLS)), ("p_state_pool", (1, 1, 15, 512)),
         ("p_cmp_k", (1, 1, TP, 2, 64)), ("p_cmp_v", (1, 1, TP, 2, 64)), ("p_slc_k", (1, 1, TP, 2, 64)),
         ("p_slc_v", (1, 1, TP, 2, 64)), ("p_win_k", (1, 1, 512, 2, 64)), ("p_win_v", (1, 1, 512, 2, 64)),
         ("p_mem_k", (1, 1, 256, 4, 128)), ("p_mem_v", (1, 1, 256, 4, 128)),
         ("s_state_rwkv", (1, DB, 8, 64, 64)), ("s_state_shift", (1, DB, A_COLS)), ("s_state_pool", (1, DB, 15, 512)),
         ("s_cmp_k", (1, DB, DT, 2, 64)), ("s_cmp_v", (1, DB, DT, 2, 64)), ("s_slc_k", (1, DB, DT, 2, 64)),
         ("s_slc_v", (1, DB, DT, 2, 64)), ("s_win_k", (1, DB, 512, 2, 64)), ("s_win_v", (1, DB, 512, 2, 64))]
_CONSTS = {"sheet": SHEET, "keep": KEEP, "onehot": ONEHOT}


def kernel(**inputs):
    import numpy as _np
    import concourse.bacc as _bacc
    from concourse import mybir as _mybir
    from concourse.bass_utils import run_bass_kernel_spmd as _run

    nc = _bacc.Bacc("TRN2", target_bir_lowering=False, num_devices=1)
    arrays, aps = {}, {}
    for name in _INS:
        a = _np.ascontiguousarray(inputs[name])
        arrays[f"in_{name}"] = a
        aps[name] = nc.dram_tensor(f"in_{name}", a.shape, _mybir.dt.from_np(a.dtype), kind="ExternalInput").ap()
    for name, a in _CONSTS.items():
        arrays[f"const_{name}"] = a
        aps[name] = nc.dram_tensor(f"const_{name}", a.shape, F32, kind="ExternalInput").ap()
    for name, shape in _OUTS:
        aps[name] = nc.dram_tensor(f"out_{name}", shape, F32, kind="ExternalOutput").ap()
    build(nc, aps)
    r = _run(nc, [arrays], core_ids=[0])
    return tuple(r.results[0][f"out_{name}"] for name, _ in _OUTS)
```

```python
from contextlib import ExitStack

import numpy as np

import concourse.bass as bass
from concourse import mybir


class Shared:
    pass


F32 = mybir.dt.float32
I32 = mybir.dt.int32
F32R = mybir.dt.float32r
ALU = mybir.AluOpType
ACT = mybir.ActivationFunctionType
AX = mybir.AxisListType

P = 128
D = 1024
KD = D // P
TP = 1024
DB, DT = 8, 4
TS = DB * DT
T = TP + TS
NC3 = 3
NW = T // NC3
TAIL = 15 + TS
T0 = T - TAIL
NTI = TP // P
A_COLS = 1792
OFF_POOL = A_COLS
OFF_Q = OFF_POOL + 512
OFF_KV = OFF_Q + 512
OFF_CG = OFF_KV + 768
OFF_MG = OFF_CG + 24
KVG = 768 + 24
PAST = 2048
PAGE = 128
NPG = PAST // PAGE
NEG = -1e30
RMS_EPS = 1e-6
LNX_EPS = 64e-5
DECAY = float(np.exp(-0.5))
REV = 2111
BVL = REV + 1025

BLOCKS = ([[(128 * c, 128)] for c in range(4)] + [[(576 + 128 * c, 128)] for c in range(4)]
          + [[(1088 + 128 * c, 128)] for c in range(4)] + [[(512, 64), (1600, 64)], [(1664, 128)]]
          + [[(OFF_POOL + 128 * c, 128)] for c in range(4)] + [[(OFF_Q + 128 * c, 128)] for c in range(4)])
B_R, B_K, B_V, B_WA, B_G, B_POOL, B_Q = 0, 4, 8, 12, 13, 14, 18
NSHIFT = 14

PARAMS = [("norm_mix_g", 8), ("shift_mu", NSHIFT), ("rwkv_w0", 4), ("rwkv_a0", 4), ("rwkv_kk", 4), ("rwkv_ka", 4),
          ("rwkv_rk", 4), ("rwkv_lnx_g", 4), ("rwkv_lnx_b", 4), ("pool_scale", 4), ("norm_memx_g", 8),
          ("norm_mem_g", 8), ("norm_ffn_g", 8), ("mem_q_g", 1), ("nsa_q_g", 1), ("kg_cmp", 1)]
PCOL = {}
_at = 0
for _n, _c in PARAMS:
    PCOL[_n] = _at
    _at += _c
NPAR = _at


def shape_constants():
    cols, sheets = {}, []

    def put(name, a):
        b = np.zeros((P, a.shape[1]), np.float32)
        b[:a.shape[0]] = a
        cols[name] = (sum(s.shape[1] for s in sheets), a.shape[1])
        sheets.append(b)

    r = np.arange(P)
    put("ident", np.eye(P))
    put("flip", np.eye(P)[::-1])
    put("headsum", (r[:, None] // 64 == r[None, :] // 64).astype(np.float32))
    put("ones", np.ones((P, P)))

    def chunk_masks(tag, n, levels, size):
        i, t = np.arange(n)[:, None], np.arange(n)[None, :]
        same = i // size == t // size
        put("strict" + tag, (same & (i < t)) * 1.0)
        put("incl" + tag, (same & (i <= t)) * 1.0)
        for l in range(levels):
            s = 1 << l
            m = (i // (2 * s) == t // (2 * s)) & (t // s % 2 == 1) & (i // s % 2 == 0)
            put(f"lvl{l}" + tag, m * 1.0)
        put("low0" + tag, ((t // 2 == i // 2) & (i % 2 == 1) & (t % 2 == 0)) * 1.0)
    chunk_masks("P", 128, 7, 128)
    chunk_masks("S", TS, 2, DT)
    i = np.arange(TS)
    put("batch", (i[:, None] // DT == np.arange(DB)[None, :]) * 1.0)
    put("batchcol", np.repeat(np.kron(np.eye(DB), np.ones((1, DT))).reshape(1, -1), P, 0))
    put("edge", np.where(r[:, None] < r[None, :], 0.0, NEG))
    put("poolcnt", np.concatenate([np.repeat((1.0 / np.minimum(w, np.arange(16) + 1))[None], P, 0)
                                   for w in (2, 4, 8, 16)], 1))
    m = np.zeros((P, 64))
    m[:64, 30] = 1 / 64
    m[64:, 31] = 1 / 64
    put("blk", m)
    t = r % 4
    put("edgeS", np.where(np.arange(4)[None, :] <= t[:, None], NEG, 0.0))
    put("grp", (r[:, None] % 32 // 16 == np.arange(2)[None, :]) * 1.0)
    put("mhead", (r[:, None] % 32 // 4 == np.arange(4)[None, :]) * 1.0)
    put("heads4", ((r[:, None] // 16 == r[None, :] // 16) & (t[:, None] == t[None, :])) * 1.0)
    m = np.arange(-14, 16)
    put("cmask", (r[:, None] - 64 * m[None, :] - 63 >= 0) * 1.0)
    keep = np.ones((1, T))
    keep[0, 0:TP:P] = 0
    keep[0, TP:T:DT] = 0
    dist = REV - np.arange(BVL)
    n = np.maximum(dist, 0)
    ratio = np.log(np.maximum(n, 1) / 16) / np.log(8)
    bucket = np.where(n < 16, n, np.minimum(16 + (ratio * 16).astype(np.int64), 31))
    onehot = (bucket[None, :] == np.arange(32)[:, None]) & (dist >= 0)[None]
    onehot = np.concatenate([onehot, (dist < 0)[None]], 0)
    return cols, np.concatenate(sheets, 1).astype(np.float32), keep.astype(np.float32), onehot.astype(np.float32)


CCOL, SHEET, KEEP, ONEHOT = shape_constants()


def stage_load(nc, K):
    ctx = ExitStack()
    with ctx:
        xin = ctx.enter_context(nc.sbuf_tensor("xin", [P, 3, D], F32))
        prow = ctx.enter_context(nc.sbuf_tensor("prow", [NPAR, P], F32))
        srow = ctx.enter_context(nc.sbuf_tensor("srow", [DB, A_COLS], F32))
        block = ctx.enter_context(nc.Block())
        s_const, s_prow, s_x = K.sem("const_in"), K.sem("param_rows_in"), K.sems("x_in", 3)
        s_par, s_parc = K.sem("params_turned"), K.sem("params_copied")
        s_xt, s_xa, s_xv = K.sem("x_turned"), K.sem("x_copied_act"), K.sem("x_copied_dve")
        s_sh = K.sem("shift_turned")

        @block.sync
        def _(e):
            e.dma_start(K.cst[:, :], K.d["sheet"]).then_inc(s_const, 16)
            e.dma_start(K.keep[:, :], K.d["keep"].partition_broadcast(P)).then_inc(s_const, 16)
            e.dma_start(srow[:, :], K.d["state_shift"][0]).then_inc(s_const, 16)
            for i in range(NTI + 1):
                if i >= 3:
                    e.wait_ge(s_xt, i - 2)
                if i < NTI:
                    e.dma_start(xin[:, i % 3, :], K.d["x_prompt"][0, P * i:P * i + P, :]).then_inc(s_x[i % 3], 16)
                else:
                    e.dma_start(xin[0:TS, i % 3, :], K.d["x_sample"].rearrange("b t d -> (b t) d")).then_inc(s_x[i % 3], 16)

        @block.scalar
        def _(e):
            for name, cnt in PARAMS:
                if name in ("nsa_q_g", "kg_cmp"):
                    src = K.d["nsa_q_g"][0:1, :] if name == "nsa_q_g" else K.d["nsa_k_g"][0, 0:1, :]
                    for z in range(2):
                        e.dma_start(prow[PCOL[name]:PCOL[name] + 1, 64 * z:64 * z + 64], src).then_inc(s_prow, 16)
                    continue
                if name == "shift_mu":
                    for b in range(NSHIFT):
                        at = 0
                        for c0, w in BLOCKS[b]:
                            e.dma_start(prow[PCOL[name] + b:PCOL[name] + b + 1, at:at + w],
                                        K.d["shift_mu"][0:1, c0:c0 + w]).then_inc(s_prow, 16)
                            at += w
                    continue
                src = K.d[name]
                if name == "rwkv_rk":
                    src = src.rearrange("a (c h) d -> (a c) (h d)", c=cnt)
                else:
                    src = src.rearrange("a (c p) -> (a c) p", p=P)
                e.dma_start(prow[PCOL[name]:PCOL[name] + cnt, :], src).then_inc(s_prow, 16)
            for i in range(NTI + 1):
                n = P if i < NTI else TS
                e.wait_ge(s_xt, i + 1)
                e.activation(K.xT[:, 0:4, P * i:P * i + n],
                             K.ps[:, 2 * (i % 2), :].rearrange("p (k n) -> p k n", k=4)[:, :, 0:n],
                             ACT.Copy).then_inc(s_xa, 1)

        @block.tensor
        def _(e):
            e.wait_ge(s_const, 48)
            ident = K.c("ident")
            e.wait_ge(s_prow, 16 * K.n_prow)
            e.transpose(K.ps[:, 4, 0:NPAR], prow[:, :], ident[0:NPAR, 0:NPAR]).then_inc(s_par, 1)
            for b in range(NSHIFT):
                at = 0
                for c0, w in BLOCKS[b]:
                    if at == 0:
                        mm = e.transpose(K.ps[0:w, 5, 8 * b:8 * b + 8], srow[:, c0:c0 + w], ident[0:DB, 0:DB])
                    else:
                        mm = e.transpose(K.ps[0:w, 6, 0:8], srow[:, c0:c0 + w], ident[0:DB, 0:DB])
                    at += w
            mm.then_inc(s_sh, 1)
            for i in range(NTI + 1):
                n = P if i < NTI else TS
                e.wait_ge(s_x[i % 3], 16 * (i // 3 + 1))
                if i >= 2:
                    e.wait_ge(s_xa, i - 1)
                    e.wait_ge(s_xv, i - 1)
                for k in range(KD):
                    mm = e.transpose(K.ps[:, 2 * (i % 2) + k // 4, P * (k % 4):P * (k % 4) + n],
                                     xin[0:n, i % 3, P * k:P * k + P], ident[0:n, 0:n])
                mm.then_inc(s_xt, 1)

        @block.vector
        def _(e):
            e.wait_ge(s_par, 1)
            e.tensor_copy(K.par[:, 0:NPAR], K.ps[:, 4, 0:NPAR])
            e.wait_ge(s_sh, 1)
            e.tensor_copy(K.shT[:, 0:B_WA, :], K.ps[:, 5, 0:8 * B_WA].rearrange("p (b n) -> p b n", n=8))
            e.tensor_copy(K.shT[:, B_G, :], K.ps[:, 5, 8 * B_G:8 * B_G + 8])
            e.tensor_copy(K.shT[0:64, B_WA, :], K.ps[0:64, 5, 8 * B_WA:8 * B_WA + 8])
            e.tensor_copy(K.shT[64:128, B_WA, :], K.ps[0:64, 6, 0:8])
            for i in range(NTI + 1):
                n = P if i < NTI else TS
                e.wait_ge(s_xt, i + 1)
                e.tensor_copy(K.xT[:, 4:8, P * i:P * i + n],
                              K.ps[:, 2 * (i % 2) + 1, :].rearrange("p (k n) -> p k n", k=4)[:, :, 0:n]).then_inc(s_xv, 1)


def stage_rms(nc, K, name, src, hi, lo, gain, ntok):
    nchunk = -(-ntok // NW)
    w = ntok // nchunk
    ctx = ExitStack()
    with ctx:
        sq = ctx.enter_context(nc.sbuf_tensor(name + "_sq", [P, 2, KD, w], F32))
        rstd = ctx.enter_context(nc.sbuf_tensor(name + "_rstd", [P, 2, w], F32))
        block = ctx.enter_context(nc.Block())
        s_sq, s_sum, s_nrm, s_hi = (K.sem(name + x) for x in ("_squared", "_summed", "_normed", "_high"))
        s_var, s_root, s_lo = K.sem(name + "_mean"), K.sem(name + "_root"), K.sem(name + "_low")

        @block.scalar
        def _(e):
            def squares(c):
                if c >= 2:
                    e.wait_ge(s_lo, c - 1)
                e.activation(sq[:, c % 2, :, :], src[:, :, w * c:w * c + w], ACT.Square).then_inc(s_sq, 1)

            squares(0)
            for c in range(nchunk):
                e.wait_ge(s_var, c + 1)
                e.activation(rstd[:, c % 2, :], rstd[:, c % 2, :], ACT.Sqrt).then_inc(s_root, 1)
                if c + 1 < nchunk:
                    squares(c + 1)
                e.wait_ge(s_nrm, c + 1)
                e.activation(hi[:, :, w * c:w * c + w], sq[:, c % 2, :, :], ACT.Copy).then_inc(s_hi, 1)

        @block.tensor
        def _(e):
            for c in range(nchunk):
                e.wait_ge(s_sq, c + 1)
                if c >= 2:
                    e.wait_ge(s_var, c - 1)
                for k in range(KD):
                    mm = e.matmul(K.ps[:, c % 2, 0:w], K.c("ones"), sq[:, c % 2, k, :], start=k == 0, stop=k == KD - 1)
                mm.then_inc(s_sum, 1)

        @block.vector
        def _(e):
            for c in range(nchunk):
                e.wait_ge(s_sum, c + 1)
                e.tensor_scalar(rstd[:, c % 2, :], K.ps[:, c % 2, 0:w], 1.0 / D, RMS_EPS,
                                ALU.mult, ALU.add).then_inc(s_var, 1)
                e.wait_ge(s_root, c + 1)
                e.reciprocal(rstd[:, c % 2, :], rstd[:, c % 2, :])
                e.drain()
                for k in range(KD):
                    e.scalar_tensor_tensor(sq[:, c % 2, k, :], src[:, k, w * c:w * c + w],
                                           K.p(gain, k), rstd[:, c % 2, :], ALU.mult, ALU.mult)
                e.drain().then_inc(s_nrm, 1)
                e.wait_ge(s_hi, c + 1)
                e.tensor_tensor(lo[:, :, w * c:w * c + w], sq[:, c % 2, :, :], hi[:, :, w * c:w * c + w].bitcast(F32),
                                ALU.subtract).then_inc(s_lo, 1)


def stage_split(nc, K, name, src, hi, lo, nblk):
    with nc.Block() as block:
        s_hi = K.sem(name + "_high")

        @block.scalar
        def _(e):
            for m in range(nblk):
                e.activation(hi[:, m, :], src[:, m, :], ACT.Copy).then_inc(s_hi, 1)

        @block.vector
        def _(e):
            for m in range(nblk):
                e.wait_ge(s_hi, m + 1)
                e.tensor_tensor(lo[:, m, :], src[:, m, :], hi[:, m, :].bitcast(F32), ALU.subtract)


NRAW = 3
NSPL = 2


def weight_slots(nc, K, ctx, tag, kb, nraw=NRAW):
    W = Shared()
    W.kb, W.nraw = kb, nraw
    W.raw = ctx.enter_context(nc.sbuf_tensor(tag + "_raw", [P, nraw, kb, P], F32))
    W.hi = ctx.enter_context(nc.sbuf_tensor(tag + "_high", [P, NSPL, kb, P], F32R))
    W.lo = ctx.enter_context(nc.sbuf_tensor(tag + "_low", [P, NSPL, kb, P], F32R))
    W.s_in = K.sems(tag + "_weights_in", nraw)
    W.s_hi, W.s_lo, W.s_mm = K.sem(tag + "_weights_high"), K.sem(tag + "_weights_low"), K.sem(tag + "_product")
    return W


def load_block(e, W, m, pieces):
    if m >= W.nraw:
        e.wait_ge(W.s_lo, m - W.nraw + 1)
    at = 0
    for src in pieces:
        w = src.shape[1]
        e.dma_start(W.raw[:, m % W.nraw, :, at:at + w], src.rearrange("(k p) n -> p k n", p=P)).then_inc(W.s_in[m % W.nraw], 16)
        at += w


def high_block(e, W, m, landed, per=1):
    e.wait_ge(W.s_in[m % W.nraw], 16 * landed)
    if m >= NSPL:
        e.wait_ge(W.s_mm, per * (m - NSPL + 1))
    e.activation(W.hi[:, m % NSPL, :, :], W.raw[:, m % W.nraw, 0:W.kb, :], ACT.Copy).then_inc(W.s_hi, 1)


def low_block(e, W, m):
    e.wait_ge(W.s_hi, m + 1)
    e.tensor_tensor(W.lo[:, m % NSPL, :, :], W.raw[:, m % W.nraw, 0:W.kb, :], W.hi[:, m % NSPL, :, :].bitcast(F32),
                    ALU.subtract).then_inc(W.s_lo, 1)


def product(e, K, W, m, rh, rl, bank, ks):
    z = m % NSPL
    for c in range(NC3):
        o, n = K.ps[:, bank + c, 0:NW], slice(NW * c, NW * c + NW)
        for k in ks:
            e.matmul(o, W.hi[:, z, k, :], rh[:, k, n], start=k == ks[0], stop=False)
            e.matmul(o, W.hi[:, z, k, :], rl[:, k, n], start=False, stop=False)
            mm = e.matmul(o, W.lo[:, z, k, :], rh[:, k, n], start=False, stop=k == ks[-1])
    return mm


def stage_proj_a(nc, K, xs, first, count, xh, xl):
    ctx = ExitStack()
    tag = f"pj{first}"
    with ctx:
        shifted = first == 0
        W = weight_slots(nc, K, ctx, tag, KD)
        if shifted:
            u = ctx.enter_context(nc.sbuf_tensor(tag + "_u", [P, 2, 1 + TP + DB * (DT + 1)], F32))
            dlt = ctx.enter_context(nc.sbuf_tensor(tag + "_d", [P, T], F32))
        block = ctx.enter_context(nc.Block())
        s_raw, s_used = K.sem(tag + "_raw_copied"), K.sem(tag + "_raw_used")
        landed = {}
        for m in range(count):
            landed[m] = landed.get(m - NRAW, 0) + len(BLOCKS[first + m])

        @block.sync
        def _(e):
            for m in range(count):
                load_block(e, W, m, [K.d["w_in"][0, :, c0:c0 + w] for c0, w in BLOCKS[first + m]])

        @block.tensor
        def _(e):
            for m in range(count):
                e.wait_ge(W.s_lo, m + 1)
                if m >= 2:
                    e.wait_ge(s_raw, m - 1)
                product(e, K, W, m, xh, xl, 3 * (m % 2), range(KD)).then_inc(W.s_mm, 1)

        @block.scalar
        def _(e):
            high_block(e, W, 0, landed[0])
            high_block(e, W, 1, landed[1])
            for m in range(count):
                e.wait_ge(W.s_mm, m + 1)
                bank = K.ps[:, 3 * (m % 2):3 * (m % 2) + 3, :]
                if shifted:
                    if m >= 2:
                        e.wait_ge(s_used, m - 1)
                    for c in range(2):
                        e.activation(u[:, m % 2, 1 + NW * c:1 + NW * c + NW], bank[:, c, 0:NW], ACT.Copy)
                    e.activation(u[:, m % 2, 1 + 2 * NW:1 + TP], bank[:, 2, 0:TP - 2 * NW], ACT.Copy)
                    us = u[:, m % 2, 1 + TP:].rearrange("p (b t) -> p b t", t=DT + 1)
                    e.activation(us[:, :, 1:], bank[:, 2, TP - 2 * NW:NW].rearrange("p (b t) -> p b t", t=DT), ACT.Copy)
                else:
                    e.activation(xs[:, m, :].rearrange("p (c n) -> p c n", c=NC3), bank[:, :, 0:NW], ACT.Copy)
                if first + m < B_Q:
                    e.activation(K.utail[:, first + m, :], bank[:, 2, NW - TAIL:NW], ACT.Copy).then_inc(s_raw, 1)
                else:
                    e.drain().then_inc(s_raw, 1)
                if m + 2 < count:
                    high_block(e, W, m + 2, landed[m + 2])

        @block.vector
        def _(e):
            low_block(e, W, 0)
            low_block(e, W, 1)
            if shifted:
                e.memset(u[:, 0, 0:1], 0.0)
                e.memset(u[:, 1, 0:1], 0.0)
            for m in range(count):
                if m + 2 < count:
                    low_block(e, W, m + 2)
                if not shifted:
                    continue
                us = u[:, m % 2, 1 + TP:].rearrange("p (b t) -> p b t", t=DT + 1)
                e.tensor_copy(us[:, :, 0:1], K.shT[:, m, :].unsqueeze(2))
                e.wait_ge(s_raw, m + 1)
                e.drain()
                up = u[:, m % 2, 0:1 + TP]
                e.tensor_tensor(dlt[:, 0:TP], up[:, 0:TP], up[:, 1:1 + TP], ALU.subtract)
                e.tensor_tensor(dlt[:, TP:T].rearrange("p (b t) -> p b t", t=DT), us[:, :, 0:DT], us[:, :, 1:DT + 1],
                                ALU.subtract)
                e.drain()
                e.scalar_tensor_tensor(xs[:, m, 0:TP], dlt[:, 0:TP], K.p("shift_mu", m), up[:, 1:1 + TP],
                                       ALU.mult, ALU.add)
                e.scalar_tensor_tensor(xs[:, m, TP:T].rearrange("p (b t) -> p b t", t=DT),
                                       dlt[:, TP:T].rearrange("p (b t) -> p b t", t=DT), K.p("shift_mu", m),
                                       us[:, :, 1:DT + 1], ALU.mult, ALU.add).then_inc(s_used, 1)
                e.drain()


def stage_rwkv_prep(nc, K, xs, ld):
    KK, A, L = K.oA, K.oB, K.oC
    ctx = ExitStack()
    with ctx:
        w2 = ctx.enter_context(nc.sbuf_tensor("rw_w2a2", [P, 512], F32))
        sq = ctx.enter_context(nc.sbuf_tensor("rw_sq", [P, T], F32))
        inv = ctx.enter_context(nc.sbuf_tensor("rw_inv", [P, T], F32))
        block = ctx.enter_context(nc.Block())
        s_w, s_th = K.sem("rw_lora_in"), K.sem("rw_tanh")
        s_z, s_sig = K.sem("rw_lora_product"), K.sem("rw_sigmoid")
        s_kk, s_sq, s_ss = K.sem("rw_kk_scaled"), K.sem("rw_kk_squared"), K.sem("rw_kk_summed")
        s_mx, s_rt = K.sem("rw_sum_guarded"), K.sem("rw_root")

        @block.sync
        def _(e):
            e.dma_start(w2[0:64, :], K.d["rwkv_w2"][0]).then_inc(s_w, 16)
            e.dma_start(w2[64:128, :], K.d["rwkv_a2"][0]).then_inc(s_w, 16)

        @block.scalar
        def _(e):
            e.activation(xs[0:64, B_WA, :], xs[0:64, B_WA, :], ACT.Tanh).then_inc(s_th, 1)
            for m in range(8):
                e.wait_ge(s_z, m + 1)
                dst = (ld if m < 4 else A)[:, m % 4, :].rearrange("p (c n) -> p c n", c=NC3)
                e.activation(dst, K.ps[:, 3 * (m % 2):3 * (m % 2) + 3, 0:NW], ACT.Sigmoid,
                             bias=K.p("rwkv_w0" if m < 4 else "rwkv_a0", m % 4)).then_inc(s_sig, 1)
            for c in range(4):
                e.wait_ge(s_kk, c + 1)
                if c >= 1:
                    e.wait_ge(s_ss, c)
                e.activation(sq[:, :], KK[:, c, :], ACT.Square).then_inc(s_sq, 1)
                e.wait_ge(s_mx, c + 1)
                e.activation(inv[:, :], inv[:, :], ACT.Sqrt).then_inc(s_rt, 1)

        @block.tensor
        def _(e):
            e.wait_ge(s_w, 32)
            e.wait_ge(s_th, 1)
            for m in range(8):
                o = 0 if m < 4 else 64
                if m >= 2:
                    e.wait_ge(s_sig, m - 1)
                for c in range(NC3):
                    mm = e.matmul(K.ps[:, 3 * (m % 2) + c, 0:NW], w2[o:o + 64, 128 * (m % 4):128 * (m % 4) + 128],
                                  xs[o:o + 64, B_WA, NW * c:NW * c + NW], start=True, stop=True)
                mm.then_inc(s_z, 1)
            e.wait_ge(s_sig, 8)
            for c in range(4):
                e.wait_ge(s_sq, c + 1)
                if c >= 1:
                    e.wait_ge(s_mx, c)
                for n in range(NC3):
                    mm = e.matmul(K.ps[:, n, 0:NW], K.c("headsum"), sq[:, NW * n:NW * n + NW], start=True, stop=True)
                mm.then_inc(s_ss, 1)

        @block.vector
        def _(e):
            for c in range(4):
                e.tensor_scalar(KK[:, c, :], xs[:, B_K + c, :], K.p("rwkv_kk", c), None, ALU.mult).then_inc(s_kk, 1)
            e.tensor_scalar(K.par[:, NPAR:NPAR + 4], K.par[:, PCOL["rwkv_ka"]:PCOL["rwkv_ka"] + 4], -1.0, 1.0,
                            ALU.mult, ALU.add)
            for c in range(4):
                e.wait_ge(s_sig, c + 1)
                e.tensor_scalar(ld[:, c, :], ld[:, c, :], -DECAY, None, ALU.mult)
                e.drain()
                e.tensor_tensor_scan(L[:, c, :], K.keep[:, :], ld[:, c, :], 0.0, ALU.mult, ALU.add)
            for c in range(4):
                e.wait_ge(s_ss, c + 1)
                e.tensor_scalar(inv[:, :].rearrange("p (c n) -> p c n", c=NC3), K.ps[:, 0:3, 0:NW], 1e-24, None,
                                ALU.max).then_inc(s_mx, 1)
                e.wait_ge(s_rt, c + 1)
                e.reciprocal(inv[:, :], inv[:, :])
                e.drain()
                e.tensor_tensor(KK[:, c, :], KK[:, c, :], inv[:, :], ALU.mult)
                e.drain()
                e.tensor_scalar(inv[:, :], A[:, c, :], K.p("rwkv_ka", c), K.par[:, NPAR + c:NPAR + c + 1],
                                ALU.mult, ALU.add)
                e.drain()
                e.tensor_tensor(xs[:, B_K + c, :], xs[:, B_K + c, :], inv[:, :], ALU.mult)
                e.tensor_tensor(A[:, c, :], A[:, c, :], KK[:, c, :], ALU.mult)
                e.drain()


def stage_rwkv_scan(nc, K, xs, ld, tag, n, levels, nchunk, tbase, S0, mid):
    KK, B, L = K.oA, K.oB, K.oC
    sample = tag == "S"
    ctx = ExitStack()
    with ctx:
        sb = lambda nm, sh: ctx.enter_context(nc.sbuf_tensor("sc" + tag + nm, sh, F32))
        D1, D2 = sb("D1", [P, 4, n]), sb("D2", [P, 4, n])
        EN = sb("EN", [P, 4, n])
        KtR = sb("KtR", [P, 4, 2, n])
        Bt, Kc, Vc = sb("Bt", [P, 4, n]), sb("Kc", [P, 4, n]), sb("Vc", [P, 4, n])
        fac = sb("fac", [P, 4])
        BtT, KcT, VT = sb("BtT", [n, 512]), sb("KcT", [n, 512]), sb("VT", [n, 512])
        MT, RBT, NT, RKT = (sb(x, [n, 8, n]) for x in ("MT", "RBT", "NT", "RKT"))
        X, XT, T1 = (sb(x, [n, 8, n]) for x in ("X", "XT", "T1"))
        Mn = [sb(f"Mn{z}", [n, 8, n]) for z in range(2 if sample else 1)]
        RH, SA = sb("RH", [n, 512]), sb("SA", [n, 512])
        if sample:
            KtB = sb("KtB", [P, 4, DB, TS])
            RB4 = sb("RB4", [P, 4, DB, TS])
            SAB = sb("SAB", [n, 2, DB, 64])
        block = ctx.enter_context(nc.Block())
        sem = lambda nm: K.sem(f"sc{tag}_{nm}")
        s_d, s_e = sem("exponents"), sem("decays")
        s_prep, s_vc = sem("operands"), sem("values_copied")
        s_tr, s_trc = sem("turned"), sem("turned_copied")
        s_ab, s_msk = sem("scores"), sem("scores_masked")
        s_mn, s_t1, s_t1c, s_z, s_x = sem("level_masked"), sem("level_half"), sem("level_half_copied"), sem("level_step"), sem("inverse_updated")
        s_rh, s_rhc, s_sa, s_sac = sem("rhs"), sem("rhs_copied"), sem("corrections"), sem("corrections_copied")
        s_y, s_yc, s_st, s_stu = sem("outputs"), sem("outputs_copied"), sem("state_sum"), sem("state_updated")
        NLV = levels - 1
        ps = K.ps
        bank = lambda h: 2 * (h % 2) + h // 4
        pos = lambda h: (h // 2) % 2

        def tok(i):
            return bass.ds(tbase + n * i, n) if not isinstance(i, int) else slice(tbase + n * i, tbase + n * i + n)

        def col(i, at):
            return bass.ds(tbase + n * i + at, 1) if not isinstance(i, int) else slice(tbase + n * i + at, tbase + n * i + at + 1)

        msk = lambda nm: K.c(nm + tag)[0:n, 0:n].unsqueeze(1)

        def mid_of(i):
            return L[:, :, col(i, mid)].to_broadcast([P, 4, n])

        @block.vector
        def _(e):
            for i in range(nchunk):
                if i >= 1:
                    e.wait_ge(s_e, 2 * i)
                if sample:
                    e.tensor_copy(D1[:, :, :], L[:, :, tok(i)])
                else:
                    e.tensor_tensor(D1[:, :, :], L[:, :, tok(i)], mid_of(i), ALU.subtract)
                e.drain()
                e.tensor_tensor(D2[:, :, :], D1[:, :, :], ld[:, :, tok(i)], ALU.subtract).then_inc(s_d, 1)
                e.wait_ge(s_e, 2 * i + 1)
                if i >= 1:
                    e.wait_ge(s_y, i)
                e.tensor_tensor(KtR[:, :, 0, :], KK[:, :, tok(i)], D2[:, :, :], ALU.mult)
                e.tensor_tensor(KtR[:, :, 1, :], xs[:, B_R:B_R + 4, tok(i)], D1[:, :, :], ALU.mult)
                e.tensor_tensor(Bt[:, :, :], B[:, :, tok(i)], EN[:, :, :], ALU.mult)
                e.tensor_tensor(Kc[:, :, :], xs[:, B_K:B_K + 4, tok(i)], EN[:, :, :], ALU.mult)
                if not sample:
                    e.tensor_tensor(fac[:, :].unsqueeze(2), L[:, :, col(i, n - 1)], L[:, :, col(i, mid)], ALU.subtract)
                    if i < nchunk - 1:
                        e.drain()
                        e.tensor_tensor(fac[:, :].unsqueeze(2), fac[:, :].unsqueeze(2), L[:, :, col(i + 1, mid)], ALU.add)
                e.drain().then_inc(s_prep, 1)
                if sample:
                    bc = K.c("batchcol").rearrange("p (b t) -> p b t", b=DB)
                    for q in range(4):
                        for dst, z in ((KtB, 0), (RB4, 1)):
                            e.tensor_tensor(dst[:, q, :, :], KtR[:, q, z, :].unsqueeze(1).to_broadcast([P, DB, TS]), bc, ALU.mult)
                    e.drain().then_inc(s_prep, 1)
                for h in range(8):
                    e.wait_ge(s_ab, 24 * i + 8)
                    v = ps[0:n, bank(h), :].rearrange("p (z n) -> p z n", z=2)[:, pos(h), 0:2 * n]
                    e.scalar_tensor_tensor(MT[:, h, :], v[:, 0:n], 3e38, K.c("strict" + tag)[0:n, 0:n], ALU.min, ALU.mult)
                    e.scalar_tensor_tensor(RBT[:, h, :], v[:, n:2 * n], 3e38, K.c("incl" + tag)[0:n, 0:n], ALU.min, ALU.mult).then_inc(s_msk, 1)
                for h in range(8):
                    e.wait_ge(s_ab, 24 * i + 16)
                    v = ps[0:n, 4 + bank(h), :].rearrange("p (z n) -> p z n", z=2)[:, pos(h), 0:2 * n]
                    e.scalar_tensor_tensor(NT[:, h, :], v[:, 0:n], 3e38, K.c("strict" + tag)[0:n, 0:n], ALU.min, ALU.mult)
                    e.scalar_tensor_tensor(RKT[:, h, :], v[:, n:2 * n], 3e38, K.c("incl" + tag)[0:n, 0:n], ALU.min, ALU.mult).then_inc(s_msk, 1)
                e.wait_ge(s_ab, 24 * i + 24)
                for z in range(2):
                    v = ps[0:n, z, 0:4 * n].rearrange("p (h n) -> p h n", h=4)
                    e.scalar_tensor_tensor(X[:, z::2, :], v, 3e38, msk("low0").to_broadcast([n, 4, n]), ALU.min, ALU.mult)
                e.tensor_tensor(XT[:, :, :], MT[:, :, :], msk("lvl0").to_broadcast([n, 8, n]), ALU.mult)
                e.drain()
                idn = K.c("ident")[0:n, 0:n].unsqueeze(1).to_broadcast([n, 8, n])
                e.tensor_tensor(X[:, :, :], idn, X[:, :, :], ALU.subtract)
                e.tensor_tensor(XT[:, :, :], idn, XT[:, :, :], ALU.subtract)
                e.drain().then_inc(s_x, 2)
                for l in range(NLV):
                    for z in range(2):
                        e.wait_ge(s_z, 2 * (NLV * i + l) + z + 1)
                        zz = ps[0:n, 2 + z, 0:4 * n].rearrange("p (h n) -> p h n", h=4)
                        e.tensor_tensor(X[:, 4 * z:4 * z + 4, :], X[:, 4 * z:4 * z + 4, :], zz, ALU.subtract)
                        zt = ps[0:n, 4 + z, 0:4 * n].rearrange("p (h n) -> p h n", h=4)
                        e.tensor_tensor(XT[:, 4 * z:4 * z + 4, :], XT[:, 4 * z:4 * z + 4, :], zt, ALU.subtract)
                        e.drain().then_inc(s_x, 1)
                e.wait_ge(s_sa, i + 1)
                e.tensor_copy(SA[:, :].rearrange("p (h z d) -> p h z d", z=2, d=64),
                              ps[0:n, 0:2, 0:256].rearrange("p z (h d) -> p h z d", d=64)).then_inc(s_sac, 1)
                if sample:
                    e.drain()
                    bm = K.c("batch")[0:n, :].unsqueeze(2).to_broadcast([n, DB, 64])
                    for h in range(8):
                        e.wait_ge(s_st, h) if h else None
                        e.tensor_tensor(SAB[:, 0, :, :], SA[:, 64 * h:64 * h + 64].unsqueeze(1).to_broadcast([n, DB, 64]), bm, ALU.mult)
                        e.tensor_tensor(SAB[:, 1, :, :], VT[:, 64 * h:64 * h + 64].unsqueeze(1).to_broadcast([n, DB, 64]), bm, ALU.mult)
                        e.drain().then_inc(s_sac, 1)
                        e.wait_ge(s_st, h + 1)
                        pp = 64 * (h % 2)
                        st = S0[pp:pp + 64, h // 2, :, :]
                        e.tensor_tensor(st, st, ps[pp:pp + 64, 4 + h % 2, :].rearrange("p (b d) -> p b d", b=DB), ALU.add)
                        e.drain()
                        e.tensor_tensor(st, st, D1[pp:pp + 64, h // 2, DT - 1::DT].unsqueeze(2).to_broadcast([64, DB, 64]), ALU.mult)
                        e.drain()
                else:
                    e.wait_ge(s_st, i + 1)
                    e.tensor_tensor(S0[:, :, :], S0[:, :, :], ps[:, 4, 0:256].rearrange("p (c d) -> p c d", c=4), ALU.add)
                    e.wait_ge(s_e, 2 * i + 2)
                    e.drain()
                    e.tensor_tensor(S0[:, :, :], S0[:, :, :], fac[:, :].unsqueeze(2).to_broadcast([P, 4, 64]), ALU.mult)
                    e.drain().then_inc(s_stu, 1)

        @block.scalar
        def _(e):
            for i in range(nchunk):
                e.wait_ge(s_d, i + 1)
                if i >= 1:
                    e.wait_ge(s_prep, i)
                e.activation(EN[:, :, :], D1[:, :, :], ACT.Exp, scale=-1.0)
                e.drain()
                e.activation(D1[:, :, :], D1[:, :, :], ACT.Exp)
                e.activation(D2[:, :, :], D2[:, :, :], ACT.Exp)
                e.drain().then_inc(s_e, 1)
                if sample:
                    e.wait_ge(s_prep, 1)
                else:
                    e.wait_ge(s_prep, i + 1)
                    e.activation(fac[:, :], fac[:, :], ACT.Exp).then_inc(s_e, 1)
                for z, dst in enumerate((BtT, KcT, VT)):
                    e.wait_ge(s_tr, 3 * i + z + 1)
                    e.activation(dst[:, :], ps[0:n, z, :], ACT.Copy).then_inc(s_trc, 1)
                for l in range(2 * NLV):
                    z = l % 2
                    e.wait_ge(s_t1, 2 * NLV * i + l + 1)
                    e.activation(T1[:, 4 * z:4 * z + 4, :], ps[0:n, z, 0:4 * n].rearrange("p (h n) -> p h n", h=4),
                                 ACT.Copy).then_inc(s_t1c, 1)
                e.wait_ge(s_rh, i + 1)
                e.activation(RH[:, :].rearrange("p (h z d) -> p h z d", z=2, d=64),
                             ps[0:n, 6:8, 0:256].rearrange("p z (h d) -> p h z d", d=64), ACT.Copy, scale=-1.0).then_inc(s_rhc, 1)
                e.wait_ge(s_y, i + 1)
                for z in range(2):
                    e.activation(KK[64 * z:64 * z + 64, :, tok(i)],
                                 ps[64 * z:64 * z + 64, 2 + z, 0:4 * n].rearrange("p (c n) -> p c n", c=4), ACT.Copy)
                e.drain().then_inc(s_yc, 1)

        @block.gpsimd
        def _(e):
            for i in range(nchunk):
                if i >= 1:
                    e.wait_ge(s_y, i)
                e.tensor_copy(Vc[:, :, :], xs[:, B_V:B_V + 4, tok(i)]).then_inc(s_vc, 1)
                e.wait_ge(s_msk, 16 * i + 8)
                for l in range(NLV):
                    if not sample:
                        if NLV * i + l >= 1:
                            e.wait_ge(s_t1, 2 * (NLV * i + l))
                    e.tensor_tensor(Mn[l % len(Mn)][:, :, :], MT[:, :, :], msk(f"lvl{l + 1}").to_broadcast([n, 8, n]),
                                    ALU.mult).then_inc(s_mn, 1)

        @block.tensor
        def _(e):
            ident = K.c("ident")
            for i in range(nchunk):
                e.wait_ge(s_prep, (2 if sample else 1) * (i + 1))
                e.wait_ge(s_vc, i + 1)
                if i >= 1:
                    e.wait_ge(s_stu, i)
                    e.wait_ge(s_yc, i)
                for z, src in enumerate((Bt, Kc, Vc)):
                    for c in range(4):
                        mm = e.transpose(ps[0:n, z, P * c:P * c + P], src[:, c, :], ident)
                    mm.then_inc(s_tr, 1)
                e.wait_ge(s_trc, 3 * i + 3)
                for src, b0 in ((Bt, 0), (Kc, 4)):
                    for h in range(8):
                        pp = 64 * (h % 2)
                        e.matmul(ps[0:n, b0 + bank(h), 256 * pos(h):256 * pos(h) + 2 * n], src[pp:pp + 64, h // 2, :],
                                 KtR[pp:pp + 64, h // 2, :, :].rearrange("p z n -> p (z n)"), start=True, stop=True).then_inc(s_ab, 1)
                e.wait_ge(s_msk, 16 * i + 8)
                for h in range(8):
                    pp = 64 * (h % 2)
                    e.matmul(ps[0:n, h % 2, n * (h // 2):n * (h // 2) + n], KtR[pp:pp + 64, h // 2, 0, :],
                             Bt[pp:pp + 64, h // 2, :], start=True, stop=True).then_inc(s_ab, 1)
                e.wait_ge(s_msk, 16 * i + 16)
                for l in range(NLV):
                    e.wait_ge(s_mn, NLV * i + l + 1)
                    for z in range(2):
                        e.wait_ge(s_x, 2 * ((NLV + 1) * i + l) + z + 1)
                        for h in range(4 * z, 4 * z + 4):
                            mm = e.matmul(ps[0:n, z, n * (h % 4):n * (h % 4) + n], Mn[l % len(Mn)][:, h, :], X[:, h, :], start=True, stop=True)
                        mm.then_inc(s_t1, 1)
                    for z in range(2):
                        e.wait_ge(s_t1c, 2 * (NLV * i + l) + z + 1)
                        for h in range(4 * z, 4 * z + 4):
                            e.matmul(ps[0:n, 2 + z, n * (h % 4):n * (h % 4) + n], XT[:, h, :], T1[:, h, :], start=True, stop=True)
                            mm = e.matmul(ps[0:n, 4 + z, n * (h % 4):n * (h % 4) + n], T1[:, h, :], XT[:, h, :], start=True, stop=True)
                        mm.then_inc(s_z, 1)
                e.wait_ge(s_x, 2 * (NLV + 1) * (i + 1))
                for h in range(8):
                    pp, hh = 64 * (h % 2), h // 2
                    o = ps[0:n, 6 + h % 2, 64 * hh:64 * hh + 64]
                    if sample:
                        for b in range(DB):
                            e.matmul(o, KtB[pp:pp + 64, hh, b, :], S0[pp:pp + 64, hh, b, :], start=b == 0, stop=False)
                    else:
                        e.matmul(o, KtR[pp:pp + 64, hh, 0, :], S0[pp:pp + 64, hh, :], start=True, stop=False)
                    mm = e.matmul(o, NT[:, h, :], VT[:, 64 * h:64 * h + 64], start=False, stop=True)
                mm.then_inc(s_rh, 1)
                e.wait_ge(s_rhc, i + 1)
                for h in range(8):
                    mm = e.matmul(ps[0:n, h % 2, 64 * (h // 2):64 * (h // 2) + 64], XT[:, h, :], RH[:, 64 * h:64 * h + 64],
                                  start=True, stop=True)
                mm.then_inc(s_sa, 1)
                e.wait_ge(s_sac, i + 1)
                for h in range(8):
                    pp, hh = 64 * (h % 2), h // 2
                    o = ps[pp:pp + 64, 2 + h % 2, n * hh:n * hh + n]
                    if sample:
                        for b in range(DB):
                            e.matmul(o, S0[pp:pp + 64, hh, b, :], RB4[pp:pp + 64, hh, b, :], start=b == 0, stop=False)
                    else:
                        e.matmul(o, S0[pp:pp + 64, hh, :], KtR[pp:pp + 64, hh, 1, :], start=True, stop=False)
                    e.matmul(o, SA[:, 64 * h:64 * h + 64], RBT[:, h, :], start=False, stop=False)
                    mm = e.matmul(o, VT[:, 64 * h:64 * h + 64], RKT[:, h, :], start=False, stop=True)
                mm.then_inc(s_y, 1)
                if sample:
                    for h in range(8):
                        pp = 64 * (h % 2)
                        e.wait_ge(s_sac, h + 2)
                        o = ps[pp:pp + 64, 4 + h % 2, :]
                        e.matmul(o, BtT[:, 64 * h:64 * h + 64], SAB[:, 0, :, :].rearrange("p b d -> p (b d)"), start=True, stop=False)
                        e.matmul(o, KcT[:, 64 * h:64 * h + 64], SAB[:, 1, :, :].rearrange("p b d -> p (b d)"), start=False, stop=True).then_inc(s_st, 1)
                else:
                    for h in range(8):
                        pp, hh = 64 * (h % 2), h // 2
                        o = ps[pp:pp + 64, 4, 64 * hh:64 * hh + 64]
                        e.matmul(o, BtT[:, 64 * h:64 * h + 64], SA[:, 64 * h:64 * h + 64], start=True, stop=False)
                        mm = e.matmul(o, KcT[:, 64 * h:64 * h + 64], VT[:, 64 * h:64 * h + 64], start=False, stop=True)
                    mm.then_inc(s_st, 1)


def stage_rwkv_states(nc, K, tag, S0, src, outs):
    nb = DB if tag == "S" else 1
    ctx = ExitStack()
    nm = f"st{tag}{'i' if src is not None else 'o'}"
    with ctx:
        rows = ctx.enter_context(nc.sbuf_tensor(nm + "rows", [64, nb, 8, 64], F32))
        low = ctx.enter_context(nc.sbuf_tensor(nm + "low", [64, nb, 8, 64], F32)) if outs is not None else None
        block = ctx.enter_context(nc.Block())
        s_in, s_t, s_c = K.sem(nm + "_in"), K.sem(nm + "_turned"), K.sem(nm + "_copied")
        s_low, s_out = K.sem(nm + "_lowered"), K.out_sem(nm + "_stored")
        st4 = S0 if tag == "S" else S0[:, :, :].unsqueeze(2)
        if src is not None:
            @block.sync
            def _(e):
                e.dma_start(rows[:, :, :, :], src.rearrange("b h i j -> i b h j")).then_inc(s_in, 16)

            @block.tensor
            def _(e):
                e.wait_ge(s_in, 16)
                for b in range(nb):
                    if b >= 2:
                        e.wait_ge(s_c, b - 1)
                    for h in range(8):
                        mm = e.transpose(K.ps[0:64, b % 2, 64 * h:64 * h + 64], rows[:, b, h, :], K.c("ident")[0:64, 0:64])
                    mm.then_inc(s_t, 1)

            @block.vector
            def _(e):
                for b in range(nb):
                    e.wait_ge(s_t, b + 1)
                    for z in range(2):
                        e.tensor_copy(st4[64 * z:64 * z + 64, :, b, :],
                                      K.ps[0:64, b % 2, :].rearrange("p (c z d) -> p c z d", z=2, d=64)[:, :, z, :])
                    e.drain().then_inc(s_c, 1)
        else:
            @block.tensor
            def _(e):
                e.wait_ge(s_low, 1)
                for b in range(nb):
                    if b >= 2:
                        e.wait_ge(s_c, b - 1)
                    for h in range(8):
                        mm = e.transpose(K.ps[0:64, b % 2, 64 * h:64 * h + 64], low[:, b, h, :], K.c("ident")[0:64, 0:64])
                    mm.then_inc(s_t, 1)

            @block.vector
            def _(e):
                for z in range(2):
                    for b in range(nb):
                        e.tensor_copy(low[:, b, z::2, :], st4[64 * z:64 * z + 64, :, b, :])
                e.drain().then_inc(s_low, 1)
                for b in range(nb):
                    e.wait_ge(s_t, b + 1)
                    e.tensor_copy(rows[:, b, :, :], K.ps[0:64, b % 2, :].rearrange("p (h d) -> p h d", h=8)).then_inc(s_c, 1)

            @block.sync
            def _(e):
                e.wait_ge(s_c, nb)
                e.dma_start(outs.rearrange("b h i j -> i b h j"), rows[:, :, :, :]).then_inc(s_out, 16)
                e.wait_ge(s_out, 16)


def stage_rwkv_out(nc, K, xs):
    Y = K.oA
    ctx = ExitStack()
    with ctx:
        g2 = ctx.enter_context(nc.sbuf_tensor("ro_g2", [P, 512], F32))
        sq = ctx.enter_context(nc.sbuf_tensor("ro_sq", [P, 2, T], F32))
        rt = ctx.enter_context(nc.sbuf_tensor("ro_root", [P, T], F32))
        block = ctx.enter_context(nc.Block())
        s_w, s_sg, s_mean, s_cen, s_sq = K.sem("ro_gate_w_in"), K.sem("ro_gate_sig"), K.sem("ro_means"), K.sem("ro_centred"), K.sem("ro_squared")
        s_rk, s_var, s_ve, s_rt, s_bon, s_g, s_fin = (K.sem("ro_" + x) for x in
                                                   ("rk", "variances", "variance_eps", "rooted", "bonus_sum", "gate", "final"))
        c3 = lambda ap: ap.rearrange("p (c n) -> p c n", c=NC3)

        @block.sync
        def _(e):
            e.dma_start(g2[:, :], K.d["rwkv_g2"][0]).then_inc(s_w, 16)

        @block.scalar
        def _(e):
            e.activation(xs[:, B_G, :], xs[:, B_G, :], ACT.Sigmoid).then_inc(s_sg, 1)
            for c in range(4):
                e.wait_ge(s_cen, c + 1)
                e.activation(sq[:, 0, :], Y[:, c, :], ACT.Square).then_inc(s_sq, 1)
                e.wait_ge(s_ve, c + 1)
                e.activation(rt[:, :], rt[:, :], ACT.Sqrt).then_inc(s_rt, 1)

        @block.tensor
        def _(e):
            hs = K.c("headsum")
            e.wait_ge(s_w, 16)
            for c in range(4):
                if c >= 1:
                    e.wait_ge(s_fin, c)
                for n in range(NC3):
                    mm = e.matmul(K.ps[:, n, 0:NW], hs, Y[:, c, NW * n:NW * n + NW], start=True, stop=True)
                mm.then_inc(s_mean, 1)
                e.wait_ge(s_rk, c + 1)
                for n in range(NC3):
                    mm = e.matmul(K.ps[:, 3 + n, 0:NW], hs, sq[:, 1, NW * n:NW * n + NW], start=True, stop=True)
                mm.then_inc(s_bon, 1)
                e.wait_ge(s_sq, c + 1)
                for n in range(NC3):
                    mm = e.matmul(K.ps[:, n, 0:NW], hs, sq[:, 0, NW * n:NW * n + NW], start=True, stop=True)
                mm.then_inc(s_var, 1)
                e.wait_ge(s_sg, 1)
                e.wait_ge(s_ve, c + 1)
                for n in range(NC3):
                    mm = e.matmul(K.ps[:, n, 0:NW], g2[:, P * c:P * c + P], xs[:, B_G, NW * n:NW * n + NW], start=True, stop=True)
                mm.then_inc(s_g, 1)

        @block.vector
        def _(e):
            for c in range(4):
                e.wait_ge(s_mean, c + 1)
                e.scalar_tensor_tensor(c3(Y[:, c, :]), K.ps[:, 0:3, 0:NW], -1.0 / 64, c3(Y[:, c, :]), ALU.mult, ALU.add).then_inc(s_cen, 1)
                e.tensor_tensor(sq[:, 1, :], xs[:, B_R + c, :], xs[:, B_K + c, :], ALU.mult)
                e.drain()
                e.tensor_scalar(sq[:, 1, :], sq[:, 1, :], K.p("rwkv_rk", c), None, ALU.mult).then_inc(s_rk, 1)
                e.wait_ge(s_var, c + 1)
                e.tensor_scalar(c3(rt[:, :]), K.ps[:, 0:3, 0:NW], 1.0 / 64, LNX_EPS, ALU.mult, ALU.add).then_inc(s_ve, 1)
                e.wait_ge(s_bon, c + 1)
                e.tensor_tensor(c3(xs[:, B_V + c, :]), c3(xs[:, B_V + c, :]), K.ps[:, 3:6, 0:NW], ALU.mult)
                e.wait_ge(s_rt, c + 1)
                e.reciprocal(rt[:, :], rt[:, :])
                e.drain()
                e.tensor_tensor(Y[:, c, :], Y[:, c, :], rt[:, :], ALU.mult)
                e.drain()
                e.tensor_scalar(Y[:, c, :], Y[:, c, :], K.p("rwkv_lnx_g", c), K.p("rwkv_lnx_b", c), ALU.mult, ALU.add)
                e.drain()
                e.tensor_tensor(Y[:, c, :], Y[:, c, :], xs[:, B_V + c, :], ALU.add)
                e.drain()
                e.wait_ge(s_g, c + 1)
                e.tensor_tensor(c3(Y[:, c, :]), c3(Y[:, c, :]), K.ps[:, 0:3, 0:NW], ALU.mult)
                e.drain().then_inc(s_fin, 1)


def stage_move(nc, K, name, moves):
    with nc.Block() as block:
        s_moved = K.sem(name)

        @block.gpsimd
        def _(e):
            for dst, src in moves:
                e.dma_start(dst, src).then_inc(s_moved, 16)
            e.wait_ge(s_moved, 16 * len(moves))


def stage_tail_rows(nc, K):
    ctx = ExitStack()
    with ctx:
        rows = ctx.enter_context(nc.sbuf_tensor("tail_rows", [TAIL, B_Q, P], F32))
        block = ctx.enter_context(nc.Block())
        s_t, s_c, s_out = K.sem("tail_turned"), K.sem("tail_copied"), K.out_sem("tail_stored")

        @block.tensor
        def _(e):
            for b in range(B_Q):
                mm = e.transpose(K.ps[0:TAIL, b // 4, P * (b % 4):P * (b % 4) + P], K.utail[:, b, :], K.c("ident"))
            mm.then_inc(s_t, 1)

        @block.vector
        def _(e):
            e.wait_ge(s_t, 1)
            e.tensor_copy(rows[:, :, :].rearrange("p b n -> p (b n)"),
                          K.ps[0:TAIL, 0:5, :].rearrange("p a n -> p (a n)")[:, 0:B_Q * P]).then_inc(s_c, 1)

        @block.sync
        def _(e):
            n = 0
            e.wait_ge(s_c, 1)
            for b in range(NSHIFT):
                at = 0
                for c0, w in BLOCKS[b]:
                    e.dma_start(K.d["p_state_shift"][0, :, c0:c0 + w], rows[14:15, b, at:at + w]).then_inc(s_out, 16)
                    e.dma_start(K.d["s_state_shift"][0, :, c0:c0 + w], rows[15 + DT - 1:TAIL:DT, b, at:at + w]).then_inc(s_out, 16)
                    at += w
                    n += 2
            e.dma_start(K.d["p_state_pool"][0, 0].rearrange("t (b n) -> t b n", n=P), rows[0:15, B_POOL:B_Q, :]).then_inc(s_out, 16)
            e.dma_start(K.d["s_state_pool"][0, :, 0:15 - DT, :], K.d["state_pool"][0, :, DT:15, :]).then_inc(s_out, 16)
            for b in range(DB):
                e.dma_start(K.d["s_state_pool"][0, b, 15 - DT:15, :].rearrange("t (b n) -> t b n", n=P),
                            rows[15 + DT * b:15 + DT * b + DT, B_POOL:B_Q, :]).then_inc(s_out, 16)
            n += 2 + DB
            e.wait_ge(s_out, 16 * n)


def stage_pool(nc, K, up):
    ctx = ExitStack()
    with ctx:
        sb = lambda nm, sh: ctx.enter_context(nc.sbuf_tensor("po_" + nm, sh, F32))
        srow = sb("state", [DB * 15, 512])
        pw = sb("w", [P, 4, P])
        EP, ES = sb("ext", [P, 4, 15 + TP]), sb("exts", [P, 4, DB, 15 + DT])
        TPp, TSs = sb("sums", [P, 2, 15 + TP]), sb("sumss", [P, 2, DB, 15 + DT])
        dd = sb("diff", [P, 4, T])
        block = ctx.enter_context(nc.Block())
        s_in, s_t, s_cp, s_c2 = K.sem("po_in"), K.sem("po_turned"), K.sem("po_extended"), K.sem("po_state_copied")
        s_d, s_z, s_w = K.sem("po_differences"), K.sem("po_mapped"), K.sem("po_scaled")

        @block.sync
        def _(e):
            e.dma_start(srow[:, :], K.d["state_pool"][0].rearrange("b t n -> (b t) n")).then_inc(s_in, 16)
            e.dma_start(pw[:, :, :], K.d["pool_w"][0].rearrange("g c n -> c g n")).then_inc(s_in, 16)

        @block.scalar
        def _(e):
            e.activation(EP[:, :, 15:], up[:, :, 0:TP], ACT.Copy)
            for g in range(4):
                e.activation(ES[:, g, :, 15:], up[:, g, TP:T].rearrange("p (b t) -> p b t", t=DT), ACT.Copy)
            e.drain().then_inc(s_cp, 1)
            for g in range(4):
                e.wait_ge(s_z, g + 1)
                e.activation(K.oB[:, g, :].rearrange("p (c n) -> p c n", c=NC3),
                             K.ps[:, 3 * (g % 2):3 * (g % 2) + 3, 0:NW], ACT.Copy, scale=K.p("pool_scale", g)).then_inc(s_w, 1)

        @block.tensor
        def _(e):
            e.wait_ge(s_in, 32)
            for g in range(4):
                mm = e.transpose(K.ps[:, 7, 120 * g:120 * g + 120], srow[:, P * g:P * g + P], K.c("ident")[0:120, 0:120])
            mm.then_inc(s_t, 1)
            for g in range(4):
                e.wait_ge(s_d, g + 1)
                if g >= 2:
                    e.wait_ge(s_w, g - 1)
                for c in range(NC3):
                    mm = e.matmul(K.ps[:, 3 * (g % 2) + c, 0:NW], pw[:, g, :], dd[:, g, NW * c:NW * c + NW], start=True, stop=True)
                mm.then_inc(s_z, 1)

        @block.vector
        def _(e):
            e.memset(EP[:, :, 0:15], 0.0)
            e.wait_ge(s_t, 1)
            for g in range(4):
                e.tensor_copy(ES[:, g, :, 0:15], K.ps[:, 7, 120 * g:120 * g + 120].rearrange("p (b t) -> p b t", t=15))
            e.wait_ge(s_cp, 1)
            e.drain()
            LP, LS = 15 + TP, 15 + DT
            for g in range(4):
                a, s = EP[:, g, :], ES[:, g, :, :]
                for l in range(g + 1):
                    w, o = 1 << l, (2 << l) - 1
                    e.tensor_tensor(TPp[:, l % 2, o:LP], a[:, o:LP], a[:, o - w:LP - w], ALU.add)
                    e.tensor_tensor(TSs[:, l % 2, :, o:LS], s[:, :, o:LS], s[:, :, o - w:LS - w], ALU.add)
                    e.drain()
                    a, s = TPp[:, l % 2, :], TSs[:, l % 2, :, :]
                inv = 1.0 / (2 << g)
                e.scalar_tensor_tensor(dd[:, g, 16:TP], a[:, 31:LP], inv, EP[:, g, 31:LP], ALU.mult, ALU.subtract)
                e.tensor_tensor(dd[:, g, 0:16], a[:, 15:31], K.c("poolcnt")[:, 16 * g:16 * g + 16], ALU.mult)
                e.scalar_tensor_tensor(dd[:, g, TP:T].rearrange("p (b t) -> p b t", t=DT), s[:, :, 15:], inv,
                                       ES[:, g, :, 15:], ALU.mult, ALU.subtract)
                e.drain()
                e.tensor_tensor(dd[:, g, 0:16], dd[:, g, 0:16], EP[:, g, 15:31], ALU.subtract)
                e.drain().then_inc(s_d, 1)


def stage_head_rms(nc, K, name, q, nblk, mask, width, gain, scale):
    ctx = ExitStack()
    with ctx:
        sq = ctx.enter_context(nc.sbuf_tensor(name + "_sq", [P, 2, T], F32))
        rt = ctx.enter_context(nc.sbuf_tensor(name + "_root", [P, 2, T], F32))
        block = ctx.enter_context(nc.Block())
        s_sq, s_sum, s_me, s_rt = (K.sem(f"{name}_{x}") for x in ("squared", "summed", "mean", "rooted"))

        @block.scalar
        def _(e):
            def squares(c):
                if c >= 2:
                    e.wait_ge(s_sum, c - 1)
                e.activation(sq[:, c % 2, :], q[:, c, :], ACT.Square).then_inc(s_sq, 1)
            squares(0)
            for c in range(nblk):
                if c + 1 < nblk:
                    squares(c + 1)
                e.wait_ge(s_me, c + 1)
                e.activation(rt[:, c % 2, :], rt[:, c % 2, :], ACT.Sqrt).then_inc(s_rt, 1)

        @block.tensor
        def _(e):
            for c in range(nblk):
                e.wait_ge(s_sq, c + 1)
                if c >= 2:
                    e.wait_ge(s_me, c - 1)
                for n in range(NC3):
                    mm = e.matmul(K.ps[:, 3 * (c % 2) + n, 0:NW], K.c(mask), sq[:, c % 2, NW * n:NW * n + NW], start=True, stop=True)
                mm.then_inc(s_sum, 1)

        @block.vector
        def _(e):
            for c in range(nblk):
                e.wait_ge(s_sum, c + 1)
                e.tensor_scalar(rt[:, c % 2, :].rearrange("p (c n) -> p c n", c=NC3), K.ps[:, 3 * (c % 2):3 * (c % 2) + 3, 0:NW],
                                1.0 / width / scale ** 2, RMS_EPS / scale ** 2, ALU.mult, ALU.add).then_inc(s_me, 1)
                e.wait_ge(s_rt, c + 1)
                e.reciprocal(rt[:, c % 2, :], rt[:, c % 2, :])
                e.drain()
                e.scalar_tensor_tensor(q[:, c, :], q[:, c, :], K.p(gain, 0), rt[:, c % 2, :], ALU.mult, ALU.mult)
                e.drain()


def stage_kv(nc, K, kvt, xh, xl):
    HW = KVG // 2
    ctx = ExitStack()
    with ctx:
        raw = ctx.enter_context(nc.sbuf_tensor("kv_raw", [P, 2, 2, HW], F32))
        wh = ctx.enter_context(nc.sbuf_tensor("kv_high", [P, KD, HW], F32R))
        wl = ctx.enter_context(nc.sbuf_tensor("kv_low", [P, KD, HW], F32R))
        block = ctx.enter_context(nc.Block())
        s_in, s_hi, s_lo, s_mm, s_cp = K.sems("kv_w_in", 2), K.sem("kv_high"), K.sem("kv_low"), K.sem("kv_product"), K.sem("kv_copied")
        NT1 = NTI + 1
        tile = lambda i: (P * i, 0) if i < NTI else (T - P, P - TS)

        @block.sync
        def _(e):
            for q in range(8):
                z, k = q // 4, 2 * (q % 4)
                if q >= 2:
                    e.wait_ge(s_lo, q - 1)
                e.dma_start(raw[:, q % 2, :, :], K.d["w_in"][0, P * k:P * k + 2 * P, OFF_KV + HW * z:OFF_KV + HW * z + HW]
                            .rearrange("(k p) n -> p k n", p=P)).then_inc(s_in[q % 2], 16)

        @block.tensor
        def _(e):
            for z in range(2):
                for i in range(NT1):
                    a = tile(i)[0]
                    G = NT1 * z + i
                    if G >= 4:
                        e.wait_ge(s_cp, G - 3)
                    for k in range(KD):
                        if i == 0:
                            e.wait_ge(s_lo, 4 * z + k // 2 + 1)
                        o = K.ps[:, G % 4, 0:HW]
                        e.matmul(o, xh[:, k, a:a + P], wh[:, k, :], start=k == 0, stop=False)
                        e.matmul(o, xl[:, k, a:a + P], wh[:, k, :], start=False, stop=False)
                        mm = e.matmul(o, xh[:, k, a:a + P], wl[:, k, :], start=False, stop=k == KD - 1)
                    mm.then_inc(s_mm, 1)

        @block.scalar
        def _(e):
            for z in range(2):
                for q in range(4 * z, 4 * z + 4):
                    e.wait_ge(s_in[q % 2], 16 * (q // 2 + 1))
                    if z:
                        e.wait_ge(s_mm, NT1)
                    k = 2 * (q % 4)
                    e.activation(wh[:, k:k + 2, :], raw[:, q % 2, :, :], ACT.Copy).then_inc(s_hi, 1)
                for i in range(NT1):
                    r0 = tile(i)[1]
                    G = NT1 * z + i
                    e.wait_ge(s_mm, G + 1)
                    e.activation(kvt[0:P - r0, i, HW * z:HW * z + HW], K.ps[r0:P, G % 4, 0:HW], ACT.Copy).then_inc(s_cp, 1)

        @block.vector
        def _(e):
            for q in range(8):
                e.wait_ge(s_hi, q + 1)
                k = 2 * (q % 4)
                e.tensor_tensor(wl[:, k:k + 2, :], raw[:, q % 2, :, :], wh[:, k:k + 2, :].bitcast(F32), ALU.subtract).then_inc(s_lo, 1)


def stage_kv_norm(nc, K, kvt):
    ctx = ExitStack()
    with ctx:
        kg = ctx.enter_context(nc.sbuf_tensor("kv_gain", [P, 2, 64], F32))
        sq = ctx.enter_context(nc.sbuf_tensor("kv_sq", [P, 2, 8, 2, 64], F32))
        ss = ctx.enter_context(nc.sbuf_tensor("kv_ss", [P, 2, 2, 16], F32))
        block = ctx.enter_context(nc.Block())
        s_g = K.sem("kv_gain_in")
        s_v, s_r, s_k, s_out = K.sem("kv_mean"), K.sem("kv_rooted"), K.sem("kv_normed"), K.out_sem("kv_stored")

        @block.sync
        def _(e):
            e.dma_start(kg[:, :, :], K.d["nsa_k_g"][0, 1:3, :].partition_broadcast(P)).then_inc(s_g, 16)
            e.wait_ge(s_k, 1)
            pr = lambda name: K.d[name][0, 0].rearrange("(i p) g d -> p i (g d)", p=P)
            n = 0
            for z, nm in enumerate(("cmp_k", "cmp_v", "slc_k", "slc_v", "win_k", "win_v")):
                lo = NTI - 4 if z >= 4 else 0
                e.dma_start(pr("p_" + nm), kvt[:, lo:NTI, P * z:P * z + P]).then_inc(s_out, 16)
                n += 1
                if z < 4:
                    e.dma_start(K.d["s_" + nm][0].rearrange("b t g d -> (b t) (g d)"), kvt[0:TS, NTI, P * z:P * z + P]).then_inc(s_out, 16)
                    n += 1
                else:
                    e.dma_start(K.d["s_" + nm][0, :, 0:512 - DT], K.d["cache_" + nm][0, :, DT:512]).then_inc(s_out, 16)
                    n += 1
                    for b in range(DB):
                        e.dma_start(K.d["s_" + nm][0, b, 512 - DT:512].rearrange("t g d -> t (g d)"),
                                    kvt[DT * b:DT * b + DT, NTI, P * z:P * z + P]).then_inc(s_out, 16)
                        n += 1
            e.wait_ge(s_out, 16 * n)

        @block.scalar
        def _(e):
            for z in range(2):
                e.wait_ge(s_v, z + 1)
                m, cnt = (P, 16) if z == 0 else (TS, 2)
                e.activation(ss[0:m, z, :, 0:cnt], ss[0:m, z, :, 0:cnt], ACT.Sqrt).then_inc(s_r, 1)
            e.activation(kvt[:, 0:NTI, 768:KVG], kvt[:, 0:NTI, 768:KVG], ACT.Sigmoid)
            e.activation(kvt[0:TS, NTI, 768:KVG], kvt[0:TS, NTI, 768:KVG], ACT.Sigmoid)

        @block.vector
        def _(e):
            e.wait_ge(s_g, 16)
            for z, (m, lo, hi) in enumerate(((P, 0, NTI), (TS, NTI, NTI + 1))):
                nt = hi - lo
                for s in range(2):
                    kk = kvt[0:m, lo:hi, 256 + 256 * s:384 + 256 * s].rearrange("p i (g d) -> p i g d", g=2)
                    e.tensor_tensor(sq[0:m, s, 0:nt, :, :], kk, kk, ALU.mult)
                    e.drain()
                    e.tensor_reduce(ss[0:m, z, s, 0:2 * nt], sq[0:m, s, 0:nt, :, :].rearrange("p i g d -> p (i g) d"), AX.X, ALU.add)
                e.drain()
                e.tensor_scalar(ss[0:m, z, :, 0:2 * nt], ss[0:m, z, :, 0:2 * nt], 1.0 / 64, RMS_EPS, ALU.mult, ALU.add).then_inc(s_v, 1)
                e.wait_ge(s_r, z + 1)
                e.reciprocal(ss[0:m, z, :, 0:2 * nt], ss[0:m, z, :, 0:2 * nt])
                e.drain()
                for s in range(2):
                    kk = kvt[0:m, lo:hi, 256 + 256 * s:384 + 256 * s].rearrange("p i (g d) -> p i g d", g=2)
                    e.tensor_tensor(kk, kk, ss[0:m, z, s, 0:2 * nt].rearrange("p (i g) -> p i g", g=2).unsqueeze(3).to_broadcast([m, nt, 2, 64]), ALU.mult)
                    e.drain()
                    for i in range(lo, hi):
                        k2 = kvt[0:m, i, 256 + 256 * s:384 + 256 * s].rearrange("p (g d) -> p g d", g=2)
                        e.tensor_tensor(k2, k2, kg[0:m, s, :].unsqueeze(1).to_broadcast([m, 2, 64]), ALU.mult)
            e.drain().then_inc(s_k, 1)


def stage_bias(nc, K, near, cb, b31):
    ctx = ExitStack()
    with ctx:
        rb = ctx.enter_context(nc.sbuf_tensor("bi_rel", [33, 8], F32))
        oh = ctx.enter_context(nc.sbuf_tensor("bi_onehot", [33, BVL], F32))
        bv = ctx.enter_context(nc.sbuf_tensor("bi_vector", [8, BVL], F32))
        block = ctx.enter_context(nc.Block())
        s_in, s_ms, s_mm, s_c, s_d, s_t, s_fl = (K.sem("bi_" + x) for x in (
            "in", "neg_set", "spread", "copied", "stored", "tiles_in", "tiles_flipped"))
        W = BVL // 7

        @block.sync
        def _(e):
            e.dma_start(oh[:, :], K.d["onehot"]).then_inc(s_in, 16)
            e.wait_ge(s_ms, 1)
            e.dma_start(rb[0:32, :], K.d["rel_bias"]).then_inc(s_in, 16)
            e.dma_start(b31[:, :], K.d["rel_bias"][31, :].partition_broadcast(P)).then_inc(s_t, 16)
            e.wait_ge(s_c, 1)
            e.dma_start(K.bvec, bv[:, :]).then_inc(s_d, 16)
            e.wait_ge(s_d, 16)
            v = K.bvec.tensor
            for h in range(8):
                e.dma_start(near[:, h, :], bass.AP(tensor=v, offset=h * BVL + REV - 2 * P + 1, ap=[[1, P], [1, 2 * P]])).then_inc(s_t, 16)
                e.dma_start(cb[:, h, :], bass.AP(tensor=v, offset=h * BVL + REV + 63 - 64 * 14 - P + 1, ap=[[1, P], [64, 30]]),
                            allow_slow_non_contiguous=True).then_inc(s_t, 16)

        @block.vector
        def _(e):
            e.memset(rb[:, :], NEG).then_inc(s_ms, 1)
            e.wait_ge(s_mm, 1)
            e.tensor_copy(bv[:, :].rearrange("p (z n) -> p z n", z=7), K.ps[0:8, 0:7, 0:W]).then_inc(s_c, 1)
            e.wait_ge(s_fl, 1)
            e.tensor_copy(near[:, :, :].rearrange("p (a h) n -> p a (h n)", h=2), K.ps[:, 0:4, :])
            e.tensor_copy(cb[:, :, :].rearrange("p h n -> p (h n)"), K.ps[:, 4, 0:240])

        @block.tensor
        def _(e):
            e.wait_ge(s_in, 32)
            for z in range(7):
                mm = e.matmul(K.ps[0:8, z, 0:W], rb[:, :], oh[:, W * z:W * z + W], start=True, stop=True)
            mm.then_inc(s_mm, 1)
            e.wait_ge(s_t, 16 * 17)
            e.wait_ge(s_c, 1)
            for a in range(4):
                e.matmul(K.ps[:, a, :], K.c("flip"), near[:, 2 * a:2 * a + 2, :].rearrange("p h n -> p (h n)"), start=True, stop=True)
            e.matmul(K.ps[:, 4, 0:240], K.c("flip"), cb[:, :, :].rearrange("p h n -> p (h n)"), start=True, stop=True).then_inc(s_fl, 1)


def stage_nsa_keys(nc, K, kvt, kcd, vc, ksd, kwd, ksn, kwn):
    ctx = ExitStack()
    with ctx:
        kc = ctx.enter_context(nc.sbuf_tensor("nk_kc", [P, 16], F32))
        sq = ctx.enter_context(nc.sbuf_tensor("nk_sq", [P, 16], F32))
        rt = ctx.enter_context(nc.sbuf_tensor("nk_rt", [P, 16], F32))
        block = ctx.enter_context(nc.Block())
        s_t, s_c, s_new, s_m, s_sq, s_s, s_v, s_r = (K.sem("nk_" + x) for x in (
            "turned", "copied", "new_turned", "means", "squared", "summed", "mean_sq", "rooted"))
        CUT = ((0, 0), (1, 1))

        @block.tensor
        def _(e):
            blk, ident = K.c("blk"), K.c("ident")
            for i in range(NTI):
                e.matmul(K.ps[:, 4, 2 * i:2 * i + 2], kvt[:, i, 0:P], blk[:, 30:32], start=True, stop=True)
            for i in range(NTI):
                mm = e.matmul(K.ps[0:16, 5, 0:P], blk[:, 30 - 2 * i:46 - 2 * i], kvt[:, i, P:2 * P], start=i == 0, stop=i == NTI - 1)
            mm.then_inc(s_m, 1)
            for z in range(4):
                for i in range(4):
                    mm = e.transpose(K.ps[:, z, P * i:P * i + P], kvt[:, 4 * (z % 2) + i, 256 + 256 * (z // 2):384 + 256 * (z // 2)], ident)
                mm.then_inc(s_t, 1)
            e.transpose(K.ps[:, 6, 0:TS], kvt[0:TS, NTI, 256:384], ident[0:TS, 0:TS])
            e.transpose(K.ps[:, 6, TS:2 * TS], kvt[0:TS, NTI, 512:640], ident[0:TS, 0:TS]).then_inc(s_new, 1)
            e.wait_ge(s_sq, 1)
            e.matmul(K.ps[:, 7, 0:16], K.c("headsum"), sq[:, :], start=True, stop=True).then_inc(s_s, 1)

        @block.scalar
        def _(e):
            e.wait_ge(s_v, 1)
            e.activation(rt[:, :], rt[:, :], ACT.Sqrt).then_inc(s_r, 1)
            for z in range(4):
                e.wait_ge(s_t, z + 1)
                dst = (ksd, kwd)[z // 2]
                cs = slice(512 * (z % 2), 512 * (z % 2) + 512)
                e.activation(dst[0:64, 0, cs], K.ps[0:64, z, :], ACT.Copy)
                e.activation(dst[64:128, 0, cs], K.ps[0:64, z, :], ACT.Copy).then_inc(s_c, 1)

        @block.vector
        def _(e):
            e.wait_ge(s_m, 1)
            e.tensor_copy(kc[:, :], K.ps[:, 4, 0:16])
            e.tensor_copy(vc[:, :], K.ps[0:16, 5, 0:P])
            e.drain()
            e.tensor_tensor(sq[:, :], kc[:, :], kc[:, :], ALU.mult).then_inc(s_sq, 1)
            e.wait_ge(s_s, 1)
            e.tensor_scalar(rt[:, :], K.ps[:, 7, 0:16], 1.0 / 64, RMS_EPS, ALU.mult, ALU.add).then_inc(s_v, 1)
            e.wait_ge(s_r, 1)
            e.reciprocal(rt[:, :], rt[:, :])
            e.drain()
            e.scalar_tensor_tensor(kc[:, :], kc[:, :], K.p("kg_cmp", 0), rt[:, :], ALU.mult, ALU.mult)
            e.drain()
            for g in range(2):
                for half in range(2):
                    e.tensor_copy(kcd[64 * half:64 * half + 64, g, :], kc[64 * g:64 * g + 64, :])
            for z in range(4):
                e.wait_ge(s_t, z + 1)
                e.wait_ge(s_c, z + 1)
                dst = (ksd, kwd)[z // 2]
                cs = slice(512 * (z % 2), 512 * (z % 2) + 512)
                e.tensor_copy(dst[0:64, 1, cs], K.ps[64:128, z, :])
                e.tensor_copy(dst[64:128, 1, cs], K.ps[64:128, z, :])
            e.wait_ge(s_new, 1)
            e.tensor_copy(ksn[:, :], K.ps[:, 6, 0:TS])
            e.tensor_copy(kwn[:, :], K.ps[:, 6, TS:2 * TS])


def stage_nsa_prompt(nc, K, qT, kvt, kcd, vc, ksd, kwd, near, cb, b31):
    units = [(i, h) for i in range(NTI) for h in range(8)]
    NU = len(units)
    SW = TP + 5 * P + 16
    win = lambda i: list(range(max(0, i - 4), i + 1))
    cols = lambda i: (P * (i + 1), P * len(win(i)))

    def blocks(i):
        return [("s", j) for j in range(i + 1)] + [("w", j) for j in win(i)] + [("c", 0)]

    groups = lambda i: [blocks(i)[a:a + 4] for a in range(0, len(blocks(i)), 4)]
    gbase = [0]
    for i, h in units:
        gbase.append(gbase[-1] + len(groups(i)))
    ctx = ExitStack()
    with ctx:
        sb = lambda nm, sh: ctx.enter_context(nc.sbuf_tensor("np_" + nm, sh, F32))
        S = sb("scores", [P, 2, SW])
        nm = sb("negmax", [P, 2, 3])
        sm = sb("sums", [P, 2, 3])
        PT = sb("probsT", [P, 2, 512])
        co = sb("coef", [P, 2, 3])
        O = sb("out", [P, 2, 512])
        block = ctx.enter_context(nc.Block())
        s_s, s_ev, s_mx, s_ex = K.sem("np_scores"), K.sem("np_scores_out"), K.sem("np_max"), K.sem("np_exps")
        s_cm, s_pt, s_pc, s_o, s_oc = K.sem("np_masked"), K.sem("np_turned"), K.sem("np_turned_copied"), K.sem("np_values"), K.sem("np_combined")
        s_ot, s_oe = K.sem("np_out_turned"), K.sem("np_out_copied")

        def col_of(i, kind, j):
            return {"s": P * j, "w": TP + P * (j - win(i)[0]), "c": TP + 5 * P}[kind]

        @block.tensor
        def _(e):
            ident = K.c("ident")

            def scores(u):
                i, h = units[u]
                g, pp, c = h // 4, 64 * (h % 2), h // 2
                q = qT[pp:pp + 64, c, P * i:P * i + P]
                if u >= 1:
                    e.wait_ge(s_ev, u)
                ns, nw = cols(i)
                for a in range(0, ns, 512):
                    e.matmul(K.ps[:, a // 512, 0:min(512, ns - a)], q, ksd[pp:pp + 64, g, a:min(a + 512, ns)], start=True, stop=True)
                lo = P * win(i)[0]
                for a in range(0, nw, 512):
                    e.matmul(K.ps[:, 2 + a // 512, 0:min(512, nw - a)], q, kwd[pp:pp + 64, g, lo + a:lo + min(a + 512, nw)], start=True, stop=True)
                e.matmul(K.ps[:, 3, 256:272], q, kcd[pp:pp + 64, g, :], start=True, stop=True).then_inc(s_s, 1)

            def values(u):
                i, h = units[u]
                g = h // 4
                e.wait_ge(s_ex, u + 1)
                e.wait_ge(s_cm, u + 1)
                if u >= 2:
                    e.wait_ge(s_oc, u - 1)
                gs = groups(i)
                seen = set()

                def turn(n):
                    G = gbase[u] + n
                    if G >= 2:
                        e.wait_ge(s_pc, G - 1)
                    for z, (kind, j) in enumerate(gs[n]):
                        a = col_of(i, kind, j)
                        m = 16 if kind == "c" else P
                        mm = e.transpose(K.ps[0:m, 4 + G % 2, P * z:P * z + P], S[:, u % 2, a:a + m], ident)
                    mm.then_inc(s_pt, 1)

                turn(0)
                for n in range(len(gs)):
                    if n + 1 < len(gs):
                        turn(n + 1)
                    G = gbase[u] + n
                    e.wait_ge(s_pc, G + 1)
                    for z, (kind, j) in enumerate(gs[n]):
                        b = "swc".index(kind)
                        m = 16 if kind == "c" else P
                        v = vc[:, 64 * g:64 * g + 64] if kind == "c" else \
                            kvt[:, j, (384 if kind == "s" else 640) + 64 * g:(384 if kind == "s" else 640) + 64 * g + 64]
                        last = kind == "c" or j == i
                        mm = e.matmul(K.ps[:, 6 + u % 2, 64 * b:64 * b + 64], PT[0:m, G % 2, P * z:P * z + P], v,
                                      start=kind not in seen, stop=last)
                        seen.add(kind)
                mm.then_inc(s_o, 1)

            def turn_out(i):
                e.wait_ge(s_oc, 8 * i + 8)
                e.wait_ge(s_pc, gbase[8 * i + 8])
                if i == NTI - 1:
                    pass
                for c in range(4):
                    mm = e.transpose(K.ps[:, 7, P * c:P * c + P], O[:, i % 2, P * c:P * c + P], ident)
                mm.then_inc(s_ot, 1)
                e.wait_ge(s_oe, i + 1)

            scores(0)
            for u in range(NU):
                if u + 1 < NU:
                    scores(u + 1)
                values(u)
                if units[u][1] == 7:
                    turn_out(units[u][0])

        @block.vector
        def _(e):
            def softmax_in(u):
                i, h = units[u]
                b = u % 2
                e.wait_ge(s_s, u + 1)
                if u >= 2:
                    e.wait_ge(s_o, u - 1)
                ns, nw = cols(i)
                far = ns - 2 * P
                if far > 0:
                    e.tensor_scalar(S[:, b, 0:far], K.ps[:, 0:2, :].rearrange("p a n -> p (a n)")[:, 0:far], b31[:, h:h + 1], None, ALU.add)
                lo = max(far, 0)
                e.tensor_tensor(S[:, b, lo:ns], K.ps[:, 0:2, :].rearrange("p a n -> p (a n)")[:, lo:ns], near[:, h, 2 * P - (ns - lo):], ALU.add)
                pw = K.ps[:, 2:4, :].rearrange("p a n -> p (a n)")
                at = 0
                if i >= 4:
                    e.scalar_tensor_tensor(S[:, b, TP:TP + P], pw[:, 0:P], b31[:, h:h + 1], K.c("edge"), ALU.add, ALU.add)
                    at = P
                if nw - 2 * P > at:
                    e.tensor_scalar(S[:, b, TP + at:TP + nw - 2 * P], pw[:, at:nw - 2 * P], b31[:, h:h + 1], None, ALU.add)
                lo = max(nw - 2 * P, 0)
                e.tensor_tensor(S[:, b, TP + lo:TP + nw], pw[:, lo:nw], near[:, h, 2 * P - (nw - lo):], ALU.add)
                e.tensor_tensor(S[:, b, TP + 5 * P:SW], pw[:, 768:784], cb[:, h, 14 - 2 * i:30 - 2 * i], ALU.add).then_inc(s_ev, 1)
                e.drain()
                e.tensor_reduce(nm[:, b, 0:1], S[:, b, 0:ns], AX.X, ALU.max, negate=True)
                e.tensor_reduce(nm[:, b, 1:2], S[:, b, TP:TP + nw], AX.X, ALU.max, negate=True)
                e.tensor_reduce(nm[:, b, 2:3], S[:, b, TP + 5 * P:SW], AX.X, ALU.max, negate=True)
                e.drain().then_inc(s_mx, 1)

            def combine(u):
                i, h = units[u]
                b = u % 2
                e.wait_ge(s_ex, u + 1)
                e.reciprocal(co[:, b, :], sm[:, b, :])
                e.drain()
                gt = kvt[:, i, 768:KVG].rearrange("p (z h) -> p z h", z=3)
                e.tensor_tensor(co[:, b, 0:2], co[:, b, 0:2], gt[:, 1:3, h], ALU.mult)
                e.tensor_tensor(co[:, b, 2:3], co[:, b, 2:3], gt[:, 0:1, h], ALU.mult)
                e.wait_ge(s_o, u + 1)
                if h == 0 and i >= 2:
                    e.wait_ge(s_ot, i - 1)
                o = O[:, i % 2, 64 * h:64 * h + 64]
                e.drain()
                e.tensor_scalar(o, K.ps[:, 6 + b, 0:64], co[:, b, 0:1], None, ALU.mult)
                e.drain()
                e.scalar_tensor_tensor(o, K.ps[:, 6 + b, 64:128], co[:, b, 1:2], o, ALU.mult, ALU.add)
                e.drain()
                e.scalar_tensor_tensor(o, K.ps[:, 6 + b, 128:192], co[:, b, 2:3], o, ALU.mult, ALU.add).then_inc(s_oc, 1)
                if h == 7:
                    e.wait_ge(s_ot, i + 1)
                    e.tensor_copy(K.oC[:, :, P * i:P * i + P], K.ps[:, 7, :].rearrange("p (c n) -> p c n", c=4)).then_inc(s_oe, 1)

            softmax_in(0)
            for u in range(NU):
                if u + 1 < NU:
                    softmax_in(u + 1)
                combine(u)

        @block.scalar
        def _(e):
            def exps(u):
                i, h = units[u]
                b = u % 2
                ns, nw = cols(i)
                e.wait_ge(s_mx, u + 1)
                if u >= 2:
                    e.wait_ge(s_oc, u - 1)
                for z, (lo, hi) in enumerate(((0, ns), (TP, TP + nw), (TP + 5 * P, SW))):
                    e.activation(S[:, b, lo:hi], S[:, b, lo:hi], ACT.Exp, bias=nm[:, b, z:z + 1], accum_out=sm[:, b, z:z + 1])
                e.drain().then_inc(s_ex, 1)

            exps(0)
            for u in range(NU):
                gs = groups(units[u][0])
                for n in range(len(gs)):
                    G = gbase[u] + n
                    e.wait_ge(s_pt, G + 1)
                    full = [z for z, (kind, _) in enumerate(gs[n]) if kind != "c"]
                    w = P * len(full)
                    if w:
                        mm = e.activation(PT[:, G % 2, 0:w], K.ps[:, 4 + G % 2, 0:w], ACT.Copy)
                    if len(full) < len(gs[n]):
                        mm = e.activation(PT[0:16, G % 2, w:w + P], K.ps[0:16, 4 + G % 2, w:w + P], ACT.Copy)
                    mm.then_inc(s_pc, 1)
                if u + 1 < NU:
                    exps(u + 1)

        @block.gpsimd
        def _(e):
            for u in range(NU):
                i, h = units[u]
                e.wait_ge(s_ex, u + 1)
                e.tensor_tensor(S[:, u % 2, TP + 5 * P:SW], S[:, u % 2, TP + 5 * P:SW], K.c("cmask")[:, 14 - 2 * i:30 - 2 * i],
                                ALU.mult).then_inc(s_cm, 1)


SS, SWN, SCM = PAST + DT, 512 + DT, 32
SROW = SS + SWN + SCM


def stage_sample_rows(nc, K, kvt, qT, Qbd, bias, grow, vnew):
    with nc.Block() as block:
        s_g, s_b, s_z, s_q = K.sem("sr_gates_stored"), K.sem("sr_in"), K.sem("sr_zeroed"), K.sem("sr_queries")

        @block.sync
        def _(e):
            v = K.bvec.tensor
            n = 0
            e.dma_start(K.gscr, kvt[0:TS, NTI, 768:KVG]).then_inc(s_g, 16)
            for q in range(4):
                for t in range(DT):
                    r = slice(32 * q + t, 32 * q + 32, DT)
                    e.dma_start(bias[r, 0:SS], bass.AP(tensor=v, offset=REV - PAST - t, ap=[[BVL, 8], [1, SS]])).then_inc(s_b, 16)
                    e.dma_start(bias[r, SS:SS + SWN], bass.AP(tensor=v, offset=REV - 512 - t, ap=[[BVL, 8], [1, SWN]])).then_inc(s_b, 16)
                    e.dma_start(bias[r, SS + SWN:SROW], bass.AP(tensor=v, offset=REV - PAST + 63 - t, ap=[[BVL, 8], [64, SCM]]),
                                allow_slow_non_contiguous=True).then_inc(s_b, 16)
                    n += 3
            for b in range(DB):
                for z, c0 in enumerate((384, 640)):
                    e.dma_start(vnew[0:DT, b, z, :], kvt[DT * b:DT * b + DT, NTI, c0:c0 + P]).then_inc(s_b, 16)
                    n += 1
            e.wait_ge(s_g, 16)
            for b in range(DB):
                for h in range(8):
                    r0 = 32 * (b % 4) + 4 * h
                    e.dma_start(grow[r0:r0 + 4, b // 4, :], bass.AP(tensor=K.gscr.tensor, offset=24 * DT * b + h, ap=[[24, DT], [8, 3]]),
                                allow_slow_non_contiguous=True).then_inc(s_b, 16)
                    n += 1
            e.wait_ge(s_b, 16 * n)

        @block.vector
        def _(e):
            e.memset(Qbd[:, :, :], 0.0)
            e.drain()
            for h in range(8):
                g, pp = h // 4, 64 * (h % 2)
                e.tensor_copy(Qbd[64 * g:64 * g + 64, :, 4 * h:4 * h + 4],
                              qT[pp:pp + 64, h // 2, TP:T].rearrange("p (b t) -> p b t", t=DT))


def stage_sample_scores(nc, K, Qbd, bias, S, vcb, ksn, kwn):
    ctx = ExitStack()
    with ctx:
        sb = lambda nm, sh: ctx.enter_context(nc.sbuf_tensor("ss_" + nm, sh, F32))
        pt = ctx.enter_context(nc.sbuf_tensor("ss_pages", [1, DB * NPG], I32))
        ck, cv, sk = (sb(x, [P, NPG, P]) for x in ("ck", "cv", "sk"))
        wk = sb("wk", [P, 4, P])
        KT = sb("KT", [P, SS + SWN])
        kc, sq, rt = sb("kc", [P, SCM]), sb("sq", [P, SCM]), sb("rt", [P, SCM])
        block = ctx.enter_context(nc.Block())
        s_pt, s_pg, s_wk = K.sem("ss_table_in"), K.sem("ss_pages_in"), K.sem("ss_window_in")
        s_used, s_t, s_tc = K.sem("ss_pages_used"), K.sem("ss_turned"), K.sem("ss_turned_copied")
        s_m, s_mc, s_sq, s_sm, s_v, s_r, s_kc = (K.sem("ss_" + x) for x in (
            "means", "means_copied", "squared", "summed", "mean_sq", "rooted", "block_keys"))
        s_s, s_ev = K.sem("ss_scores"), K.sem("ss_scores_out")
        NTG = 5

        @block.sync
        def _(e):
            e.dma_start(pt[:, :], K.d["page_table"].rearrange("b n -> (b n)").unsqueeze(0)).then_inc(s_pt, 16)
            e.wait_ge(s_pt, 16)
            for b in range(DB):
                if b >= 1:
                    e.wait_ge(s_used, b)
                e.dma_start(wk[:, :, :], K.d["cache_win_k"][0, b].rearrange("(i p) g d -> p i (g d)", p=P)).then_inc(s_wk, 16)
                for j in range(NPG):
                    page = e.value_load(pt[0:1, NPG * b + j:NPG * b + j + 1], min_val=0, max_val=159)
                    for dst, src in ((ck, K.d["cache_cmp_k"]), (cv, K.d["cache_cmp_v"]), (sk, K.d["cache_slc_k"])):
                        e.dma_start(dst[:, j, :], src[0, bass.ds(page, 1), :, :, :].rearrange("a p g d -> p (a g d)")).then_inc(s_pg, 16)

        @block.tensor
        def _(e):
            ident, blk = K.c("ident"), K.c("blk")
            for b in range(DB):
                q, bb = b // 4, b % 4
                e.wait_ge(s_pg, 48 * NPG * (b + 1))
                e.wait_ge(s_wk, 16 * (b + 1))
                if b >= 1:
                    e.wait_ge(s_mc, b)
                    e.wait_ge(s_v, b)
                for j in range(NPG):
                    e.matmul(K.ps[:, 6, 2 * j:2 * j + 2], ck[:, j, :], blk[:, 30:32], start=True, stop=True)
                for j in range(NPG):
                    mm = e.matmul(K.ps[0:SCM, 7, 0:P], blk[:, 30 - 2 * j:62 - 2 * j], cv[:, j, :], start=j == 0, stop=j == NPG - 1)
                mm.then_inc(s_m, 1)
                for z in range(NTG):
                    G = NTG * b + z
                    if G >= 2:
                        e.wait_ge(s_tc, G - 1)
                    for j in range(4):
                        src = sk[:, 4 * z + j, :] if z < 4 else wk[:, j, :]
                        mm = e.transpose(K.ps[:, G % 2, P * j:P * j + P], src, ident)
                    mm.then_inc(s_t, 1)
                e.wait_ge(s_sq, b + 1)
                e.matmul(K.ps[:, 5, 0:SCM], K.c("headsum"), sq[:, :], start=True, stop=True).then_inc(s_sm, 1)
                e.wait_ge(s_tc, NTG * (b + 1))
                e.wait_ge(s_kc, b + 1)
                pr = slice(32 * bb, 32 * bb + 32)
                new = slice(DT * b, DT * b + DT)
                qb = Qbd[:, b, :]
                for z in range(4):
                    c = 2 + z % 3
                    if z == 0 and b >= 1:
                        e.wait_ge(s_ev, 6 * b)
                    if z == 3:
                        e.wait_ge(s_ev, 6 * b + 1)
                    e.matmul(K.ps[pr, c, :], qb, KT[:, 512 * z:512 * z + 512], start=True, stop=True).then_inc(s_s, 1)
                e.wait_ge(s_ev, 6 * b + 2)
                e.matmul(K.ps[pr, 3, 0:512], qb, KT[:, SS:SS + 512], start=True, stop=True).then_inc(s_s, 1)
                e.wait_ge(s_ev, 6 * b + 3)
                e.matmul(K.ps[pr, 4, 0:DT], qb, ksn[:, new], start=True, stop=True)
                e.matmul(K.ps[pr, 4, 8:8 + DT], qb, kwn[:, new], start=True, stop=True)
                e.matmul(K.ps[pr, 4, 16:16 + SCM], qb, kc[:, :], start=True, stop=True).then_inc(s_s, 1)

        @block.scalar
        def _(e):
            for b in range(DB):
                for z in range(NTG):
                    G = NTG * b + z
                    e.wait_ge(s_t, G + 1)
                    if z == 0 and b >= 1:
                        e.wait_ge(s_s, 6 * b)
                    lo = 512 * z if z < 4 else SS
                    e.activation(KT[:, lo:lo + 512], K.ps[:, G % 2, :], ACT.Copy).then_inc(s_tc, 1)
                e.wait_ge(s_v, b + 1)
                e.activation(rt[:, :], rt[:, :], ACT.Sqrt).then_inc(s_r, 1)
                e.wait_ge(s_m, b + 1)
                e.drain().then_inc(s_used, 1)

        @block.vector
        def _(e):
            for b in range(DB):
                q, bb = b // 4, b % 4
                pr = slice(32 * bb, 32 * bb + 32)
                e.wait_ge(s_m, b + 1)
                if b >= 1:
                    e.wait_ge(s_s, 6 * b)
                e.tensor_copy(kc[:, :], K.ps[:, 6, 0:SCM])
                e.tensor_copy(vcb[:, b, :], K.ps[0:SCM, 7, 0:P]).then_inc(s_mc, 1)
                e.drain()
                e.tensor_tensor(sq[:, :], kc[:, :], kc[:, :], ALU.mult).then_inc(s_sq, 1)
                e.wait_ge(s_sm, b + 1)
                e.tensor_scalar(rt[:, :], K.ps[:, 5, 0:SCM], 1.0 / 64, RMS_EPS, ALU.mult, ALU.add).then_inc(s_v, 1)
                e.wait_ge(s_r, b + 1)
                e.reciprocal(rt[:, :], rt[:, :])
                e.drain()
                e.scalar_tensor_tensor(kc[:, :], kc[:, :], K.p("kg_cmp", 0), rt[:, :], ALU.mult, ALU.mult).then_inc(s_kc, 1)
                for z in range(4):
                    e.wait_ge(s_s, 6 * b + z + 1)
                    lo = 512 * z
                    e.tensor_tensor(S[pr, q, lo:lo + 512], K.ps[pr, 2 + z % 3, :], bias[pr, lo:lo + 512], ALU.add).then_inc(s_ev, 1)
                e.wait_ge(s_s, 6 * b + 5)
                e.tensor_tensor(S[pr, q, SS:SS + 512], K.ps[pr, 3, :], bias[pr, SS:SS + 512], ALU.add).then_inc(s_ev, 1)
                e.wait_ge(s_s, 6 * b + 6)
                e.tensor_tensor(S[pr, q, PAST:SS], K.ps[pr, 4, 0:DT], bias[pr, PAST:SS], ALU.add)
                e.tensor_tensor(S[pr, q, SS + 512:SS + SWN], K.ps[pr, 4, 8:8 + DT], bias[pr, SS + 512:SS + SWN], ALU.add)
                e.tensor_tensor(S[pr, q, SS + SWN:SROW], K.ps[pr, 4, 16:16 + SCM], bias[pr, SS + SWN:SROW], ALU.add).then_inc(s_ev, 1)


def stage_sample_softmax(nc, K, S, coef, grow):
    ctx = ExitStack()
    with ctx:
        sb = lambda nm, sh: ctx.enter_context(nc.sbuf_tensor("sx_" + nm, sh, F32))
        nm, sm, rc = sb("negmax", [P, 2, 3]), sb("sums", [P, 2, 3]), sb("rec", [P, 2, 3])
        pc, sc, s1, s2 = sb("pc", [P, SCM]), sb("score", [P, 33]), sb("left", [P, 33]), sb("left2", [P, 33])
        m1, m2 = sb("top", [P, 8]), sb("top2", [P, 8])
        block = ctx.enter_context(nc.Block())
        s_mx, s_ex, s_pc, s_sc = K.sem("sx_max"), K.sem("sx_exps"), K.sem("sx_block_probs"), K.sem("sx_block_scores")
        RNG = ((0, SS), (SS, SS + SWN), (SS + SWN, SROW))
        OUT = -3e30

        @block.vector
        def _(e):
            for q in range(2):
                e.tensor_tensor(S[:, q, SS:SS + 4], S[:, q, SS:SS + 4], K.c("edgeS"), ALU.add)
                e.drain()
                for z in (2, 1):
                    lo, hi = RNG[z]
                    e.tensor_reduce(nm[:, q, z:z + 1], S[:, q, lo:hi], AX.X, ALU.max, negate=True).then_inc(s_mx, 1)
                e.wait_ge(s_ex, 3 * q + 1)
                e.reciprocal(rc[:, q, 2:3], sm[:, q, 2:3])
                e.drain()
                e.tensor_scalar(pc[:, :], S[:, q, SS + SWN:SROW], rc[:, q, 2:3], None, ALU.mult).then_inc(s_pc, 1)
                e.wait_ge(s_sc, q + 1)
                e.tensor_copy(sc[:, 0:SCM], K.ps[:, q, 0:SCM])
                e.drain()
                e.memset(sc[:, 0:1], 1e4)
                e.memset(sc[:, 31:33], 1e4)
                e.drain()
                e.max(m1[:, :], sc[:, :])
                e.drain()
                e.match_replace(s1[:, :], m1[:, :], sc[:, :], OUT)
                e.drain()
                e.max(m2[:, :], s1[:, :])
                e.drain()
                e.match_replace(s2[:, :], m2[:, :], s1[:, :], OUT)
                e.drain()
                e.tensor_scalar(s1[:, :], s2[:, :], OUT / 2, NEG, ALU.is_gt, ALU.mult)
                e.drain()
                sv = S[:, q, 0:PAST].rearrange("p (j n) -> p j n", n=64)
                e.tensor_tensor(sv, sv, s1[:, 0:32].unsqueeze(2).to_broadcast([P, 32, 64]), ALU.add)
                e.drain()
                e.tensor_reduce(nm[:, q, 0:1], S[:, q, 0:SS], AX.X, ALU.max, negate=True).then_inc(s_mx, 1)
                e.wait_ge(s_ex, 3 * q + 3)
                e.reciprocal(rc[:, q, 0:2], sm[:, q, 0:2])
                e.drain()
                e.tensor_tensor(coef[:, q, 0:2], rc[:, q, 0:2], grow[:, q, 1:3], ALU.mult)
                e.tensor_tensor(coef[:, q, 2:3], rc[:, q, 2:3], grow[:, q, 0:1], ALU.mult)

        @block.scalar
        def _(e):
            for q in range(2):
                for n, z in enumerate((2, 1, 0)):
                    lo, hi = RNG[z]
                    e.wait_ge(s_mx, 3 * q + n + 1)
                    e.activation(S[:, q, lo:hi], S[:, q, lo:hi], ACT.Exp, bias=nm[:, q, z:z + 1], accum_out=sm[:, q, z:z + 1])
                    e.drain().then_inc(s_ex, 1)

        @block.tensor
        def _(e):
            for q in range(2):
                e.wait_ge(s_pc, q + 1)
                e.matmul(K.ps[:, q, 0:SCM], K.c("heads4"), pc[:, :], start=True, stop=True).then_inc(s_sc, 1)


def stage_sample_values(nc, K, S, coef, vcb, vnew):
    ctx = ExitStack()
    NB4 = 20
    with ctx:
        sb = lambda nm, sh: ctx.enter_context(nc.sbuf_tensor("sv_" + nm, sh, F32))
        pt = ctx.enter_context(nc.sbuf_tensor("sv_pages", [1, DB * NPG], I32))
        sv = sb("v", [P, 2, NPG, P])
        wv = sb("wv", [P, 2, 4, P])
        PT = sb("PT", [P, NB4, P])
        PN = sb("PN", [SCM, 3, P])
        o1, o2 = sb("o1", [P, P]), sb("o2", [P, 64])
        block = ctx.enter_context(nc.Block())
        s_pt, s_wv = K.sem("sv_table_in"), K.sem("sv_window_in")
        s_pgs = K.sems("sv_pages_in", 2)
        s_t, s_tc, s_used, s_o, s_oc, s_ot, s_fin = (K.sem("sv_" + x) for x in (
            "turned", "turned_copied", "values_used", "values", "combined", "out_turned", "out_copied"))

        @block.sync
        def _(e):
            e.dma_start(pt[:, :], K.d["page_table"].rearrange("b n -> (b n)").unsqueeze(0)).then_inc(s_pt, 16)
            e.wait_ge(s_pt, 16)
            for b in range(DB):
                if b >= 2:
                    e.wait_ge(s_used, b - 1)
                e.dma_start(wv[:, b % 2, :, :], K.d["cache_win_v"][0, b].rearrange("(i p) g d -> p i (g d)", p=P)).then_inc(s_pgs[b % 2], 16)
                for j in range(NPG):
                    page = e.value_load(pt[0:1, NPG * b + j:NPG * b + j + 1], min_val=0, max_val=159)
                    e.dma_start(sv[:, b % 2, j, :], K.d["cache_slc_v"][0, bass.ds(page, 1), :, :, :].rearrange("a p g d -> p (a g d)")).then_inc(s_pgs[b % 2], 16)

        @block.tensor
        def _(e):
            ident = K.c("ident")
            for q in range(2):
                if q:
                    e.wait_ge(s_used, 4)
                for z in range(6):
                    G = 6 * q + z
                    if G >= 2:
                        e.wait_ge(s_tc, G - 1)
                    if z < 5:
                        for j in range(4):
                            lo = 512 * z + P * j if z < 4 else SS + P * j
                            mm = e.transpose(K.ps[:, G % 2, P * j:P * j + P], S[:, q, lo:lo + P], ident)
                    else:
                        e.transpose(K.ps[0:DT, G % 2, 0:P], S[:, q, PAST:SS], ident)
                        e.transpose(K.ps[0:DT, G % 2, P:2 * P], S[:, q, SS + 512:SS + SWN], ident)
                        mm = e.transpose(K.ps[0:SCM, G % 2, 2 * P:3 * P], S[:, q, SS + SWN:SROW], ident)
                    mm.then_inc(s_t, 1)
                e.wait_ge(s_tc, 6 * q + 6)
                if q:
                    e.wait_ge(s_oc, 1)
                for bb in range(4):
                    b = 4 * q + bb
                    e.wait_ge(s_pgs[b % 2], 16 * (NPG + 1) * (b // 2 + 1))
                    r = slice(32 * bb, 32 * bb + 32)
                    for j in range(NPG):
                        e.matmul(K.ps[r, 2, 0:P], PT[:, j, r], sv[:, b % 2, j, :], start=j == 0, stop=False)
                    e.matmul(K.ps[r, 2, 0:P], PN[0:DT, 0, r], vnew[0:DT, b, 0, :], start=False, stop=True)
                    for j in range(4):
                        e.matmul(K.ps[r, 3, 0:P], PT[:, NPG + j, r], wv[:, b % 2, j, :], start=j == 0, stop=False)
                    e.matmul(K.ps[r, 3, 0:P], PN[0:DT, 1, r], vnew[0:DT, b, 1, :], start=False, stop=True)
                    e.matmul(K.ps[r, 4, 0:P], PN[:, 2, r], vcb[:, b, :], start=True, stop=True).then_inc(s_used, 1)
                e.wait_ge(s_oc, q + 1)
                e.transpose(K.ps[0:64, 5, 0:P], o2[:, :], ident).then_inc(s_ot, 1)

        @block.scalar
        def _(e):
            for q in range(2):
                if q:
                    e.wait_ge(s_used, 4)
                for z in range(6):
                    G = 6 * q + z
                    e.wait_ge(s_t, G + 1)
                    if z < 5:
                        e.activation(PT[:, 4 * z:4 * z + 4, :].rearrange("p j n -> p (j n)"), K.ps[:, G % 2, :], ACT.Copy).then_inc(s_tc, 1)
                    else:
                        for k, n in enumerate((DT, DT, SCM)):
                            mm = e.activation(PN[0:n, k, :], K.ps[0:n, G % 2, P * k:P * k + P], ACT.Copy)
                        mm.then_inc(s_tc, 1)

        @block.vector
        def _(e):
            for q in range(2):
                e.wait_ge(s_used, 4 * q + 4)
                e.tensor_scalar(o1[:, :], K.ps[:, 2, 0:P], coef[:, q, 0:1], None, ALU.mult)
                e.drain()
                e.scalar_tensor_tensor(o1[:, :], K.ps[:, 3, 0:P], coef[:, q, 1:2], o1[:, :], ALU.mult, ALU.add)
                e.drain()
                e.scalar_tensor_tensor(o1[:, :], K.ps[:, 4, 0:P], coef[:, q, 2:3], o1[:, :], ALU.mult, ALU.add)
                e.drain()
                e.tensor_scalar(o2[:, :], o1[:, 0:64], K.c("grp")[:, 0:1], None, ALU.mult)
                e.drain()
                e.scalar_tensor_tensor(o2[:, :], o1[:, 64:P], K.c("grp")[:, 1:2], o2[:, :], ALU.mult, ALU.add).then_inc(s_oc, 1)
                e.wait_ge(s_ot, q + 1)
                t = K.ps[0:64, 5, 0:P].rearrange("p (b h t) -> p b h t", b=4, h=8)
                for h in range(8):
                    e.tensor_copy(K.oC[64 * (h % 2):64 * (h % 2) + 64, h // 2, TP + 16 * q:TP + 16 * q + 16].rearrange("p (b t) -> p b t", t=DT),
                                  t[:, :, h, :])
                e.drain()


def stage_merge(nc, K, h, xh, xl, spare):
    names = ("w_br_a", "w_br_b", "w_br_c")
    srcs = (K.oA, K.oB, K.oC)
    ctx = ExitStack()
    with ctx:
        W = weight_slots(nc, K, ctx, "me", KD, 2)
        wb = ctx.enter_context(nc.sbuf_tensor("me_branch_w", [P, 2, 4, P], F32))
        sg, tmp = spare[:, 0:2, :], spare[:, 2, :]
        block = ctx.enter_context(nc.Block())
        s_bin = K.sems("me_branch_in", 2)
        s_b, s_sg, s_h = K.sem("me_branch_product"), K.sem("me_gate_sigmoid"), K.sem("me_weighted")
        NU = 3 * KD

        @block.sync
        def _(e):
            for u in range(NU):
                m, br = u // 3, u % 3
                c0 = OFF_MG + D * br + P * m
                load_block(e, W, u, [K.d["w_in"][0, :, c0:c0 + P]])
                if u >= 2:
                    e.wait_ge(s_b, u - 1)
                e.dma_start(wb[:, u % 2, :, :], K.d[names[br]][0, :, P * m:P * m + P].rearrange("(k p) n -> p k n", p=P)).then_inc(s_bin[u % 2], 16)

        @block.tensor
        def _(e):
            for u in range(NU):
                br = u % 3
                e.wait_ge(W.s_lo, u + 1)
                if u >= 1:
                    e.wait_ge(s_sg, u)
                product(e, K, W, u, xh, xl, 0, range(KD)).then_inc(W.s_mm, 1)
                e.wait_ge(s_bin[u % 2], 16 * (u // 2 + 1))
                if u >= 1:
                    e.wait_ge(s_h, u)
                for c in range(NC3):
                    for k in range(4):
                        mm = e.matmul(K.ps[:, 3 + c, 0:NW], wb[:, u % 2, k, :], srcs[br][:, k, NW * c:NW * c + NW], start=k == 0, stop=k == 3)
                mm.then_inc(s_b, 1)

        @block.scalar
        def _(e):
            high_block(e, W, 0, 1)
            high_block(e, W, 1, 1)
            for u in range(NU):
                e.wait_ge(W.s_mm, u + 1)
                if u >= 2:
                    e.wait_ge(s_h, u - 1)
                e.activation(sg[:, u % 2, :].rearrange("p (c n) -> p c n", c=NC3), K.ps[:, 0:3, 0:NW], ACT.Sigmoid).then_inc(s_sg, 1)
                if u + 2 < NU:
                    high_block(e, W, u + 2, (u + 2) // 2 + 1)

        @block.vector
        def _(e):
            c3 = lambda ap: ap.rearrange("p (c n) -> p c n", c=NC3)
            low_block(e, W, 0)
            low_block(e, W, 1)
            for u in range(NU):
                m, br = u // 3, u % 3
                if u + 2 < NU:
                    low_block(e, W, u + 2)
                e.wait_ge(s_sg, u + 1)
                e.wait_ge(s_b, u + 1)
                dst = h[:, m, :] if br == 0 else tmp
                e.tensor_tensor(c3(dst), c3(sg[:, u % 2, :]), K.ps[:, 3:6, 0:NW], ALU.mult).then_inc(s_h, 1)
                e.drain()
                if br:
                    e.tensor_tensor(h[:, m, :], h[:, m, :], tmp, ALU.add)
                    e.drain()


def stage_product(nc, K, tag, w, kb, nblk, rh, rl, dst, add):
    ctx = ExitStack()
    with ctx:
        W = weight_slots(nc, K, ctx, tag, kb)
        block = ctx.enter_context(nc.Block())
        s_out = K.sem(tag + "_taken")
        c3 = lambda ap: ap.rearrange("p (c n) -> p c n", c=NC3)
        bank = lambda m: K.ps[:, 3 * (m % 2):3 * (m % 2) + 3, 0:NW]

        @block.sync
        def _(e):
            for m in range(nblk):
                load_block(e, W, m, [w(m)])

        @block.tensor
        def _(e):
            for m in range(nblk):
                e.wait_ge(W.s_lo, m + 1)
                if m >= 2:
                    e.wait_ge(s_out, m - 1)
                product(e, K, W, m, rh, rl, 3 * (m % 2), range(kb)).then_inc(W.s_mm, 1)

        @block.scalar
        def _(e):
            for m in range(nblk):
                high_block(e, W, m, m // NRAW + 1)

        @block.vector
        def _(e):
            low_block(e, W, 0)
            low_block(e, W, 1)
            for m in range(nblk):
                e.wait_ge(W.s_mm, m + 1)
                if add:
                    e.tensor_tensor(c3(dst[:, m, :]), c3(dst[:, m, :]), bank(m), ALU.add).then_inc(s_out, 1)
                else:
                    e.tensor_copy(c3(dst[:, m, :]), bank(m)).then_inc(s_out, 1)
                if m + 2 < nblk:
                    low_block(e, W, m + 2)


def stage_ffn(nc, K, xh, xl, x):
    GB = 4
    NG = 4 * D // P // GB
    RING = GB + 1
    units = [("up", j) for j in range(GB)]
    for g in range(NG):
        up = [("up", GB * (g + 1) + j) for j in range(GB)] if g + 1 < NG else []
        units += up[:1] + [("down", g, q) for q in range(KD // 2)] + up[1:]
    NU = len(units)
    done = []
    for un in units:
        done.append((done[-1] if done else 0) + (1 if un[0] == "up" else 2))
    kinds = [un[0] for un in units for _ in range(1 if un[0] == "up" else 2)]
    ctx = ExitStack()
    with ctx:
        W = weight_slots(nc, K, ctx, "ff", KD)
        hh = ctx.enter_context(nc.sbuf_tensor("ff_hidden_high", [P, RING, T], F32R))
        hl = ctx.enter_context(nc.sbuf_tensor("ff_hidden_low", [P, RING, T], F32R))
        act = ctx.enter_context(nc.sbuf_tensor("ff_act", [P, 2, T], F32))
        block = ctx.enter_context(nc.Block())
        s_hh, s_hl, s_read_up, s_read_down = (K.sem("ff_" + x) for x in (
            "hidden_high", "hidden_low", "up_read", "down_read"))
        c3 = lambda ap: ap.rearrange("p (c n) -> p c n", c=NC3)
        bank = lambda n: K.ps[:, 3 * (n % 2):3 * (n % 2) + 3, 0:NW]

        @block.sync
        def _(e):
            for u, un in enumerate(units):
                if un[0] == "up":
                    load_block(e, W, u, [K.d["w_ff1"][0][:, P * un[1]:P * un[1] + P]])
                    continue
                if u >= NRAW:
                    e.wait_ge(W.s_lo, u - NRAW + 1)
                src = K.d["w_ff2"][0][GB * P * un[1]:GB * P * (un[1] + 1), 2 * P * un[2]:2 * P * un[2] + 2 * P]
                e.dma_start(W.raw[:, u % NRAW, :, :].rearrange("p (k z) n -> p k (z n)", z=2),
                            src.rearrange("(k p) n -> p k n", p=P)).then_inc(W.s_in[u % NRAW], 16)

        @block.tensor
        def _(e):
            def bank_free(n):
                if n >= 2:
                    e.wait_ge(s_read_up if kinds[n - 2] == "up" else s_read_down, kinds[:n - 1].count(kinds[n - 2]))

            n = 0
            for u, un in enumerate(units):
                e.wait_ge(W.s_lo, u + 1)
                if un[0] == "up":
                    bank_free(n)
                    mm = product(e, K, W, u, xh, xl, 3 * (n % 2), range(KD))
                    mm.then_inc(W.s_mm, 1)
                    n += 1
                    continue
                g = un[1]
                e.wait_ge(s_hl, GB * (g + 1))
                for z in range(2):
                    bank_free(n)
                    for c in range(NC3):
                        o, ns = K.ps[:, 3 * (n % 2) + c, 0:NW], slice(NW * c, NW * c + NW)
                        for k in range(GB):
                            r = (GB * g + k) % RING
                            e.matmul(o, W.hi[:, u % NSPL, 2 * k + z, :], hh[:, r, ns], start=k == 0, stop=False)
                            e.matmul(o, W.hi[:, u % NSPL, 2 * k + z, :], hl[:, r, ns], start=False, stop=False)
                            mm = e.matmul(o, W.lo[:, u % NSPL, 2 * k + z, :], hh[:, r, ns], start=False, stop=k == GB - 1)
                    mm.then_inc(W.s_mm, 1)
                    n += 1

        def weights_high(e, u):
            e.wait_ge(W.s_in[u % NRAW], 16 * (u // NRAW + 1))
            if u >= NSPL:
                e.wait_ge(W.s_mm, done[u - NSPL])
            e.activation(W.hi[:, u % NSPL, :, :], W.raw[:, u % NRAW, :, :], ACT.Copy).then_inc(W.s_hi, 1)

        @block.scalar
        def _(e):
            weights_high(e, 0)
            weights_high(e, 1)
            for u, un in enumerate(units):
                if un[0] == "up":
                    j = un[1]
                    e.wait_ge(W.s_mm, done[u])
                    if j >= 2:
                        e.wait_ge(s_hl, j - 1)
                    e.activation(c3(act[:, j % 2, :]), bank(done[u] - 1), ACT.Relu).then_inc(s_read_up, 1)
                    e.drain()
                    e.activation(act[:, j % 2, :], act[:, j % 2, :], ACT.Square)
                    e.drain()
                    e.activation(hh[:, j % RING, :], act[:, j % 2, :], ACT.Copy).then_inc(s_hh, 1)
                if u + 2 < NU:
                    weights_high(e, u + 2)

        @block.vector
        def _(e):
            low_block(e, W, 0)
            low_block(e, W, 1)
            for u, un in enumerate(units):
                if un[0] == "up":
                    j = un[1]
                    e.wait_ge(s_hh, j + 1)
                    e.tensor_tensor(hl[:, j % RING, :], act[:, j % 2, :], hh[:, j % RING, :].bitcast(F32), ALU.subtract).then_inc(s_hl, 1)
                else:
                    for z in range(2):
                        n = done[u] - 2 + z
                        e.wait_ge(W.s_mm, n + 1)
                        m = 2 * un[2] + z
                        e.tensor_tensor(c3(x[:, m, :]), c3(x[:, m, :]), bank(n), ALU.add).then_inc(s_read_down, 1)
                if u + 2 < NU:
                    low_block(e, W, u + 2)


def stage_mem_load(nc, K, mT):
    ctx = ExitStack()
    with ctx:
        rows = ctx.enter_context(nc.sbuf_tensor("ml_rows", [P, 2, D], F32))
        block = ctx.enter_context(nc.Block())
        s_in, s_t, s_c = K.sem("ml_in"), K.sem("ml_turned"), K.sem("ml_copied")

        @block.sync
        def _(e):
            e.dma_start(rows[:, :, :], K.d["mem_prompt"][0].rearrange("(i p) d -> p i d", p=P)).then_inc(s_in, 16)

        @block.tensor
        def _(e):
            e.wait_ge(s_in, 16)
            for i in range(2):
                for k in range(KD):
                    mm = e.transpose(K.ps[:, 2 * i + k // 4, P * (k % 4):P * (k % 4) + P], rows[:, i, P * k:P * k + P], K.c("ident"))
                mm.then_inc(s_t, 1)

        @block.vector
        def _(e):
            for i in range(2):
                e.wait_ge(s_t, i + 1)
                for z in range(2):
                    e.tensor_copy(mT[:, 4 * z:4 * z + 4, P * i:P * i + P], K.ps[:, 2 * i + z, :].rearrange("p (k n) -> p k n", k=4))


def stage_mem_kv(nc, K, mh, ml, mkT, mv):
    ctx = ExitStack()
    with ctx:
        sb = lambda nm, sh: ctx.enter_context(nc.sbuf_tensor("mk_" + nm, sh, F32))
        w = sb("w", [P, 2, KD, 512])
        wh, wl = (ctx.enter_context(nc.sbuf_tensor("mk_" + x, [P, KD, 512], F32R)) for x in ("high", "low"))
        mk = sb("k", [P, 2, 512])
        sq, kg, ss = sb("sq", [P, 2, 512]), sb("gain", [P, P]), sb("ss", [P, 8])
        block = ctx.enter_context(nc.Block())
        s_in, s_g, s_mm, s_c, s_v, s_r, s_k, s_t, s_hi, s_lo = (K.sem("mk_" + x) for x in (
            "w_in", "gain_in", "product", "copied", "mean", "rooted", "normed", "turned", "high", "low"))
        s_out = K.out_sem("mk_stored")

        @block.sync
        def _(e):
            e.dma_start(w[:, 0, :, :], K.d["w_mk"][0].rearrange("(k p) n -> p k n", p=P)).then_inc(s_in, 16)
            e.dma_start(w[:, 1, :, :], K.d["w_mv"][0].rearrange("(k p) n -> p k n", p=P)).then_inc(s_in, 16)
            e.dma_start(kg[:, :], K.d["mem_k_g"][0, :].partition_broadcast(P)).then_inc(s_g, 16)
            e.wait_ge(s_k, 1)
            e.dma_start(K.d["p_mem_k"][0, 0].rearrange("(i p) h d -> p i (h d)", p=P), mk[:, :, :]).then_inc(s_out, 16)
            e.wait_ge(s_c, 2)
            e.dma_start(K.d["p_mem_v"][0, 0].rearrange("(i p) h d -> p i (h d)", p=P), mv[:, :, :]).then_inc(s_out, 16)
            e.wait_ge(s_out, 32)

        @block.tensor
        def _(e):
            for z in range(2):
                e.wait_ge(s_lo, z + 1)
                for i in range(2):
                    for k in range(KD):
                        o, r = K.ps[:, 2 * z + i, :], slice(P * i, P * i + P)
                        e.matmul(o, mh[:, k, r], wh[:, k, :], start=k == 0, stop=False)
                        e.matmul(o, ml[:, k, r], wh[:, k, :], start=False, stop=False)
                        mm = e.matmul(o, mh[:, k, r], wl[:, k, :], start=False, stop=k == KD - 1)
                mm.then_inc(s_mm, 1)
            e.wait_ge(s_k, 1)
            for h in range(4):
                for i in range(2):
                    mm = e.transpose(K.ps[:, 4 + h // 2, 256 * (h % 2) + P * i:256 * (h % 2) + P * i + P], mk[:, i, P * h:P * h + P], K.c("ident"))
            mm.then_inc(s_t, 1)

        @block.scalar
        def _(e):
            for z, dst in ((0, mk), (1, mv)):
                e.wait_ge(s_in, 32)
                e.activation(wh[:, :, :], w[:, z, :, :], ACT.Copy).then_inc(s_hi, 1)
                e.wait_ge(s_mm, z + 1)
                e.activation(dst[:, :, :], K.ps[:, 2 * z:2 * z + 2, :], ACT.Copy).then_inc(s_c, 1)
            e.wait_ge(s_v, 1)
            e.activation(ss[:, :], ss[:, :], ACT.Sqrt).then_inc(s_r, 1)

        @block.vector
        def _(e):
            k8 = mk[:, :, :].rearrange("p i (h d) -> p (i h) d", d=P)
            for z in range(2):
                e.wait_ge(s_hi, z + 1)
                e.tensor_tensor(wl[:, :, :], w[:, z, :, :], wh[:, :, :].bitcast(F32), ALU.subtract).then_inc(s_lo, 1)
            e.wait_ge(s_c, 1)
            e.tensor_tensor(sq[:, :, :], mk[:, :, :], mk[:, :, :], ALU.mult)
            e.drain()
            e.tensor_reduce(ss[:, :], sq[:, :, :].rearrange("p i (h d) -> p (i h) d", d=P), AX.X, ALU.add)
            e.drain()
            e.tensor_scalar(ss[:, :], ss[:, :], 1.0 / P, RMS_EPS, ALU.mult, ALU.add).then_inc(s_v, 1)
            e.wait_ge(s_r, 1)
            e.reciprocal(ss[:, :], ss[:, :])
            e.drain()
            e.tensor_tensor(k8, k8, ss[:, :].unsqueeze(2).to_broadcast([P, 8, P]), ALU.mult)
            e.drain()
            e.wait_ge(s_g, 16)
            e.tensor_tensor(k8, k8, kg[:, :].unsqueeze(1).to_broadcast([P, 8, P]), ALU.mult).then_inc(s_k, 1)
            e.wait_ge(s_t, 1)
            e.tensor_copy(mkT[:, :, :].rearrange("p h n -> p (h n)"), K.ps[:, 4:6, :].rearrange("p a n -> p (a n)"))


def stage_mem_prompt(nc, K, q, mkT, mv, o):
    SC = P ** -0.5
    ctx = ExitStack()
    with ctx:
        sb = lambda nm, sh: ctx.enter_context(nc.sbuf_tensor("mp_" + nm, sh, F32))
        Pr = sb("probs", [P, 2, 4, 256])
        nm, sm = sb("negmax", [P, 2, 4]), sb("sums", [P, 2, 4])
        PT = sb("probsT", [P, 8, P])
        block = ctx.enter_context(nc.Block())
        s_s, s_mx, s_ex, s_pr, s_t, s_tc, s_o, s_oc = (K.sem("mp_" + x) for x in (
            "scores", "max", "exps", "probs", "turned", "turned_copied", "values", "values_copied"))

        def sbank(i):
            return K.ps[:, 2 * (i % 2):2 * (i % 2) + 2, :].rearrange("p a (h n) -> p (a h) n", h=2)

        @block.tensor
        def _(e):
            def scores(i):
                if i >= 2:
                    e.wait_ge(s_ex, i - 1)
                for h in range(4):
                    mm = e.matmul(K.ps[:, 2 * (i % 2) + h // 2, 256 * (h % 2):256 * (h % 2) + 256], q[:, h, P * i:P * i + P], mkT[:, h, :],
                                  start=True, stop=True)
                mm.then_inc(s_s, 1)

            scores(0)
            for i in range(NTI):
                if i + 1 < NTI:
                    scores(i + 1)
                e.wait_ge(s_pr, i + 1)
                if i >= 1:
                    e.wait_ge(s_tc, i)
                for h in range(4):
                    for j in range(2):
                        mm = e.transpose(K.ps[:, 4 + h // 2, 256 * (h % 2) + P * j:256 * (h % 2) + P * j + P],
                                         Pr[:, i % 2, h, P * j:P * j + P], K.c("ident"))
                mm.then_inc(s_t, 1)
                e.wait_ge(s_tc, i + 1)
                if i >= 2:
                    e.wait_ge(s_oc, i - 1)
                for h in range(4):
                    for j in range(2):
                        mm = e.matmul(K.ps[:, 6 + i % 2, P * h:P * h + P], mv[:, j, P * h:P * h + P], PT[:, 2 * h + j, :], start=j == 0, stop=j == 1)
                mm.then_inc(s_o, 1)

        @block.vector
        def _(e):
            def maxes(i):
                e.wait_ge(s_s, i + 1)
                if i >= 2:
                    e.wait_ge(s_ex, i - 1)
                e.tensor_reduce(nm[:, i % 2, :], sbank(i), AX.X, ALU.max, negate=True)
                e.drain()
                e.tensor_scalar(nm[:, i % 2, :], nm[:, i % 2, :], SC, None, ALU.mult).then_inc(s_mx, 1)

            maxes(0)
            for i in range(NTI):
                if i + 1 < NTI:
                    maxes(i + 1)
                e.wait_ge(s_ex, i + 1)
                e.reciprocal(sm[:, i % 2, :], sm[:, i % 2, :])
                e.drain()
                e.tensor_tensor(Pr[:, i % 2, :, :], Pr[:, i % 2, :, :], sm[:, i % 2, :].unsqueeze(2).to_broadcast([P, 4, 256]), ALU.mult).then_inc(s_pr, 1)
                e.wait_ge(s_o, i + 1)
                e.tensor_copy(o[:, :, P * i:P * i + P], K.ps[:, 6 + i % 2, :].rearrange("p (h n) -> p h n", h=4)).then_inc(s_oc, 1)

        @block.scalar
        def _(e):
            for i in range(NTI):
                e.wait_ge(s_mx, i + 1)
                if i >= 2:
                    e.wait_ge(s_t, i - 1)
                for h in range(4):
                    e.activation(Pr[:, i % 2, h, :], sbank(i)[:, h, :], ACT.Exp, bias=nm[:, i % 2, h:h + 1], scale=SC, accum_out=sm[:, i % 2, h:h + 1])
                e.drain().then_inc(s_ex, 1)
                e.wait_ge(s_t, i + 1)
                if i >= 1:
                    e.wait_ge(s_o, i)
                e.activation(PT[:, :, :].rearrange("p (a h) n -> p a (h n)", a=2), K.ps[:, 4:6, :], ACT.Copy).then_inc(s_tc, 1)


def stage_mem_sample(nc, K, q, o):
    SC = P ** -0.5
    ctx = ExitStack()
    with ctx:
        sb = lambda nm, sh: ctx.enter_context(nc.sbuf_tensor("ms_" + nm, sh, F32))
        kb, vb = sb("k", [P, 2, 2, 512]), sb("v", [P, DB, 2, 512])
        KT = sb("KT", [P, 2, 1024])
        Q = sb("Q", [P, 4, DB, 32])
        Pr, PT = sb("probs", [P, 256]), sb("probsT", [P, 2, P])
        nm, sm = sb("negmax", [P, 1]), sb("sums", [P, 1])
        o1 = sb("o1", [P, P])
        block = ctx.enter_context(nc.Block())
        s_k, s_v = K.sems("ms_keys_in", 2), K.sem("ms_values_in")
        s_q, s_t, s_tc, s_s, s_mx, s_ex, s_pr, s_pt, s_ptc, s_o, s_oc, s_ot, s_oe = (K.sem("ms_" + x) for x in (
            "queries", "keys_turned", "keys_copied", "scores", "max", "exps", "probs", "probs_turned", "probs_copied",
            "values", "combined", "out_turned", "out_copied"))

        @block.sync
        def _(e):
            for b in range(DB):
                if b >= 2:
                    e.wait_ge(s_t, b - 1)
                e.dma_start(kb[:, b % 2, :, :], K.d["cache_mem_k"][0, b].rearrange("(i p) h d -> p i (h d)", p=P)).then_inc(s_k[b % 2], 16)
                if b == 1:
                    for z in range(DB):
                        e.dma_start(vb[:, z, :, :], K.d["cache_mem_v"][0, z].rearrange("(i p) h d -> p i (h d)", p=P)).then_inc(s_v, 16)

        @block.tensor
        def _(e):
            ident = K.c("ident")
            e.wait_ge(s_q, 1)
            for b in range(DB):
                qd, bb = b // 4, b % 4
                e.wait_ge(s_k[b % 2], 16 * (b // 2 + 1))
                if b >= 1:
                    e.wait_ge(s_tc, b)
                for h in range(4):
                    for j in range(2):
                        mm = e.transpose(K.ps[:, h // 2, 256 * (h % 2) + P * j:256 * (h % 2) + P * j + P], kb[:, b % 2, j, P * h:P * h + P], ident)
                mm.then_inc(s_t, 1)
                e.wait_ge(s_tc, b + 1)
                if b == 4:
                    e.wait_ge(s_ex, 1)
                for h in range(4):
                    mm = e.matmul(K.ps[32 * bb:32 * bb + 32, 2, 0:256], Q[:, h, b, :], KT[:, b % 2, 256 * h:256 * h + 256], start=h == 0, stop=h == 3)
                mm.then_inc(s_s, 1)
                if bb == 3:
                    e.wait_ge(s_pr, qd + 1)
                    for j in range(2):
                        mm = e.transpose(K.ps[:, 3, P * j:P * j + P], Pr[:, P * j:P * j + P], ident)
                    mm.then_inc(s_pt, 1)
                    e.wait_ge(s_ptc, qd + 1)
                    e.wait_ge(s_v, 16 * DB)
                    if qd:
                        e.wait_ge(s_oc, 1)
                    for z in range(4):
                        for j in range(2):
                            mm = e.matmul(K.ps[32 * z:32 * z + 32, 4, :], PT[:, j, 32 * z:32 * z + 32], vb[:, 4 * qd + z, j, :], start=j == 0, stop=j == 1)
                    mm.then_inc(s_o, 1)
                    e.wait_ge(s_oc, qd + 1)
                    e.transpose(K.ps[:, 5, 0:P], o1[:, :], ident).then_inc(s_ot, 1)

        @block.scalar
        def _(e):
            for b in range(DB):
                qd = b // 4
                e.wait_ge(s_t, b + 1)
                if b >= 2:
                    e.wait_ge(s_s, b - 1)
                e.activation(KT[:, b % 2, :].rearrange("p (a n) -> p a n", a=2), K.ps[:, 0:2, :], ACT.Copy).then_inc(s_tc, 1)
                if b % 4 == 3:
                    e.wait_ge(s_mx, qd + 1)
                    e.activation(Pr[:, :], K.ps[:, 2, 0:256], ACT.Exp, bias=nm[:, :], scale=SC, accum_out=sm[:, :])
                    e.drain().then_inc(s_ex, 1)
                    e.wait_ge(s_pt, qd + 1)
                    e.activation(PT[:, :, :].rearrange("p j n -> p (j n)"), K.ps[:, 3, 0:256], ACT.Copy).then_inc(s_ptc, 1)

        @block.vector
        def _(e):
            e.memset(Q[:, :, :, :], 0.0)
            e.drain()
            for h in range(4):
                e.tensor_copy(Q[:, h, :, 4 * h:4 * h + 4], q[:, h, TP:T].rearrange("p (b t) -> p b t", t=DT))
            e.drain().then_inc(s_q, 1)
            for qd in range(2):
                e.wait_ge(s_s, 4 * qd + 4)
                e.tensor_reduce(nm[:, :], K.ps[:, 2, 0:256], AX.X, ALU.max, negate=True)
                e.drain()
                e.tensor_scalar(nm[:, :], nm[:, :], SC, None, ALU.mult).then_inc(s_mx, 1)
                e.wait_ge(s_ex, qd + 1)
                e.reciprocal(sm[:, :], sm[:, :])
                e.drain()
                e.tensor_scalar(Pr[:, :], Pr[:, :], sm[:, 0:1], None, ALU.mult).then_inc(s_pr, 1)
                e.wait_ge(s_o, qd + 1)
                e.tensor_scalar(o1[:, :], K.ps[:, 4, 0:P], K.c("mhead")[:, 0:1], None, ALU.mult)
                for h in range(1, 4):
                    e.drain()
                    mm = e.scalar_tensor_tensor(o1[:, :], K.ps[:, 4, P * h:P * h + P], K.c("mhead")[:, h:h + 1], o1[:, :], ALU.mult, ALU.add)
                mm.then_inc(s_oc, 1)
                e.wait_ge(s_ot, qd + 1)
                t = K.ps[:, 5, 0:P].rearrange("p (b h t) -> p b h t", b=4, h=8)
                for h in range(4):
                    e.tensor_copy(o[:, h, TP + 16 * qd:TP + 16 * qd + 16].rearrange("p (b t) -> p b t", t=DT), t[:, :, h, :])
                e.drain()


def stage_store(nc, K, x):
    ctx = ExitStack()
    with ctx:
        rows = ctx.enter_context(nc.sbuf_tensor("so_rows", [P, 3, D], F32))
        block = ctx.enter_context(nc.Block())
        s_t, s_a, s_v = K.sem("so_turned"), K.sem("so_copied_act"), K.sem("so_copied_dve")
        s_out = [K.out_sem(f"so_stored{z}") for z in range(3)]

        @block.tensor
        def _(e):
            for i in range(NTI + 1):
                n = P if i < NTI else TS
                if i >= 2:
                    e.wait_ge(s_a, i - 1)
                    e.wait_ge(s_v, i - 1)
                for k in range(KD):
                    mm = e.transpose(K.ps[0:n, 2 * (i % 2) + k // 4, P * (k % 4):P * (k % 4) + P], x[:, k, P * i:P * i + n], K.c("ident"))
                mm.then_inc(s_t, 1)

        @block.scalar
        def _(e):
            for i in range(NTI + 1):
                n = P if i < NTI else TS
                e.wait_ge(s_t, i + 1)
                if i >= 3:
                    e.wait_ge(s_out[i % 3], 16 * (i // 3))
                e.activation(rows[0:n, i % 3, 0:512], K.ps[0:n, 2 * (i % 2), :], ACT.Copy).then_inc(s_a, 1)

        @block.vector
        def _(e):
            for i in range(NTI + 1):
                n = P if i < NTI else TS
                e.wait_ge(s_t, i + 1)
                if i >= 3:
                    e.wait_ge(s_out[i % 3], 16 * (i // 3))
                e.tensor_copy(rows[0:n, i % 3, 512:1024], K.ps[0:n, 2 * (i % 2) + 1, :]).then_inc(s_v, 1)

        @block.sync
        def _(e):
            for i in range(NTI + 1):
                e.wait_ge(s_a, i + 1)
                e.wait_ge(s_v, i + 1)
                if i < NTI:
                    e.dma_start(K.d["y_prompt"][0, P * i:P * i + P, :], rows[:, i % 3, :]).then_inc(s_out[i % 3], 16)
                else:
                    e.dma_start(K.d["y_sample"].rearrange("b t d -> (b t) d"), rows[0:TS, i % 3, :]).then_inc(s_out[i % 3], 16)
            for z in range(3):
                e.wait_ge(s_out[z], 48)


def stage_zero(nc, tile):
    with nc.Block() as block:
        @block.vector
        def _(e):
            e.memset(tile[:, :, :], 0.0)


def build(nc, aps):
    with ExitStack() as ctx:
        K = Shared()
        K.d = aps
        K.turn = {}
        K.n_prow = sum(2 if n in ("nsa_q_g", "kg_cmp") else 15 if n == "shift_mu" else 1 for n, _ in PARAMS)
        K.live = []

        def sem(name):
            K.live.append(nc.alloc_semaphore(name))
            return K.live[-1]

        def reuse_semaphores():
            nc.clear_and_free_semaphores(K.live)
            nc.all_engine_barrier()
            K.live = []

        K.sem = sem
        stores = {n: nc.alloc_semaphore(n) for n in ("tail_stored", "kv_stored", "stPo_stored", "stSo_stored", "stSi_stored",
                                                      "mk_stored", "so_stored0", "so_stored1", "so_stored2")}
        K.out_sem = lambda name: stores[name]
        K.sems = lambda name, n: [K.sem(f"{name}{i}") for i in range(n)]
        K.c = lambda name: K.cst[:, CCOL[name][0]:CCOL[name][0] + CCOL[name][1]]
        K.p = lambda name, k: K.par[:, PCOL[name] + k:PCOL[name] + k + 1]
        sb = lambda name, shape: ctx.enter_context(nc.sbuf_tensor(name, shape, F32))
        K.ps = ctx.enter_context(nc.psum_tensor("ps", [P, 8, 512], F32))
        K.cst = sb("cst", [P, SHEET.shape[1]])
        K.par = sb("par", [P, NPAR + 4])
        K.utail = sb("utail", [P, B_Q, TAIL])
        K.shT = sb("shT", [P, NSHIFT, DB])
        slab = nc.sbuf_base
        sb("slab", [P, 16, T])

        def on_slab(name, at, blocks, dtype=F32):
            return nc.alloc_sbuf_tensor_at(name, [P, blocks, T], dtype, offset=slab + at * T * 4)

        K.oA, K.oB, K.oC = (on_slab(n, 4 * z, 4) for z, n in enumerate(("oA", "oB", "oC")))
        K.x_dram = nc.dram_tensor("x_channel_major", (P, KD * T), F32).ap()
        K.xh_dram = nc.dram_tensor("xn_high", (P, KD * T), F32R).ap()
        K.xl_dram = nc.dram_tensor("xn_low", (P, KD * T), F32R).ap()
        K.bvec = nc.dram_tensor("bias_vectors", (8, BVL), F32).ap()
        K.gscr = nc.dram_tensor("gate_rows", (TS, 24), F32).ap()
        flat = lambda t: t[:, :, :].rearrange("p k n -> p (k n)")
        with nc.sbuf_tensor("keep", [P, T], F32) as K.keep, nc.sbuf_tensor("xs", [P, NSHIFT, T], F32) as xs:
            xh, xl = on_slab("xn_h", 0, KD, F32R), on_slab("xn_l", KD, KD, F32R)
            with nc.sbuf_tensor("xT", [P, KD, T], F32) as K.xT:
                stage_load(nc, K)
                stage_rms(nc, K, "mix", K.xT, xh, xl, "norm_mix_g", T)
                stage_move(nc, K, "x_spilled", ((K.x_dram, flat(K.xT)), (K.xh_dram, flat(xh)), (K.xl_dram, flat(xl))))
            stage_proj_a(nc, K, xs, 0, NSHIFT, xh, xl)
            ld = on_slab("ld", 12, 4)
            stage_rwkv_prep(nc, K, xs, ld)
            with nc.sbuf_tensor("stP", [P, 4, 64], F32) as stP:
                stage_zero(nc, stP)
                stage_rwkv_scan(nc, K, xs, ld, "P", 128, 7, NTI, 0, stP, 63)
                stage_rwkv_states(nc, K, "P", stP, None, K.d["p_state_rwkv"][0])
            with nc.sbuf_tensor("stS", [P, 4, DB, 64], F32) as stS:
                stage_rwkv_states(nc, K, "S", stS, K.d["state_rwkv"][0], None)
                stage_rwkv_scan(nc, K, xs, ld, "S", TS, 2, 1, TP, stS, None)
                stage_rwkv_states(nc, K, "S", stS, None, K.d["s_state_rwkv"][0])
            stage_rwkv_out(nc, K, xs)
        reuse_semaphores()
        with ExitStack() as c1:
            s1 = lambda name, shape: c1.enter_context(nc.sbuf_tensor(name, shape, F32))
            kvt = s1("kvt", [P, NTI + 1, KVG])
            b31, ksn, kwn = s1("b31", [P, 8]), s1("ksn", [P, TS]), s1("kwn", [P, TS])
            up, qT = on_slab("up", 8, 4), on_slab("qT", 12, 4)
            with nc.sbuf_tensor("xn_h2", [P, KD, T], F32R) as xh, nc.sbuf_tensor("xn_l2", [P, KD, T], F32R) as xl:
                stage_move(nc, K, "xn_back", ((flat(xh), K.xh_dram), (flat(xl), K.xl_dram)))
                stage_proj_a(nc, K, up, B_POOL, 4, xh, xl)
                stage_kv(nc, K, kvt, xh, xl)
                stage_proj_a(nc, K, qT, B_Q, 4, xh, xl)
            stage_pool(nc, K, up)
            stage_tail_rows(nc, K)
            stage_head_rms(nc, K, "nsaq", qT, 4, "headsum", 64, "nsa_q_g", 0.125)
            stage_kv_norm(nc, K, kvt)
            with ExitStack() as c2:
                sc = lambda name, shape: c2.enter_context(nc.sbuf_tensor(name, shape, F32))
                near, cb = sc("near", [P, 8, 2 * P]), sc("cb", [P, 8, 30])
                kcd, vc = sc("kcd", [P, 2, 16]), sc("vc", [16, P])
                ksd, kwd = sc("ksd", [P, 2, TP]), sc("kwd", [P, 2, TP])
                stage_bias(nc, K, near, cb, b31)
                stage_nsa_keys(nc, K, kvt, kcd, vc, ksd, kwd, ksn, kwn)
                stage_nsa_prompt(nc, K, qT, kvt, kcd, vc, ksd, kwd, near, cb, b31)
            reuse_semaphores()
            with ExitStack() as c2:
                sc = lambda name, shape: c2.enter_context(nc.sbuf_tensor(name, shape, F32))
                Ssc = sc("s_scores", [P, 2, SROW])
                coef, grow = sc("s_coef", [P, 2, 3]), sc("s_gates", [P, 2, 3])
                vnew, vcb = sc("s_vnew", [DT, DB, 2, P]), sc("s_vcb", [SCM, DB, P])
                with nc.sbuf_tensor("s_qbd", [P, DB, 32], F32) as Qbd, nc.sbuf_tensor("s_bias", [P, SROW], F32) as bias:
                    stage_sample_rows(nc, K, kvt, qT, Qbd, bias, grow, vnew)
                    stage_sample_scores(nc, K, Qbd, bias, Ssc, vcb, ksn, kwn)
                stage_sample_softmax(nc, K, Ssc, coef, grow)
                stage_sample_values(nc, K, Ssc, coef, vcb, vnew)
        reuse_semaphores()
        block_of = lambda w: lambda m: w[:, P * m:P * m + P]
        place = nc.sbuf_base
        x = sb("x", [P, KD, T])
        h = nc.alloc_sbuf_tensor_at("h", [P, KD, T], F32, offset=place)
        with nc.sbuf_tensor("xn_h3", [P, KD, T], F32R) as xh, nc.sbuf_tensor("xn_l3", [P, KD, T], F32R) as xl:
            stage_move(nc, K, "xn_again", ((flat(xh), K.xh_dram), (flat(xl), K.xl_dram)))
            stage_merge(nc, K, h, xh, xl, on_slab("merge_spare", 12, 4))
        with nc.sbuf_tensor("h_h", [P, KD, T], F32R) as hh, nc.sbuf_tensor("h_l", [P, KD, T], F32R) as hl:
            stage_split(nc, K, "h", h, hh, hl, KD)
            stage_move(nc, K, "x_back", ((flat(x), K.x_dram),))
            stage_product(nc, K, "wo", block_of(K.d["w_out"][0]), KD, KD, hh, hl, x, True)
        mkT, mv = sb("mkT", [P, 4, 256]), sb("mv", [P, 2, 512])
        mT, mh, ml = (nc.alloc_sbuf_tensor_at(n, [P, KD, 256], d, offset=slab + z * KD * 256 * 4)
                      for z, (n, d) in enumerate((("mT", F32), ("mT_h", F32R), ("mT_l", F32R))))
        stage_mem_load(nc, K, mT)
        stage_rms(nc, K, "mem", mT, mh, ml, "norm_mem_g", 256)
        stage_mem_kv(nc, K, mh, ml, mkT, mv)
        xh = on_slab("xm_h", 0, KD, F32R)
        with nc.sbuf_tensor("xm_l", [P, KD, T], F32R) as xl:
            stage_rms(nc, K, "memx", x, xh, xl, "norm_memx_g", T)
            stage_product(nc, K, "mq", block_of(K.d["w_mq"][0]), KD, 4, xh, xl, K.oC, False)
        stage_head_rms(nc, K, "memq", K.oC, 4, "ones", P, "mem_q_g", 1.0)
        stage_mem_prompt(nc, K, K.oC, mkT, mv, K.oA)
        stage_mem_sample(nc, K, K.oC, K.oA)
        oh, ol = on_slab("om_h", 4, 4, F32R), on_slab("om_l", 8, 4, F32R)
        stage_split(nc, K, "om", K.oA, oh, ol, 4)
        stage_product(nc, K, "mo", block_of(K.d["w_mo"][0]), 4, KD, oh, ol, x, True)
        reuse_semaphores()
        xh, xl = on_slab("xf_h", 0, KD, F32R), on_slab("xf_l", KD, KD, F32R)
        stage_rms(nc, K, "ffn", x, xh, xl, "norm_ffn_g", T)
        stage_ffn(nc, K, xh, xl, x)
        stage_store(nc, K, x)


_INS = ["x_prompt", "x_sample", "state_rwkv", "state_shift", "state_pool", "cache_cmp_k", "cache_cmp_v", "cache_slc_k",
        "cache_slc_v", "cache_win_k", "cache_win_v", "cache_mem_k", "cache_mem_v", "page_table", "mem_prompt", "rel_bias",
        "norm_mix_g", "w_in", "shift_mu", "rwkv_w0", "rwkv_w2", "rwkv_a0", "rwkv_a2", "rwkv_g2", "rwkv_kk", "rwkv_ka",
        "rwkv_rk", "rwkv_lnx_g", "rwkv_lnx_b", "pool_w", "pool_scale", "nsa_q_g", "nsa_k_g", "w_br_a", "w_br_b", "w_br_c",
        "w_out", "norm_memx_g", "norm_mem_g", "w_mq", "w_mk", "w_mv", "mem_q_g", "mem_k_g", "w_mo", "norm_ffn_g",
        "w_ff1", "w_ff2"]
_OUTS = [("y_prompt", (1, TP, D)), ("y_sample", (DB, DT, D)),
         ("p_state_rwkv", (1, 1, 8, 64, 64)), ("p_state_shift", (1, 1, A_COLS)), ("p_state_pool", (1, 1, 15, 512)),
         ("p_cmp_k", (1, 1, TP, 2, 64)), ("p_cmp_v", (1, 1, TP, 2, 64)), ("p_slc_k", (1, 1, TP, 2, 64)),
         ("p_slc_v", (1, 1, TP, 2, 64)), ("p_win_k", (1, 1, 512, 2, 64)), ("p_win_v", (1, 1, 512, 2, 64)),
         ("p_mem_k", (1, 1, 256, 4, 128)), ("p_mem_v", (1, 1, 256, 4, 128)),
         ("s_state_rwkv", (1, DB, 8, 64, 64)), ("s_state_shift", (1, DB, A_COLS)), ("s_state_pool", (1, DB, 15, 512)),
         ("s_cmp_k", (1, DB, DT, 2, 64)), ("s_cmp_v", (1, DB, DT, 2, 64)), ("s_slc_k", (1, DB, DT, 2, 64)),
         ("s_slc_v", (1, DB, DT, 2, 64)), ("s_win_k", (1, DB, 512, 2, 64)), ("s_win_v", (1, DB, 512, 2, 64))]
_CONSTS = {"sheet": SHEET, "keep": KEEP, "onehot": ONEHOT}


def kernel(**inputs):
    import numpy as _np
    import concourse.bacc as _bacc
    from concourse import mybir as _mybir
    from concourse.bass_utils import run_bass_kernel_spmd as _run

    nc = _bacc.Bacc("TRN2", target_bir_lowering=False, num_devices=1)
    arrays, aps = {}, {}
    for name in _INS:
        a = _np.ascontiguousarray(inputs[name])
        arrays[f"in_{name}"] = a
        aps[name] = nc.dram_tensor(f"in_{name}", a.shape, _mybir.dt.from_np(a.dtype), kind="ExternalInput").ap()
    for name, a in _CONSTS.items():
        arrays[f"const_{name}"] = a
        aps[name] = nc.dram_tensor(f"const_{name}", a.shape, F32, kind="ExternalInput").ap()
    for name, shape in _OUTS:
        aps[name] = nc.dram_tensor(f"out_{name}", shape, F32, kind="ExternalOutput").ap()
    build(nc, aps)
    r = _run(nc, [arrays], core_ids=[0])
    return tuple(r.results[0][f"out_{name}"] for name, _ in _OUTS)
```

```python
from contextlib import ExitStack

import numpy as np

import concourse.bass as bass
from concourse import mybir


class Shared:
    pass


F32 = mybir.dt.float32
I32 = mybir.dt.int32
F32R = mybir.dt.float32r
ALU = mybir.AluOpType
ACT = mybir.ActivationFunctionType
AX = mybir.AxisListType

P = 128
D = 1024
KD = D // P
TP = 1024
DB, DT = 8, 4
TS = DB * DT
T = TP + TS
NC3 = 3
NW = T // NC3
TAIL = 15 + TS
T0 = T - TAIL
NTI = TP // P
A_COLS = 1792
OFF_POOL = A_COLS
OFF_Q = OFF_POOL + 512
OFF_KV = OFF_Q + 512
OFF_CG = OFF_KV + 768
OFF_MG = OFF_CG + 24
KVG = 768 + 24
PAST = 2048
PAGE = 128
NPG = PAST // PAGE
NEG = -1e30
RMS_EPS = 1e-6
LNX_EPS = 64e-5
DECAY = float(np.exp(-0.5))
REV = 2111
BVL = REV + 1025

BLOCKS = ([[(128 * c, 128)] for c in range(4)] + [[(576 + 128 * c, 128)] for c in range(4)]
          + [[(1088 + 128 * c, 128)] for c in range(4)] + [[(512, 64), (1600, 64)], [(1664, 128)]]
          + [[(OFF_POOL + 128 * c, 128)] for c in range(4)] + [[(OFF_Q + 128 * c, 128)] for c in range(4)])
B_R, B_K, B_V, B_WA, B_G, B_POOL, B_Q = 0, 4, 8, 12, 13, 14, 18
NSHIFT = 14

PARAMS = [("norm_mix_g", 8), ("shift_mu", NSHIFT), ("rwkv_w0", 4), ("rwkv_a0", 4), ("rwkv_kk", 4), ("rwkv_ka", 4),
          ("rwkv_rk", 4), ("rwkv_lnx_g", 4), ("rwkv_lnx_b", 4), ("pool_scale", 4), ("norm_memx_g", 8),
          ("norm_mem_g", 8), ("norm_ffn_g", 8), ("mem_q_g", 1), ("nsa_q_g", 1), ("kg_cmp", 1)]
PCOL = {}
_at = 0
for _n, _c in PARAMS:
    PCOL[_n] = _at
    _at += _c
NPAR = _at


def shape_constants():
    cols, sheets = {}, []

    def put(name, a):
        b = np.zeros((P, a.shape[1]), np.float32)
        b[:a.shape[0]] = a
        cols[name] = (sum(s.shape[1] for s in sheets), a.shape[1])
        sheets.append(b)

    r = np.arange(P)
    put("ident", np.eye(P))
    put("flip", np.eye(P)[::-1])
    put("headsum", (r[:, None] // 64 == r[None, :] // 64).astype(np.float32))
    put("ones", np.ones((P, P)))

    def chunk_masks(tag, n, levels, size):
        i, t = np.arange(n)[:, None], np.arange(n)[None, :]
        same = i // size == t // size
        put("strict" + tag, (same & (i < t)) * 1.0)
        put("incl" + tag, (same & (i <= t)) * 1.0)
        c = np.arange(32)[None, :]
        r = i % 32
        put("eye" + tag, (r == c) * 1.0)
        for l in range(levels):
            s = 1 << l
            put(f"lvl{l}" + tag, ((r // (2 * s) == c // (2 * s)) & (c // s % 2 == 1) & (r // s % 2 == 0)) * 1.0)
        put("low0" + tag, ((c // 2 == r // 2) & (r % 2 == 1) & (c % 2 == 0)) * 1.0)
    chunk_masks("P", 128, 5, 128)
    chunk_masks("S", TS, 2, DT)
    i = np.arange(TS)
    put("batch", (i[:, None] // DT == np.arange(DB)[None, :]) * 1.0)
    put("batchcol", np.repeat(np.kron(np.eye(DB), np.ones((1, DT))).reshape(1, -1), P, 0))
    put("edge", np.where(r[:, None] < r[None, :], 0.0, NEG))
    put("poolcnt", np.concatenate([np.repeat((1.0 / np.minimum(w, np.arange(16) + 1))[None], P, 0)
                                   for w in (2, 4, 8, 16)], 1))
    c, late = np.arange(4), []
    for tag, per in (("H", 2), ("M", 1)):
        own = np.arange(8)[None, :, None] == per * c[:, None, None] + (r * per // P)[None, None, :]
        put("tohead" + tag, own.transpose(2, 0, 1).reshape(P, 32) * 1.0)
        late.append(("tochan" + tag, own.transpose(1, 0, 2).reshape(8, 4 * P) * 1.0))
    m = np.zeros((P, 64))
    m[:64, 30] = 1 / 64
    m[64:, 31] = 1 / 64
    put("blk", m)
    put("blk16", (r[:, None] // 4 == np.arange(32)[None, :]) / 64.0)
    put("eighth", (r[:, None] % 8) * 1.0)
    t = r % 4
    put("edgeS", np.where(np.arange(4)[None, :] <= t[:, None], NEG, 0.0))
    put("grp", (r[:, None] % 32 // 16 == np.arange(2)[None, :]) * 1.0)
    put("mhead", (r[:, None] % 32 // 4 == np.arange(4)[None, :]) * 1.0)
    put("heads4", ((r[:, None] // 16 == r[None, :] // 16) & (t[:, None] == t[None, :])) * 1.0)
    m = np.arange(-14, 16)
    put("cmask", (r[:, None] - 64 * m[None, :] - 63 >= 0) * 1.0)
    resident = sum(x.shape[1] for x in sheets)
    for name, m in late:
        put(name, m)
    keep = np.ones((1, T))
    keep[0, 0:TP:P] = 0
    keep[0, TP:T:DT] = 0
    dist = REV - np.arange(BVL)
    n = np.maximum(dist, 0)
    ratio = np.log(np.maximum(n, 1) / 16) / np.log(8)
    bucket = np.where(n < 16, n, np.minimum(16 + (ratio * 16).astype(np.int64), 31))
    onehot = (bucket[None, :] == np.arange(32)[:, None]) & (dist >= 0)[None]
    onehot = np.concatenate([onehot, (dist < 0)[None]], 0)
    return cols, resident, np.concatenate(sheets, 1).astype(np.float32), keep.astype(np.float32), onehot.astype(np.float32)


CCOL, RESIDENT, SHEET, KEEP, ONEHOT = shape_constants()


def stage_load(nc, K):
    ctx = ExitStack()
    with ctx:
        xin = ctx.enter_context(nc.sbuf_tensor("xin", [P, 3, D], F32))
        prow = ctx.enter_context(nc.sbuf_tensor("prow", [NPAR, P], F32))
        srow = ctx.enter_context(nc.sbuf_tensor("srow", [DB, A_COLS], F32))
        block = ctx.enter_context(nc.Block())
        s_const, s_prow, s_x = K.sem("const_in"), K.sem("param_rows_in"), K.sems("x_in", 3)
        s_par, s_parc = K.sem("params_turned"), K.sem("params_copied")
        s_xt, s_xa, s_xv = K.sem("x_turned"), K.sem("x_copied_act"), K.sem("x_copied_dve")
        s_sh = K.sem("shift_turned")

        @block.sync
        def _(e):
            e.dma_start(K.cst[:, :], K.d["sheet"][:, 0:RESIDENT]).then_inc(s_const, 16)
            e.dma_start(K.keep[:, :], K.d["keep"].partition_broadcast(P)).then_inc(s_const, 16)
            e.dma_start(srow[:, :], K.d["state_shift"][0]).then_inc(s_const, 16)
            for i in range(NTI + 1):
                if i >= 3:
                    e.wait_ge(s_xt, i - 2)
                if i < NTI:
                    e.dma_start(xin[:, i % 3, :], K.d["x_prompt"][0, P * i:P * i + P, :]).then_inc(s_x[i % 3], 16)
                else:
                    e.dma_start(xin[0:TS, i % 3, :], K.d["x_sample"].rearrange("b t d -> (b t) d")).then_inc(s_x[i % 3], 16)

        @block.scalar
        def _(e):
            for name, cnt in PARAMS:
                if name in ("nsa_q_g", "kg_cmp"):
                    src = K.d["nsa_q_g"][0:1, :] if name == "nsa_q_g" else K.d["nsa_k_g"][0, 0:1, :]
                    for z in range(2):
                        e.dma_start(prow[PCOL[name]:PCOL[name] + 1, 64 * z:64 * z + 64], src).then_inc(s_prow, 16)
                    continue
                if name == "shift_mu":
                    for b in range(NSHIFT):
                        at = 0
                        for c0, w in BLOCKS[b]:
                            e.dma_start(prow[PCOL[name] + b:PCOL[name] + b + 1, at:at + w],
                                        K.d["shift_mu"][0:1, c0:c0 + w]).then_inc(s_prow, 16)
                            at += w
                    continue
                src = K.d[name]
                if name == "rwkv_rk":
                    src = src.rearrange("a (c h) d -> (a c) (h d)", c=cnt)
                else:
                    src = src.rearrange("a (c p) -> (a c) p", p=P)
                e.dma_start(prow[PCOL[name]:PCOL[name] + cnt, :], src).then_inc(s_prow, 16)
            for i in range(NTI + 1):
                n = P if i < NTI else TS
                e.wait_ge(s_xt, i + 1)
                e.activation(K.xT[:, 0:4, P * i:P * i + n],
                             K.ps[:, 2 * (i % 2), :].rearrange("p (k n) -> p k n", k=4)[:, :, 0:n],
                             ACT.Copy).then_inc(s_xa, 1)

        @block.tensor
        def _(e):
            e.wait_ge(s_const, 48)
            ident = K.c("ident")
            e.wait_ge(s_prow, 16 * K.n_prow)
            e.transpose(K.ps[:, 4, 0:NPAR], prow[:, :], ident[0:NPAR, 0:NPAR]).then_inc(s_par, 1)
            for b in range(NSHIFT):
                at = 0
                for c0, w in BLOCKS[b]:
                    if at == 0:
                        mm = e.transpose(K.ps[0:w, 5, 8 * b:8 * b + 8], srow[:, c0:c0 + w], ident[0:DB, 0:DB])
                    else:
                        mm = e.transpose(K.ps[0:w, 6, 0:8], srow[:, c0:c0 + w], ident[0:DB, 0:DB])
                    at += w
            mm.then_inc(s_sh, 1)
            for i in range(NTI + 1):
                n = P if i < NTI else TS
                e.wait_ge(s_x[i % 3], 16 * (i // 3 + 1))
                if i >= 2:
                    e.wait_ge(s_xa, i - 1)
                    e.wait_ge(s_xv, i - 1)
                for k in range(KD):
                    mm = e.transpose(K.ps[:, 2 * (i % 2) + k // 4, P * (k % 4):P * (k % 4) + n],
                                     xin[0:n, i % 3, P * k:P * k + P], ident[0:n, 0:n])
                mm.then_inc(s_xt, 1)

        @block.vector
        def _(e):
            e.wait_ge(s_par, 1)
            e.tensor_copy(K.par[:, 0:NPAR], K.ps[:, 4, 0:NPAR])
            e.wait_ge(s_sh, 1)
            e.tensor_copy(K.shT[:, 0:B_WA, :], K.ps[:, 5, 0:8 * B_WA].rearrange("p (b n) -> p b n", n=8))
            e.tensor_copy(K.shT[:, B_G, :], K.ps[:, 5, 8 * B_G:8 * B_G + 8])
            e.tensor_copy(K.shT[0:64, B_WA, :], K.ps[0:64, 5, 8 * B_WA:8 * B_WA + 8])
            e.tensor_copy(K.shT[64:128, B_WA, :], K.ps[0:64, 6, 0:8])
            for i in range(NTI + 1):
                n = P if i < NTI else TS
                e.wait_ge(s_xt, i + 1)
                e.tensor_copy(K.xT[:, 4:8, P * i:P * i + n],
                              K.ps[:, 2 * (i % 2) + 1, :].rearrange("p (k n) -> p k n", k=4)[:, :, 0:n]).then_inc(s_xv, 1)


def side_moves(block, K, name, moves):
    s_moved = K.sem(name + "_moved")

    @block.gpsimd
    def _(e):
        for dst, src in moves:
            e.dma_start(dst, src).then_inc(s_moved, 16)
        e.wait_ge(s_moved, 16 * len(moves))


def stage_rms(nc, K, name, src, hi, lo, gain, ntok, moves=()):
    nchunk = -(-ntok // NW)
    w = ntok // nchunk
    ctx = ExitStack()
    with ctx:
        sq = ctx.enter_context(nc.sbuf_tensor(name + "_sq", [P, 2, KD, w], F32))
        rstd = ctx.enter_context(nc.sbuf_tensor(name + "_rstd", [P, 2, w], F32))
        block = ctx.enter_context(nc.Block())
        s_sq, s_sum, s_nrm, s_hi = (K.sem(name + x) for x in ("_squared", "_summed", "_normed", "_high"))
        s_var, s_root, s_lo = K.sem(name + "_mean"), K.sem(name + "_root"), K.sem(name + "_low")
        if moves:
            side_moves(block, K, name, moves)

        @block.scalar
        def _(e):
            def squares(c):
                if c >= 2:
                    e.wait_ge(s_lo, c - 1)
                e.activation(sq[:, c % 2, :, :], src[:, :, w * c:w * c + w], ACT.Square).then_inc(s_sq, 1)

            squares(0)
            for c in range(nchunk):
                e.wait_ge(s_var, c + 1)
                e.activation(rstd[:, c % 2, :], rstd[:, c % 2, :], ACT.Sqrt).then_inc(s_root, 1)
                if c + 1 < nchunk:
                    squares(c + 1)
                e.wait_ge(s_nrm, c + 1)
                e.activation(hi[:, :, w * c:w * c + w], sq[:, c % 2, :, :], ACT.Copy).then_inc(s_hi, 1)

        @block.tensor
        def _(e):
            for c in range(nchunk):
                e.wait_ge(s_sq, c + 1)
                if c >= 2:
                    e.wait_ge(s_var, c - 1)
                for k in range(KD):
                    mm = e.matmul(K.ps[:, c % 2, 0:w], K.c("ones"), sq[:, c % 2, k, :], start=k == 0, stop=k == KD - 1)
                mm.then_inc(s_sum, 1)

        @block.vector
        def _(e):
            for c in range(nchunk):
                e.wait_ge(s_sum, c + 1)
                e.tensor_scalar(rstd[:, c % 2, :], K.ps[:, c % 2, 0:w], 1.0 / D, RMS_EPS,
                                ALU.mult, ALU.add).then_inc(s_var, 1)
                e.wait_ge(s_root, c + 1)
                e.reciprocal(rstd[:, c % 2, :], rstd[:, c % 2, :])
                e.drain()
                for k in range(KD):
                    e.scalar_tensor_tensor(sq[:, c % 2, k, :], src[:, k, w * c:w * c + w],
                                           K.p(gain, k), rstd[:, c % 2, :], ALU.mult, ALU.mult)
                e.drain().then_inc(s_nrm, 1)
                e.wait_ge(s_hi, c + 1)
                e.tensor_tensor(lo[:, :, w * c:w * c + w], sq[:, c % 2, :, :], hi[:, :, w * c:w * c + w].bitcast(F32),
                                ALU.subtract).then_inc(s_lo, 1)


def stage_split(nc, K, name, src, hi, lo, nblk):
    with nc.Block() as block:
        s_hi = K.sem(name + "_high")

        @block.scalar
        def _(e):
            for m in range(nblk):
                e.activation(hi[:, m, :], src[:, m, :], ACT.Copy).then_inc(s_hi, 1)

        @block.vector
        def _(e):
            for m in range(nblk):
                e.wait_ge(s_hi, m + 1)
                e.tensor_tensor(lo[:, m, :], src[:, m, :], hi[:, m, :].bitcast(F32), ALU.subtract)


NRAW = 3
NSPL = 2


def weight_slots(nc, K, ctx, tag, kb, nraw=NRAW):
    W = Shared()
    W.kb, W.nraw = kb, nraw
    W.raw = ctx.enter_context(nc.sbuf_tensor(tag + "_raw", [P, nraw, kb, P], F32))
    W.hi = ctx.enter_context(nc.sbuf_tensor(tag + "_high", [P, NSPL, kb, P], F32R))
    W.lo = ctx.enter_context(nc.sbuf_tensor(tag + "_low", [P, NSPL, kb, P], F32R))
    W.s_in = K.sems(tag + "_weights_in", nraw)
    W.s_hi, W.s_lo, W.s_mm = K.sem(tag + "_weights_high"), K.sem(tag + "_weights_low"), K.sem(tag + "_product")
    return W


def load_block(e, W, m, pieces):
    if m >= W.nraw:
        e.wait_ge(W.s_lo, m - W.nraw + 1)
    at = 0
    for src in pieces:
        w = src.shape[1]
        e.dma_start(W.raw[:, m % W.nraw, :, at:at + w], src.rearrange("(k p) n -> p k n", p=P)).then_inc(W.s_in[m % W.nraw], 16)
        at += w


def high_block(e, W, m, landed, per=1):
    e.wait_ge(W.s_in[m % W.nraw], 16 * landed)
    if m >= NSPL:
        e.wait_ge(W.s_mm, per * (m - NSPL + 1))
    e.activation(W.hi[:, m % NSPL, :, :], W.raw[:, m % W.nraw, 0:W.kb, :], ACT.Copy).then_inc(W.s_hi, 1)


def low_block(e, W, m):
    e.wait_ge(W.s_hi, m + 1)
    e.tensor_tensor(W.lo[:, m % NSPL, :, :], W.raw[:, m % W.nraw, 0:W.kb, :], W.hi[:, m % NSPL, :, :].bitcast(F32),
                    ALU.subtract).then_inc(W.s_lo, 1)


def product(e, K, W, m, rh, rl, bank, ks):
    z = m % NSPL
    for c in range(NC3):
        o, n = K.ps[:, bank + c, 0:NW], slice(NW * c, NW * c + NW)
        for k in ks:
            e.matmul(o, W.hi[:, z, k, :], rh[:, k, n], start=k == ks[0], stop=False)
            e.matmul(o, W.hi[:, z, k, :], rl[:, k, n], start=False, stop=False)
            mm = e.matmul(o, W.lo[:, z, k, :], rh[:, k, n], start=False, stop=k == ks[-1])
    return mm


def stage_proj_a(nc, K, xs, first, count, xh, xl, moves=()):
    ctx = ExitStack()
    tag = f"pj{first}"
    with ctx:
        shifted = first == 0
        W = weight_slots(nc, K, ctx, tag, KD)
        if shifted:
            u = ctx.enter_context(nc.sbuf_tensor(tag + "_u", [P, 2, 1 + TP + DB * (DT + 1)], F32))
            dlt = ctx.enter_context(nc.sbuf_tensor(tag + "_d", [P, T], F32))
        block = ctx.enter_context(nc.Block())
        s_raw, s_used = K.sem(tag + "_raw_copied"), K.sem(tag + "_raw_used")
        if moves:
            side_moves(block, K, tag, moves)
        landed = {}
        for m in range(count):
            landed[m] = landed.get(m - NRAW, 0) + len(BLOCKS[first + m])

        @block.sync
        def _(e):
            for m in range(count):
                load_block(e, W, m, [K.d["w_in"][0, :, c0:c0 + w] for c0, w in BLOCKS[first + m]])

        @block.tensor
        def _(e):
            for m in range(count):
                e.wait_ge(W.s_lo, m + 1)
                if m >= 2:
                    e.wait_ge(s_raw, m - 1)
                product(e, K, W, m, xh, xl, 3 * (m % 2), range(KD)).then_inc(W.s_mm, 1)

        @block.scalar
        def _(e):
            high_block(e, W, 0, landed[0])
            high_block(e, W, 1, landed[1])
            for m in range(count):
                e.wait_ge(W.s_mm, m + 1)
                bank = K.ps[:, 3 * (m % 2):3 * (m % 2) + 3, :]
                if shifted:
                    if m >= 2:
                        e.wait_ge(s_used, m - 1)
                    for c in range(2):
                        e.activation(u[:, m % 2, 1 + NW * c:1 + NW * c + NW], bank[:, c, 0:NW], ACT.Copy)
                    e.activation(u[:, m % 2, 1 + 2 * NW:1 + TP], bank[:, 2, 0:TP - 2 * NW], ACT.Copy)
                    us = u[:, m % 2, 1 + TP:].rearrange("p (b t) -> p b t", t=DT + 1)
                    e.activation(us[:, :, 1:], bank[:, 2, TP - 2 * NW:NW].rearrange("p (b t) -> p b t", t=DT), ACT.Copy)
                else:
                    e.activation(xs[:, m, :].rearrange("p (c n) -> p c n", c=NC3), bank[:, :, 0:NW], ACT.Copy)
                if first + m < B_Q:
                    e.activation(K.utail[:, first + m, :], bank[:, 2, NW - TAIL:NW], ACT.Copy).then_inc(s_raw, 1)
                else:
                    e.drain().then_inc(s_raw, 1)
                if m + 2 < count:
                    high_block(e, W, m + 2, landed[m + 2])

        @block.vector
        def _(e):
            low_block(e, W, 0)
            low_block(e, W, 1)
            if shifted:
                e.memset(u[:, 0, 0:1], 0.0)
                e.memset(u[:, 1, 0:1], 0.0)
            for m in range(count):
                if m + 2 < count:
                    low_block(e, W, m + 2)
                if not shifted:
                    continue
                us = u[:, m % 2, 1 + TP:].rearrange("p (b t) -> p b t", t=DT + 1)
                e.tensor_copy(us[:, :, 0:1], K.shT[:, m, :].unsqueeze(2))
                e.wait_ge(s_raw, m + 1)
                e.drain()
                up = u[:, m % 2, 0:1 + TP]
                e.tensor_tensor(dlt[:, 0:TP], up[:, 0:TP], up[:, 1:1 + TP], ALU.subtract)
                e.tensor_tensor(dlt[:, TP:T].rearrange("p (b t) -> p b t", t=DT), us[:, :, 0:DT], us[:, :, 1:DT + 1],
                                ALU.subtract)
                e.drain()
                e.scalar_tensor_tensor(xs[:, m, 0:TP], dlt[:, 0:TP], K.p("shift_mu", m), up[:, 1:1 + TP],
                                       ALU.mult, ALU.add)
                e.scalar_tensor_tensor(xs[:, m, TP:T].rearrange("p (b t) -> p b t", t=DT),
                                       dlt[:, TP:T].rearrange("p (b t) -> p b t", t=DT), K.p("shift_mu", m),
                                       us[:, :, 1:DT + 1], ALU.mult, ALU.add).then_inc(s_used, 1)
                e.drain()


def stage_rwkv_prep(nc, K, xs, ld):
    KK, A, L = K.oA, K.oB, K.oC
    ctx = ExitStack()
    with ctx:
        w2 = ctx.enter_context(nc.sbuf_tensor("rw_w2a2", [P, 512], F32))
        sq = ctx.enter_context(nc.sbuf_tensor("rw_sq", [P, T], F32))
        inv = ctx.enter_context(nc.sbuf_tensor("rw_inv", [P, T], F32))
        block = ctx.enter_context(nc.Block())
        s_w, s_th = K.sem("rw_lora_in"), K.sem("rw_tanh")
        s_z, s_sig = K.sem("rw_lora_product"), K.sem("rw_sigmoid")
        s_kk, s_sq, s_ss = K.sem("rw_kk_scaled"), K.sem("rw_kk_squared"), K.sem("rw_kk_summed")
        s_mx, s_rt = K.sem("rw_sum_guarded"), K.sem("rw_root")

        @block.sync
        def _(e):
            e.dma_start(w2[0:64, :], K.d["rwkv_w2"][0]).then_inc(s_w, 16)
            e.dma_start(w2[64:128, :], K.d["rwkv_a2"][0]).then_inc(s_w, 16)

        @block.scalar
        def _(e):
            e.activation(xs[0:64, B_WA, :], xs[0:64, B_WA, :], ACT.Tanh).then_inc(s_th, 1)
            for m in range(8):
                e.wait_ge(s_z, m + 1)
                dst = (ld if m < 4 else A)[:, m % 4, :].rearrange("p (c n) -> p c n", c=NC3)
                e.activation(dst, K.ps[:, 3 * (m % 2):3 * (m % 2) + 3, 0:NW], ACT.Sigmoid,
                             bias=K.p("rwkv_w0" if m < 4 else "rwkv_a0", m % 4)).then_inc(s_sig, 1)
            for c in range(4):
                e.wait_ge(s_kk, c + 1)
                if c >= 1:
                    e.wait_ge(s_ss, c)
                e.activation(sq[:, :], KK[:, c, :], ACT.Square).then_inc(s_sq, 1)
                e.wait_ge(s_mx, c + 1)
                e.activation(inv[:, :], inv[:, :], ACT.Sqrt).then_inc(s_rt, 1)

        @block.tensor
        def _(e):
            e.wait_ge(s_w, 32)
            e.wait_ge(s_th, 1)
            for m in range(8):
                o = 0 if m < 4 else 64
                if m >= 2:
                    e.wait_ge(s_sig, m - 1)
                for c in range(NC3):
                    mm = e.matmul(K.ps[:, 3 * (m % 2) + c, 0:NW], w2[o:o + 64, 128 * (m % 4):128 * (m % 4) + 128],
                                  xs[o:o + 64, B_WA, NW * c:NW * c + NW], start=True, stop=True)
                mm.then_inc(s_z, 1)
            e.wait_ge(s_sig, 8)
            for c in range(4):
                e.wait_ge(s_sq, c + 1)
                if c >= 1:
                    e.wait_ge(s_mx, c)
                for n in range(NC3):
                    mm = e.matmul(K.ps[:, n, 0:NW], K.c("headsum"), sq[:, NW * n:NW * n + NW], start=True, stop=True)
                mm.then_inc(s_ss, 1)

        @block.vector
        def _(e):
            for c in range(4):
                e.tensor_scalar(KK[:, c, :], xs[:, B_K + c, :], K.p("rwkv_kk", c), None, ALU.mult).then_inc(s_kk, 1)
            e.tensor_scalar(K.par[:, NPAR:NPAR + 4], K.par[:, PCOL["rwkv_ka"]:PCOL["rwkv_ka"] + 4], -1.0, 1.0,
                            ALU.mult, ALU.add)
            for c in range(4):
                e.wait_ge(s_sig, c + 1)
                e.tensor_scalar(ld[:, c, :], ld[:, c, :], -DECAY, None, ALU.mult)
                e.drain()
                e.tensor_tensor_scan(L[:, c, :], K.keep[:, :], ld[:, c, :], 0.0, ALU.mult, ALU.add)
            for c in range(4):
                e.wait_ge(s_ss, c + 1)
                e.tensor_scalar(inv[:, :].rearrange("p (c n) -> p c n", c=NC3), K.ps[:, 0:3, 0:NW], 1e-24, None,
                                ALU.max).then_inc(s_mx, 1)
                e.wait_ge(s_rt, c + 1)
                e.reciprocal(inv[:, :], inv[:, :])
                e.drain()
                e.tensor_tensor(KK[:, c, :], KK[:, c, :], inv[:, :], ALU.mult)
                e.drain()
                e.tensor_scalar(inv[:, :], A[:, c, :], K.p("rwkv_ka", c), K.par[:, NPAR + c:NPAR + c + 1],
                                ALU.mult, ALU.add)
                e.drain()
                e.tensor_tensor(xs[:, B_K + c, :], xs[:, B_K + c, :], inv[:, :], ALU.mult)
                e.tensor_tensor(A[:, c, :], A[:, c, :], KK[:, c, :], ALU.mult)
                e.drain()


def stage_rwkv_scan(nc, K, xs, ld, tag, n, levels, nchunk, tbase, S0, mid):
    KK, B, L = K.oA, K.oB, K.oC
    sample = tag == "S"
    ctx = ExitStack()
    with ctx:
        C = 32
        FINE, COARSE = levels
        nb = n // C
        sb = lambda nm, sh: ctx.enter_context(nc.sbuf_tensor("sc" + tag + nm, sh, F32))
        D1, D2 = sb("D1", [P, 4, n]), sb("D2", [P, 4, n])
        EN = sb("EN", [P, 4, n])
        NB = min(2, nchunk)
        KtR2 = sb("KtR", [P, NB, 4, 2, n])
        Bt2, Kc2 = sb("Bt", [P, NB, 4, n]), sb("Kc", [P, NB, 4, n])
        fac = sb("fac", [P, NB, 4])
        BtT, KcT, VT = sb("BtT", [n, 512]), sb("KcT", [n, 512]), sb("VT", [n, 512])
        MT, RBT, NT, RKT = (sb(x, [n, 8, n]) for x in ("MT", "RBT", "NT", "RKT"))
        X, XT = (sb(x, [n, 8, C]) for x in ("X", "XT"))
        MD, Mn = sb("MD", [n, 8, C]), sb("Mn", [n, FINE, 8, C])
        T1 = sb("T1", [n, 8, 2 * C])
        if sample:
            XTF = XT
        else:
            XTF = sb("XTF", [n, 8, n])
            X00 = sb("X00", [64, 8, 64])
        RH, SA = xs[0:n, B_WA, 0:512], xs[0:n, B_WA, 512:1024]
        if sample:
            KtB = sb("KtB", [P, 4, DB, TS])
            RB4 = sb("RB4", [P, 4, DB, TS])
            SAB = sb("SAB", [n, 2, DB, 64])
        block = ctx.enter_context(nc.Block())
        sem = lambda nm: K.sem(f"sc{tag}_{nm}")
        s_d, s_e = sem("exponents"), sem("decays")
        s_prep = sem("operands")
        s_tr, s_trc = sem("turned"), sem("turned_copied")
        s_ab, s_msk = sem("scores"), sem("scores_masked")
        s_mn, s_t1, s_t1c, s_z, s_x = sem("level_masked"), sem("level_half"), sem("level_half_copied"), sem("level_step"), sem("inverse_updated")
        s_rh, s_rhc, s_sa, s_sac = sem("rhs"), sem("rhs_copied"), sem("corrections"), sem("corrections_copied")
        s_y, s_yc, s_st, s_stu = sem("outputs"), sem("outputs_copied"), sem("state_sum"), sem("state_updated")
        s_dg, s_md, s_zero = sem("blocks_unpacked"), sem("blocks_packed"), sem("inverse_zeroed")
        NST = FINE + COARSE
        ps = K.ps
        bank = lambda h: 2 * (h % 2) + h // 4
        pos = lambda h: (h // 2) % 2

        def tok(i):
            return bass.ds(tbase + n * i, n) if not isinstance(i, int) else slice(tbase + n * i, tbase + n * i + n)

        def col(i, at):
            return bass.ds(tbase + n * i + at, 1) if not isinstance(i, int) else slice(tbase + n * i + at, tbase + n * i + at + 1)

        def part(b, at, w=32):
            return ps[0:n, b, at:at + 4 * w].rearrange("p (h c) -> p h c", h=4)

        msk = lambda nm: K.c(nm + tag)[0:n, 0:C].unsqueeze(1)

        def mid_of(i):
            return L[:, :, col(i, mid)].to_broadcast([P, 4, n])

        @block.vector
        def _(e):
            def exponents(i):
                if sample:
                    e.tensor_copy(D1[:, :, :], L[:, :, tok(i)])
                else:
                    e.tensor_tensor(D1[:, :, :], L[:, :, tok(i)], mid_of(i), ALU.subtract)
                e.drain()
                e.tensor_tensor(D2[:, :, :], D1[:, :, :], ld[:, :, tok(i)], ALU.subtract).then_inc(s_d, 1)

            def rows(i):
                e.wait_ge(s_e, 2 * i + 1)
                if i >= NB:
                    e.wait_ge(s_y, i - NB + 1)
                e.tensor_tensor(KtR2[:, i % NB, :, 0, :], KK[:, :, tok(i)], D2[:, :, :], ALU.mult)
                e.tensor_tensor(KtR2[:, i % NB, :, 1, :], xs[:, B_R:B_R + 4, tok(i)], D1[:, :, :], ALU.mult)

            def columns(i):
                e.tensor_tensor(Bt2[:, i % NB, :, :], B[:, :, tok(i)], EN[:, :, :], ALU.mult)
                e.tensor_tensor(Kc2[:, i % NB, :, :], xs[:, B_K:B_K + 4, tok(i)], EN[:, :, :], ALU.mult)
                f = fac[:, i % NB, :].unsqueeze(2)
                if not sample:
                    e.tensor_tensor(f, L[:, :, col(i, n - 1)], L[:, :, col(i, mid)], ALU.subtract)
                    if i < nchunk - 1:
                        e.drain()
                        e.tensor_tensor(f, f, L[:, :, col(i + 1, mid)], ALU.add)
                e.drain().then_inc(s_prep, 1)

            exponents(0)
            rows(0)
            columns(0)
            for i in range(nchunk):
                KtR = KtR2[:, i % NB, :, :, :]
                if sample:
                    bc = K.c("batchcol").rearrange("p (b t) -> p b t", b=DB)
                    for q in range(4):
                        for dst, z in ((KtB, 0), (RB4, 1)):
                            e.tensor_tensor(dst[:, q, :, :], KtR[:, q, z, :].unsqueeze(1).to_broadcast([P, DB, TS]), bc, ALU.mult)
                    e.drain().then_inc(s_prep, 1)
                for h in range(8):
                    e.wait_ge(s_ab, 24 * i + (4 if h < 4 else 8))
                    v = ps[0:n, bank(h), :].rearrange("p (z n) -> p z n", z=2)[:, pos(h), 0:2 * n]
                    e.scalar_tensor_tensor(MT[:, h, :], v[:, 0:n], 3e38, K.c("strict" + tag)[0:n, 0:n], ALU.min, ALU.mult)
                    e.scalar_tensor_tensor(RBT[:, h, :], v[:, n:2 * n], 3e38, K.c("incl" + tag)[0:n, 0:n], ALU.min, ALU.mult).then_inc(s_msk, 1)
                e.wait_ge(s_ab, 24 * i + 24)
                for z in range(2):
                    v = ps[0:n, z, 0:4 * C].rearrange("p (h n) -> p h n", h=4)
                    e.scalar_tensor_tensor(X[:, z::2, :], v, 3e38, msk("low0").to_broadcast([n, 4, C]), ALU.min, ALU.mult)
                e.wait_ge(s_md, i + 1)
                if i == 0 and not sample:
                    e.wait_ge(s_zero, 1)
                e.tensor_tensor(XT[:, :, :], MD[:, :, :], msk("lvl0").to_broadcast([n, 8, C]), ALU.mult)
                e.drain()
                idn = msk("eye").to_broadcast([n, 8, C])
                e.tensor_tensor(X[:, :, :], idn, X[:, :, :], ALU.subtract)
                e.tensor_tensor(XT[:, :, :], idn, XT[:, :, :], ALU.subtract)
                e.drain().then_inc(s_x, 2)

                def late_masks(h):
                    e.wait_ge(s_ab, 24 * i + 16)
                    v = ps[0:n, 4 + bank(h), :].rearrange("p (z n) -> p z n", z=2)[:, pos(h), 0:2 * n]
                    e.scalar_tensor_tensor(NT[:, h, :], v[:, 0:n], 3e38, K.c("strict" + tag)[0:n, 0:n], ALU.min, ALU.mult)
                    e.scalar_tensor_tensor(RKT[:, h, :], v[:, n:2 * n], 3e38, K.c("incl" + tag)[0:n, 0:n], ALU.min, ALU.mult).then_inc(s_msk, 1)

                for l in range(NST):
                    for z in range(2):
                        e.wait_ge(s_z, 2 * (NST * i + l) + z + 1)
                        hs = slice(4 * z, 4 * z + 4)
                        if l < FINE:
                            e.tensor_tensor(X[:, hs, :], X[:, hs, :], part(2 + z, 0), ALU.subtract)
                            e.tensor_tensor(XT[:, hs, :], XT[:, hs, :], part(2 + z, 128), ALU.subtract)
                        elif l == FINE:
                            e.tensor_scalar(X00[32:64, hs, 0:32], part(2 + z, 0)[32:64, :, :], -1.0, None, ALU.mult)
                            for p in (0, 64):
                                e.tensor_scalar(XTF[p:p + 32, hs, p + 32:p + 64], part(2 + z, 128)[p:p + 32, :, :], -1.0, None, ALU.mult)
                        else:
                            e.tensor_scalar(XTF[0:64, hs, 64:128], part(2 + z, 0, 64)[0:64, :, :], -1.0, None, ALU.mult)
                        e.drain().then_inc(s_x, 1)
                    if sample:
                        for h in range(8):
                            late_masks(h)
                    elif l < 4:
                        late_masks(2 * l)
                        late_masks(2 * l + 1)
                    if i + 1 < nchunk and l in (0, 2, 4):
                        {0: exponents, 2: rows, 4: columns}[l](i + 1)
                e.wait_ge(s_sa, i + 1)
                e.tensor_copy(SA[:, :].rearrange("p (h z d) -> p h z d", z=2, d=64),
                              ps[0:n, 0:2, 0:256].rearrange("p z (h d) -> p h z d", d=64)).then_inc(s_sac, 1)
                if sample:
                    e.drain()
                    bm = K.c("batch")[0:n, :].unsqueeze(2).to_broadcast([n, DB, 64])
                    for h in range(8):
                        e.wait_ge(s_st, h) if h else None
                        e.tensor_tensor(SAB[:, 0, :, :], SA[:, 64 * h:64 * h + 64].unsqueeze(1).to_broadcast([n, DB, 64]), bm, ALU.mult)
                        e.tensor_tensor(SAB[:, 1, :, :], VT[:, 64 * h:64 * h + 64].unsqueeze(1).to_broadcast([n, DB, 64]), bm, ALU.mult)
                        e.drain().then_inc(s_sac, 1)
                        e.wait_ge(s_st, h + 1)
                        pp = 64 * (h % 2)
                        st = S0[pp:pp + 64, h // 2, :, :]
                        e.tensor_tensor(st, st, ps[pp:pp + 64, 4 + h % 2, :].rearrange("p (b d) -> p b d", b=DB), ALU.add)
                        e.drain()
                        e.tensor_tensor(st, st, D1[pp:pp + 64, h // 2, DT - 1::DT].unsqueeze(2).to_broadcast([64, DB, 64]), ALU.mult)
                        e.drain()
                else:
                    e.wait_ge(s_st, i + 1)
                    e.tensor_tensor(S0[:, :, :], S0[:, :, :], ps[:, 4, 0:256].rearrange("p (c d) -> p c d", c=4), ALU.add)
                    e.wait_ge(s_e, 2 * i + 2)
                    e.drain()
                    e.tensor_tensor(S0[:, :, :], S0[:, :, :], fac[:, i % NB, :].unsqueeze(2).to_broadcast([P, 4, 64]), ALU.mult)
                    e.drain().then_inc(s_stu, 1)

        @block.scalar
        def _(e):
            def exps(i):
                e.wait_ge(s_d, i + 1)
                e.activation(EN[:, :, :], D1[:, :, :], ACT.Exp, scale=-1.0)
                e.drain()
                e.activation(D1[:, :, :], D1[:, :, :], ACT.Exp)
                e.activation(D2[:, :, :], D2[:, :, :], ACT.Exp)
                e.drain().then_inc(s_e, 1)

            exps(0)
            for i in range(nchunk):
                if sample:
                    e.wait_ge(s_prep, 1)
                else:
                    e.wait_ge(s_prep, i + 1)
                    e.activation(fac[:, i % NB, :], fac[:, i % NB, :], ACT.Exp).then_inc(s_e, 1)
                for z, dst in enumerate((BtT, KcT, VT)):
                    e.wait_ge(s_tr, 3 * i + z + 1)
                    e.activation(dst[:, :], ps[0:n, 5 + z, :], ACT.Copy).then_inc(s_trc, 1)
                e.wait_ge(s_msk, 16 * i + 8)
                if i >= 1:
                    e.wait_ge(s_mn, FINE * i)
                for q in range(nb):
                    mm = e.activation(MD[C * q:C * q + C, :, :], MT[C * q:C * q + C, :, C * q:C * q + C], ACT.Copy)
                mm.then_inc(s_md, 1)
                for l in range(NST):
                    for z in range(2):
                        e.wait_ge(s_t1, 2 * (NST * i + l) + z + 1)
                        hs = slice(4 * z, 4 * z + 4)
                        if l < FINE:
                            mm = e.activation(T1[:, hs, 0:C], part(z, 0), ACT.Copy)
                        elif l == FINE:
                            for p in (32, 96):
                                mm = e.activation(T1[p:p + 32, hs, 0:C], part(z, 0)[p:p + 32, :, :], ACT.Copy)
                        else:
                            mm = e.activation(T1[64:128, hs, :], part(z, 0, 64)[64:128, :, :], ACT.Copy)
                        mm.then_inc(s_t1c, 1)
                    if l == 1 and i + 1 < nchunk:
                        exps(i + 1)
                    if l == FINE and not sample:
                        e.wait_ge(s_zero, 1)
                        e.wait_ge(s_x, 2 * (NST + 1) * i + 2 * (FINE + 1))
                        if i >= 1:
                            e.wait_ge(s_sa, i)
                        for q in range(nb):
                            b = slice(C * q, C * q + C)
                            if q < 2:
                                e.activation(X00[b, :, b], X[b, :, :], ACT.Copy)
                            mm = e.activation(XTF[b, :, b], XT[b, :, :], ACT.Copy)
                        mm.then_inc(s_dg, 1)
                e.wait_ge(s_rh, i + 1)
                e.activation(RH[:, :].rearrange("p (h z d) -> p h z d", z=2, d=64),
                             ps[0:n, 6:8, 0:256].rearrange("p z (h d) -> p h z d", d=64), ACT.Copy, scale=-1.0).then_inc(s_rhc, 1)
                e.wait_ge(s_y, i + 1)
                for z in range(2):
                    e.activation(KK[64 * z:64 * z + 64, :, tok(i)],
                                 ps[64 * z:64 * z + 64, 2 + z, 0:4 * n].rearrange("p (c n) -> p c n", c=4), ACT.Copy)
                e.drain().then_inc(s_yc, 1)

        @block.gpsimd
        def _(e):
            if not sample:
                e.memset(XTF[:, :, :], 0.0)
                e.memset(X00[:, :, :], 0.0)
                e.drain().then_inc(s_zero, 1)
            for i in range(nchunk):
                e.wait_ge(s_md, i + 1)
                if i >= 1:
                    e.wait_ge(s_x, 2 * (NST + 1) * i)
                for l in range(FINE):
                    e.tensor_tensor(Mn[:, l, :, :], MD[:, :, :], msk(f"lvl{l + 1}").to_broadcast([n, 8, C]),
                                    ALU.mult).then_inc(s_mn, 1)
        @block.tensor
        def _(e):
            ident = K.c("ident")
            for i in range(nchunk):
                e.wait_ge(s_prep, (2 if sample else 1) * (i + 1))
                KtR, Bt, Kc = KtR2[:, i % NB, :, :, :], Bt2[:, i % NB, :, :], Kc2[:, i % NB, :, :]
                for z, src in enumerate((Bt, Kc, xs[:, B_V:B_V + 4, tok(i)])):
                    for c in range(4):
                        mm = e.transpose(ps[0:n, 5 + z, P * c:P * c + P], src[:, c, :], ident)
                    mm.then_inc(s_tr, 1)
                if i >= 1:
                    e.wait_ge(s_yc, i)
                for src, b0 in ((Bt, 0), (Kc, 4)):
                    if b0:
                        e.wait_ge(s_trc, 3 * i + 3)
                        if i >= 1:
                            e.wait_ge(s_stu, i)
                    for h in range(8):
                        pp = 64 * (h % 2)
                        e.matmul(ps[0:n, b0 + bank(h), 256 * pos(h):256 * pos(h) + 2 * n], src[pp:pp + 64, h // 2, :],
                                 KtR[pp:pp + 64, h // 2, :, :].rearrange("p z n -> p (z n)"), start=True, stop=True).then_inc(s_ab, 1)
                e.wait_ge(s_msk, 16 * i + 8)
                for h in range(8):
                    pp = 64 * (h % 2)
                    for q in range(nb):
                        b = slice(C * q, C * q + C)
                        mm = e.matmul(ps[b, h % 2, C * (h // 2):C * (h // 2) + C], KtR[pp:pp + 64, h // 2, 0, b],
                                      Bt[pp:pp + 64, h // 2, b], start=True, stop=True)
                    mm.then_inc(s_ab, 1)
                for l in range(NST):
                    if l < FINE:
                        e.wait_ge(s_mn, FINE * i + l + 1)
                    elif l == FINE + 1:
                        e.wait_ge(s_dg, i + 1)
                    for z in range(2):
                        e.wait_ge(s_x, 2 * ((NST + 1) * i + l) + z + 1)
                        for h in range(4 * z, 4 * z + 4):
                            at = h % 4
                            if l < FINE:
                                for q in range(nb):
                                    b = slice(C * q, C * q + C)
                                    mm = e.matmul(ps[b, z, C * at:C * at + C], Mn[b, l, h, :], X[b, h, :], start=True, stop=True)
                            elif l == FINE:
                                for p in (0, 64):
                                    mm = e.matmul(ps[p + 32:p + 64, z, C * at:C * at + C], MT[p:p + 32, h, p + 32:p + 64], X[p:p + 32, h, :],
                                                  start=True, stop=True)
                            else:
                                mm = e.matmul(ps[64:128, z, 64 * at:64 * at + 64], MT[0:64, h, 64:128], X00[:, h, :], start=True, stop=True)
                        mm.then_inc(s_t1, 1)
                    for z in range(2):
                        e.wait_ge(s_t1c, 2 * (NST * i + l) + z + 1)
                        for h in range(4 * z, 4 * z + 4):
                            at = h % 4
                            x0, x1 = C * at, 128 + C * at
                            if l < FINE:
                                for q in range(nb):
                                    b = slice(C * q, C * q + C)
                                    e.matmul(ps[b, 2 + z, x0:x0 + C], XT[b, h, :], T1[b, h, 0:C], start=True, stop=True)
                                for q in range(nb):
                                    b = slice(C * q, C * q + C)
                                    mm = e.matmul(ps[b, 2 + z, x1:x1 + C], T1[b, h, 0:C], XT[b, h, :], start=True, stop=True)
                            elif l == FINE:
                                e.matmul(ps[32:64, 2 + z, x0:x0 + C], XT[32:64, h, :], T1[32:64, h, 0:C], start=True, stop=True)
                                for p in (0, 64):
                                    mm = e.matmul(ps[p:p + 32, 2 + z, x1:x1 + C], T1[p + 32:p + 64, h, 0:C], XT[p + 32:p + 64, h, :],
                                                  start=True, stop=True)
                            else:
                                mm = e.matmul(ps[0:64, 2 + z, 64 * at:64 * at + 64], T1[64:128, h, :], XTF[64:128, h, 64:128], start=True, stop=True)
                        mm.then_inc(s_z, 1)
                e.wait_ge(s_x, 2 * (NST + 1) * (i + 1))
                e.wait_ge(s_msk, 16 * i + 16)
                for h in range(8):
                    pp, hh = 64 * (h % 2), h // 2
                    o = ps[0:n, 6 + h % 2, 64 * hh:64 * hh + 64]
                    if sample:
                        for b in range(DB):
                            e.matmul(o, KtB[pp:pp + 64, hh, b, :], S0[pp:pp + 64, hh, b, :], start=b == 0, stop=False)
                    else:
                        e.matmul(o, KtR[pp:pp + 64, hh, 0, :], S0[pp:pp + 64, hh, :], start=True, stop=False)
                    mm = e.matmul(o, NT[:, h, :], VT[:, 64 * h:64 * h + 64], start=False, stop=True)
                mm.then_inc(s_rh, 1)
                e.wait_ge(s_rhc, i + 1)
                for h in range(8):
                    mm = e.matmul(ps[0:n, h % 2, 64 * (h // 2):64 * (h // 2) + 64], XTF[:, h, :], RH[:, 64 * h:64 * h + 64],
                                  start=True, stop=True)
                mm.then_inc(s_sa, 1)
                e.wait_ge(s_sac, i + 1)
                for h in range(8):
                    pp, hh = 64 * (h % 2), h // 2
                    o = ps[pp:pp + 64, 2 + h % 2, n * hh:n * hh + n]
                    if sample:
                        for b in range(DB):
                            e.matmul(o, S0[pp:pp + 64, hh, b, :], RB4[pp:pp + 64, hh, b, :], start=b == 0, stop=False)
                    else:
                        e.matmul(o, S0[pp:pp + 64, hh, :], KtR[pp:pp + 64, hh, 1, :], start=True, stop=False)
                    e.matmul(o, SA[:, 64 * h:64 * h + 64], RBT[:, h, :], start=False, stop=False)
                    mm = e.matmul(o, VT[:, 64 * h:64 * h + 64], RKT[:, h, :], start=False, stop=True)
                mm.then_inc(s_y, 1)
                if sample:
                    for h in range(8):
                        pp = 64 * (h % 2)
                        e.wait_ge(s_sac, h + 2)
                        o = ps[pp:pp + 64, 4 + h % 2, :]
                        e.matmul(o, BtT[:, 64 * h:64 * h + 64], SAB[:, 0, :, :].rearrange("p b d -> p (b d)"), start=True, stop=False)
                        e.matmul(o, KcT[:, 64 * h:64 * h + 64], SAB[:, 1, :, :].rearrange("p b d -> p (b d)"), start=False, stop=True).then_inc(s_st, 1)
                else:
                    for h in range(8):
                        pp, hh = 64 * (h % 2), h // 2
                        o = ps[pp:pp + 64, 4, 64 * hh:64 * hh + 64]
                        e.matmul(o, BtT[:, 64 * h:64 * h + 64], SA[:, 64 * h:64 * h + 64], start=True, stop=False)
                        mm = e.matmul(o, KcT[:, 64 * h:64 * h + 64], VT[:, 64 * h:64 * h + 64], start=False, stop=True)
                    mm.then_inc(s_st, 1)


def stage_rwkv_states(nc, K, tag, S0, src, outs):
    nb = DB if tag == "S" else 1
    ctx = ExitStack()
    nm = f"st{tag}{'i' if src is not None else 'o'}"
    with ctx:
        rows = ctx.enter_context(nc.sbuf_tensor(nm + "rows", [64, nb, 8, 64], F32))
        low = ctx.enter_context(nc.sbuf_tensor(nm + "low", [64, nb, 8, 64], F32)) if outs is not None else None
        block = ctx.enter_context(nc.Block())
        s_in, s_t, s_c = K.sem(nm + "_in"), K.sem(nm + "_turned"), K.sem(nm + "_copied")
        s_low, s_out = K.sem(nm + "_lowered"), K.out_sem(nm + "_stored")
        st4 = S0 if tag == "S" else S0[:, :, :].unsqueeze(2)
        if src is not None:
            @block.sync
            def _(e):
                e.dma_start(rows[:, :, :, :], src.rearrange("b h i j -> i b h j")).then_inc(s_in, 16)

            @block.tensor
            def _(e):
                e.wait_ge(s_in, 16)
                for b in range(nb):
                    if b >= 2:
                        e.wait_ge(s_c, b - 1)
                    for h in range(8):
                        mm = e.transpose(K.ps[0:64, b % 2, 64 * h:64 * h + 64], rows[:, b, h, :], K.c("ident")[0:64, 0:64])
                    mm.then_inc(s_t, 1)

            @block.vector
            def _(e):
                for b in range(nb):
                    e.wait_ge(s_t, b + 1)
                    for z in range(2):
                        e.tensor_copy(st4[64 * z:64 * z + 64, :, b, :],
                                      K.ps[0:64, b % 2, :].rearrange("p (c z d) -> p c z d", z=2, d=64)[:, :, z, :])
                    e.drain().then_inc(s_c, 1)
        else:
            @block.tensor
            def _(e):
                e.wait_ge(s_low, 1)
                for b in range(nb):
                    if b >= 2:
                        e.wait_ge(s_c, b - 1)
                    for h in range(8):
                        mm = e.transpose(K.ps[0:64, b % 2, 64 * h:64 * h + 64], low[:, b, h, :], K.c("ident")[0:64, 0:64])
                    mm.then_inc(s_t, 1)

            @block.vector
            def _(e):
                for z in range(2):
                    for b in range(nb):
                        e.tensor_copy(low[:, b, z::2, :], st4[64 * z:64 * z + 64, :, b, :])
                e.drain().then_inc(s_low, 1)
                for b in range(nb):
                    e.wait_ge(s_t, b + 1)
                    e.tensor_copy(rows[:, b, :, :], K.ps[0:64, b % 2, :].rearrange("p (h d) -> p h d", h=8)).then_inc(s_c, 1)

            @block.sync
            def _(e):
                e.wait_ge(s_c, nb)
                e.dma_start(outs.rearrange("b h i j -> i b h j"), rows[:, :, :, :]).then_inc(s_out, 16)
                e.wait_ge(s_out, 16)


def stage_rwkv_out(nc, K, xs):
    Y = K.oA
    ctx = ExitStack()
    with ctx:
        g2 = ctx.enter_context(nc.sbuf_tensor("ro_g2", [P, 512], F32))
        sq = ctx.enter_context(nc.sbuf_tensor("ro_sq", [P, 2, T], F32))
        rkk = ctx.enter_context(nc.sbuf_tensor("ro_rk", [P, 2, T], F32))
        rt = ctx.enter_context(nc.sbuf_tensor("ro_root", [8, T], F32))
        spread = ctx.enter_context(nc.sbuf_tensor("ro_to_channels", [8, 4 * P], F32))
        block = ctx.enter_context(nc.Block())
        s_w, s_sg, s_mean, s_cen, s_sq, s_rk, s_var, s_ve, s_rt, s_inv, s_bon, s_bonu, s_sp, s_spu, s_g = (K.sem("ro_" + x) for x in (
            "gate_w_in", "gate_sig", "means", "centred", "squared", "rk", "variances", "variance_eps", "rooted",
            "inverted", "bonus_sum", "bonus_used", "spread", "spread_used", "gate"))
        c3 = lambda ap: ap.rearrange("p (c n) -> p c n", c=NC3)
        bank = lambda z: K.ps[:, 3 * z:3 * z + 3, 0:NW]

        @block.sync
        def _(e):
            e.dma_start(g2[:, :], K.d["rwkv_g2"][0]).then_inc(s_w, 16)
            e.dma_start(spread[:, :], head_map(K, "H")).then_inc(s_w, 16)

        @block.scalar
        def _(e):
            e.activation(xs[:, B_G, :], xs[:, B_G, :], ACT.Sigmoid).then_inc(s_sg, 1)
            for c in range(4):
                e.wait_ge(s_cen, c + 1)
                if c >= 2:
                    e.wait_ge(s_var, c - 1)
                e.activation(sq[:, c % 2, :], Y[:, c, :], ACT.Square).then_inc(s_sq, 1)
            e.wait_ge(s_ve, 1)
            e.activation(rt[:, :], rt[:, :], ACT.Sqrt).then_inc(s_rt, 1)

        @block.tensor
        def _(e):
            hs = K.c("headsum")

            def over(z, lhs, rhs):
                for n in range(NC3):
                    mm = e.matmul(K.ps[:, 3 * z + n, 0:NW], lhs, rhs[:, NW * n:NW * n + NW], start=True, stop=True)
                return mm

            for c in range(4):
                if c >= 2:
                    e.wait_ge(s_cen, c - 1)
                over(c % 2, hs, Y[:, c, :]).then_inc(s_mean, 1)
            e.wait_ge(s_cen, 3)
            for c in range(4):
                e.wait_ge(s_sq, c + 1)
                for n in range(NC3):
                    mm = e.matmul(K.ps[0:8, n, 0:NW], K.c("toheadH")[:, 8 * c:8 * c + 8], sq[:, c % 2, NW * n:NW * n + NW],
                                  start=c == 0, stop=c == 3)
                mm.then_inc(s_var, 1)
            e.wait_ge(s_cen, 4)
            for c in range(4):
                e.wait_ge(s_rk, c + 1)
                if c >= 1:
                    e.wait_ge(s_bonu, c)
                over(1, hs, rkk[:, c % 2, :]).then_inc(s_bon, 1)
            e.wait_ge(s_inv, 1)
            e.wait_ge(s_w, 32)
            e.wait_ge(s_sg, 1)
            e.wait_ge(s_bonu, 4)
            for c in range(4):
                if c >= 1:
                    e.wait_ge(s_spu, 2 * c - 1)
                over(0, spread[:, P * c:P * c + P], rt[:, :]).then_inc(s_sp, 1)
                if c >= 1:
                    e.wait_ge(s_spu, 2 * c)
                over(1, g2[:, P * c:P * c + P], xs[:, B_G, :]).then_inc(s_g, 1)

        @block.vector
        def _(e):
            for c in range(4):
                e.wait_ge(s_mean, c + 1)
                e.scalar_tensor_tensor(c3(Y[:, c, :]), bank(c % 2), -1.0 / 64, c3(Y[:, c, :]), ALU.mult, ALU.add).then_inc(s_cen, 1)

            def bonus_terms(c):
                if c >= 2:
                    e.wait_ge(s_bon, c - 1)
                e.scalar_tensor_tensor(rkk[:, c % 2, :], xs[:, B_R + c, :], K.p("rwkv_rk", c), xs[:, B_K + c, :], ALU.mult, ALU.mult).then_inc(s_rk, 1)

            bonus_terms(0)
            bonus_terms(1)
            e.wait_ge(s_var, 4)
            e.tensor_scalar(c3(rt[:, :]), K.ps[0:8, 0:3, 0:NW], 1.0 / 64, LNX_EPS, ALU.mult, ALU.add).then_inc(s_ve, 1)
            for c in range(4):
                e.wait_ge(s_bon, c + 1)
                e.tensor_tensor(c3(xs[:, B_V + c, :]), c3(xs[:, B_V + c, :]), bank(1), ALU.mult).then_inc(s_bonu, 1)
                if c + 2 < 4:
                    bonus_terms(c + 2)
                if c == 0:
                    e.wait_ge(s_rt, 1)
                    e.reciprocal(rt[:, :], rt[:, :]).then_inc(s_inv, 1)
            for c in range(4):
                e.wait_ge(s_sp, c + 1)
                e.tensor_tensor(c3(Y[:, c, :]), c3(Y[:, c, :]), bank(0), ALU.mult).then_inc(s_spu, 1)
                e.drain()
                e.tensor_scalar(Y[:, c, :], Y[:, c, :], K.p("rwkv_lnx_g", c), K.p("rwkv_lnx_b", c), ALU.mult, ALU.add)
                e.drain()
                e.tensor_tensor(Y[:, c, :], Y[:, c, :], xs[:, B_V + c, :], ALU.add)
                e.drain()
                e.wait_ge(s_g, c + 1)
                e.tensor_tensor(c3(Y[:, c, :]), c3(Y[:, c, :]), bank(1), ALU.mult).then_inc(s_spu, 1)


def stage_move(nc, K, name, moves):
    with nc.Block() as block:
        s_moved = K.sem(name)

        @block.gpsimd
        def _(e):
            for dst, src in moves:
                e.dma_start(dst, src).then_inc(s_moved, 16)
            e.wait_ge(s_moved, 16 * len(moves))


def stage_tail_rows(nc, K, rows):
    ctx = ExitStack()
    with ctx:
        block = ctx.enter_context(nc.Block())
        s_t, s_c, s_out = K.sem("tail_turned"), K.sem("tail_copied"), K.out_sem("tail_stored")

        @block.tensor
        def _(e):
            for b in range(B_Q):
                mm = e.transpose(K.ps[0:TAIL, b // 4, P * (b % 4):P * (b % 4) + P], K.utail[:, b, :], K.c("ident"))
            mm.then_inc(s_t, 1)

        @block.vector
        def _(e):
            e.wait_ge(s_t, 1)
            e.tensor_copy(rows[:, :, :].rearrange("p b n -> p (b n)"),
                          K.ps[0:TAIL, 0:5, :].rearrange("p a n -> p (a n)")[:, 0:B_Q * P]).then_inc(s_c, 1)

        pieces = [(b, at, c0, w) for b in range(NSHIFT) for at, (c0, w) in zip((0, 64), BLOCKS[b])]
        K.tail_stores = 2 * len(pieces) + 2 + DB

        @block.sync
        def _(e):
            e.dma_start(K.d["s_state_pool"][0, :, 0:15 - DT, :], K.d["state_pool"][0, :, DT:15, :]).then_inc(s_out, 16)
            e.wait_ge(s_c, 1)
            for b, at, c0, w in pieces:
                e.dma_start(K.d["p_state_shift"][0, :, c0:c0 + w], rows[14:15, b, at:at + w]).then_inc(s_out, 16)

        @block.scalar
        def _(e):
            e.wait_ge(s_c, 1)
            for b, at, c0, w in pieces:
                e.dma_start(K.d["s_state_shift"][0, :, c0:c0 + w], rows[15 + DT - 1:TAIL:DT, b, at:at + w]).then_inc(s_out, 16)
            e.dma_start(K.d["p_state_pool"][0, 0].rearrange("t (b n) -> t b n", n=P), rows[0:15, B_POOL:B_Q, :]).then_inc(s_out, 16)
            for b in range(DB):
                e.dma_start(K.d["s_state_pool"][0, b, 15 - DT:15, :].rearrange("t (b n) -> t b n", n=P),
                            rows[15 + DT * b:15 + DT * b + DT, B_POOL:B_Q, :]).then_inc(s_out, 16)


def stage_pool(nc, K, up):
    ctx = ExitStack()
    with ctx:
        sb = lambda nm, sh: ctx.enter_context(nc.sbuf_tensor("po_" + nm, sh, F32))
        srow = sb("state", [DB * 15, 512])
        pw = sb("w", [P, 4, P])
        EP, ES = sb("ext", [P, 4, 15 + TP]), sb("exts", [P, 4, DB, 15 + DT])
        TPp, TSs = sb("sums", [P, 2, 15 + TP]), sb("sumss", [P, 2, DB, 15 + DT])
        dd = sb("diff", [P, 4, T])
        block = ctx.enter_context(nc.Block())
        s_in, s_t, s_cp, s_c2 = K.sem("po_in"), K.sem("po_turned"), K.sem("po_extended"), K.sem("po_state_copied")
        s_d, s_z, s_w = K.sem("po_differences"), K.sem("po_mapped"), K.sem("po_scaled")

        @block.sync
        def _(e):
            e.dma_start(srow[:, :], K.d["state_pool"][0].rearrange("b t n -> (b t) n")).then_inc(s_in, 16)
            e.dma_start(pw[:, :, :], K.d["pool_w"][0].rearrange("g c n -> c g n")).then_inc(s_in, 16)

        @block.scalar
        def _(e):
            e.activation(EP[:, :, 15:], up[:, :, 0:TP], ACT.Copy)
            for g in range(4):
                e.activation(ES[:, g, :, 15:], up[:, g, TP:T].rearrange("p (b t) -> p b t", t=DT), ACT.Copy)
            e.drain().then_inc(s_cp, 1)
            for g in range(4):
                e.wait_ge(s_z, g + 1)
                e.activation(K.oB[:, g, :].rearrange("p (c n) -> p c n", c=NC3),
                             K.ps[:, 3 * (g % 2):3 * (g % 2) + 3, 0:NW], ACT.Copy, scale=K.p("pool_scale", g)).then_inc(s_w, 1)

        @block.tensor
        def _(e):
            e.wait_ge(s_in, 32)
            for g in range(4):
                mm = e.transpose(K.ps[:, 7, 120 * g:120 * g + 120], srow[:, P * g:P * g + P], K.c("ident")[0:120, 0:120])
            mm.then_inc(s_t, 1)
            for g in range(4):
                e.wait_ge(s_d, g + 1)
                if g >= 2:
                    e.wait_ge(s_w, g - 1)
                for c in range(NC3):
                    mm = e.matmul(K.ps[:, 3 * (g % 2) + c, 0:NW], pw[:, g, :], dd[:, g, NW * c:NW * c + NW], start=True, stop=True)
                mm.then_inc(s_z, 1)

        @block.vector
        def _(e):
            e.memset(EP[:, :, 0:15], 0.0)
            e.wait_ge(s_t, 1)
            for g in range(4):
                e.tensor_copy(ES[:, g, :, 0:15], K.ps[:, 7, 120 * g:120 * g + 120].rearrange("p (b t) -> p b t", t=15))
            e.wait_ge(s_cp, 1)
            e.drain()
            LP, LS = 15 + TP, 15 + DT
            for g in range(4):
                a, s = EP[:, g, :], ES[:, g, :, :]
                for l in range(g + 1):
                    w, o = 1 << l, (2 << l) - 1
                    e.tensor_tensor(TPp[:, l % 2, o:LP], a[:, o:LP], a[:, o - w:LP - w], ALU.add)
                    e.tensor_tensor(TSs[:, l % 2, :, o:LS], s[:, :, o:LS], s[:, :, o - w:LS - w], ALU.add)
                    e.drain()
                    a, s = TPp[:, l % 2, :], TSs[:, l % 2, :, :]
                inv = 1.0 / (2 << g)
                e.scalar_tensor_tensor(dd[:, g, 16:TP], a[:, 31:LP], inv, EP[:, g, 31:LP], ALU.mult, ALU.subtract)
                e.tensor_tensor(dd[:, g, 0:16], a[:, 15:31], K.c("poolcnt")[:, 16 * g:16 * g + 16], ALU.mult)
                e.scalar_tensor_tensor(dd[:, g, TP:T].rearrange("p (b t) -> p b t", t=DT), s[:, :, 15:], inv,
                                       ES[:, g, :, 15:], ALU.mult, ALU.subtract)
                e.drain()
                e.tensor_tensor(dd[:, g, 0:16], dd[:, g, 0:16], EP[:, g, 15:31], ALU.subtract)
                e.drain().then_inc(s_d, 1)


def head_map(K, heads):
    at = CCOL["tochan" + heads][0]
    return K.d["sheet"][0:8, at:at + 4 * P]


def stage_head_rms(nc, K, name, q, heads, width, gain, scale):
    ctx = ExitStack()
    with ctx:
        sq = ctx.enter_context(nc.sbuf_tensor(name + "_sq", [P, 2, T], F32))
        rt = ctx.enter_context(nc.sbuf_tensor(name + "_root", [8, T], F32))
        spread = ctx.enter_context(nc.sbuf_tensor(name + "_to_channels", [8, 4 * P], F32))
        block = ctx.enter_context(nc.Block())
        s_map = K.sem(name + "_map_in")

        @block.sync
        def _(e):
            e.dma_start(spread[:, :], head_map(K, heads)).then_inc(s_map, 16)

        s_sq, s_sum, s_me, s_rt, s_inv, s_sp, s_used = (K.sem(f"{name}_{x}") for x in (
            "squared", "summed", "mean", "rooted", "inverted", "spread", "spread_used"))
        c3 = lambda ap: ap.rearrange("p (c n) -> p c n", c=NC3)

        @block.scalar
        def _(e):
            for c in range(4):
                if c >= 2:
                    e.wait_ge(s_sum, c - 1)
                e.activation(sq[:, c % 2, :], q[:, c, :], ACT.Square).then_inc(s_sq, 1)
            e.wait_ge(s_me, 1)
            e.activation(rt[:, :], rt[:, :], ACT.Sqrt).then_inc(s_rt, 1)

        @block.tensor
        def _(e):
            for c in range(4):
                e.wait_ge(s_sq, c + 1)
                for n in range(NC3):
                    mm = e.matmul(K.ps[0:8, n, 0:NW], K.c("tohead" + heads)[:, 8 * c:8 * c + 8], sq[:, c % 2, NW * n:NW * n + NW],
                                  start=c == 0, stop=c == 3)
                mm.then_inc(s_sum, 1)
            e.wait_ge(s_inv, 1)
            e.wait_ge(s_map, 16)
            for c in range(4):
                if c >= 2:
                    e.wait_ge(s_used, c - 1)
                for n in range(NC3):
                    mm = e.matmul(K.ps[:, 3 * (c % 2) + n, 0:NW], spread[:, P * c:P * c + P], rt[:, NW * n:NW * n + NW],
                                  start=True, stop=True)
                mm.then_inc(s_sp, 1)

        @block.vector
        def _(e):
            e.wait_ge(s_sum, 4)
            e.tensor_scalar(c3(rt[:, :]), K.ps[0:8, 0:3, 0:NW], 1.0 / width / scale ** 2, RMS_EPS / scale ** 2,
                            ALU.mult, ALU.add).then_inc(s_me, 1)
            e.wait_ge(s_rt, 1)
            e.reciprocal(rt[:, :], rt[:, :]).then_inc(s_inv, 1)
            for c in range(4):
                e.wait_ge(s_sp, c + 1)
                e.scalar_tensor_tensor(c3(q[:, c, :]), c3(q[:, c, :]), K.p(gain, 0), K.ps[:, 3 * (c % 2):3 * (c % 2) + 3, 0:NW],
                                       ALU.mult, ALU.mult).then_inc(s_used, 1)


def stage_kv(nc, K, kvt, xh, xl):
    HW = KVG // 2
    ctx = ExitStack()
    with ctx:
        raw = ctx.enter_context(nc.sbuf_tensor("kv_raw", [P, 2, 2, HW], F32))
        wh = ctx.enter_context(nc.sbuf_tensor("kv_high", [P, KD, HW], F32R))
        wl = ctx.enter_context(nc.sbuf_tensor("kv_low", [P, KD, HW], F32R))
        block = ctx.enter_context(nc.Block())
        s_in, s_hi, s_lo, s_mm, s_cp = K.sems("kv_w_in", 2), K.sem("kv_high"), K.sem("kv_low"), K.sem("kv_product"), K.sem("kv_copied")
        NT1 = NTI + 1
        tile = lambda i: (P * i, 0) if i < NTI else (T - P, P - TS)

        @block.sync
        def _(e):
            for q in range(8):
                z, k = q // 4, 2 * (q % 4)
                if q >= 2:
                    e.wait_ge(s_lo, q - 1)
                e.dma_start(raw[:, q % 2, :, :], K.d["w_in"][0, P * k:P * k + 2 * P, OFF_KV + HW * z:OFF_KV + HW * z + HW]
                            .rearrange("(k p) n -> p k n", p=P)).then_inc(s_in[q % 2], 16)

        @block.tensor
        def _(e):
            for z in range(2):
                for i in range(NT1):
                    a = tile(i)[0]
                    G = NT1 * z + i
                    if G >= 4:
                        e.wait_ge(s_cp, G - 3)
                    for k in range(KD):
                        if i == 0:
                            e.wait_ge(s_lo, 4 * z + k // 2 + 1)
                        o = K.ps[:, G % 4, 0:HW]
                        e.matmul(o, xh[:, k, a:a + P], wh[:, k, :], start=k == 0, stop=False)
                        e.matmul(o, xl[:, k, a:a + P], wh[:, k, :], start=False, stop=False)
                        mm = e.matmul(o, xh[:, k, a:a + P], wl[:, k, :], start=False, stop=k == KD - 1)
                    mm.then_inc(s_mm, 1)

        @block.scalar
        def _(e):
            for z in range(2):
                for q in range(4 * z, 4 * z + 4):
                    e.wait_ge(s_in[q % 2], 16 * (q // 2 + 1))
                    if z:
                        e.wait_ge(s_mm, NT1)
                    k = 2 * (q % 4)
                    e.activation(wh[:, k:k + 2, :], raw[:, q % 2, :, :], ACT.Copy).then_inc(s_hi, 1)
                for i in range(NT1):
                    r0 = tile(i)[1]
                    G = NT1 * z + i
                    e.wait_ge(s_mm, G + 1)
                    e.activation(kvt[0:P - r0, i, HW * z:HW * z + HW], K.ps[r0:P, G % 4, 0:HW], ACT.Copy).then_inc(s_cp, 1)

        @block.vector
        def _(e):
            for q in range(8):
                e.wait_ge(s_hi, q + 1)
                k = 2 * (q % 4)
                e.tensor_tensor(wl[:, k:k + 2, :], raw[:, q % 2, :, :], wh[:, k:k + 2, :].bitcast(F32), ALU.subtract).then_inc(s_lo, 1)


def stage_kv_norm(nc, K, kvt):
    ctx = ExitStack()
    with ctx:
        kg = ctx.enter_context(nc.sbuf_tensor("kv_gain", [P, 2, 64], F32))
        sq = ctx.enter_context(nc.sbuf_tensor("kv_sq", [P, 2, 8, 2, 64], F32))
        ss = ctx.enter_context(nc.sbuf_tensor("kv_ss", [P, 2, 2, 16], F32))
        block = ctx.enter_context(nc.Block())
        s_g = K.sem("kv_gain_in")
        names = ("cmp_k", "cmp_v", "slc_k", "slc_v", "win_k", "win_v")
        K.kv_stores = 6 + 4 + 2 + 2 * DB
        s_v, s_r, s_k, s_out = K.sem("kv_mean"), K.sem("kv_rooted"), K.sem("kv_normed"), K.out_sem("kv_stored")

        @block.sync
        def _(e):
            e.dma_start(kg[:, :, :], K.d["nsa_k_g"][0, 1:3, :].partition_broadcast(P)).then_inc(s_g, 16)
            for nm in names[4:]:
                e.dma_start(K.d["s_" + nm][0, :, 0:512 - DT], K.d["cache_" + nm][0, :, DT:512]).then_inc(s_out, 16)
            e.wait_ge(s_k, 1)
            pr = lambda name: K.d[name][0, 0].rearrange("(i p) g d -> p i (g d)", p=P)
            for z, nm in enumerate(names):
                lo = NTI - 4 if z >= 4 else 0
                e.dma_start(pr("p_" + nm), kvt[:, lo:NTI, P * z:P * z + P]).then_inc(s_out, 16)
                if z < 4:
                    e.dma_start(K.d["s_" + nm][0].rearrange("b t g d -> (b t) (g d)"), kvt[0:TS, NTI, P * z:P * z + P]).then_inc(s_out, 16)

        @block.scalar
        def _(e):
            for z in range(2):
                e.wait_ge(s_v, z + 1)
                m, cnt = (P, 16) if z == 0 else (TS, 2)
                e.activation(ss[0:m, z, :, 0:cnt], ss[0:m, z, :, 0:cnt], ACT.Sqrt).then_inc(s_r, 1)
            e.activation(kvt[:, 0:NTI, 768:KVG], kvt[:, 0:NTI, 768:KVG], ACT.Sigmoid)
            e.activation(kvt[0:TS, NTI, 768:KVG], kvt[0:TS, NTI, 768:KVG], ACT.Sigmoid)
            e.wait_ge(s_k, 1)
            for z in (4, 5):
                for b in range(DB):
                    e.dma_start(K.d["s_" + names[z]][0, b, 512 - DT:512].rearrange("t g d -> t (g d)"),
                                kvt[DT * b:DT * b + DT, NTI, P * z:P * z + P]).then_inc(s_out, 16)

        @block.vector
        def _(e):
            e.wait_ge(s_g, 16)
            for z, (m, lo, hi) in enumerate(((P, 0, NTI), (TS, NTI, NTI + 1))):
                nt = hi - lo
                for s in range(2):
                    kk = kvt[0:m, lo:hi, 256 + 256 * s:384 + 256 * s].rearrange("p i (g d) -> p i g d", g=2)
                    e.tensor_tensor(sq[0:m, s, 0:nt, :, :], kk, kk, ALU.mult)
                    e.drain()
                    e.tensor_reduce(ss[0:m, z, s, 0:2 * nt], sq[0:m, s, 0:nt, :, :].rearrange("p i g d -> p (i g) d"), AX.X, ALU.add)
                e.drain()
                e.tensor_scalar(ss[0:m, z, :, 0:2 * nt], ss[0:m, z, :, 0:2 * nt], 1.0 / 64, RMS_EPS, ALU.mult, ALU.add).then_inc(s_v, 1)
                e.wait_ge(s_r, z + 1)
                e.reciprocal(ss[0:m, z, :, 0:2 * nt], ss[0:m, z, :, 0:2 * nt])
                e.drain()
                for s in range(2):
                    kk = kvt[0:m, lo:hi, 256 + 256 * s:384 + 256 * s].rearrange("p i (g d) -> p i g d", g=2)
                    e.tensor_tensor(kk, kk, ss[0:m, z, s, 0:2 * nt].rearrange("p (i g) -> p i g", g=2).unsqueeze(3).to_broadcast([m, nt, 2, 64]), ALU.mult)
                    e.drain()
                    for i in range(lo, hi):
                        k2 = kvt[0:m, i, 256 + 256 * s:384 + 256 * s].rearrange("p (g d) -> p g d", g=2)
                        e.tensor_tensor(k2, k2, kg[0:m, s, :].unsqueeze(1).to_broadcast([m, 2, 64]), ALU.mult)
            e.drain().then_inc(s_k, 1)


def stage_bias(nc, K, near, cb, b31):
    ctx = ExitStack()
    with ctx:
        rb = ctx.enter_context(nc.sbuf_tensor("bi_rel", [33, 8], F32))
        oh = ctx.enter_context(nc.sbuf_tensor("bi_onehot", [33, BVL], F32))
        bv = ctx.enter_context(nc.sbuf_tensor("bi_vector", [8, BVL], F32))
        block = ctx.enter_context(nc.Block())
        s_in, s_ms, s_mm, s_c, s_d, s_t, s_fl = (K.sem("bi_" + x) for x in (
            "in", "neg_set", "spread", "copied", "stored", "tiles_in", "tiles_flipped"))
        W = BVL // 7

        @block.sync
        def _(e):
            e.dma_start(oh[:, :], K.d["onehot"]).then_inc(s_in, 16)
            e.wait_ge(s_ms, 1)
            e.dma_start(rb[0:32, :], K.d["rel_bias"]).then_inc(s_in, 16)
            e.dma_start(b31[:, :], K.d["rel_bias"][31, :].partition_broadcast(P)).then_inc(s_t, 16)
            e.wait_ge(s_c, 1)
            e.dma_start(K.bvec, bv[:, :]).then_inc(s_d, 16)
            e.wait_ge(s_d, 16)
            v = K.bvec.tensor
            for h in range(8):
                e.dma_start(near[:, h, :], bass.AP(tensor=v, offset=h * BVL + REV - 2 * P + 1, ap=[[1, P], [1, 2 * P]])).then_inc(s_t, 16)

        @block.scalar
        def _(e):
            e.wait_ge(s_d, 16)
            v = K.bvec.tensor
            for h in range(8):
                e.dma_start(cb[:, h, :], bass.AP(tensor=v, offset=h * BVL + REV + 63 - 64 * 14 - P + 1, ap=[[1, P], [64, 30]]),
                            allow_slow_non_contiguous=True).then_inc(s_t, 16)

        @block.vector
        def _(e):
            e.memset(rb[:, :], NEG).then_inc(s_ms, 1)
            e.wait_ge(s_mm, 1)
            e.tensor_copy(bv[:, :].rearrange("p (z n) -> p z n", z=7), K.ps[0:8, 0:7, 0:W]).then_inc(s_c, 1)
            e.wait_ge(s_fl, 1)
            e.tensor_copy(near[:, :, :].rearrange("p (a h) n -> p a (h n)", h=2), K.ps[:, 0:4, :])
            e.tensor_copy(cb[:, :, :].rearrange("p h n -> p (h n)"), K.ps[:, 4, 0:240])

        @block.tensor
        def _(e):
            e.wait_ge(s_in, 32)
            for z in range(7):
                mm = e.matmul(K.ps[0:8, z, 0:W], rb[:, :], oh[:, W * z:W * z + W], start=True, stop=True)
            mm.then_inc(s_mm, 1)
            e.wait_ge(s_t, 16 * 17)
            e.wait_ge(s_c, 1)
            for a in range(4):
                e.matmul(K.ps[:, a, :], K.c("flip"), near[:, 2 * a:2 * a + 2, :].rearrange("p h n -> p (h n)"), start=True, stop=True)
            e.matmul(K.ps[:, 4, 0:240], K.c("flip"), cb[:, :, :].rearrange("p h n -> p (h n)"), start=True, stop=True).then_inc(s_fl, 1)


def stage_nsa_keys(nc, K, kvt, kcd, vc, kh, kl, ksn, kwn):
    ctx = ExitStack()
    with ctx:
        kc = ctx.enter_context(nc.sbuf_tensor("nk_kc", [P, 16], F32))
        sq = ctx.enter_context(nc.sbuf_tensor("nk_sq", [P, 16], F32))
        rt = ctx.enter_context(nc.sbuf_tensor("nk_rt", [P, 16], F32))
        block = ctx.enter_context(nc.Block())
        s_t, s_c, s_new, s_m, s_sq, s_s, s_v, s_r = (K.sem("nk_" + x) for x in (
            "turned", "copied", "new_turned", "means", "squared", "summed", "mean_sq", "rooted"))

        @block.tensor
        def _(e):
            blk, ident = K.c("blk"), K.c("ident")
            for i in range(NTI):
                e.matmul(K.ps[:, 4, 2 * i:2 * i + 2], kvt[:, i, 0:P], blk[:, 30:32], start=True, stop=True)
            for i in range(NTI):
                mm = e.matmul(K.ps[0:16, 5, 0:P], blk[:, 30 - 2 * i:46 - 2 * i], kvt[:, i, P:2 * P], start=i == 0, stop=i == NTI - 1)
            mm.then_inc(s_m, 1)
            for z in range(4):
                for i in range(4):
                    mm = e.transpose(K.ps[:, z, P * i:P * i + P], kvt[:, 4 * (z % 2) + i, 256 + 256 * (z // 2):384 + 256 * (z // 2)], ident)
                mm.then_inc(s_t, 1)
            e.transpose(K.ps[:, 6, 0:TS], kvt[0:TS, NTI, 256:384], ident[0:TS, 0:TS])
            e.transpose(K.ps[:, 6, TS:2 * TS], kvt[0:TS, NTI, 512:640], ident[0:TS, 0:TS]).then_inc(s_new, 1)
            e.wait_ge(s_sq, 1)
            e.matmul(K.ps[:, 7, 0:16], K.c("headsum"), sq[:, :], start=True, stop=True).then_inc(s_s, 1)

        @block.scalar
        def _(e):
            e.wait_ge(s_v, 1)
            e.activation(rt[:, :], rt[:, :], ACT.Sqrt).then_inc(s_r, 1)
            for z in range(4):
                e.wait_ge(s_t, z + 1)
                cs = slice(512 * (z % 2), 512 * (z % 2) + 512)
                for g in range(2):
                    src = K.ps[64 * g:64 * g + 64, z, :]
                    e.activation(kh[0:64, z // 2, g, cs], src, ACT.Copy)
                    mm = e.activation(kh[64:128, z // 2, g, cs], src, ACT.Copy)
                mm.then_inc(s_c, 1)

        @block.vector
        def _(e):
            e.wait_ge(s_m, 1)
            e.tensor_copy(kc[:, :], K.ps[:, 4, 0:16])
            e.tensor_copy(vc[:, :], K.ps[0:16, 5, 0:P])
            e.drain()
            e.tensor_tensor(sq[:, :], kc[:, :], kc[:, :], ALU.mult).then_inc(s_sq, 1)
            e.wait_ge(s_s, 1)
            e.tensor_scalar(rt[:, :], K.ps[:, 7, 0:16], 1.0 / 64, RMS_EPS, ALU.mult, ALU.add).then_inc(s_v, 1)
            e.wait_ge(s_r, 1)
            e.reciprocal(rt[:, :], rt[:, :])
            e.drain()
            e.scalar_tensor_tensor(kc[:, :], kc[:, :], K.p("kg_cmp", 0), rt[:, :], ALU.mult, ALU.mult)
            e.drain()
            for g in range(2):
                for half in range(2):
                    e.tensor_copy(kcd[64 * half:64 * half + 64, g, :], kc[64 * g:64 * g + 64, :])
            for z in range(4):
                e.wait_ge(s_c, z + 1)
                cs = slice(512 * (z % 2), 512 * (z % 2) + 512)
                for g in range(2):
                    src, hi = K.ps[64 * g:64 * g + 64, z, :], kh[64 * g:64 * g + 64, z // 2, g, cs].bitcast(F32)
                    e.tensor_tensor(kl[0:64, z // 2, g, cs], src, hi, ALU.subtract)
                    e.tensor_tensor(kl[64:128, z // 2, g, cs], src, hi, ALU.subtract)
            e.wait_ge(s_new, 1)
            e.tensor_copy(ksn[:, :], K.ps[:, 6, 0:TS])
            e.tensor_copy(kwn[:, :], K.ps[:, 6, TS:2 * TS])


def stage_nsa_prompt(nc, K, qT, kvt, kcd, vc, kh, kl, near, cb, b31):
    units = [(i, h) for i in range(NTI) for h in range(8)]
    NU = len(units)
    AHEAD = 2
    NS = AHEAD + 1
    SW = TP + 5 * P + 16
    win = lambda i: list(range(max(0, i - 4), i + 1))
    cols = lambda i: (P * (i + 1), P * len(win(i)))

    def blocks(i):
        return [("s", j) for j in range(i + 1)] + [("w", j) for j in win(i)] + [("c", 0)]

    groups = lambda i: [blocks(i)[a:a + 4] for a in range(0, len(blocks(i)), 4)]
    gbase = [0]
    for i, h in units:
        gbase.append(gbase[-1] + len(groups(i)))
    ctx = ExitStack()
    with ctx:
        sb = lambda nm, sh: ctx.enter_context(nc.sbuf_tensor("np_" + nm, sh, F32))
        S = sb("scores", [P, AHEAD + 1, SW])
        nm = sb("negmax", [P, AHEAD + 1, 3])
        sm = sb("sums", [P, AHEAD + 1, 3])
        Q = ctx.enter_context(nc.sbuf_tensor("np_query_parts", [P, 2, 8, P], F32R))
        PT = sb("probsT", [P, 2, 512])
        co = sb("coef", [P, 2, 3])
        O = sb("out", [P, 2, 512])
        block = ctx.enter_context(nc.Block())
        s_s, s_ev, s_mx, s_ex = K.sem("np_scores"), K.sem("np_scores_out"), K.sem("np_max"), K.sem("np_exps")
        s_cm, s_pt, s_pc, s_o, s_oc = K.sem("np_masked"), K.sem("np_turned"), K.sem("np_turned_copied"), K.sem("np_values"), K.sem("np_combined")
        s_ot, s_oe, s_qh, s_ql = (K.sem("np_" + x) for x in ("out_turned", "out_copied", "queries_high", "queries_low"))

        def col_of(i, kind, j):
            return {"s": P * j, "w": TP + P * (j - win(i)[0]), "c": TP + 5 * P}[kind]

        @block.tensor
        def _(e):
            ident = K.c("ident")

            def scores(u):
                i, h = units[u]
                g, pp, c = h // 4, 64 * (h % 2), h // 2
                q = qT[pp:pp + 64, c, P * i:P * i + P]
                if u >= 1:
                    e.wait_ge(s_ev, u)
                if h == 0:
                    e.wait_ge(s_ql, i + 1)
                for z, (n, lo) in enumerate(zip(cols(i), (0, P * win(i)[0]))):
                    for a in range(0, n, 512):
                        w = min(512, n - a)
                        o = K.ps[:, 2 * z + a // 512, 0:w]
                        e.matmul(o, Q[:, i % 2, h, :], kh[:, z, g, lo + a:lo + a + w], start=True, stop=False)
                        e.matmul(o, Q[pp:pp + 64, i % 2, h, :], kl[pp:pp + 64, z, g, lo + a:lo + a + w], start=False, stop=True)
                e.matmul(K.ps[:, 3, 256:272], q, kcd[pp:pp + 64, g, :], start=True, stop=True).then_inc(s_s, 1)

            def values(u):
                i, h = units[u]
                g = h // 4
                e.wait_ge(s_ex, u + 1)
                e.wait_ge(s_cm, u + 1)
                if u >= 2:
                    e.wait_ge(s_oc, u - 1)
                if h == 1 and i >= 1:
                    e.wait_ge(s_oe, i)
                gs = groups(i)
                seen = set()

                def turn(n):
                    G = gbase[u] + n
                    if G >= 2:
                        e.wait_ge(s_pc, G - 1)
                    for z, (kind, j) in enumerate(gs[n]):
                        a = col_of(i, kind, j)
                        m = 16 if kind == "c" else P
                        mm = e.transpose(K.ps[0:m, 4 + G % 2, P * z:P * z + P], S[:, u % NS, a:a + m], ident)
                    mm.then_inc(s_pt, 1)

                turn(0)
                for n in range(len(gs)):
                    if n + 1 < len(gs):
                        turn(n + 1)
                    G = gbase[u] + n
                    e.wait_ge(s_pc, G + 1)
                    for z, (kind, j) in enumerate(gs[n]):
                        b = "swc".index(kind)
                        m = 16 if kind == "c" else P
                        v = vc[:, 64 * g:64 * g + 64] if kind == "c" else \
                            kvt[:, j, (384 if kind == "s" else 640) + 64 * g:(384 if kind == "s" else 640) + 64 * g + 64]
                        last = kind == "c" or j == i
                        mm = e.matmul(K.ps[:, 6 + u % 2, 64 * b:64 * b + 64], PT[0:m, G % 2, P * z:P * z + P], v,
                                      start=kind not in seen, stop=last)
                        seen.add(kind)
                mm.then_inc(s_o, 1)

            def turn_out(i):
                e.wait_ge(s_oc, 8 * i + 8)
                for c in range(4):
                    mm = e.transpose(K.ps[:, 7, P * c:P * c + P], O[:, i % 2, P * c:P * c + P], ident)
                mm.then_inc(s_ot, 1)

            for u in range(AHEAD):
                scores(u)
            for u in range(NU):
                i, h = units[u]
                if u + AHEAD < NU:
                    scores(u + AHEAD)
                values(u)
                if h == 0 and i >= 1:
                    turn_out(i - 1)
            turn_out(NTI - 1)

        @block.vector
        def _(e):
            def softmax_in(u):
                i, h = units[u]
                b = u % NS
                e.wait_ge(s_s, u + 1)
                if u >= NS:
                    e.wait_ge(s_o, u - NS + 1)
                ns, nw = cols(i)
                far = ns - 2 * P
                if far > 0:
                    e.tensor_scalar(S[:, b, 0:far], K.ps[:, 0:2, :].rearrange("p a n -> p (a n)")[:, 0:far], b31[:, h:h + 1], None, ALU.add)
                lo = max(far, 0)
                e.tensor_tensor(S[:, b, lo:ns], K.ps[:, 0:2, :].rearrange("p a n -> p (a n)")[:, lo:ns], near[:, h, 2 * P - (ns - lo):], ALU.add)
                pw = K.ps[:, 2:4, :].rearrange("p a n -> p (a n)")
                at = 0
                if i >= 4:
                    e.scalar_tensor_tensor(S[:, b, TP:TP + P], pw[:, 0:P], b31[:, h:h + 1], K.c("edge"), ALU.add, ALU.add)
                    at = P
                if nw - 2 * P > at:
                    e.tensor_scalar(S[:, b, TP + at:TP + nw - 2 * P], pw[:, at:nw - 2 * P], b31[:, h:h + 1], None, ALU.add)
                lo = max(nw - 2 * P, 0)
                e.tensor_tensor(S[:, b, TP + lo:TP + nw], pw[:, lo:nw], near[:, h, 2 * P - (nw - lo):], ALU.add)
                e.tensor_tensor(S[:, b, TP + 5 * P:SW], pw[:, 768:784], cb[:, h, 14 - 2 * i:30 - 2 * i], ALU.add).then_inc(s_ev, 1)
                e.drain()
                e.tensor_reduce(nm[:, b, 0:1], S[:, b, 0:ns], AX.X, ALU.max, negate=True)
                e.tensor_reduce(nm[:, b, 1:2], S[:, b, TP:TP + nw], AX.X, ALU.max, negate=True)
                e.tensor_reduce(nm[:, b, 2:3], S[:, b, TP + 5 * P:SW], AX.X, ALU.max, negate=True)
                e.drain().then_inc(s_mx, 1)

            def combine(u):
                i, h = units[u]
                b, ob = u % NS, u % 2
                e.wait_ge(s_ex, u + 1)
                e.reciprocal(co[:, ob, :], sm[:, b, :])
                e.drain()
                gt = kvt[:, i, 768:KVG].rearrange("p (z h) -> p z h", z=3)
                e.tensor_tensor(co[:, ob, 0:2], co[:, ob, 0:2], gt[:, 1:3, h], ALU.mult)
                e.tensor_tensor(co[:, ob, 2:3], co[:, ob, 2:3], gt[:, 0:1, h], ALU.mult)
                e.wait_ge(s_o, u + 1)
                if h == 0 and i >= 2:
                    e.wait_ge(s_ot, i - 1)
                o = O[:, i % 2, 64 * h:64 * h + 64]
                e.drain()
                e.tensor_scalar(o, K.ps[:, 6 + ob, 0:64], co[:, ob, 0:1], None, ALU.mult)
                e.drain()
                e.scalar_tensor_tensor(o, K.ps[:, 6 + ob, 64:128], co[:, ob, 1:2], o, ALU.mult, ALU.add)
                e.drain()
                e.scalar_tensor_tensor(o, K.ps[:, 6 + ob, 128:192], co[:, ob, 2:3], o, ALU.mult, ALU.add).then_inc(s_oc, 1)

            def out(i):
                e.wait_ge(s_ot, i + 1)
                e.tensor_copy(K.oC[:, :, P * i:P * i + P], K.ps[:, 7, :].rearrange("p (c n) -> p c n", c=4)).then_inc(s_oe, 1)

            def queries_low(i):
                e.wait_ge(s_qh, i + 1)
                for pp in (0, 64):
                    src, at = qT[pp:pp + 64, :, P * i:P * i + P], Q[pp:pp + 64, i % 2, pp // 64::2, :]
                    mm = e.tensor_tensor(Q[64 - pp:128 - pp, i % 2, pp // 64::2, :], src, at.bitcast(F32), ALU.subtract)
                mm.then_inc(s_ql, 1)

            queries_low(0)
            for u in range(AHEAD):
                softmax_in(u)
            for u in range(NU):
                i, h = units[u]
                if u + AHEAD < NU:
                    softmax_in(u + AHEAD)
                combine(u)
                if h == 0 and i >= 1:
                    out(i - 1)
                if h == 2 and i + 1 < NTI:
                    queries_low(i + 1)
            out(NTI - 1)

        @block.scalar
        def _(e):
            def exps(u):
                i, h = units[u]
                b = u % NS
                ns, nw = cols(i)
                e.wait_ge(s_mx, u + 1)
                if u >= NS:
                    e.wait_ge(s_oc, u - NS + 1)
                for z, (lo, hi) in enumerate(((0, ns), (TP, TP + nw), (TP + 5 * P, SW))):
                    e.activation(S[:, b, lo:hi], S[:, b, lo:hi], ACT.Exp, bias=nm[:, b, z:z + 1], accum_out=sm[:, b, z:z + 1])
                e.drain().then_inc(s_ex, 1)

            def queries_high(i):
                if i >= 2:
                    e.wait_ge(s_s, 8 * i - 8)
                for pp in (0, 64):
                    mm = e.activation(Q[pp:pp + 64, i % 2, pp // 64::2, :], qT[pp:pp + 64, :, P * i:P * i + P], ACT.Copy)
                mm.then_inc(s_qh, 1)

            queries_high(0)
            for u in range(AHEAD):
                exps(u)
            for u in range(NU):
                i, h = units[u]
                if h == 2 and i + 1 < NTI:
                    queries_high(i + 1)
                gs = groups(i)
                for n in range(len(gs)):
                    G = gbase[u] + n
                    e.wait_ge(s_pt, G + 1)
                    full = [z for z, (kind, _) in enumerate(gs[n]) if kind != "c"]
                    w = P * len(full)
                    if w:
                        mm = e.activation(PT[:, G % 2, 0:w], K.ps[:, 4 + G % 2, 0:w], ACT.Copy)
                    if len(full) < len(gs[n]):
                        mm = e.activation(PT[0:16, G % 2, w:w + P], K.ps[0:16, 4 + G % 2, w:w + P], ACT.Copy)
                    mm.then_inc(s_pc, 1)
                if u + AHEAD < NU:
                    exps(u + AHEAD)

        @block.sync
        def _(e):
            e.wait_ge(K.out_sem("kv_stored"), 16 * K.kv_stores)
            e.wait_ge(K.out_sem("tail_stored"), 16 * K.tail_stores)

        @block.gpsimd
        def _(e):
            for u in range(NU):
                i, h = units[u]
                e.wait_ge(s_ex, u + 1)
                e.tensor_tensor(S[:, u % NS, TP + 5 * P:SW], S[:, u % NS, TP + 5 * P:SW], K.c("cmask")[:, 14 - 2 * i:30 - 2 * i],
                                ALU.mult).then_inc(s_cm, 1)


SS, SWN, SCM = PAST + DT, 512 + DT, 32
SROW = SS + SWN + SCM


def stage_sample_rows(nc, K, kvt, qT, Qbd, bias, grow, vnew):
    with nc.sbuf_tensor("sr_gates", [TS, 24], F32) as gates, nc.Block() as block:
        s_hz = K.sem("sr_gates_by_head")
        s_g, s_b, s_r = K.sem("sr_rows_stored"), K.sem("sr_biases_in"), K.sem("sr_rows_in")

        @block.sync
        def _(e):
            v = K.bvec.tensor
            for t in range(DT):
                r = slice(t, P, DT)
                e.dma_start(bias[r, 0:SS], bass.AP(tensor=v, offset=REV - PAST - t, ap=[[0, 4], [BVL, 8], [1, SS]])).then_inc(s_b, 16)
                e.dma_start(bias[r, SS:SS + SWN], bass.AP(tensor=v, offset=REV - 512 - t, ap=[[0, 4], [BVL, 8], [1, SWN]])).then_inc(s_b, 16)

        @block.scalar
        def _(e):
            e.dma_start(K.gscr[:, 0:768], kvt[0:TS, NTI, 0:768]).then_inc(s_g, 16)
            e.wait_ge(s_hz, 1)
            e.dma_start(K.gscr[:, 768:KVG], gates[:, :]).then_inc(s_g, 16)
            e.wait_ge(s_g, 32)
            g = K.gscr.tensor
            for q in range(2):
                for t in range(DT):
                    e.dma_start(grow[t:P:DT, q, :], bass.AP(tensor=g, offset=KVG * (16 * q + t) + 768, ap=[[DT * KVG, 4], [3, 8], [1, 3]])).then_inc(s_r, 16)
            for z, c0 in enumerate((384, 640)):
                e.dma_start(vnew[0:DT, :, z, :], bass.AP(tensor=g, offset=c0, ap=[[KVG, DT], [DT * KVG, DB], [1, P]])).then_inc(s_r, 16)
            e.wait_ge(s_r, 16 * (2 * DT + 2))

        @block.vector
        def _(e):
            e.tensor_copy(gates[:, :].rearrange("p (h z) -> p h z", z=3),
                          kvt[0:TS, NTI, 768:KVG].rearrange("p (z h) -> p h z", z=3)).then_inc(s_hz, 1)
            e.memset(Qbd[:, :, :], 0.0)
            e.drain()
            for h in range(8):
                g, pp = h // 4, 64 * (h % 2)
                e.tensor_copy(Qbd[64 * g:64 * g + 64, :, 4 * h:4 * h + 4],
                              qT[pp:pp + 64, h // 2, TP:T].rearrange("p (b t) -> p b t", t=DT))
            e.wait_ge(s_b, 16 * 2 * DT)
            e.tensor_copy(bias[:, SS + SWN:SROW], bias[:, 63:PAST:64])


SLOTS = PAST // P


def stage_page_index(nc, K, idx):
    with nc.sbuf_tensor("pi_pages", [P, DB], I32) as pages, nc.Block() as block:
        s_in = K.sem("pi_pages_in")

        @block.sync
        def _(e):
            for b in range(DB):
                e.dma_start(pages[:, b:b + 1], bass.AP(tensor=K.d["page_table"].tensor, offset=NPG * b, ap=[[1, NPG], [0, 8], [1, 1]]),
                            allow_slow_non_contiguous=True).then_inc(s_in, 16)

        @block.vector
        def _(e):
            e.wait_ge(s_in, 16 * DB)
            e.tensor_scalar(idx[:, :], pages[:, :], 8.0, K.c("eighth"), ALU.mult, ALU.add)


def gather(e, dst, cache, idx, b):
    rows = cache[0].rearrange("g (e s) h d -> (g e) (s h d)", s=SLOTS)
    return e.indirect_dma_start(dst, None, rows, bass.IndirectOffsetOnAxis(ap=idx[:, b:b + 1], axis=0))


def stage_sample_scores(nc, K, Qbd, bias, S, vcb, ksn, kwn, idx, KT):
    ctx = ExitStack()
    with ctx:
        sb = lambda nm, sh: ctx.enter_context(nc.sbuf_tensor("ss_" + nm, sh, F32))
        ck, cv, sk = (sb(x, [P, 2, SLOTS * P]) for x in ("ck", "cv", "sk"))
        wk = sb("wk", [P, 2, 4, P])
        kc, sq, rt = sb("kc", [P, SCM]), sb("sq", [P, SCM]), sb("rt", [P, SCM])
        block = ctx.enter_context(nc.Block())
        s_c, s_k, s_wk = (K.sems("ss_" + x, 2) for x in ("means_in", "keys_in", "window_in"))
        s_t, s_tc = K.sem("ss_turned"), K.sem("ss_turned_copied")
        s_m, s_mc, s_sq, s_sm, s_v, s_r, s_kc = (K.sem("ss_" + x) for x in (
            "means", "means_copied", "squared", "summed", "mean_sq", "rooted", "block_keys"))
        s_s, s_ev = K.sem("ss_scores"), K.sem("ss_scores_out")
        NTG = 5

        tile = lambda t, b, s: t[:, b % 2, P * s:P * s + P]

        @block.gpsimd
        def _(e):
            for b in range(DB):
                z = b % 2
                if b >= 2:
                    e.wait_ge(s_m, b - 1)
                gather(e, ck[:, z, :], K.d["cache_cmp_k"], idx, b).then_inc(s_c[z], 16)
                gather(e, cv[:, z, :], K.d["cache_cmp_v"], idx, b).then_inc(s_c[z], 16)
                if b >= 2:
                    e.wait_ge(s_t, NTG * (b - 1))
                gather(e, sk[:, z, :], K.d["cache_slc_k"], idx, b).then_inc(s_k[z], 16)

        @block.sync
        def _(e):
            for b in range(DB):
                if b >= 2:
                    e.wait_ge(s_t, NTG * (b - 1))
                e.dma_start(wk[:, b % 2, :, :], K.d["cache_win_k"][0, b].rearrange("(i p) g d -> p i (g d)", p=P)).then_inc(s_wk[b % 2], 16)

        @block.tensor
        def _(e):
            ident, blk = K.c("ident"), K.c("blk16")

            def means(b):
                e.wait_ge(s_c[b % 2], 32 * (b // 2 + 1))
                if b >= 1:
                    e.wait_ge(s_mc, b)
                for j in range(SLOTS):
                    e.matmul(K.ps[:, 6, 0:SCM], tile(ck, b, j), blk, start=j == 0, stop=j == SLOTS - 1)
                for j in range(SLOTS):
                    mm = e.matmul(K.ps[0:SCM, 7, 0:P], blk, tile(cv, b, j), start=j == 0, stop=j == SLOTS - 1)
                mm.then_inc(s_m, 1)

            means(0)
            for b in range(DB):
                q, bb = b // 4, b % 4
                e.wait_ge(s_k[b % 2], 16 * (b // 2 + 1))
                for z in range(NTG):
                    G = NTG * b + z
                    if G >= 2:
                        e.wait_ge(s_tc, G - 1)
                    if z == 2:
                        e.wait_ge(s_sq, b + 1)
                        if b >= 1:
                            e.wait_ge(s_v, b)
                        e.matmul(K.ps[:, 5, 0:SCM], K.c("headsum"), sq[:, :], start=True, stop=True).then_inc(s_sm, 1)
                    if z == 4:
                        e.wait_ge(s_wk[b % 2], 16 * (b // 2 + 1))
                    for j in range(4):
                        src = tile(sk, b, 4 * z + j) if z < 4 else wk[:, b % 2, j, :]
                        mm = e.transpose(K.ps[:, G % 2, P * j:P * j + P], src, ident)
                    mm.then_inc(s_t, 1)
                pr = slice(32 * bb, 32 * bb + 32)
                new = slice(DT * b, DT * b + DT)
                qb = Qbd[:, b, :]
                for z in range(6):
                    n = 6 * b + z
                    if n >= 3:
                        e.wait_ge(s_ev, n - 2)
                    c = 2 + z % 3
                    if z < 5:
                        e.wait_ge(s_tc, NTG * b + z + 1)
                        lo = 512 * z if z < 4 else SS
                        e.matmul(K.ps[pr, c, :], qb, KT[:, lo:lo + 512], start=True, stop=True).then_inc(s_s, 1)
                    else:
                        if b + 1 < DB:
                            means(b + 1)
                        e.wait_ge(s_kc, b + 1)
                        e.matmul(K.ps[pr, c, 0:DT], qb, ksn[:, new], start=True, stop=True)
                        e.matmul(K.ps[pr, c, 8:8 + DT], qb, kwn[:, new], start=True, stop=True)
                        e.matmul(K.ps[pr, c, 16:16 + SCM], qb, kc[:, :], start=True, stop=True).then_inc(s_s, 1)

        @block.scalar
        def _(e):
            for b in range(DB):
                for z in range(NTG):
                    G = NTG * b + z
                    e.wait_ge(s_t, G + 1)
                    if b >= 1:
                        e.wait_ge(s_s, 6 * (b - 1) + z + 1)
                    lo = 512 * z if z < 4 else SS
                    e.activation(KT[:, lo:lo + 512], K.ps[:, G % 2, :], ACT.Copy).then_inc(s_tc, 1)
                    if z == 3:
                        e.wait_ge(s_v, b + 1)
                        e.activation(rt[:, :], rt[:, :], ACT.Sqrt).then_inc(s_r, 1)

        @block.vector
        def _(e):
            def means_out(b):
                e.wait_ge(s_m, b + 1)
                if b >= 1:
                    e.wait_ge(s_s, 6 * b)
                e.tensor_copy(kc[:, :], K.ps[:, 6, 0:SCM])
                e.tensor_copy(vcb[:, b, :], K.ps[0:SCM, 7, 0:P]).then_inc(s_mc, 1)
                e.drain()
                e.tensor_tensor(sq[:, :], kc[:, :], kc[:, :], ALU.mult).then_inc(s_sq, 1)

            means_out(0)
            for b in range(DB):
                q, bb = b // 4, b % 4
                pr = slice(32 * bb, 32 * bb + 32)
                e.wait_ge(s_sm, b + 1)
                e.tensor_scalar(rt[:, :], K.ps[:, 5, 0:SCM], 1.0 / 64, RMS_EPS, ALU.mult, ALU.add).then_inc(s_v, 1)
                for z in range(5):
                    e.wait_ge(s_s, 6 * b + z + 1)
                    src = K.ps[pr, 2 + z % 3, :]
                    if z < 4:
                        nat = lambda ap: ap.rearrange("r (p s) -> r s p", s=SLOTS)[:, 4 * z:4 * z + 4, :]
                        e.tensor_tensor(nat(S[pr, q, 0:PAST]), src.rearrange("r (s p) -> r s p", s=4),
                                        nat(bias[pr, 0:PAST]), ALU.add).then_inc(s_ev, 1)
                    else:
                        e.tensor_tensor(S[pr, q, SS:SS + 512], src, bias[pr, SS:SS + 512], ALU.add).then_inc(s_ev, 1)
                    if z == 3:
                        e.wait_ge(s_r, b + 1)
                        e.reciprocal(rt[:, :], rt[:, :])
                        e.drain()
                        e.scalar_tensor_tensor(kc[:, :], kc[:, :], K.p("kg_cmp", 0), rt[:, :], ALU.mult, ALU.mult).then_inc(s_kc, 1)
                e.wait_ge(s_s, 6 * b + 6)
                e.tensor_tensor(S[pr, q, PAST:SS], K.ps[pr, 4, 0:DT], bias[pr, PAST:SS], ALU.add)
                e.tensor_tensor(S[pr, q, SS + 512:SS + SWN], K.ps[pr, 4, 8:8 + DT], bias[pr, SS + 512:SS + SWN], ALU.add)
                e.tensor_tensor(S[pr, q, SS + SWN:SROW], K.ps[pr, 4, 16:16 + SCM], bias[pr, SS + SWN:SROW], ALU.add).then_inc(s_ev, 1)
                if b + 1 < DB:
                    means_out(b + 1)


def stage_sample_softmax(nc, K, S, coef, grow):
    ctx = ExitStack()
    with ctx:
        sb = lambda nm, sh: ctx.enter_context(nc.sbuf_tensor("sx_" + nm, sh, F32))
        nm, sm, rc = sb("negmax", [P, 2, 3]), sb("sums", [P, 2, 3]), sb("rec", [P, 2, 3])
        pc, sc, s1, s2 = sb("pc", [P, SCM]), sb("score", [P, 33]), sb("left", [P, 33]), sb("left2", [P, 33])
        m1, m2 = sb("top", [P, 8]), sb("top2", [P, 8])
        block = ctx.enter_context(nc.Block())
        s_mx, s_ex, s_pc, s_sc = K.sem("sx_max"), K.sem("sx_exps"), K.sem("sx_block_probs"), K.sem("sx_block_scores")
        RNG = ((0, SS), (SS, SS + SWN), (SS + SWN, SROW))
        OUT = -3e30

        @block.vector
        def _(e):
            for q in range(2):
                e.tensor_tensor(S[:, q, SS:SS + 4], S[:, q, SS:SS + 4], K.c("edgeS"), ALU.add)
                e.drain()
                for z in (2, 1):
                    lo, hi = RNG[z]
                    e.tensor_reduce(nm[:, q, z:z + 1], S[:, q, lo:hi], AX.X, ALU.max, negate=True).then_inc(s_mx, 1)
                e.wait_ge(s_ex, 3 * q + 1)
                e.reciprocal(rc[:, q, 2:3], sm[:, q, 2:3])
                e.drain()
                e.tensor_scalar(pc[:, :], S[:, q, SS + SWN:SROW], rc[:, q, 2:3], None, ALU.mult).then_inc(s_pc, 1)
                e.wait_ge(s_sc, q + 1)
                e.tensor_copy(sc[:, 0:SCM], K.ps[:, q, 0:SCM])
                e.drain()
                e.memset(sc[:, 0:1], 1e4)
                e.memset(sc[:, 31:33], 1e4)
                e.drain()
                e.max(m1[:, :], sc[:, :])
                e.drain()
                e.match_replace(s1[:, :], m1[:, :], sc[:, :], OUT)
                e.drain()
                e.max(m2[:, :], s1[:, :])
                e.drain()
                e.match_replace(s2[:, :], m2[:, :], s1[:, :], OUT)
                e.drain()
                e.tensor_scalar(s1[:, :], s2[:, :], OUT / 2, NEG, ALU.is_gt, ALU.mult)
                e.drain()
                sv = S[:, q, 0:PAST].rearrange("p (j n) -> p j n", n=64)
                e.tensor_tensor(sv, sv, s1[:, 0:32].unsqueeze(2).to_broadcast([P, 32, 64]), ALU.add)
                e.drain()
                e.tensor_reduce(nm[:, q, 0:1], S[:, q, 0:SS], AX.X, ALU.max, negate=True).then_inc(s_mx, 1)
                e.wait_ge(s_ex, 3 * q + 3)
                e.reciprocal(rc[:, q, 0:2], sm[:, q, 0:2])
                e.drain()
                e.tensor_tensor(coef[:, q, 0:2], rc[:, q, 0:2], grow[:, q, 1:3], ALU.mult)
                e.tensor_tensor(coef[:, q, 2:3], rc[:, q, 2:3], grow[:, q, 0:1], ALU.mult)

        @block.scalar
        def _(e):
            for q in range(2):
                for n, z in enumerate((2, 1, 0)):
                    lo, hi = RNG[z]
                    e.wait_ge(s_mx, 3 * q + n + 1)
                    e.activation(S[:, q, lo:hi], S[:, q, lo:hi], ACT.Exp, bias=nm[:, q, z:z + 1], accum_out=sm[:, q, z:z + 1])
                    e.drain().then_inc(s_ex, 1)

        @block.tensor
        def _(e):
            for q in range(2):
                e.wait_ge(s_pc, q + 1)
                e.matmul(K.ps[:, q, 0:SCM], K.c("heads4"), pc[:, :], start=True, stop=True).then_inc(s_sc, 1)


def stage_sample_values(nc, K, S, coef, vcb, vnew, idx):
    ctx = ExitStack()
    NB4 = 20
    with ctx:
        sb = lambda nm, sh: ctx.enter_context(nc.sbuf_tensor("sv_" + nm, sh, F32))
        sv = sb("v", [P, 3, SLOTS * P])
        wv = sb("wv", [P, 2, 4, P])
        PT = sb("PT", [P, NB4, P])
        PN = sb("PN", [SCM, 3, P])
        o1, o2 = sb("o1", [P, P]), sb("o2", [P, 64])
        block = ctx.enter_context(nc.Block())
        s_pgs, s_wv = K.sems("sv_pages_in", 3), K.sems("sv_window_in", 2)
        s_t, s_tc, s_used, s_o, s_oc, s_ot, s_fin = (K.sem("sv_" + x) for x in (
            "turned", "turned_copied", "values_used", "values", "combined", "out_turned", "out_copied"))

        @block.gpsimd
        def _(e):
            for b in range(DB):
                if b >= 3:
                    e.wait_ge(s_used, b - 2)
                gather(e, sv[:, b % 3, :], K.d["cache_slc_v"], idx, b).then_inc(s_pgs[b % 3], 16)

        @block.sync
        def _(e):
            for b in range(DB):
                if b >= 2:
                    e.wait_ge(s_used, b - 1)
                e.dma_start(wv[:, b % 2, :, :], K.d["cache_win_v"][0, b].rearrange("(i p) g d -> p i (g d)", p=P)).then_inc(s_wv[b % 2], 16)

        @block.tensor
        def _(e):
            ident = K.c("ident")
            for q in range(2):
                if q:
                    e.wait_ge(s_used, 4)
                for z in range(6):
                    G = 6 * q + z
                    if G >= 2:
                        e.wait_ge(s_tc, G - 1)
                    if z < 5:
                        for j in range(4):
                            keys = slice(4 * z + j, PAST, SLOTS) if z < 4 else slice(SS + P * j, SS + P * j + P)
                            mm = e.transpose(K.ps[:, G % 2, P * j:P * j + P], S[:, q, keys], ident)
                    else:
                        e.transpose(K.ps[0:DT, G % 2, 0:P], S[:, q, PAST:SS], ident)
                        e.transpose(K.ps[0:DT, G % 2, P:2 * P], S[:, q, SS + 512:SS + SWN], ident)
                        mm = e.transpose(K.ps[0:SCM, G % 2, 2 * P:3 * P], S[:, q, SS + SWN:SROW], ident)
                    mm.then_inc(s_t, 1)
                e.wait_ge(s_tc, 6 * q + 6)
                if q:
                    e.wait_ge(s_oc, 1)
                for bb in range(4):
                    b = 4 * q + bb
                    e.wait_ge(s_pgs[b % 3], 16 * (b // 3 + 1))
                    e.wait_ge(s_wv[b % 2], 16 * (b // 2 + 1))
                    r = slice(32 * bb, 32 * bb + 32)
                    for j in range(SLOTS):
                        e.matmul(K.ps[r, 2, 0:P], PT[:, j, r], sv[:, b % 3, P * j:P * j + P], start=j == 0, stop=False)
                    e.matmul(K.ps[r, 2, 0:P], PN[0:DT, 0, r], vnew[0:DT, b, 0, :], start=False, stop=True)
                    for j in range(4):
                        e.matmul(K.ps[r, 3, 0:P], PT[:, NPG + j, r], wv[:, b % 2, j, :], start=j == 0, stop=False)
                    e.matmul(K.ps[r, 3, 0:P], PN[0:DT, 1, r], vnew[0:DT, b, 1, :], start=False, stop=True)
                    e.matmul(K.ps[r, 4, 0:P], PN[:, 2, r], vcb[:, b, :], start=True, stop=True).then_inc(s_used, 1)
                e.wait_ge(s_oc, q + 1)
                e.transpose(K.ps[0:64, 5, 0:P], o2[:, :], ident).then_inc(s_ot, 1)

        @block.scalar
        def _(e):
            for q in range(2):
                if q:
                    e.wait_ge(s_used, 4)
                for z in range(6):
                    G = 6 * q + z
                    e.wait_ge(s_t, G + 1)
                    if z < 5:
                        e.activation(PT[:, 4 * z:4 * z + 4, :].rearrange("p j n -> p (j n)"), K.ps[:, G % 2, :], ACT.Copy).then_inc(s_tc, 1)
                    else:
                        for k, n in enumerate((DT, DT, SCM)):
                            mm = e.activation(PN[0:n, k, :], K.ps[0:n, G % 2, P * k:P * k + P], ACT.Copy)
                        mm.then_inc(s_tc, 1)

        @block.vector
        def _(e):
            for q in range(2):
                e.wait_ge(s_used, 4 * q + 4)
                e.tensor_scalar(o1[:, :], K.ps[:, 2, 0:P], coef[:, q, 0:1], None, ALU.mult)
                e.drain()
                e.scalar_tensor_tensor(o1[:, :], K.ps[:, 3, 0:P], coef[:, q, 1:2], o1[:, :], ALU.mult, ALU.add)
                e.drain()
                e.scalar_tensor_tensor(o1[:, :], K.ps[:, 4, 0:P], coef[:, q, 2:3], o1[:, :], ALU.mult, ALU.add)
                e.drain()
                e.tensor_scalar(o2[:, :], o1[:, 0:64], K.c("grp")[:, 0:1], None, ALU.mult)
                e.drain()
                e.scalar_tensor_tensor(o2[:, :], o1[:, 64:P], K.c("grp")[:, 1:2], o2[:, :], ALU.mult, ALU.add).then_inc(s_oc, 1)
                e.wait_ge(s_ot, q + 1)
                t = K.ps[0:64, 5, 0:P].rearrange("p (b h t) -> p b h t", b=4, h=8)
                for h in range(8):
                    e.tensor_copy(K.oC[64 * (h % 2):64 * (h % 2) + 64, h // 2, TP + 16 * q:TP + 16 * q + 16].rearrange("p (b t) -> p b t", t=DT),
                                  t[:, :, h, :])
                e.drain()


def stage_merge(nc, K, h, xh, xl, spare):
    names = ("w_br_a", "w_br_b", "w_br_c")
    srcs = (K.oA, K.oB, K.oC)
    ctx = ExitStack()
    with ctx:
        W = weight_slots(nc, K, ctx, "me", KD, 2)
        wb = ctx.enter_context(nc.sbuf_tensor("me_branch_w", [P, 2, 4, P], F32))
        sg, tmp = spare[:, 0:2, :], spare[:, 2, :]
        block = ctx.enter_context(nc.Block())
        s_bin = K.sems("me_branch_in", 2)
        s_b, s_sg, s_h = K.sem("me_branch_product"), K.sem("me_gate_sigmoid"), K.sem("me_weighted")
        NU = 3 * KD

        @block.sync
        def _(e):
            for u in range(NU):
                m, br = u // 3, u % 3
                c0 = OFF_MG + D * br + P * m
                load_block(e, W, u, [K.d["w_in"][0, :, c0:c0 + P]])
                if u >= 2:
                    e.wait_ge(s_b, u - 1)
                e.dma_start(wb[:, u % 2, :, :], K.d[names[br]][0, :, P * m:P * m + P].rearrange("(k p) n -> p k n", p=P)).then_inc(s_bin[u % 2], 16)

        @block.tensor
        def _(e):
            for u in range(NU):
                br = u % 3
                e.wait_ge(W.s_lo, u + 1)
                if u >= 1:
                    e.wait_ge(s_sg, u)
                product(e, K, W, u, xh, xl, 0, range(KD)).then_inc(W.s_mm, 1)
                e.wait_ge(s_bin[u % 2], 16 * (u // 2 + 1))
                if u >= 1:
                    e.wait_ge(s_h, u)
                for c in range(NC3):
                    for k in range(4):
                        mm = e.matmul(K.ps[:, 3 + c, 0:NW], wb[:, u % 2, k, :], srcs[br][:, k, NW * c:NW * c + NW], start=k == 0, stop=k == 3)
                mm.then_inc(s_b, 1)

        @block.scalar
        def _(e):
            high_block(e, W, 0, 1)
            high_block(e, W, 1, 1)
            for u in range(NU):
                e.wait_ge(W.s_mm, u + 1)
                if u >= 2:
                    e.wait_ge(s_h, u - 1)
                e.activation(sg[:, u % 2, :].rearrange("p (c n) -> p c n", c=NC3), K.ps[:, 0:3, 0:NW], ACT.Sigmoid).then_inc(s_sg, 1)
                if u + 2 < NU:
                    high_block(e, W, u + 2, (u + 2) // 2 + 1)

        @block.vector
        def _(e):
            c3 = lambda ap: ap.rearrange("p (c n) -> p c n", c=NC3)
            low_block(e, W, 0)
            low_block(e, W, 1)
            for u in range(NU):
                m, br = u // 3, u % 3
                if u + 2 < NU:
                    low_block(e, W, u + 2)
                e.wait_ge(s_sg, u + 1)
                e.wait_ge(s_b, u + 1)
                dst = h[:, m, :] if br == 0 else tmp
                e.tensor_tensor(c3(dst), c3(sg[:, u % 2, :]), K.ps[:, 3:6, 0:NW], ALU.mult).then_inc(s_h, 1)
                e.drain()
                if br:
                    e.tensor_tensor(h[:, m, :], h[:, m, :], tmp, ALU.add)
                    e.drain()


def stage_product(nc, K, tag, w, kb, nblk, rh, rl, dst, add):
    ctx = ExitStack()
    with ctx:
        W = weight_slots(nc, K, ctx, tag, kb)
        block = ctx.enter_context(nc.Block())
        s_out = K.sem(tag + "_taken")
        c3 = lambda ap: ap.rearrange("p (c n) -> p c n", c=NC3)
        bank = lambda m: K.ps[:, 3 * (m % 2):3 * (m % 2) + 3, 0:NW]

        @block.sync
        def _(e):
            for m in range(nblk):
                load_block(e, W, m, [w(m)])

        @block.tensor
        def _(e):
            for m in range(nblk):
                e.wait_ge(W.s_lo, m + 1)
                if m >= 2:
                    e.wait_ge(s_out, m - 1)
                product(e, K, W, m, rh, rl, 3 * (m % 2), range(kb)).then_inc(W.s_mm, 1)

        @block.scalar
        def _(e):
            for m in range(nblk):
                high_block(e, W, m, m // NRAW + 1)

        @block.vector
        def _(e):
            low_block(e, W, 0)
            low_block(e, W, 1)
            for m in range(nblk):
                e.wait_ge(W.s_mm, m + 1)
                if add:
                    e.tensor_tensor(c3(dst[:, m, :]), c3(dst[:, m, :]), bank(m), ALU.add).then_inc(s_out, 1)
                else:
                    e.tensor_copy(c3(dst[:, m, :]), bank(m)).then_inc(s_out, 1)
                if m + 2 < nblk:
                    low_block(e, W, m + 2)


def stage_ffn(nc, K, xh, xl, x):
    GB = 4
    NG = 4 * D // P // GB
    RING = GB + 1
    units = [("up", j) for j in range(GB)]
    for g in range(NG):
        up = [("up", GB * (g + 1) + j) for j in range(GB)] if g + 1 < NG else []
        units += up[:1] + [("down", g, q) for q in range(KD // 2)] + up[1:]
    NU = len(units)
    done = []
    for un in units:
        done.append((done[-1] if done else 0) + (1 if un[0] == "up" else 2))
    kinds = [un[0] for un in units for _ in range(1 if un[0] == "up" else 2)]
    ctx = ExitStack()
    with ctx:
        W = weight_slots(nc, K, ctx, "ff", KD)
        hh = ctx.enter_context(nc.sbuf_tensor("ff_hidden_high", [P, RING, T], F32R))
        hl = ctx.enter_context(nc.sbuf_tensor("ff_hidden_low", [P, RING, T], F32R))
        act = ctx.enter_context(nc.sbuf_tensor("ff_act", [P, 2, T], F32))
        block = ctx.enter_context(nc.Block())
        s_hh, s_hl, s_read_up, s_read_down = (K.sem("ff_" + x) for x in (
            "hidden_high", "hidden_low", "up_read", "down_read"))
        c3 = lambda ap: ap.rearrange("p (c n) -> p c n", c=NC3)
        bank = lambda n: K.ps[:, 3 * (n % 2):3 * (n % 2) + 3, 0:NW]

        @block.sync
        def _(e):
            for u, un in enumerate(units):
                if un[0] == "up":
                    load_block(e, W, u, [K.d["w_ff1"][0][:, P * un[1]:P * un[1] + P]])
                    continue
                if u >= NRAW:
                    e.wait_ge(W.s_lo, u - NRAW + 1)
                src = K.d["w_ff2"][0][GB * P * un[1]:GB * P * (un[1] + 1), 2 * P * un[2]:2 * P * un[2] + 2 * P]
                e.dma_start(W.raw[:, u % NRAW, :, :].rearrange("p (k z) n -> p k (z n)", z=2),
                            src.rearrange("(k p) n -> p k n", p=P)).then_inc(W.s_in[u % NRAW], 16)

        @block.tensor
        def _(e):
            def bank_free(n):
                if n >= 2:
                    e.wait_ge(s_read_up if kinds[n - 2] == "up" else s_read_down, kinds[:n - 1].count(kinds[n - 2]))

            n = 0
            for u, un in enumerate(units):
                e.wait_ge(W.s_lo, u + 1)
                if un[0] == "up":
                    bank_free(n)
                    mm = product(e, K, W, u, xh, xl, 3 * (n % 2), range(KD))
                    mm.then_inc(W.s_mm, 1)
                    n += 1
                    continue
                g = un[1]
                e.wait_ge(s_hl, GB * (g + 1))
                for z in range(2):
                    bank_free(n)
                    for c in range(NC3):
                        o, ns = K.ps[:, 3 * (n % 2) + c, 0:NW], slice(NW * c, NW * c + NW)
                        for k in range(GB):
                            r = (GB * g + k) % RING
                            e.matmul(o, W.hi[:, u % NSPL, 2 * k + z, :], hh[:, r, ns], start=k == 0, stop=False)
                            e.matmul(o, W.hi[:, u % NSPL, 2 * k + z, :], hl[:, r, ns], start=False, stop=False)
                            mm = e.matmul(o, W.lo[:, u % NSPL, 2 * k + z, :], hh[:, r, ns], start=False, stop=k == GB - 1)
                    mm.then_inc(W.s_mm, 1)
                    n += 1

        def weights_high(e, u):
            e.wait_ge(W.s_in[u % NRAW], 16 * (u // NRAW + 1))
            if u >= NSPL:
                e.wait_ge(W.s_mm, done[u - NSPL])
            e.activation(W.hi[:, u % NSPL, :, :], W.raw[:, u % NRAW, :, :], ACT.Copy).then_inc(W.s_hi, 1)

        @block.scalar
        def _(e):
            weights_high(e, 0)
            weights_high(e, 1)
            for u, un in enumerate(units):
                if un[0] == "up":
                    j = un[1]
                    e.wait_ge(W.s_mm, done[u])
                    if j >= 2:
                        e.wait_ge(s_hl, j - 1)
                    e.activation(c3(act[:, j % 2, :]), bank(done[u] - 1), ACT.Relu).then_inc(s_read_up, 1)
                    e.drain()
                    e.activation(act[:, j % 2, :], act[:, j % 2, :], ACT.Square)
                    e.drain()
                    e.activation(hh[:, j % RING, :], act[:, j % 2, :], ACT.Copy).then_inc(s_hh, 1)
                if u + 2 < NU:
                    weights_high(e, u + 2)

        @block.vector
        def _(e):
            low_block(e, W, 0)
            low_block(e, W, 1)
            for u, un in enumerate(units):
                if un[0] == "up":
                    j = un[1]
                    e.wait_ge(s_hh, j + 1)
                    e.tensor_tensor(hl[:, j % RING, :], act[:, j % 2, :], hh[:, j % RING, :].bitcast(F32), ALU.subtract).then_inc(s_hl, 1)
                else:
                    for z in range(2):
                        n = done[u] - 2 + z
                        e.wait_ge(W.s_mm, n + 1)
                        m = 2 * un[2] + z
                        e.tensor_tensor(c3(x[:, m, :]), c3(x[:, m, :]), bank(n), ALU.add).then_inc(s_read_down, 1)
                if u + 2 < NU:
                    low_block(e, W, u + 2)


def stage_mem_load(nc, K, mT):
    ctx = ExitStack()
    with ctx:
        rows = ctx.enter_context(nc.sbuf_tensor("ml_rows", [P, 2, D], F32))
        block = ctx.enter_context(nc.Block())
        s_in, s_t, s_c = K.sem("ml_in"), K.sem("ml_turned"), K.sem("ml_copied")

        @block.sync
        def _(e):
            e.dma_start(rows[:, :, :], K.d["mem_prompt"][0].rearrange("(i p) d -> p i d", p=P)).then_inc(s_in, 16)

        @block.tensor
        def _(e):
            e.wait_ge(s_in, 16)
            for i in range(2):
                for k in range(KD):
                    mm = e.transpose(K.ps[:, 2 * i + k // 4, P * (k % 4):P * (k % 4) + P], rows[:, i, P * k:P * k + P], K.c("ident"))
                mm.then_inc(s_t, 1)

        @block.vector
        def _(e):
            for i in range(2):
                e.wait_ge(s_t, i + 1)
                for z in range(2):
                    e.tensor_copy(mT[:, 4 * z:4 * z + 4, P * i:P * i + P], K.ps[:, 2 * i + z, :].rearrange("p (k n) -> p k n", k=4))


def stage_mem_kv(nc, K, mh, ml, mkT, mv):
    ctx = ExitStack()
    with ctx:
        sb = lambda nm, sh: ctx.enter_context(nc.sbuf_tensor("mk_" + nm, sh, F32))
        w = sb("w", [P, 2, KD, 512])
        wh, wl = (ctx.enter_context(nc.sbuf_tensor("mk_" + x, [P, KD, 512], F32R)) for x in ("high", "low"))
        mk = sb("k", [P, 2, 512])
        sq, kg, ss = sb("sq", [P, 2, 512]), sb("gain", [P, P]), sb("ss", [P, 8])
        block = ctx.enter_context(nc.Block())
        s_in, s_g, s_mm, s_c, s_v, s_r, s_k, s_t, s_hi, s_lo = (K.sem("mk_" + x) for x in (
            "w_in", "gain_in", "product", "copied", "mean", "rooted", "normed", "turned", "high", "low"))
        s_out = K.out_sem("mk_stored")

        @block.sync
        def _(e):
            e.dma_start(w[:, 0, :, :], K.d["w_mk"][0].rearrange("(k p) n -> p k n", p=P)).then_inc(s_in, 16)
            e.dma_start(w[:, 1, :, :], K.d["w_mv"][0].rearrange("(k p) n -> p k n", p=P)).then_inc(s_in, 16)
            e.dma_start(kg[:, :], K.d["mem_k_g"][0, :].partition_broadcast(P)).then_inc(s_g, 16)
            e.wait_ge(s_k, 1)
            e.dma_start(K.d["p_mem_k"][0, 0].rearrange("(i p) h d -> p i (h d)", p=P), mk[:, :, :]).then_inc(s_out, 16)
            e.wait_ge(s_c, 2)
            e.dma_start(K.d["p_mem_v"][0, 0].rearrange("(i p) h d -> p i (h d)", p=P), mv[:, :, :]).then_inc(s_out, 16)
            e.wait_ge(s_out, 32)

        @block.tensor
        def _(e):
            for z in range(2):
                e.wait_ge(s_lo, z + 1)
                for i in range(2):
                    for k in range(KD):
                        o, r = K.ps[:, 2 * z + i, :], slice(P * i, P * i + P)
                        e.matmul(o, mh[:, k, r], wh[:, k, :], start=k == 0, stop=False)
                        e.matmul(o, ml[:, k, r], wh[:, k, :], start=False, stop=False)
                        mm = e.matmul(o, mh[:, k, r], wl[:, k, :], start=False, stop=k == KD - 1)
                mm.then_inc(s_mm, 1)
            e.wait_ge(s_k, 1)
            for h in range(4):
                for i in range(2):
                    mm = e.transpose(K.ps[:, 4 + h // 2, 256 * (h % 2) + P * i:256 * (h % 2) + P * i + P], mk[:, i, P * h:P * h + P], K.c("ident"))
            mm.then_inc(s_t, 1)

        @block.scalar
        def _(e):
            for z, dst in ((0, mk), (1, mv)):
                e.wait_ge(s_in, 32)
                e.activation(wh[:, :, :], w[:, z, :, :], ACT.Copy).then_inc(s_hi, 1)
                e.wait_ge(s_mm, z + 1)
                e.activation(dst[:, :, :], K.ps[:, 2 * z:2 * z + 2, :], ACT.Copy).then_inc(s_c, 1)
            e.wait_ge(s_v, 1)
            e.activation(ss[:, :], ss[:, :], ACT.Sqrt).then_inc(s_r, 1)

        @block.vector
        def _(e):
            k8 = mk[:, :, :].rearrange("p i (h d) -> p (i h) d", d=P)
            for z in range(2):
                e.wait_ge(s_hi, z + 1)
                e.tensor_tensor(wl[:, :, :], w[:, z, :, :], wh[:, :, :].bitcast(F32), ALU.subtract).then_inc(s_lo, 1)
            e.wait_ge(s_c, 1)
            e.tensor_tensor(sq[:, :, :], mk[:, :, :], mk[:, :, :], ALU.mult)
            e.drain()
            e.tensor_reduce(ss[:, :], sq[:, :, :].rearrange("p i (h d) -> p (i h) d", d=P), AX.X, ALU.add)
            e.drain()
            e.tensor_scalar(ss[:, :], ss[:, :], 1.0 / P, RMS_EPS, ALU.mult, ALU.add).then_inc(s_v, 1)
            e.wait_ge(s_r, 1)
            e.reciprocal(ss[:, :], ss[:, :])
            e.drain()
            e.tensor_tensor(k8, k8, ss[:, :].unsqueeze(2).to_broadcast([P, 8, P]), ALU.mult)
            e.drain()
            e.wait_ge(s_g, 16)
            e.tensor_tensor(k8, k8, kg[:, :].unsqueeze(1).to_broadcast([P, 8, P]), ALU.mult).then_inc(s_k, 1)
            e.wait_ge(s_t, 1)
            e.tensor_copy(mkT[:, :, :].rearrange("p h n -> p (h n)"), K.ps[:, 4:6, :].rearrange("p a n -> p (a n)"))


def stage_mem_prompt(nc, K, q, mkT, mv, o):
    SC = P ** -0.5
    ctx = ExitStack()
    with ctx:
        sb = lambda nm, sh: ctx.enter_context(nc.sbuf_tensor("mp_" + nm, sh, F32))
        Pr = sb("probs", [P, 2, 4, 256])
        nm, sm = sb("negmax", [P, 2, 4]), sb("sums", [P, 2, 4])
        PT = sb("probsT", [P, 8, P])
        block = ctx.enter_context(nc.Block())
        s_s, s_mx, s_ex, s_pr, s_t, s_tc, s_o, s_oc = (K.sem("mp_" + x) for x in (
            "scores", "max", "exps", "probs", "turned", "turned_copied", "values", "values_copied"))

        def sbank(i):
            return K.ps[:, 2 * (i % 2):2 * (i % 2) + 2, :].rearrange("p a (h n) -> p (a h) n", h=2)

        @block.tensor
        def _(e):
            def scores(i):
                if i >= 2:
                    e.wait_ge(s_ex, i - 1)
                for h in range(4):
                    mm = e.matmul(K.ps[:, 2 * (i % 2) + h // 2, 256 * (h % 2):256 * (h % 2) + 256], q[:, h, P * i:P * i + P], mkT[:, h, :],
                                  start=True, stop=True)
                mm.then_inc(s_s, 1)

            scores(0)
            for i in range(NTI):
                if i + 1 < NTI:
                    scores(i + 1)
                e.wait_ge(s_pr, i + 1)
                if i >= 1:
                    e.wait_ge(s_tc, i)
                for h in range(4):
                    for j in range(2):
                        mm = e.transpose(K.ps[:, 4 + h // 2, 256 * (h % 2) + P * j:256 * (h % 2) + P * j + P],
                                         Pr[:, i % 2, h, P * j:P * j + P], K.c("ident"))
                mm.then_inc(s_t, 1)
                e.wait_ge(s_tc, i + 1)
                if i >= 2:
                    e.wait_ge(s_oc, i - 1)
                for h in range(4):
                    for j in range(2):
                        mm = e.matmul(K.ps[:, 6 + i % 2, P * h:P * h + P], mv[:, j, P * h:P * h + P], PT[:, 2 * h + j, :], start=j == 0, stop=j == 1)
                mm.then_inc(s_o, 1)

        @block.vector
        def _(e):
            def maxes(i):
                e.wait_ge(s_s, i + 1)
                if i >= 2:
                    e.wait_ge(s_ex, i - 1)
                e.tensor_reduce(nm[:, i % 2, :], sbank(i), AX.X, ALU.max, negate=True)
                e.drain()
                e.tensor_scalar(nm[:, i % 2, :], nm[:, i % 2, :], SC, None, ALU.mult).then_inc(s_mx, 1)

            maxes(0)
            for i in range(NTI):
                if i + 1 < NTI:
                    maxes(i + 1)
                e.wait_ge(s_ex, i + 1)
                e.reciprocal(sm[:, i % 2, :], sm[:, i % 2, :])
                e.drain()
                e.tensor_tensor(Pr[:, i % 2, :, :], Pr[:, i % 2, :, :], sm[:, i % 2, :].unsqueeze(2).to_broadcast([P, 4, 256]), ALU.mult).then_inc(s_pr, 1)
                e.wait_ge(s_o, i + 1)
                e.tensor_copy(o[:, :, P * i:P * i + P], K.ps[:, 6 + i % 2, :].rearrange("p (h n) -> p h n", h=4)).then_inc(s_oc, 1)

        @block.scalar
        def _(e):
            for i in range(NTI):
                e.wait_ge(s_mx, i + 1)
                if i >= 2:
                    e.wait_ge(s_t, i - 1)
                for h in range(4):
                    e.activation(Pr[:, i % 2, h, :], sbank(i)[:, h, :], ACT.Exp, bias=nm[:, i % 2, h:h + 1], scale=SC, accum_out=sm[:, i % 2, h:h + 1])
                e.drain().then_inc(s_ex, 1)
                e.wait_ge(s_t, i + 1)
                if i >= 1:
                    e.wait_ge(s_o, i)
                e.activation(PT[:, :, :].rearrange("p (a h) n -> p a (h n)", a=2), K.ps[:, 4:6, :], ACT.Copy).then_inc(s_tc, 1)


def stage_mem_sample(nc, K, q, o):
    SC = P ** -0.5
    ctx = ExitStack()
    with ctx:
        sb = lambda nm, sh: ctx.enter_context(nc.sbuf_tensor("ms_" + nm, sh, F32))
        kb, vb = sb("k", [P, 2, 2, 512]), sb("v", [P, DB, 2, 512])
        KT = sb("KT", [P, 2, 1024])
        Q = sb("Q", [P, 4, DB, 32])
        Pr, PT = sb("probs", [P, 256]), sb("probsT", [P, 2, P])
        nm, sm = sb("negmax", [P, 1]), sb("sums", [P, 1])
        o1 = sb("o1", [P, P])
        block = ctx.enter_context(nc.Block())
        s_k, s_v = K.sems("ms_keys_in", 2), K.sem("ms_values_in")
        s_q, s_t, s_tc, s_s, s_mx, s_ex, s_pr, s_pt, s_ptc, s_o, s_oc, s_ot, s_oe = (K.sem("ms_" + x) for x in (
            "queries", "keys_turned", "keys_copied", "scores", "max", "exps", "probs", "probs_turned", "probs_copied",
            "values", "combined", "out_turned", "out_copied"))

        @block.sync
        def _(e):
            for b in range(DB):
                if b >= 2:
                    e.wait_ge(s_t, b - 1)
                e.dma_start(kb[:, b % 2, :, :], K.d["cache_mem_k"][0, b].rearrange("(i p) h d -> p i (h d)", p=P)).then_inc(s_k[b % 2], 16)
                if b == 1:
                    for z in range(DB):
                        e.dma_start(vb[:, z, :, :], K.d["cache_mem_v"][0, z].rearrange("(i p) h d -> p i (h d)", p=P)).then_inc(s_v, 16)

        @block.tensor
        def _(e):
            ident = K.c("ident")
            e.wait_ge(s_q, 1)
            for b in range(DB):
                qd, bb = b // 4, b % 4
                e.wait_ge(s_k[b % 2], 16 * (b // 2 + 1))
                if b >= 1:
                    e.wait_ge(s_tc, b)
                for h in range(4):
                    for j in range(2):
                        mm = e.transpose(K.ps[:, h // 2, 256 * (h % 2) + P * j:256 * (h % 2) + P * j + P], kb[:, b % 2, j, P * h:P * h + P], ident)
                mm.then_inc(s_t, 1)
                e.wait_ge(s_tc, b + 1)
                if b == 4:
                    e.wait_ge(s_ex, 1)
                for h in range(4):
                    mm = e.matmul(K.ps[32 * bb:32 * bb + 32, 2, 0:256], Q[:, h, b, :], KT[:, b % 2, 256 * h:256 * h + 256], start=h == 0, stop=h == 3)
                mm.then_inc(s_s, 1)
                if bb == 3:
                    e.wait_ge(s_pr, qd + 1)
                    for j in range(2):
                        mm = e.transpose(K.ps[:, 3, P * j:P * j + P], Pr[:, P * j:P * j + P], ident)
                    mm.then_inc(s_pt, 1)
                    e.wait_ge(s_ptc, qd + 1)
                    e.wait_ge(s_v, 16 * DB)
                    if qd:
                        e.wait_ge(s_oc, 1)
                    for z in range(4):
                        for j in range(2):
                            mm = e.matmul(K.ps[32 * z:32 * z + 32, 4, :], PT[:, j, 32 * z:32 * z + 32], vb[:, 4 * qd + z, j, :], start=j == 0, stop=j == 1)
                    mm.then_inc(s_o, 1)
                    e.wait_ge(s_oc, qd + 1)
                    e.transpose(K.ps[:, 5, 0:P], o1[:, :], ident).then_inc(s_ot, 1)

        @block.scalar
        def _(e):
            for b in range(DB):
                qd = b // 4
                e.wait_ge(s_t, b + 1)
                if b >= 2:
                    e.wait_ge(s_s, b - 1)
                e.activation(KT[:, b % 2, :].rearrange("p (a n) -> p a n", a=2), K.ps[:, 0:2, :], ACT.Copy).then_inc(s_tc, 1)
                if b % 4 == 3:
                    e.wait_ge(s_mx, qd + 1)
                    e.activation(Pr[:, :], K.ps[:, 2, 0:256], ACT.Exp, bias=nm[:, :], scale=SC, accum_out=sm[:, :])
                    e.drain().then_inc(s_ex, 1)
                    e.wait_ge(s_pt, qd + 1)
                    e.activation(PT[:, :, :].rearrange("p j n -> p (j n)"), K.ps[:, 3, 0:256], ACT.Copy).then_inc(s_ptc, 1)

        @block.vector
        def _(e):
            e.memset(Q[:, :, :, :], 0.0)
            e.drain()
            for h in range(4):
                e.tensor_copy(Q[:, h, :, 4 * h:4 * h + 4], q[:, h, TP:T].rearrange("p (b t) -> p b t", t=DT))
            e.drain().then_inc(s_q, 1)
            for qd in range(2):
                e.wait_ge(s_s, 4 * qd + 4)
                e.tensor_reduce(nm[:, :], K.ps[:, 2, 0:256], AX.X, ALU.max, negate=True)
                e.drain()
                e.tensor_scalar(nm[:, :], nm[:, :], SC, None, ALU.mult).then_inc(s_mx, 1)
                e.wait_ge(s_ex, qd + 1)
                e.reciprocal(sm[:, :], sm[:, :])
                e.drain()
                e.tensor_scalar(Pr[:, :], Pr[:, :], sm[:, 0:1], None, ALU.mult).then_inc(s_pr, 1)
                e.wait_ge(s_o, qd + 1)
                e.tensor_scalar(o1[:, :], K.ps[:, 4, 0:P], K.c("mhead")[:, 0:1], None, ALU.mult)
                for h in range(1, 4):
                    e.drain()
                    mm = e.scalar_tensor_tensor(o1[:, :], K.ps[:, 4, P * h:P * h + P], K.c("mhead")[:, h:h + 1], o1[:, :], ALU.mult, ALU.add)
                mm.then_inc(s_oc, 1)
                e.wait_ge(s_ot, qd + 1)
                t = K.ps[:, 5, 0:P].rearrange("p (b h t) -> p b h t", b=4, h=8)
                for h in range(4):
                    e.tensor_copy(o[:, h, TP + 16 * qd:TP + 16 * qd + 16].rearrange("p (b t) -> p b t", t=DT), t[:, :, h, :])
                e.drain()


def stage_store(nc, K, x):
    ctx = ExitStack()
    with ctx:
        rows = ctx.enter_context(nc.sbuf_tensor("so_rows", [P, 3, D], F32))
        block = ctx.enter_context(nc.Block())
        s_t, s_a, s_v = K.sem("so_turned"), K.sem("so_copied_act"), K.sem("so_copied_dve")
        s_out = [K.out_sem(f"so_stored{z}") for z in range(3)]

        @block.tensor
        def _(e):
            for i in range(NTI + 1):
                n = P if i < NTI else TS
                if i >= 2:
                    e.wait_ge(s_a, i - 1)
                    e.wait_ge(s_v, i - 1)
                for k in range(KD):
                    mm = e.transpose(K.ps[0:n, 2 * (i % 2) + k // 4, P * (k % 4):P * (k % 4) + P], x[:, k, P * i:P * i + n], K.c("ident"))
                mm.then_inc(s_t, 1)

        @block.scalar
        def _(e):
            for i in range(NTI + 1):
                n = P if i < NTI else TS
                e.wait_ge(s_t, i + 1)
                if i >= 3:
                    e.wait_ge(s_out[i % 3], 16 * (i // 3))
                e.activation(rows[0:n, i % 3, 0:512], K.ps[0:n, 2 * (i % 2), :], ACT.Copy).then_inc(s_a, 1)

        @block.vector
        def _(e):
            for i in range(NTI + 1):
                n = P if i < NTI else TS
                e.wait_ge(s_t, i + 1)
                if i >= 3:
                    e.wait_ge(s_out[i % 3], 16 * (i // 3))
                e.tensor_copy(rows[0:n, i % 3, 512:1024], K.ps[0:n, 2 * (i % 2) + 1, :]).then_inc(s_v, 1)

        @block.sync
        def _(e):
            for i in range(NTI + 1):
                e.wait_ge(s_a, i + 1)
                e.wait_ge(s_v, i + 1)
                if i < NTI:
                    e.dma_start(K.d["y_prompt"][0, P * i:P * i + P, :], rows[:, i % 3, :]).then_inc(s_out[i % 3], 16)
                else:
                    e.dma_start(K.d["y_sample"].rearrange("b t d -> (b t) d"), rows[0:TS, i % 3, :]).then_inc(s_out[i % 3], 16)
            for z in range(3):
                e.wait_ge(s_out[z], 48)


def stage_zero(nc, tile):
    with nc.Block() as block:
        @block.vector
        def _(e):
            e.memset(tile[:, :, :], 0.0)


def build(nc, aps):
    with ExitStack() as ctx:
        K = Shared()
        K.d = aps
        K.turn = {}
        K.n_prow = sum(2 if n in ("nsa_q_g", "kg_cmp") else 15 if n == "shift_mu" else 1 for n, _ in PARAMS)
        K.live = []

        def sem(name):
            K.live.append(nc.alloc_semaphore(name))
            return K.live[-1]

        def reuse_semaphores():
            nc.clear_and_free_semaphores(K.live)
            nc.all_engine_barrier()
            K.live = []

        K.sem = sem
        stores = {n: nc.alloc_semaphore(n) for n in ("tail_stored", "kv_stored", "stPo_stored", "stSo_stored", "stSi_stored",
                                                      "mk_stored", "so_stored0", "so_stored1", "so_stored2")}
        K.out_sem = lambda name: stores[name]
        K.sems = lambda name, n: [K.sem(f"{name}{i}") for i in range(n)]
        K.c = lambda name: K.cst[:, CCOL[name][0]:CCOL[name][0] + CCOL[name][1]]
        K.p = lambda name, k: K.par[:, PCOL[name] + k:PCOL[name] + k + 1]
        sb = lambda name, shape: ctx.enter_context(nc.sbuf_tensor(name, shape, F32))
        K.ps = ctx.enter_context(nc.psum_tensor("ps", [P, 8, 512], F32))
        K.cst = sb("cst", [P, RESIDENT])
        K.par = sb("par", [P, NPAR + 4])
        K.utail = sb("utail", [P, B_Q, TAIL])
        K.shT = sb("shT", [P, NSHIFT, DB])
        slab = nc.sbuf_base
        sb("slab", [P, 16, T])

        def on_slab(name, at, blocks, dtype=F32):
            return nc.alloc_sbuf_tensor_at(name, [P, blocks, T], dtype, offset=slab + at * T * 4)

        K.oA, K.oB, K.oC = (on_slab(n, 4 * z, 4) for z, n in enumerate(("oA", "oB", "oC")))
        K.x_dram = nc.dram_tensor("x_channel_major", (P, KD * T), F32).ap()
        K.xh_dram = nc.dram_tensor("xn_high", (P, KD * T), F32R).ap()
        K.xl_dram = nc.dram_tensor("xn_low", (P, KD * T), F32R).ap()
        K.bvec = nc.dram_tensor("bias_vectors", (8, BVL), F32).ap()
        K.gscr = nc.dram_tensor("sample_rows", (TS, KVG), F32).ap()
        flat = lambda t: t[:, :, :].rearrange("p k n -> p (k n)")
        with nc.sbuf_tensor("keep", [P, T], F32) as K.keep, nc.sbuf_tensor("xs", [P, NSHIFT, T], F32) as xs:
            xh, xl = on_slab("xn_h", 0, KD, F32R), on_slab("xn_l", KD, KD, F32R)
            with nc.sbuf_tensor("xT", [P, KD, T], F32) as K.xT:
                stage_load(nc, K)
                stage_rms(nc, K, "mix", K.xT, xh, xl, "norm_mix_g", T, ((K.x_dram, flat(K.xT)),))
            stage_proj_a(nc, K, xs, 0, NSHIFT, xh, xl, ((K.xh_dram, flat(xh)), (K.xl_dram, flat(xl))))
            ld = on_slab("ld", 12, 4)
            stage_rwkv_prep(nc, K, xs, ld)
            with nc.sbuf_tensor("stP", [P, 4, 64], F32) as stP:
                stage_zero(nc, stP)
                stage_rwkv_scan(nc, K, xs, ld, "P", 128, (4, 2), NTI, 0, stP, 63)
                stage_rwkv_states(nc, K, "P", stP, None, K.d["p_state_rwkv"][0])
            with nc.sbuf_tensor("stS", [P, 4, DB, 64], F32) as stS:
                stage_rwkv_states(nc, K, "S", stS, K.d["state_rwkv"][0], None)
                stage_rwkv_scan(nc, K, xs, ld, "S", TS, (1, 0), 1, TP, stS, None)
                stage_rwkv_states(nc, K, "S", stS, None, K.d["s_state_rwkv"][0])
            stage_rwkv_out(nc, K, xs)
        reuse_semaphores()
        with ExitStack() as c1:
            s1 = lambda name, shape: c1.enter_context(nc.sbuf_tensor(name, shape, F32))
            kvt = s1("kvt", [P, NTI + 1, KVG])
            b31, ksn, kwn = s1("b31", [P, 8]), s1("ksn", [P, TS]), s1("kwn", [P, TS])
            up, qT = on_slab("up", 8, 4), on_slab("qT", 12, 4)
            with nc.sbuf_tensor("xn_h2", [P, KD, T], F32R) as xh, nc.sbuf_tensor("xn_l2", [P, KD, T], F32R) as xl:
                stage_move(nc, K, "xn_back", ((flat(xh), K.xh_dram), (flat(xl), K.xl_dram)))
                stage_proj_a(nc, K, up, B_POOL, 4, xh, xl)
                stage_kv(nc, K, kvt, xh, xl)
                stage_proj_a(nc, K, qT, B_Q, 4, xh, xl)
            stage_pool(nc, K, up)
            stage_head_rms(nc, K, "nsaq", qT, "H", 64, "nsa_q_g", 0.125)
            stage_kv_norm(nc, K, kvt)
            with ExitStack() as c2:
                sc = lambda name, shape: c2.enter_context(nc.sbuf_tensor(name, shape, F32))
                near, cb = sc("near", [P, 8, 2 * P]), sc("cb", [P, 8, 30])
                kcd, vc = sc("kcd", [P, 2, 16]), sc("vc", [16, P])
                kh, kl = (c2.enter_context(nc.sbuf_tensor(n, [P, 2, 2, TP], F32R)) for n in ("keys_high", "keys_low"))
                tail = c2.enter_context(nc.sbuf_tensor("tail_rows", [TAIL, B_Q, P], F32))
                stage_bias(nc, K, near, cb, b31)
                stage_tail_rows(nc, K, tail)
                stage_nsa_keys(nc, K, kvt, kcd, vc, kh, kl, ksn, kwn)
                stage_nsa_prompt(nc, K, qT, kvt, kcd, vc, kh, kl, near, cb, b31)
            reuse_semaphores()
            with ExitStack() as c2:
                sc = lambda name, shape: c2.enter_context(nc.sbuf_tensor(name, shape, F32))
                Ssc = sc("s_scores", [P, 2, SROW])
                coef, grow = sc("s_coef", [P, 2, 3]), sc("s_gates", [P, 2, 3])
                idx = c2.enter_context(nc.sbuf_tensor("s_page_rows", [P, DB], mybir.dt.uint32))
                vnew, vcb = sc("s_vnew", [DT, DB, 2, P]), sc("s_vcb", [SCM, DB, P])
                with nc.sbuf_tensor("s_qbd", [P, DB, 32], F32) as Qbd, nc.sbuf_tensor("s_bias", [P, SROW], F32) as bias:
                    stage_page_index(nc, K, idx)
                    stage_sample_rows(nc, K, kvt, qT, Qbd, bias, grow, vnew)
                    KT = nc.alloc_sbuf_tensor_at("s_keys_turned", [P, SS + SWN], F32, offset=slab + 12 * T * 4)
                    stage_sample_scores(nc, K, Qbd, bias, Ssc, vcb, ksn, kwn, idx, KT)
                stage_sample_softmax(nc, K, Ssc, coef, grow)
                stage_sample_values(nc, K, Ssc, coef, vcb, vnew, idx)
        reuse_semaphores()
        block_of = lambda w: lambda m: w[:, P * m:P * m + P]
        place = nc.sbuf_base
        x = sb("x", [P, KD, T])
        h = nc.alloc_sbuf_tensor_at("h", [P, KD, T], F32, offset=place)
        with nc.sbuf_tensor("xn_h3", [P, KD, T], F32R) as xh, nc.sbuf_tensor("xn_l3", [P, KD, T], F32R) as xl:
            stage_move(nc, K, "xn_again", ((flat(xh), K.xh_dram), (flat(xl), K.xl_dram)))
            stage_merge(nc, K, h, xh, xl, on_slab("merge_spare", 12, 4))
        with nc.sbuf_tensor("h_h", [P, KD, T], F32R) as hh, nc.sbuf_tensor("h_l", [P, KD, T], F32R) as hl:
            stage_split(nc, K, "h", h, hh, hl, KD)
            stage_move(nc, K, "x_back", ((flat(x), K.x_dram),))
            stage_product(nc, K, "wo", block_of(K.d["w_out"][0]), KD, KD, hh, hl, x, True)
        mkT, mv = sb("mkT", [P, 4, 256]), sb("mv", [P, 2, 512])
        mT, mh, ml = (nc.alloc_sbuf_tensor_at(n, [P, KD, 256], d, offset=slab + z * KD * 256 * 4)
                      for z, (n, d) in enumerate((("mT", F32), ("mT_h", F32R), ("mT_l", F32R))))
        stage_mem_load(nc, K, mT)
        stage_rms(nc, K, "mem", mT, mh, ml, "norm_mem_g", 256)
        stage_mem_kv(nc, K, mh, ml, mkT, mv)
        xh = on_slab("xm_h", 0, KD, F32R)
        with nc.sbuf_tensor("xm_l", [P, KD, T], F32R) as xl:
            stage_rms(nc, K, "memx", x, xh, xl, "norm_memx_g", T)
            stage_product(nc, K, "mq", block_of(K.d["w_mq"][0]), KD, 4, xh, xl, K.oC, False)
        stage_head_rms(nc, K, "memq", K.oC, "M", P, "mem_q_g", 1.0)
        stage_mem_prompt(nc, K, K.oC, mkT, mv, K.oA)
        stage_mem_sample(nc, K, K.oC, K.oA)
        oh, ol = on_slab("om_h", 4, 4, F32R), on_slab("om_l", 8, 4, F32R)
        stage_split(nc, K, "om", K.oA, oh, ol, 4)
        stage_product(nc, K, "mo", block_of(K.d["w_mo"][0]), 4, KD, oh, ol, x, True)
        reuse_semaphores()
        xh, xl = on_slab("xf_h", 0, KD, F32R), on_slab("xf_l", KD, KD, F32R)
        stage_rms(nc, K, "ffn", x, xh, xl, "norm_ffn_g", T)
        stage_ffn(nc, K, xh, xl, x)
        stage_store(nc, K, x)


_INS = ["x_prompt", "x_sample", "state_rwkv", "state_shift", "state_pool", "cache_cmp_k", "cache_cmp_v", "cache_slc_k",
        "cache_slc_v", "cache_win_k", "cache_win_v", "cache_mem_k", "cache_mem_v", "page_table", "mem_prompt", "rel_bias",
        "norm_mix_g", "w_in", "shift_mu", "rwkv_w0", "rwkv_w2", "rwkv_a0", "rwkv_a2", "rwkv_g2", "rwkv_kk", "rwkv_ka",
        "rwkv_rk", "rwkv_lnx_g", "rwkv_lnx_b", "pool_w", "pool_scale", "nsa_q_g", "nsa_k_g", "w_br_a", "w_br_b", "w_br_c",
        "w_out", "norm_memx_g", "norm_mem_g", "w_mq", "w_mk", "w_mv", "mem_q_g", "mem_k_g", "w_mo", "norm_ffn_g",
        "w_ff1", "w_ff2"]
_OUTS = [("y_prompt", (1, TP, D)), ("y_sample", (DB, DT, D)),
         ("p_state_rwkv", (1, 1, 8, 64, 64)), ("p_state_shift", (1, 1, A_COLS)), ("p_state_pool", (1, 1, 15, 512)),
         ("p_cmp_k", (1, 1, TP, 2, 64)), ("p_cmp_v", (1, 1, TP, 2, 64)), ("p_slc_k", (1, 1, TP, 2, 64)),
         ("p_slc_v", (1, 1, TP, 2, 64)), ("p_win_k", (1, 1, 512, 2, 64)), ("p_win_v", (1, 1, 512, 2, 64)),
         ("p_mem_k", (1, 1, 256, 4, 128)), ("p_mem_v", (1, 1, 256, 4, 128)),
         ("s_state_rwkv", (1, DB, 8, 64, 64)), ("s_state_shift", (1, DB, A_COLS)), ("s_state_pool", (1, DB, 15, 512)),
         ("s_cmp_k", (1, DB, DT, 2, 64)), ("s_cmp_v", (1, DB, DT, 2, 64)), ("s_slc_k", (1, DB, DT, 2, 64)),
         ("s_slc_v", (1, DB, DT, 2, 64)), ("s_win_k", (1, DB, 512, 2, 64)), ("s_win_v", (1, DB, 512, 2, 64))]
_CONSTS = {"sheet": SHEET, "keep": KEEP, "onehot": ONEHOT}


def kernel(**inputs):
    import numpy as _np
    import concourse.bacc as _bacc
    from concourse import mybir as _mybir
    from concourse.bass_utils import run_bass_kernel_spmd as _run

    nc = _bacc.Bacc("TRN2", target_bir_lowering=False, num_devices=1)
    arrays, aps = {}, {}
    for name in _INS:
        a = _np.ascontiguousarray(inputs[name])
        arrays[f"in_{name}"] = a
        aps[name] = nc.dram_tensor(f"in_{name}", a.shape, _mybir.dt.from_np(a.dtype), kind="ExternalInput").ap()
    for name, a in _CONSTS.items():
        arrays[f"const_{name}"] = a
        aps[name] = nc.dram_tensor(f"const_{name}", a.shape, F32, kind="ExternalInput").ap()
    for name, shape in _OUTS:
        aps[name] = nc.dram_tensor(f"out_{name}", shape, F32, kind="ExternalOutput").ap()
    build(nc, aps)
    r = _run(nc, [arrays], core_ids=[0])
    return tuple(r.results[0][f"out_{name}"] for name, _ in _OUTS)
```
